# Optimizing a Trainium2 kernel written in Bass

```python
import jax, jax.numpy as jnp
from jax import lax
import numpy as np
import math
import jax
import jax.numpy as jnp

D_MODEL = 1024
BATCH = 1
SEQ = 512
DEPTH = 1

SSM_INNER = D_MODEL
SSM_HEAD_DIM = 64
SSM_HEADS = SSM_INNER // SSM_HEAD_DIM
SSM_GROUPS = 2
SSM_STATE = 128
SSM_CONV = 5
SSM_CHUNK = 128
SSM_CONV_DIM = SSM_INNER + 2 * SSM_GROUPS * SSM_STATE
RWKV_DIM = D_MODEL // 2
RWKV_HEAD_DIM = 64
RWKV_HEADS = RWKV_DIM // RWKV_HEAD_DIM
RWKV_W_RANK = 64
RWKV_A_RANK = 64
RWKV_G_RANK = 128
RWKV_COLS = 3 * RWKV_DIM + RWKV_W_RANK + RWKV_A_RANK + RWKV_G_RANK
RWKV_DECAY_SCALE = 0.6065306597
RWKV_LN_EPS = 64e-5
HGRN_DIM = D_MODEL // 2
HGRN_HEAD_DIM = 128
HGRN_HEADS = HGRN_DIM // HGRN_HEAD_DIM
HGRN_CHUNK = 64
HGRN_COLS = 5 * HGRN_DIM
N_BRANCH = 3
GATE_COLS = N_BRANCH * D_MODEL
N_IN = SSM_INNER + SSM_CONV_DIM + 2 * SSM_HEADS + RWKV_COLS + HGRN_COLS + GATE_COLS
D_FF = (8 * D_MODEL + 3 * 256 - 1) // (3 * 256) * 256
NORM_EPS = 1e-6


def _split_points(sizes):
    pts, acc = [], 0
    for s in sizes[:-1]:
        acc += s
        pts.append(acc)
    return pts

def rmsnorm(x, w, eps=NORM_EPS):
    xf = x.astype(jnp.float32)
    y = xf * lax.rsqrt(jnp.mean(xf * xf, axis=-1, keepdims=True) + eps)
    return (y * w.astype(jnp.float32)).astype(x.dtype)

def head_rmsnorm(x, w, n_heads, eps=NORM_EPS):
    b, l, d = x.shape
    xf = x.astype(jnp.float32).reshape(b, l, n_heads, d // n_heads)
    y = xf * lax.rsqrt(jnp.mean(xf * xf, axis=-1, keepdims=True) + eps)
    return (y.reshape(b, l, d) * w.astype(jnp.float32)).astype(x.dtype)

def flip_t(t):
    return jnp.flip(t, axis=1)

def centred_depthwise_conv(x, w, b):
    pad = (w.shape[0] - 1) // 2
    y = lax.conv_general_dilated(x, w, window_strides=(1,), padding=[(pad, pad)],
                                 dimension_numbers=('NWC', 'WIO', 'NWC'),
                                 feature_group_count=x.shape[-1])
    return y + b

def ssd_chunked(x, dt, a, bm, cm):
    b, L, H, P = x.shape
    G, N = bm.shape[2], bm.shape[3]
    hg = H // G
    c = L // SSM_CHUNK
    Q = SSM_CHUNK
    x = x.reshape(b, c, Q, G, hg, P)
    dt = dt.reshape(b, c, Q, G, hg)
    bm = bm.reshape(b, c, Q, G, N)
    cm = cm.reshape(b, c, Q, G, N)
    a_cum = jnp.cumsum(dt * a.reshape(G, hg), axis=2)
    xdt = x * dt[..., None]
    seg = a_cum[:, :, :, None] - a_cum[:, :, None]
    mask = jnp.tril(jnp.ones((Q, Q), dtype=bool))[:, :, None, None]
    lmat = jnp.exp(jnp.where(mask, seg, -jnp.inf))
    cb = jnp.einsum('bcqgn,bcsgn->bcqsg', cm, bm)
    y_diag = jnp.einsum('bcqsgh,bcsghp->bcqghp', cb[..., None] * lmat, xdt)
    decay_to_end = jnp.exp(a_cum[:, :, -1:] - a_cum)
    chunk_states = jnp.einsum('bcsgn,bcsghp->bcghpn', bm, xdt * decay_to_end[..., None])
    chunk_decay = jnp.exp(a_cum[:, :, -1])

    def step(s, inp):
        st, dec = inp
        return dec[..., None, None] * s + st, s

    s0 = jnp.zeros((b, G, hg, P, N), dtype=x.dtype)
    _, prev = lax.scan(step, s0, (jnp.moveaxis(chunk_states, 1, 0), jnp.moveaxis(chunk_decay, 1, 0)))
    prev = jnp.moveaxis(prev, 0, 1)
    y_off = jnp.einsum('bcqgn,bcghpn->bcqghp', cm, prev) * jnp.exp(a_cum)[..., None]
    return (y_diag + y_off).reshape(b, L, H, P)

def ssd_branch(z, xbc, dt_raw, conv_w, conv_b, dt_bias, a_log, d_skip, norm_w):
    b, L, _ = z.shape
    xbc = jax.nn.silu(centred_depthwise_conv(xbc, conv_w, conv_b))
    xs, bm, cm = jnp.split(xbc, [SSM_INNER, SSM_INNER + SSM_GROUPS * SSM_STATE], axis=-1)
    xs = xs.reshape(b, L, SSM_HEADS, SSM_HEAD_DIM)
    bm = bm.reshape(b, L, SSM_GROUPS, SSM_STATE)
    cm = cm.reshape(b, L, SSM_GROUPS, SSM_STATE)
    dt = jax.nn.softplus(dt_raw.reshape(b, L, 2, SSM_HEADS) + dt_bias)
    a = -jnp.exp(a_log)
    y_f = ssd_chunked(xs, dt[:, :, 0], a[0], bm, cm)
    y_b = flip_t(ssd_chunked(flip_t(xs), flip_t(dt[:, :, 1]), a[1], flip_t(bm), flip_t(cm)))
    y = y_f + y_b + xs * d_skip[:, None]
    y = y.reshape(b, L, SSM_INNER) * jax.nn.silu(z)
    return rmsnorm(y, norm_w)

def token_shift_bidir(p, mu):
    prev = jnp.pad(p[:, :-1], ((0, 0), (1, 0), (0, 0)))
    nxt = jnp.pad(p[:, 1:], ((0, 0), (0, 1), (0, 0)))
    return p + mu[0] * (prev - p) + mu[1] * (nxt - p)

def rwkv7_scan(r, w, k, v, kk, a, reverse):
    b = r.shape[0]
    s0 = jnp.zeros((b, RWKV_HEADS, RWKV_HEAD_DIM, RWKV_HEAD_DIM), dtype=r.dtype)

    def step(s, inp):
        r_t, w_t, k_t, v_t, kk_t, a_t = inp
        sa = jnp.einsum('bhvk,bhk->bhv', s, -kk_t)
        s = (s * w_t[:, :, None, :] + sa[..., None] * (kk_t * a_t)[:, :, None, :]
             + v_t[..., None] * k_t[:, :, None, :])
        return s, jnp.einsum('bhvk,bhk->bhv', s, r_t)

    xs = (jnp.moveaxis(r, 1, 0), jnp.moveaxis(w, 1, 0), jnp.moveaxis(k, 1, 0),
          jnp.moveaxis(v, 1, 0), jnp.moveaxis(kk, 1, 0), jnp.moveaxis(a, 1, 0))
    _, y = lax.scan(step, s0, xs, reverse=reverse)
    return jnp.moveaxis(y, 0, 1)

def rwkv7_branch(p, mu, w0, w_up, a0, a_up, g_up, k_k, k_a, r_k, ln_w, ln_b):
    b, L, _ = p.shape
    p = token_shift_bidir(p, mu)
    r, k, v, wd, ad, gd = jnp.split(p, _split_points(
        [RWKV_DIM, RWKV_DIM, RWKV_DIM, RWKV_W_RANK, RWKV_A_RANK, RWKV_G_RANK]), axis=-1)

    def heads(t):
        return t.reshape(b, L, RWKV_HEADS, RWKV_HEAD_DIM)

    tw = jnp.tanh(wd)
    w_f = jnp.exp(-RWKV_DECAY_SCALE * jax.nn.sigmoid(w0[0] + tw @ w_up[0]))
    w_b = jnp.exp(-RWKV_DECAY_SCALE * jax.nn.sigmoid(w0[1] + tw @ w_up[1]))
    a = jax.nn.sigmoid(a0 + ad @ a_up)
    g = jax.nn.sigmoid(gd) @ g_up
    kk = heads(k * k_k).astype(jnp.float32)
    kk = (kk * lax.rsqrt(jnp.sum(kk * kk, axis=-1, keepdims=True) + 1e-12)).astype(p.dtype)
    k = k * (1.0 + (a - 1.0) * k_a)
    r, k, v, a = heads(r), heads(k), heads(v), heads(a)
    y = (rwkv7_scan(r, heads(w_f), k, v, kk, a, False)
         + rwkv7_scan(r, heads(w_b), k, v, kk, a, True))
    yf = y.astype(jnp.float32)
    mean = jnp.mean(yf, axis=-1, keepdims=True)
    var = jnp.mean(jnp.square(yf - mean), axis=-1, keepdims=True)
    yn = ((yf - mean) * lax.rsqrt(var + RWKV_LN_EPS)).reshape(b, L, RWKV_DIM)
    yn = (yn * ln_w.astype(jnp.float32) + ln_b.astype(jnp.float32)).astype(p.dtype)
    r_k_h = r_k.reshape(RWKV_HEADS, RWKV_HEAD_DIM)
    bonus = jnp.sum(r * k * r_k_h, axis=-1, keepdims=True) * v
    return (yn + bonus.reshape(b, L, RWKV_DIM)) * g

def hgrn2_chunk_scan(q, k, v, log_f):
    b, L, h, dk = q.shape
    dv = v.shape[-1]
    c = L // HGRN_CHUNK

    def chunks(t):
        return jnp.transpose(t.reshape(b, c, HGRN_CHUNK, h, t.shape[-1]), (1, 0, 3, 2, 4))

    mask = jnp.tril(jnp.ones((HGRN_CHUNK, HGRN_CHUNK), dtype=bool))[:, :, None]

    def step(s, inp):
        q_c, k_c, v_c, g_c = inp
        cum = jnp.cumsum(g_c, axis=2)
        o_inter = jnp.einsum('bhtk,bhkv->bhtv', q_c * jnp.exp(cum), s)
        diff = cum[:, :, :, None, :] - cum[:, :, None, :, :]
        decay = jnp.exp(jnp.where(mask, diff, -jnp.inf))
        scores = jnp.einsum('bhtsk,bhsk->bhts', q_c[:, :, :, None, :] * decay, k_c)
        o_intra = jnp.einsum('bhts,bhsv->bhtv', scores, v_c)
        last = cum[:, :, -1:, :]
        s = (jnp.exp(last[:, :, 0, :])[..., None] * s
             + jnp.einsum('bhsk,bhsv->bhkv', k_c * jnp.exp(last - cum), v_c))
        return s, o_inter + o_intra

    s0 = jnp.zeros((b, h, dk, dv), dtype=q.dtype)
    _, o = lax.scan(step, s0, (chunks(q), chunks(k), chunks(v), chunks(log_f)))
    return jnp.transpose(o, (1, 0, 3, 2, 4)).reshape(b, L, h, dv)

def hgrn2_branch(p, lb, norm_w):
    b, L, _ = p.shape
    q, f_fwd, f_bwd, i, g = jnp.split(p, 5, axis=-1)

    def heads(t):
        return t.reshape(b, L, HGRN_HEADS, HGRN_HEAD_DIM)

    def forget(f):
        ff = lb + (1.0 - lb) * jax.nn.sigmoid(f)
        return heads(jnp.log(ff)), heads(1.0 - ff)

    logf_f, k_f = forget(f_fwd)
    logf_b, k_b = forget(f_bwd)
    qh, ih = heads(q), heads(i)
    o_f = hgrn2_chunk_scan(qh, k_f, ih, logf_f)
    o_b = flip_t(hgrn2_chunk_scan(flip_t(qh), flip_t(k_b), flip_t(ih), flip_t(logf_b)))
    o = (o_f + o_b).reshape(b, L, HGRN_DIM)
    return head_rmsnorm(o, norm_w, HGRN_HEADS) * jax.nn.silu(g)

def first_inputs(seed: int = 0) -> dict:
    key = jax.random.key(seed)
    ks = iter(jax.random.split(key, 48))
    f32 = jnp.float32

    def nrm(shape, fan_in, scale=1.0):
        return scale * fan_in ** -0.5 * jax.random.normal(next(ks), shape, f32)

    def unif(shape, lo, hi):
        return jax.random.uniform(next(ks), shape, f32, lo, hi)

    def gain(shape):
        return 1.0 + 0.05 * jax.random.normal(next(ks), shape, f32)

    x = jax.random.normal(next(ks), (BATCH, SEQ, D_MODEL), f32)
    norm1_w = gain((DEPTH, D_MODEL))
    w_in = nrm((DEPTH, D_MODEL, N_IN), D_MODEL)
    ssm_conv_w = nrm((DEPTH, SSM_CONV, 1, SSM_CONV_DIM), SSM_CONV)
    ssm_conv_b = 0.02 * jax.random.normal(next(ks), (DEPTH, SSM_CONV_DIM), f32)
    dt0 = jnp.exp(unif((DEPTH, 2, SSM_HEADS), float(np.log(1e-3)), float(np.log(1e-1))))
    ssm_dt_bias = dt0 + jnp.log(-jnp.expm1(-dt0))
    ssm_a_log = jnp.log(unif((DEPTH, 2, SSM_HEADS), 1.0, 16.0))
    ssm_d = gain((DEPTH, SSM_HEADS))
    ssm_norm_w = gain((DEPTH, SSM_INNER))
    rwkv_mu = unif((DEPTH, 2, RWKV_COLS), 0.0, 0.5)
    rwkv_w0 = 0.5 * jax.random.normal(next(ks), (DEPTH, 2, RWKV_DIM), f32)
    rwkv_w_up = nrm((DEPTH, 2, RWKV_W_RANK, RWKV_DIM), RWKV_W_RANK, 0.5)
    rwkv_a0 = 0.1 * jax.random.normal(next(ks), (DEPTH, RWKV_DIM), f32)
    rwkv_a_up = nrm((DEPTH, RWKV_A_RANK, RWKV_DIM), RWKV_A_RANK, 0.1)
    rwkv_g_up = nrm((DEPTH, RWKV_G_RANK, RWKV_DIM), RWKV_G_RANK)
    rwkv_k_k = 0.85 + 0.05 * jax.random.normal(next(ks), (DEPTH, RWKV_DIM), f32)
    rwkv_k_a = gain((DEPTH, RWKV_DIM))
    rwkv_r_k = 0.1 * jax.random.normal(next(ks), (DEPTH, RWKV_DIM), f32)
    rwkv_ln_w = gain((DEPTH, RWKV_DIM))
    rwkv_ln_b = 0.02 * jax.random.normal(next(ks), (DEPTH, RWKV_DIM), f32)
    hgrn_lb_logits = 0.1 * jax.random.normal(next(ks), (DEPTH, HGRN_DIM), f32)
    hgrn_norm_w = gain((DEPTH, HGRN_DIM))
    w_branch_ssm = nrm((DEPTH, SSM_INNER, D_MODEL), SSM_INNER)
    w_branch_rwkv = nrm((DEPTH, RWKV_DIM, D_MODEL), RWKV_DIM)
    w_branch_hgrn = nrm((DEPTH, HGRN_DIM, D_MODEL), HGRN_DIM)
    w_out = nrm((DEPTH, D_MODEL, D_MODEL), D_MODEL)
    norm2_w = gain((DEPTH, D_MODEL))
    ffn_w_in = nrm((DEPTH, D_MODEL, 2 * D_FF), D_MODEL)
    ffn_w_down = nrm((DEPTH, D_FF, D_MODEL), D_FF)
    final_norm_w = gain((D_MODEL,))
    return {"x": x, "norm1_w": norm1_w, "w_in": w_in,
            "ssm_conv_w": ssm_conv_w, "ssm_conv_b": ssm_conv_b, "ssm_dt_bias": ssm_dt_bias,
            "ssm_a_log": ssm_a_log, "ssm_d": ssm_d, "ssm_norm_w": ssm_norm_w,
            "rwkv_mu": rwkv_mu, "rwkv_w0": rwkv_w0, "rwkv_w_up": rwkv_w_up, "rwkv_a0": rwkv_a0,
            "rwkv_a_up": rwkv_a_up, "rwkv_g_up": rwkv_g_up, "rwkv_k_k": rwkv_k_k,
            "rwkv_k_a": rwkv_k_a, "rwkv_r_k": rwkv_r_k, "rwkv_ln_w": rwkv_ln_w,
            "rwkv_ln_b": rwkv_ln_b, "hgrn_lb_logits": hgrn_lb_logits, "hgrn_norm_w": hgrn_norm_w,
            "w_branch_ssm": w_branch_ssm, "w_branch_rwkv": w_branch_rwkv,
            "w_branch_hgrn": w_branch_hgrn, "w_out": w_out, "norm2_w": norm2_w,
            "ffn_w_in": ffn_w_in, "ffn_w_down": ffn_w_down, "final_norm_w": final_norm_w}

def first_block(x, norm1_w, w_in, ssm_conv_w, ssm_conv_b, ssm_dt_bias, ssm_a_log, ssm_d,
              ssm_norm_w, rwkv_mu, rwkv_w0, rwkv_w_up, rwkv_a0, rwkv_a_up, rwkv_g_up,
              rwkv_k_k, rwkv_k_a, rwkv_r_k, rwkv_ln_w, rwkv_ln_b, hgrn_lb_logits, hgrn_norm_w,
              w_branch_ssm, w_branch_rwkv, w_branch_hgrn, w_out, norm2_w, ffn_w_in,
              ffn_w_down, final_norm_w):
    b, L, _ = x.shape
    lb_p = jax.nn.softmax(hgrn_lb_logits.astype(jnp.float32), axis=0)
    lower_bounds = (jnp.cumsum(lb_p, axis=0) - lb_p[0]).astype(x.dtype)
    in_splits = _split_points([SSM_INNER, SSM_CONV_DIM, 2 * SSM_HEADS, RWKV_COLS, HGRN_COLS,
                               GATE_COLS])
    for l in range(DEPTH):
        xn = rmsnorm(x, norm1_w[l])
        p = xn @ w_in[l]
        z, xbc, dt_raw, p_rwkv, p_hgrn, p_gate = jnp.split(p, in_splits, axis=-1)
        y_ssm = ssd_branch(z, xbc, dt_raw, ssm_conv_w[l], ssm_conv_b[l], ssm_dt_bias[l],
                           ssm_a_log[l], ssm_d[l], ssm_norm_w[l]) @ w_branch_ssm[l]
        y_rwkv = rwkv7_branch(p_rwkv, rwkv_mu[l], rwkv_w0[l], rwkv_w_up[l], rwkv_a0[l],
                              rwkv_a_up[l], rwkv_g_up[l], rwkv_k_k[l], rwkv_k_a[l],
                              rwkv_r_k[l], rwkv_ln_w[l], rwkv_ln_b[l]) @ w_branch_rwkv[l]
        y_hgrn = hgrn2_branch(p_hgrn, lower_bounds[l], hgrn_norm_w[l]) @ w_branch_hgrn[l]
        gates = jax.nn.sigmoid(p_gate).reshape(b, L, N_BRANCH, D_MODEL)
        mixed = gates[:, :, 0] * y_ssm + gates[:, :, 1] * y_rwkv + gates[:, :, 2] * y_hgrn
        x = x + mixed @ w_out[l]
        h_gate, h_up = jnp.split(rmsnorm(x, norm2_w[l]) @ ffn_w_in[l], 2, axis=-1)
        x = x + (jax.nn.silu(h_gate) * h_up) @ ffn_w_down[l]
    return rmsnorm(x, final_norm_w)


DEPTH_2 = 2

GRID_W = 64
BLOCK_Q = 128
EPS = 1e-6
N_BRANCH_2 = 4

A_HEADS = 4
A_DH = 128
A_WIDTH = A_HEADS * A_DH
A_CHUNK = 128
A_CONV = 3
B_HEADS = 8
B_KV = 2
B_DH = 64
B_WIDTH = B_HEADS * B_DH
ROPE_THETA = 10000.0
C_HEADS = 8
C_DH = 64
C_WIDTH = C_HEADS * C_DH
C_WIN_R = 8
C_WIN_C = 16
D_HEADS = 4
D_DH = 64
D_DV = 2 * D_DH
D_WIDTH = D_HEADS * D_DV
D_FF_2 = ((8 * D_MODEL + 3 * 256 - 1) // (3 * 256)) * 256

SPLIT_SIZES = (
    A_WIDTH, A_WIDTH, A_WIDTH, A_WIDTH, 4 * A_HEADS,
    B_WIDTH, B_KV * B_DH, B_KV * B_DH,
    C_WIDTH, C_WIDTH, C_WIDTH,
    2 * D_HEADS * D_DH, 2 * D_HEADS * D_DH, D_WIDTH,
    N_BRANCH_2 * D_MODEL,
)
D_IN = sum(SPLIT_SIZES)


F32 = jnp.float32

def rms_norm(x, g):
    xf = x.astype(F32)
    y = xf * lax.rsqrt(jnp.mean(xf * xf, axis=-1, keepdims=True) + EPS)
    return (y * g.astype(F32)).astype(x.dtype)

def centred_dwconv(x, w):
    k = w.shape[0]
    p = k // 2
    s = x.shape[1]
    xp = jnp.pad(x, ((0, 0), (p, p), (0, 0)))
    return sum(xp[:, j:j + s, :] * w[j] for j in range(k))

def sweep_query_blocks(fn, q):
    bsz, s = q.shape[:2]
    nb = s // BLOCK_Q
    qb = jnp.moveaxis(q.reshape((bsz, nb, BLOCK_Q) + q.shape[2:]), 1, 0)
    out = lax.map(lambda a: fn(a[0], a[1]), (jnp.arange(nb), qb))
    return jnp.moveaxis(out, 0, 1).reshape((bsz, s) + out.shape[3:])

def mlstm_scan(q, k, v, li, lf):
    bsz, nh, s, d = q.shape
    nc = s // A_CHUNK

    def chunks(t):
        t = t.reshape(t.shape[:2] + (nc, A_CHUNK) + t.shape[3:])
        return jnp.moveaxis(t, 2, 0)

    qc, kc, vc, lic = chunks(q), chunks(k), chunks(v), chunks(li)
    bc = jnp.cumsum(chunks(lf), axis=-1)
    lower = jnp.tril(jnp.ones((A_CHUNK, A_CHUNK), dtype=bool))

    def step(carry, xs):
        c_mat, n_vec, m = carry
        qt, kt, vt, it, bt = xs
        dmat = jnp.where(lower, bt[..., :, None] - bt[..., None, :] + it[..., None, :], -jnp.inf)
        inter = bt + m[..., None]
        mt = jnp.maximum(inter, dmat.max(-1))
        w_inter = jnp.exp(inter - mt)
        sqk = jnp.einsum('bhtd,bhsd->bhts', qt, kt) * jnp.exp(dmat - mt[..., None])
        num = (w_inter[..., None] * jnp.einsum('bhtk,bhkv->bhtv', qt, c_mat)
               + jnp.einsum('bhts,bhsv->bhtv', sqk, vt))
        den = w_inter * jnp.einsum('bhtk,bhk->bht', qt, n_vec) + sqk.sum(-1)
        ht = num / jnp.maximum(jnp.abs(den), jnp.exp(-mt))[..., None]
        bl = bt[..., -1]
        g = bl[..., None] - bt + it
        m_new = jnp.maximum(bl + m, g.max(-1))
        wc = jnp.exp(bl + m - m_new)
        ws = jnp.exp(g - m_new[..., None])
        c_new = wc[..., None, None] * c_mat + jnp.einsum('bhs,bhsk,bhsv->bhkv', ws, kt, vt)
        n_new = wc[..., None] * n_vec + jnp.einsum('bhs,bhsk->bhk', ws, kt)
        return (c_new, n_new, m_new), ht

    init = (jnp.zeros((bsz, nh, d, d), F32), jnp.zeros((bsz, nh, d), F32), jnp.zeros((bsz, nh), F32))
    _, h = lax.scan(step, init, (qc, kc, vc, lic, bc))
    return jnp.moveaxis(h, 0, 2).reshape(bsz, nh, s, d)

def mlstm_branch(q, k, v, o, gates, conv_w, gate_bias, norm_g):
    bsz, s, _ = q.shape
    dt = q.dtype
    qk = jax.nn.silu(centred_dwconv(jnp.concatenate([q, k], axis=-1), conv_w))
    q, k = jnp.split(qk, 2, axis=-1)

    def heads(t):
        return t.reshape(bsz, s, A_HEADS, A_DH).transpose(0, 2, 1, 3).astype(F32)

    qh, kh, vh = heads(q), heads(k) * (A_DH ** -0.5), heads(v)
    g = (gates.astype(F32) + gate_bias.astype(F32)).reshape(bsz, s, 4, A_HEADS).transpose(2, 0, 3, 1)
    i_fwd, f_fwd, i_bwd, f_bwd = g[0], g[1], g[2], g[3]
    h_fwd = mlstm_scan(qh, kh, vh, i_fwd, jax.nn.log_sigmoid(f_fwd))
    flip = lambda t: jnp.flip(t, axis=2)
    h_bwd = flip(mlstm_scan(flip(qh), flip(kh), flip(vh), flip(i_bwd), flip(jax.nn.log_sigmoid(f_bwd))))
    h = h_fwd + h_bwd
    mu = jnp.mean(h, axis=-1, keepdims=True)
    var = jnp.mean(jnp.square(h - mu), axis=-1, keepdims=True)
    h = (h - mu) * lax.rsqrt(var + EPS)
    h = h.transpose(0, 2, 1, 3).reshape(bsz, s, A_WIDTH) * norm_g.astype(F32)
    return (h * jax.nn.sigmoid(o.astype(F32))).astype(dt)

def axial_rope_angles(s):
    t = jnp.arange(s)
    row = (t // GRID_W).astype(F32)
    col = (t % GRID_W).astype(F32)
    n_freq = B_DH // 4
    inv = ROPE_THETA ** (-jnp.arange(n_freq, dtype=F32) / n_freq)
    return row[:, None] * inv, col[:, None] * inv

def rotate_half_rope(x, ang):
    x1, x2 = jnp.split(x, 2, axis=-1)
    c = jnp.cos(ang)[None, :, None, :]
    sn = jnp.sin(ang)[None, :, None, :]
    return jnp.concatenate([x1 * c - x2 * sn, x2 * c + x1 * sn], axis=-1)

def axial_rope(x, ang_r, ang_c):
    xr, xc = jnp.split(x, 2, axis=-1)
    return jnp.concatenate([rotate_half_rope(xr, ang_r), rotate_half_rope(xc, ang_c)], axis=-1)

def gqa_branch(q, k, v, qn_g, kn_g):
    bsz, s, _ = q.shape
    dt = q.dtype
    q = rms_norm(q.reshape(bsz, s, B_HEADS, B_DH), qn_g).astype(F32)
    k = rms_norm(k.reshape(bsz, s, B_KV, B_DH), kn_g).astype(F32)
    v = v.reshape(bsz, s, B_KV, B_DH).astype(F32)
    ang_r, ang_c = axial_rope_angles(s)
    q = axial_rope(q, ang_r, ang_c).reshape(bsz, s, B_KV, B_HEADS // B_KV, B_DH) * (B_DH ** -0.5)
    k = axial_rope(k, ang_r, ang_c)

    def block(_, qb):
        sc = jnp.einsum('bqgrd,bkgd->bgrqk', qb, k)
        p = jax.nn.softmax(sc, axis=-1)
        return jnp.einsum('bgrqk,bkgd->bqgrd', p, v)

    o = sweep_query_blocks(block, q)
    return o.reshape(bsz, s, B_WIDTH).astype(dt)

def natten_indices(s):
    rows = s // GRID_W
    wr = min(C_WIN_R, rows)
    t = jnp.arange(s)
    r = t // GRID_W
    c = t % GRID_W
    rs = jnp.clip(r - wr // 2, 0, rows - wr)
    cs = jnp.clip(c - C_WIN_C // 2, 0, GRID_W - C_WIN_C)
    kr = rs[:, None, None] + jnp.arange(wr)[None, :, None]
    kc = cs[:, None, None] + jnp.arange(C_WIN_C)[None, None, :]
    shape = (s, wr, C_WIN_C)
    idx = jnp.broadcast_to(kr * GRID_W + kc, shape).reshape(s, wr * C_WIN_C)
    off_r = jnp.broadcast_to(kr - r[:, None, None] + (C_WIN_R - 1), shape).reshape(s, wr * C_WIN_C)
    off_c = jnp.broadcast_to(kc - c[:, None, None] + (C_WIN_C - 1), shape).reshape(s, wr * C_WIN_C)
    return idx, off_r, off_c

def natten_branch(q, k, v, rpb):
    bsz, s, _ = q.shape
    dt = q.dtype
    rows = s // GRID_W
    idx, off_r, off_c = natten_indices(s)
    nk = idx.shape[-1]
    bias = rpb.astype(F32)[:, off_r, off_c]
    q = q.reshape(bsz, rows, GRID_W, C_HEADS, C_DH).astype(F32) * (C_DH ** -0.5)
    k = k.reshape(bsz, s, C_HEADS, C_DH).astype(F32)
    v = v.reshape(bsz, s, C_HEADS, C_DH).astype(F32)
    idx_rows = idx.reshape(rows, GRID_W, nk)
    bias_rows = jnp.moveaxis(bias.reshape(C_HEADS, rows, GRID_W, nk), 1, 0)

    def row_block(args):
        qr, ir, br = args
        kg = jnp.take(k, ir, axis=1)
        vg = jnp.take(v, ir, axis=1)
        sc = jnp.einsum('bqhd,bqnhd->bhqn', qr, kg) + br[None]
        p = jax.nn.softmax(sc, axis=-1)
        return jnp.einsum('bhqn,bqnhd->bqhd', p, vg)

    o = lax.map(row_block, (jnp.moveaxis(q, 1, 0), idx_rows, bias_rows))
    return jnp.moveaxis(o, 0, 1).reshape(bsz, s, C_WIDTH).astype(dt)

def diff_branch(q, k, v, lq1, lk1, lq2, lk2, subln_g, lambda_init):
    bsz, s, _ = q.shape
    dt = q.dtype
    q = q.reshape(bsz, s, 2, D_HEADS, D_DH).astype(F32) * (D_DH ** -0.5)
    k = k.reshape(bsz, s, 2, D_HEADS, D_DH).astype(F32)
    v = v.reshape(bsz, s, D_HEADS, D_DV).astype(F32)
    lam = (jnp.exp(jnp.sum(lq1.astype(F32) * lk1.astype(F32)))
           - jnp.exp(jnp.sum(lq2.astype(F32) * lk2.astype(F32))) + lambda_init)
    slopes = 2.0 ** (-8.0 * jnp.arange(1, D_HEADS + 1, dtype=F32) / D_HEADS)
    kpos = jnp.arange(s, dtype=F32)

    def block(i, qb):
        qpos = (i * BLOCK_Q + jnp.arange(BLOCK_Q)).astype(F32)
        alibi = -slopes[:, None, None] * jnp.abs(qpos[:, None] - kpos[None, :])
        sc = jnp.einsum('bqchd,bkchd->bchqk', qb, k) + alibi[None, None]
        p = jax.nn.softmax(sc, axis=-1)
        a = p[:, 0] - lam * p[:, 1]
        return jnp.einsum('bhqk,bkhv->bqhv', a, v)

    o = sweep_query_blocks(block, q)
    o = rms_norm(o, subln_g) * (1.0 - lambda_init)
    return o.reshape(bsz, s, D_WIDTH).astype(dt)

def hybrid_layer(x, layer_idx, norm1_g, w_in, a_conv_w, a_gate_bias, a_norm_g, b_qnorm_g, b_knorm_g,
                 c_rpb, d_lq1, d_lk1, d_lq2, d_lk2, d_subln_g, w_up_a, w_up_b, w_up_c, w_up_d,
                 w_out, norm2_g, w_ffn_gate, w_ffn_up, w_ffn_down):
    bsz, s, _ = x.shape
    dt = x.dtype
    h = rms_norm(x, norm1_g)
    proj = jnp.einsum('bsd,de->bse', h, w_in)
    points = [sum(SPLIT_SIZES[:i + 1]) for i in range(len(SPLIT_SIZES) - 1)]
    (aq, ak, av, ao, ag, bq, bk, bv, cq, ck, cv, dq, dk, dv, gl) = jnp.split(proj, points, axis=-1)
    y_a = mlstm_branch(aq, ak, av, ao, ag, a_conv_w, a_gate_bias, a_norm_g)
    y_b = gqa_branch(bq, bk, bv, b_qnorm_g, b_knorm_g)
    y_c = natten_branch(cq, ck, cv, c_rpb)
    lambda_init = 0.8 - 0.6 * math.exp(-0.3 * layer_idx)
    y_d = diff_branch(dq, dk, dv, d_lq1, d_lk1, d_lq2, d_lk2, d_subln_g, lambda_init)
    g = jax.nn.sigmoid(gl.astype(F32)).reshape(bsz, s, N_BRANCH_2, D_MODEL)
    merged = (g[:, :, 0] * (y_a @ w_up_a) + g[:, :, 1] * (y_b @ w_up_b)
              + g[:, :, 2] * (y_c @ w_up_c) + g[:, :, 3] * (y_d @ w_up_d))
    x = x + merged.astype(dt) @ w_out
    h2 = rms_norm(x, norm2_g)
    ffn = (jax.nn.silu(h2 @ w_ffn_gate) * (h2 @ w_ffn_up)) @ w_ffn_down
    return x + ffn

def second_inputs(seed: int = 0) -> dict:
    key = jax.random.key(seed)
    ks = jax.random.split(key, 26)
    L = DEPTH_2
    nrm = lambda k, shape, scale: jax.random.normal(k, shape, F32) * scale
    gain = lambda k, shape: 1.0 + 0.02 * jax.random.normal(k, shape, F32)
    fb = jnp.linspace(3.0, 6.0, A_HEADS, dtype=F32)
    zh = jnp.zeros((A_HEADS,), F32)
    gate_offset = jnp.concatenate([zh, fb, zh, fb])
    return {
        "x": jax.random.normal(ks[0], (BATCH, SEQ, D_MODEL), F32),
        "norm1_g": gain(ks[1], (L, D_MODEL)),
        "w_in": nrm(ks[2], (L, D_MODEL, D_IN), D_MODEL ** -0.5),
        "a_conv_w": nrm(ks[3], (L, A_CONV, 2 * A_WIDTH), A_CONV ** -0.5),
        "a_gate_bias": gate_offset[None] + nrm(ks[4], (L, 4 * A_HEADS), 0.1),
        "a_norm_g": gain(ks[5], (L, A_WIDTH)),
        "b_qnorm_g": gain(ks[6], (L, B_DH)),
        "b_knorm_g": gain(ks[7], (L, B_DH)),
        "c_rpb": nrm(ks[8], (L, C_HEADS, 2 * C_WIN_R - 1, 2 * C_WIN_C - 1), 0.02),
        "d_lambda_q1": nrm(ks[9], (L, D_DH), 0.1),
        "d_lambda_k1": nrm(ks[10], (L, D_DH), 0.1),
        "d_lambda_q2": nrm(ks[11], (L, D_DH), 0.1),
        "d_lambda_k2": nrm(ks[12], (L, D_DH), 0.1),
        "d_subln_g": gain(ks[13], (L, D_DV)),
        "w_up_a": nrm(ks[14], (L, A_WIDTH, D_MODEL), A_WIDTH ** -0.5),
        "w_up_b": nrm(ks[15], (L, B_WIDTH, D_MODEL), B_WIDTH ** -0.5),
        "w_up_c": nrm(ks[16], (L, C_WIDTH, D_MODEL), C_WIDTH ** -0.5),
        "w_up_d": nrm(ks[17], (L, D_WIDTH, D_MODEL), D_WIDTH ** -0.5),
        "w_out": nrm(ks[18], (L, D_MODEL, D_MODEL), D_MODEL ** -0.5),
        "norm2_g": gain(ks[19], (L, D_MODEL)),
        "w_ffn_gate": nrm(ks[20], (L, D_MODEL, D_FF_2), D_MODEL ** -0.5),
        "w_ffn_up": nrm(ks[21], (L, D_MODEL, D_FF_2), D_MODEL ** -0.5),
        "w_ffn_down": nrm(ks[22], (L, D_FF_2, D_MODEL), D_FF_2 ** -0.5),
        "final_g": gain(ks[23], (D_MODEL,)),
    }

def second_block(x, norm1_g, w_in, a_conv_w, a_gate_bias, a_norm_g, b_qnorm_g, b_knorm_g, c_rpb,
              d_lambda_q1, d_lambda_k1, d_lambda_q2, d_lambda_k2, d_subln_g,
              w_up_a, w_up_b, w_up_c, w_up_d, w_out, norm2_g, w_ffn_gate, w_ffn_up, w_ffn_down, final_g):
    for l in range(DEPTH_2):
        x = hybrid_layer(x, l, norm1_g[l], w_in[l], a_conv_w[l], a_gate_bias[l], a_norm_g[l],
                         b_qnorm_g[l], b_knorm_g[l], c_rpb[l],
                         d_lambda_q1[l], d_lambda_k1[l], d_lambda_q2[l], d_lambda_k2[l], d_subln_g[l],
                         w_up_a[l], w_up_b[l], w_up_c[l], w_up_d[l], w_out[l],
                         norm2_g[l], w_ffn_gate[l], w_ffn_up[l], w_ffn_down[l])
    return rms_norm(x, final_g)


def setup_inputs(seed=0):
    out = dict(first_inputs(seed))
    for name, value in second_inputs(seed + 1).items():
        if name != "x":
            out[name + "_2"] = value
    return out


def reference(
    x, norm1_w, w_in, ssm_conv_w, ssm_conv_b, ssm_dt_bias, ssm_a_log, ssm_d, ssm_norm_w,
    rwkv_mu, rwkv_w0, rwkv_w_up, rwkv_a0, rwkv_a_up, rwkv_g_up, rwkv_k_k, rwkv_k_a, rwkv_r_k,
    rwkv_ln_w, rwkv_ln_b, hgrn_lb_logits, hgrn_norm_w, w_branch_ssm, w_branch_rwkv,
    w_branch_hgrn, w_out, norm2_w, ffn_w_in, ffn_w_down, final_norm_w, norm1_g_2, w_in_2,
    a_conv_w_2, a_gate_bias_2, a_norm_g_2, b_qnorm_g_2, b_knorm_g_2, c_rpb_2, d_lambda_q1_2,
    d_lambda_k1_2, d_lambda_q2_2, d_lambda_k2_2, d_subln_g_2, w_up_a_2, w_up_b_2, w_up_c_2,
    w_up_d_2, w_out_2, norm2_g_2, w_ffn_gate_2, w_ffn_up_2, w_ffn_down_2, final_g_2,
):
    x = first_block(
        x, norm1_w, w_in, ssm_conv_w, ssm_conv_b, ssm_dt_bias, ssm_a_log, ssm_d, ssm_norm_w,
        rwkv_mu, rwkv_w0, rwkv_w_up, rwkv_a0, rwkv_a_up, rwkv_g_up, rwkv_k_k, rwkv_k_a,
        rwkv_r_k, rwkv_ln_w, rwkv_ln_b, hgrn_lb_logits, hgrn_norm_w, w_branch_ssm,
        w_branch_rwkv, w_branch_hgrn, w_out, norm2_w, ffn_w_in, ffn_w_down, final_norm_w,
    )
    return second_block(
        x, norm1_g_2, w_in_2, a_conv_w_2, a_gate_bias_2, a_norm_g_2, b_qnorm_g_2, b_knorm_g_2,
        c_rpb_2, d_lambda_q1_2, d_lambda_k1_2, d_lambda_q2_2, d_lambda_k2_2, d_subln_g_2,
        w_up_a_2, w_up_b_2, w_up_c_2, w_up_d_2, w_out_2, norm2_g_2, w_ffn_gate_2, w_ffn_up_2,
        w_ffn_down_2, final_g_2,
    )


_drawn_inputs = setup_inputs


def setup_inputs(seed=0):
    import zlib

    import numpy as np

    out = dict(_drawn_inputs(seed))
    spreads = {}
    factors = {'ssm_d': 3.551,
     'rwkv_w_up': 2.707,
     'rwkv_a0': 2.855,
     'rwkv_a_up': 4.016,
     'rwkv_k_k': 8.0,
     'rwkv_ln_w': 3.586,
     'rwkv_ln_b': 3.554,
     'hgrn_norm_w': 2.932,
     'a_norm_g_2': 6.912,
     'b_qnorm_g_2': 8.0,
     'b_knorm_g_2': 8.0,
     'c_rpb_2': 55.042,
     'd_lambda_k1_2': 3.564,
     'd_subln_g_2': 4.379,
     'norm2_g_2': 3.052,
     'final_g_2': 8.149}
    for name, (base, spread) in spreads.items():
        noise = np.random.default_rng([zlib.crc32(name.encode()), seed]).standard_normal(out[name].shape)
        drawn = base * np.exp(spread * noise) if base else spread * noise
        out[name] = jnp.asarray(drawn.astype(out[name].dtype))
    for name, factor in factors.items():
        out[name] = (out[name] * factor).astype(out[name].dtype)
    return out
```

```python
from contextlib import ExitStack

import concourse.bass as bass
import numpy as np
from concourse import mybir

F32 = mybir.dt.float32
ALU = mybir.AluOpType
ACT = mybir.ActivationFunctionType
AX = mybir.AxisListType

P = 128
T = 512
NT = T // P
D = 1024
KD = D // P
GW = 256

SSM_HEADS, SSM_P, SSM_CONV = 16, 64, 5
SSM_INNER, SSM_XBC = 1024, 1536
RWKV_W = 512
RWKV_COLS = 3 * RWKV_W + 256
RWKV_DECAY = 0.6065306597
HGRN_W = 512
D_FF = 2816
KF = D_FF // P
NORM_EPS = 1e-6
RWKV_LN_EPS = 64e-5
CH = 32
NC = T // CH
LAYERS = 2
GRID_W, WIN_R, WIN_C = 64, 8, 16
A_HEADS, A_CONV, A_WIDTH = 4, 3, 512
B_HEADS, C_HEADS, D_HEADS = 8, 8, 4
LAMBDA_INIT = [0.8 - 0.6 * float(np.exp(-0.3 * n)) for n in range(LAYERS)]


def constants():
    p = np.arange(P)
    s, t = p[:, None], p[None, :]
    block = (s // CH) == (t // CH)
    tok = np.arange(T)
    c = {
        "ident": np.eye(P),
        "ones": np.ones((P, P)),
        "pair": (s // 64) == (t // 64),
        "eye64": s % 64 == t[:, :64],
        "le": s <= t,
        "ge": s >= t,
        "c_le": block & (s <= t),
        "c_lt": block & (s < t),
        "c_ge": block & (s >= t),
        "c_gt": block & (s > t),
        "reset": np.broadcast_to(np.stack([tok % CH != 0, tok % CH != CH - 1]).reshape(1, -1), (P, 2 * T)),
        "eps": np.broadcast_to(np.array([[NORM_EPS, RWKV_LN_EPS, 1e-12, 64 * NORM_EPS]
                                        + [NORM_EPS / (1 - LAMBDA_INIT[n]) ** 2 for n in range(LAYERS)]]),
                               (P, 4 + LAYERS)),
    }
    d = p % 64
    inv = (10000.0 ** (-np.arange(16, dtype=np.float32) / 16)).astype(np.float32)
    pos = np.where((d < 32)[:, None], tok[None] // GRID_W, tok[None] % GRID_W).astype(np.float32)
    ang = (pos * inv[d % 16][:, None]).astype(np.float32)
    c["cos"], c["sin"] = np.cos(ang), np.sin(ang)
    turn = np.zeros((P, P))
    first = (p % 32) < 16
    turn[(p + 16)[first], p[first]] = -1.0
    turn[(p - 16)[~first], p[~first]] = 1.0
    c["turn"] = turn
    c["dup"] = np.concatenate([(s == t % 64), (s == 64 + t % 64)], 1)
    c["distance"] = np.abs(s - (np.arange(896)[None] - 384))
    band = np.zeros((P, 191))
    for a in range(2):
        for o in range(31):
            band[32 * a + o, 64 * a + 78 - o] = 1.0
    c["band"] = band
    col = p % 64
    start = np.clip(col - WIN_C // 2, 0, GRID_W - WIN_C)
    kc = np.arange(64)[None]
    c["window"] = np.where((kc >= start[:, None]) & (kc < start[:, None] + WIN_C), 0.0, -1e30)
    return {n: np.ascontiguousarray(np.broadcast_to(v, (P, v.shape[1])), dtype=np.float32) for n, v in c.items()}


def places(widths):
    at, out = 0, {}
    for name, w in widths.items():
        out[name] = (at, at + w)
        at += w
    return out, at


def grouped(w, width=GW):
    k, n = w.shape
    return np.ascontiguousarray(
        w.reshape(k // P, P, n // width, width).transpose(2, 1, 0, 3)).reshape(n // width, P, -1)


def side_by_side(a, b):
    return np.concatenate([grouped(a), grouped(b)], axis=2)


def columns(v):
    v = np.asarray(v).reshape(-1, P)
    return v.T


def short(v):
    v = np.asarray(v).reshape(-1)
    out = np.zeros((P, 1), v.dtype)
    out[: len(v), 0] = v
    return out


def first_layout(x):
    w = x["w_in"][0]
    o_xbc = SSM_INNER
    o_dt = o_xbc + SSM_XBC
    o_rwkv = o_dt + 2 * SSM_HEADS
    o_hgrn = o_rwkv + RWKV_COLS
    o_gate = o_hgrn + 5 * HGRN_W
    gate = w[:, o_gate:]
    weights = {
        "w_z": grouped(w[:, :o_xbc]),
        "w_xbc": grouped(w[:, o_xbc:o_dt]),
        "w_dt": grouped(w[:, o_dt:o_rwkv], 2 * SSM_HEADS),
        "w_rwkv": grouped(w[:, o_rwkv:o_hgrn]),
        "w_hgrn": grouped(w[:, o_hgrn:o_gate]),
        "w_mix_ssm": side_by_side(gate[:, :D], x["w_branch_ssm"][0]),
        "w_mix_rwkv": side_by_side(gate[:, D:2 * D], x["w_branch_rwkv"][0]),
        "w_mix_hgrn": side_by_side(gate[:, 2 * D:], x["w_branch_hgrn"][0]),
        "w_out": grouped(x["w_out"][0]),
        "w_ffn": side_by_side(x["ffn_w_in"][0][:, :D_FF], x["ffn_w_in"][0][:, D_FF:]),
        "w_down": grouped(x["ffn_w_down"][0], P),
        "w_lora": np.concatenate([
            np.concatenate([x["rwkv_w_up"][0, 0], x["rwkv_w_up"][0, 1]], 1),
            np.concatenate([x["rwkv_a_up"][0], np.zeros_like(x["rwkv_a_up"][0])], 1)], 0),
        "w_g_up": x["rwkv_g_up"][0],
    }
    heads = lambda v: np.repeat(np.asarray(v).reshape(-1), 64)
    cols = {
        "norm1": columns(x["norm1_w"][0]),
        "conv_w": np.concatenate([columns(x["ssm_conv_w"][0, j, 0]) for j in range(SSM_CONV)], 1),
        "conv_b": columns(x["ssm_conv_b"][0]),
        "dt_bias": np.concatenate([short(x["ssm_dt_bias"][0, r]) for r in range(2)], 1),
        "a_log": np.concatenate([short(x["ssm_a_log"][0, r]) for r in range(2)], 1),
        "d_skip": columns(heads(x["ssm_d"][0])),
        "ssm_norm": columns(x["ssm_norm_w"][0]),
        "mu": np.concatenate([columns(x["rwkv_mu"][0, r]) for r in range(2)], 1),
        "w0": np.concatenate([columns(x["rwkv_w0"][0, r]) for r in range(2)], 1),
        "a0": columns(x["rwkv_a0"][0]),
        "k_k": columns(x["rwkv_k_k"][0]),
        "k_a": columns(x["rwkv_k_a"][0]),
        "r_k": columns(x["rwkv_r_k"][0]),
        "ln_w": columns(x["rwkv_ln_w"][0]),
        "ln_b": columns(x["rwkv_ln_b"][0]),
        "lb": columns(x["hgrn_lb_logits"][0]),
        "hgrn_norm": columns(x["hgrn_norm_w"][0]),
        "norm2": columns(x["norm2_w"][0]),
        "norm3": columns(x["final_norm_w"]),
    }
    return weights, cols


def second_layout(x):
    weights, cols = {}, {}
    widths = {"aq": 512, "ak": 512, "av": 512, "ao": 512, "ag": 16, "bq": 512, "bk": 128, "bv": 128,
              "cq": 512, "ck": 512, "cv": 512, "dq": 512, "dk": 512, "dv": 512, "gate": 4 * D}
    at, _ = places(widths)
    for n in range(LAYERS):
        w = x["w_in_2"][n]
        part = lambda *names: np.concatenate([w[:, at[m][0]:at[m][1]] for m in names], 1)
        weights |= {
            f"w_a_qk{n}": grouped(part("aq", "ak")),
            f"w_a_o{n}": grouped(part("ao")),
            f"w_a_gates{n}": grouped(part("ag"), 16),
            f"w_a_v{n}": grouped(part("av"), 512),
            f"w_b_q{n}": grouped(part("bq")),
            f"w_b_k{n}": grouped(part("bk"), P),
            f"w_b_v{n}": grouped(part("bv"), P),
            f"w_c_qk{n}": grouped(part("cq", "ck")),
            f"w_c_v{n}": grouped(part("cv"), 512),
            f"w_d_qk{n}": grouped(part("dq", "dk")),
            f"w_d_v{n}": grouped(part("dv"), 512),
            f"w_out{n}": grouped(x["w_out_2"][n]),
            f"w_ffn{n}": side_by_side(x["w_ffn_gate_2"][n], x["w_ffn_up_2"][n]),
            f"w_down{n}": grouped(x["w_ffn_down_2"][n], P),
        }
        for b, name in enumerate("abcd"):
            g = part("gate")[:, b * D:(b + 1) * D]
            weights[f"w_mix_{name}{n}"] = side_by_side(g, x[f"w_up_{name}_2"][n])
        rpb = np.zeros((P, C_HEADS, 16), np.float32)
        for a in range(2):
            rpb[32 * a:32 * a + 31, :, a:a + 15] = np.asarray(x["c_rpb_2"][n]).transpose(2, 0, 1)
        weights[f"rpb{n}"] = rpb.reshape(P, -1)
        twice = lambda v: np.concatenate([short(v)[:64], short(v)[:64]], 0)
        cols |= {
            f"norm1_{n}": columns(x["norm1_g_2"][n]),
            f"a_conv{n}": np.concatenate([columns(x["a_conv_w_2"][n, j]) for j in range(A_CONV)], 1),
            f"a_bias{n}": short(x["a_gate_bias_2"][n]),
            f"a_norm{n}": columns(x["a_norm_g_2"][n]),
            f"b_qnorm{n}": twice(x["b_qnorm_g_2"][n]),
            f"b_knorm{n}": twice(x["b_knorm_g_2"][n]),
            f"lambda{n}": np.concatenate([short(x[f"d_lambda_{m}_2"][n]) for m in ("q1", "q2", "k1", "k2")], 1),
            f"d_subln{n}": np.repeat(columns(x["d_subln_g_2"][n]), D_HEADS, 1),
            f"norm2_{n}": columns(x["norm2_g_2"][n]),
        }
    cols["final"] = columns(x["final_g_2"])
    return weights, cols


class Kernel:

    def __init__(self, nc, dram, const_at, col_at):
        self.nc, self.dram, self.const_at, self.col_at = nc, dram, const_at, col_at
        self.made = 0
        self.free = sorted(nc.free_semaphores)

    def sbuf(self, ctx, name, shape):
        self.made += 1
        return ctx.enter_context(self.nc.sbuf_tensor(f"{name}_{self.made}", shape, F32))

    def const(self, name, rows=P):
        a, b = self.const_at[name]
        return self.consts[0:rows, a:b]

    def col(self, name, j=0, rows=P):
        a, _ = self.col_at[name]
        return self.cols[0:rows, a + j:a + j + 1]


def semaphores(k, ctx, names):
    sems = [k.nc.alloc_semaphore(f"{n}_{k.nc.next_id()}", num=k.free.pop(0)) for n in names.split()]

    def give_back():
        for s in sems:
            k.nc.gpsimd.sem_clear(s)
            k.nc.release_semaphore(s)
            k.free.append(s.num)

    ctx.callback(give_back)
    return sems


def bank(ps, b):
    return ps[:, b, :]


def wide(ap, n):
    rows, m = ap.shape
    return ap[:, None, :].broadcast_to([rows, n, m])


def load_constants(k, col_array):
    nc = k.nc
    with ExitStack() as ctx:
        consts_in, cols_in = semaphores(k, ctx, "consts_in cols_in")
        block = ctx.enter_context(nc.Block())

        @block.sync
        def _(sp):
            sp.dma_start(k.consts[:, :], k.dram["consts"]).then_inc(consts_in, 16)
            sp.wait_ge(consts_in, 16)

        @block.scalar
        def _(act):
            act.dma_start(k.cols[:, 0:col_array.shape[1]], col_array).then_inc(cols_in, 16)
            act.wait_ge(cols_in, 16)


def load_x(k):
    nc = k.nc
    with ExitStack() as ctx:
        rows = k.sbuf(ctx, "x_rows", [P, NT, D])
        x_in, turned, x_ready = semaphores(k, ctx, "x_in turned x_ready")
        block = ctx.enter_context(nc.Block())

        @block.sync
        def _(sp):
            sp.dma_start(rows[:, :, :], k.dram["x"].rearrange("(j p) d -> p j d", p=P)).then_inc(x_in, 16)

        @block.tensor
        def _(pe):
            pe.wait_ge(x_in, 16)
            for m in range(KD):
                if m >= 2:
                    pe.wait_ge(x_ready, m - 1)
                for j in range(NT):
                    mm = pe.transpose(k.ps[:, m % 2, j * P:(j + 1) * P], rows[:, j, m * P:(m + 1) * P],
                                      k.const("ident"))
                mm.then_inc(turned, 1)

        @block.scalar
        def _(act):
            for m in range(KD):
                act.wait_ge(turned, m + 1)
                act.activation(k.x[:, m, :], bank(k.ps, m % 2), ACT.Copy).then_inc(x_ready, 1)


def store_x(k, src):
    nc = k.nc
    with ExitStack() as ctx:
        rows = k.sbuf(ctx, "out_rows", [P, NT, D])
        turned, row_ready, stored = semaphores(k, ctx, "turned row_ready stored")
        block = ctx.enter_context(nc.Block())

        @block.tensor
        def _(pe):
            for n in range(2 * NT):
                j, half = n // 2, n % 2
                if n >= 2:
                    pe.wait_ge(row_ready, n - 1)
                for q in range(NT):
                    mm = pe.transpose(k.ps[:, n % 2, q * P:(q + 1) * P],
                                      src[:, NT * half + q, j * P:(j + 1) * P], k.const("ident"))
                mm.then_inc(turned, 1)

        @block.scalar
        def _(act):
            for n in range(2 * NT):
                act.wait_ge(turned, n + 1)
                act.activation(rows[:, n // 2, (n % 2) * T:(n % 2 + 1) * T], bank(k.ps, n % 2),
                               ACT.Copy).then_inc(row_ready, 1)

        @block.sync
        def _(sp):
            for j in range(NT):
                sp.wait_ge(row_ready, 2 * j + 2)
                sp.dma_start(k.dram["out"][j * P:(j + 1) * P, :], rows[:, j, :]).then_inc(stored, 16)
            sp.wait_ge(stored, 16 * NT)


def rms_norm(k, src, dst, weight, tiles=KD, name="n"):
    nc = k.nc
    with ExitStack() as ctx:
        sq = k.sbuf(ctx, "squares", [P, 3, T])
        rstd = k.sbuf(ctx, "rstd", [P, T])
        squared, summed, root, inverse, normed = semaphores(k, ctx, "squared summed root inverse normed")
        block = ctx.enter_context(nc.Block())

        @block.scalar
        def _(act):
            for m in range(tiles):
                if m >= 3:
                    act.wait_ge(summed, m - 2)
                act.activation(sq[:, m % 3, :], src[:, m, :], ACT.Square).then_inc(squared, 1)
            act.wait_ge(summed, tiles)
            act.activation(rstd[:, :], bank(k.ps, 0), ACT.Sqrt, bias=k.const("eps")[:, 0:1],
                           scale=1.0 / (tiles * P)).then_inc(root, 1)

        @block.tensor
        def _(pe):
            for m in range(tiles):
                pe.wait_ge(squared, m + 1)
                pe.matmul(bank(k.ps, 0), k.const("ones"), sq[:, m % 3, :], start=(m == 0),
                          stop=(m == tiles - 1)).then_inc(summed, 1)

        @block.vector
        def _(dve):
            dve.wait_ge(root, 1)
            dve.reciprocal(rstd[:, :], rstd[:, :]).then_inc(inverse, 1)
            dve.wait_ge(inverse, 1)
            for m in range(tiles):
                dve.scalar_tensor_tensor(out=dst[:, m, :], in0=src[:, m, :], scalar=k.col(weight, m),
                                         in1=rstd[:, :], op0=ALU.mult, op1=ALU.mult).then_inc(normed, 1)


def by_pairs(eng, groups, body):
    if groups >= 2:
        body(0, 2)
    if groups >= 4:
        with eng.Fori(1, groups // 2) as i:
            body(i, 2)
    if groups % 2:
        body(groups // 2, 1)


def project(k, jobs):
    nc = k.nc
    with ExitStack() as ctx:
        weights_in = semaphores(k, ctx, "weights_in_0 weights_in_1")
        tile_done, tile_used = semaphores(k, ctx, "tile_done tile_used")
        block = ctx.enter_context(nc.Block())
        plans = []
        g0 = 0
        for w, src, dst, scale in jobs:
            groups, kt = w.shape[0], src.shape[1]
            plans.append((w, src, dst, scale, groups, kt, w.shape[2] // kt // P, g0))
            g0 += groups
        tpg = plans[0][6]
        assert all(p[6] == tpg for p in plans)
        banks = 2 * tpg

        @block.sync
        def _(sp):
            for w, src, dst, scale, groups, kt, _, g0 in plans:
                def load(i, n):
                    for h in range(n):
                        row = i * 2 + h if isinstance(i, int) else sp.snap(i * 2 + h)
                        if not isinstance(i, int) or g0 + 2 * i + h >= 2:
                            sp.wait_ge(tile_done, i * (2 * tpg) + (g0 + h - 1) * tpg)
                        b = (g0 + h) % 2
                        srow = w[row, :, :] if isinstance(i, int) else w[bass.ds(row, 1), :, :].rearrange("a p n -> (a p) n")
                        sp.dma_start(k.wbuf[:, b, 0:w.shape[2]], srow).then_inc(weights_in[b], 16)
                by_pairs(sp, groups, load)

        @block.tensor
        def _(pe):
            for w, src, dst, scale, groups, kt, _, g0 in plans:
                def multiply(i, n):
                    for h in range(n):
                        b = (g0 + h) % 2
                        pe.wait_ge(weights_in[b], i * 16 + ((g0 + h) // 2 + 1) * 16)
                        for m in range(tpg):
                            local = h * tpg + m
                            t0 = g0 * tpg + local
                            if not isinstance(i, int) or t0 + 2 * tpg * i >= banks:
                                pe.wait_ge(tile_used, i * (2 * tpg) + t0 - banks + 1)
                            bk = t0 % banks
                            for q in range(kt):
                                c = (q * tpg + m) * P
                                mm = pe.matmul(bank(k.ps, bk), k.wbuf[:, b, c:c + P], src[:, q, :],
                                               start=(q == 0), stop=(q == kt - 1))
                            mm.then_inc(tile_done, 1)
                by_pairs(pe, groups, multiply)

        def evacuate(eng, adding):
            for w, src, dst, scale, groups, kt, _, g0 in plans:
                if (scale == "add") != adding:
                    continue
                def take(i, n):
                    for h in range(n):
                        for m in range(tpg):
                            local = h * tpg + m
                            t0 = g0 * tpg + local
                            eng.wait_ge(tile_done, i * (2 * tpg) + t0 + 1)
                            bk = t0 % banks
                            o = dst[:, bass.ds(i * (2 * tpg) + local, 1), :].rearrange("p a t -> p (a t)")
                            if adding:
                                ins = eng.tensor_tensor(o, o, bank(k.ps, bk), ALU.add)
                            else:
                                ins = eng.activation(o, bank(k.ps, bk), ACT.Copy, scale=scale)
                            ins.then_inc(tile_used, 1)
                by_pairs(eng, groups, take)

        if any(p[3] == "add" for p in plans):
            assert len(plans) == 1

            @block.vector
            def _(dve):
                evacuate(dve, True)
        else:
            @block.scalar
            def _(act):
                evacuate(act, False)


def gated_product(k, w, src_a, src_b, func, dst, accumulate):
    nc = k.nc
    ka, kb = src_a.shape[1], src_b.shape[1]
    groups = w.shape[0]
    with ExitStack() as ctx:
        gate = k.sbuf(ctx, "gate", [P, 2, T])
        weights_in = semaphores(k, ctx, "weights_in_0 weights_in_1")
        a_done, b_done, gate_ready, tile_used, product_ready = semaphores(
            k, ctx, "a_done b_done gate_ready tile_used product_ready")
        block = ctx.enter_context(nc.Block())

        @block.sync
        def _(sp):
            def load(i, n):
                for h in range(n):
                    row = i * 2 + h if isinstance(i, int) else sp.snap(i * 2 + h)
                    if not isinstance(i, int) or i > 0:
                        sp.wait_ge(b_done, i * 4 + 2 * h - 2)
                    srow = w[row, :, :] if isinstance(i, int) else w[bass.ds(row, 1), :, :].rearrange("a p n -> (a p) n")
                    sp.dma_start(k.wbuf[:, h, 0:w.shape[2]], srow).then_inc(weights_in[h], 16)
            by_pairs(sp, groups, load)

        @block.tensor
        def _(pe):
            def multiply(i, n):
                for h in range(n):
                    pe.wait_ge(weights_in[h], i * 16 + 16)
                    for m in range(2):
                        t = 2 * h + m
                        if not isinstance(i, int) or 4 * i + t >= 2:
                            pe.wait_ge(tile_used, i * 4 + t - 1)
                        for q in range(ka):
                            c = (2 * q + m) * P
                            mm = pe.matmul(bank(k.ps, 2 * m), k.wbuf[:, h, c:c + P], src_a[:, q, :],
                                           start=(q == 0), stop=(q == ka - 1))
                        mm.then_inc(a_done, 1)
                        for q in range(kb):
                            c = (2 * (ka + q) + m) * P
                            mm = pe.matmul(bank(k.ps, 2 * m + 1), k.wbuf[:, h, c:c + P], src_b[:, q, :],
                                           start=(q == 0), stop=(q == kb - 1))
                        mm.then_inc(b_done, 1)
            by_pairs(pe, groups, multiply)

        @block.scalar
        def _(act):
            def gates(i, n):
                for t in range(2 * n):
                    act.wait_ge(a_done, i * 4 + t + 1)
                    if not isinstance(i, int) or 4 * i + t >= 2:
                        act.wait_ge(tile_used, i * 4 + t - 1)
                    act.activation(gate[:, t % 2, :], bank(k.ps, 2 * (t % 2)), func).then_inc(gate_ready, 1)
            by_pairs(act, groups, gates)

        @block.vector
        def _(dve):
            def products(i, n):
                for t in range(2 * n):
                    dve.wait_ge(gate_ready, i * 4 + t + 1)
                    dve.wait_ge(b_done, i * 4 + t + 1)
                    o = dst[:, bass.ds(i * 4 + t, 1), :].rearrange("p a t -> p (a t)")
                    g = gate[:, t % 2, :]
                    if not accumulate:
                        dve.tensor_tensor(o, g, bank(k.ps, 2 * (t % 2) + 1), ALU.mult).then_inc(tile_used, 1)
                        continue
                    dve.tensor_tensor(g, g, bank(k.ps, 2 * (t % 2) + 1), ALU.mult).then_inc(product_ready, 1)
                    dve.wait_ge(product_ready, i * 4 + t + 1)
                    dve.tensor_tensor(o, o, g, ALU.add).then_inc(tile_used, 1)
            by_pairs(dve, groups, products)


def skinny(k, w, src, rows, dst):
    nc = k.nc
    kt = src.shape[1]
    with ExitStack() as ctx:
        weights_in, done, taken = semaphores(k, ctx, "weights_in done taken")
        block = ctx.enter_context(nc.Block())
        wide_w = w.shape[1] // kt

        @block.sync
        def _(sp):
            sp.dma_start(k.wbuf[:, 0, 0:w.shape[1]], w).then_inc(weights_in, 16)

        @block.tensor
        def _(pe):
            pe.wait_ge(weights_in, 16)
            for n, (r0, nr, _) in enumerate(rows):
                for q in range(kt):
                    c = q * wide_w + r0
                    mm = pe.matmul(k.ps[0:nr, n, :], k.wbuf[:, 0, c:c + nr], src[:, q, :],
                                   start=(q == 0), stop=(q == kt - 1))
                mm.then_inc(done, 1)

        @block.scalar
        def _(act):
            for n, (_, nr, o) in enumerate(rows):
                act.wait_ge(done, n + 1)
                act.activation(o, k.ps[0:nr, n, :], ACT.Copy).then_inc(taken, 1)


def ssm_branch(k, y):
    nc = k.nc
    H, N, PAD = SSM_HEADS, SSM_XBC // P, SSM_CONV // 2
    W2 = T + 2 * PAD
    NX = SSM_INNER // P
    with ExitStack() as ctx:
        sb = lambda name, shape: k.sbuf(ctx, name, shape)
        raw = sb("xbc_raw", [P, N, W2])
        act_x = sb("xbc", [P, N, T])
        cbm = sb("cb_masked", [P, 2, NT, T + P])
        decay = sb("decay", [P, 2, T + P])
        prob = sb("prob", [P, 2, T + P])
        dt_raw = decay[0:H, :, 0:T]
        dt = sb("dt", [H, 2, T])
        acum = sb("acum", [H, 2, T])
        colneg = sb("acum_cols", [P, NT, 2, H])
        coldt = sb("dt_cols", [P, NT, 2, H])
        a_exp = sb("a_exp", [H, 2])
        xdt = [raw[:, :, :].rearrange("p a b -> p (a b)")[:, 0:NT * D].rearrange("p (j d) -> p j d", j=NT),
               y[:, 8:16, :].rearrange("p a t -> p (a t)").rearrange("p (j d) -> p j d", j=NT)]

        project(k, [(k.dram["w_xbc"], k.xn, raw[:, :, PAD:PAD + T], 1.0)])
        skinny(k, k.dram["w_dt"][0, :, :], k.xn, [(0, H, dt_raw[:, 0, :]), (H, H, dt_raw[:, 1, :])], None)

        with ExitStack() as inner:
            tap = prob[:, :, 0:T]
            edges, tapped, activated, dt_steps, dt_ready, scanned = semaphores(
                k, inner, "edges tapped activated dt_steps dt_ready scanned")
            block = inner.enter_context(nc.Block())

            @block.gpsimd
            def _(pool):
                pool.memset(raw[:, :, 0:PAD], 0.0).then_inc(edges, 1)
                pool.memset(raw[:, :, PAD + T:W2], 0.0).then_inc(edges, 1)

            @block.vector
            def _(dve):
                dve.wait_ge(edges, 2)
                for m in range(N):
                    o = tap[:, m % 2, :]
                    if m >= 2:
                        dve.wait_ge(activated, m - 1)
                    dve.tensor_scalar(o, raw[:, m, 0:T], k.col("conv_w", m), k.col("conv_b", m),
                                      ALU.mult, ALU.add).then_inc(tapped, 1)
                    for j in range(1, SSM_CONV):
                        dve.wait_ge(tapped, SSM_CONV * m + j)
                        dve.scalar_tensor_tensor(out=o, in0=raw[:, m, j:j + T], scalar=k.col("conv_w", j * N + m),
                                                 in1=o, op0=ALU.mult, op1=ALU.add).then_inc(tapped, 1)
                for r in range(2):
                    dve.wait_ge(dt_ready, r + 1)
                    dve.scalar_tensor_tensor(out=dt[:, r, :], in0=dt_raw[:, r, :], scalar=0.0, in1=dt[:, r, :],
                                             op0=ALU.max, op1=ALU.add).then_inc(scanned, 1)
                    dve.wait_ge(scanned, 3 * r + 1)
                    dve.tensor_scalar(dt_raw[:, r, :], dt[:, r, :], a_exp[:, r:r + 1], -1.0, ALU.mult,
                                      ALU.mult).then_inc(scanned, 1)
                    dve.wait_ge(scanned, 3 * r + 2)
                    step = -1 if r else 1
                    dve.tensor_tensor_scan(acum[:, r, ::step], k.const("ones", H)[:, 0:1].broadcast_to([H, T]),
                                           dt_raw[:, r, ::step], 0.0, ALU.mult, ALU.add).then_inc(scanned, 1)

            @block.scalar
            def _(act):
                for r in range(2):
                    act.activation(dt_raw[:, r, :], dt_raw[:, r, :], ACT.Identity,
                                   bias=k.col("dt_bias", r, H)).then_inc(dt_steps, 1)
                    act.wait_ge(dt_steps, 4 * r + 1)
                    act.activation(dt[:, r, :], dt_raw[:, r, :], ACT.Abs).then_inc(dt_steps, 1)
                    act.wait_ge(dt_steps, 4 * r + 2)
                    act.activation(dt[:, r, :], dt[:, r, :], ACT.Exp, scale=-1.0).then_inc(dt_steps, 1)
                    act.activation(a_exp[:, r:r + 1], k.col("a_log", r, H), ACT.Exp).then_inc(dt_steps, 1)
                    act.wait_ge(dt_steps, 4 * r + 4)
                    act.activation(dt[:, r, :], dt[:, r, :], ACT.Ln, bias=k.const("ones", H)[:, 0:1])\
                        .then_inc(dt_ready, 1)
                for m in range(N):
                    act.wait_ge(tapped, SSM_CONV * (m + 1))
                    act.activation(act_x[:, m, :], tap[:, m % 2, :], ACT.Silu).then_inc(activated, 1)

        with ExitStack() as inner:
            cols_turned, cols_ready, dt_cols_ready, x_turned, x_used, cb_done, cb_used = semaphores(
                k, inner, "cols_turned cols_ready dt_cols_ready x_turned x_used cb_done cb_used")
            block = inner.enter_context(nc.Block())
            small = k.ps[:, 0, 0:NT * 4 * H].rearrange("p (j r h) -> p j r h", j=NT, r=4)

            @block.tensor
            def _(pe):
                for j in range(NT):
                    for r in range(2):
                        pe.transpose(small[:, j, r, :], acum[:, r, j * P:(j + 1) * P], k.const("ident", H)[:, 0:H])
                        mm = pe.transpose(small[:, j, 2 + r, :], dt[:, r, j * P:(j + 1) * P],
                                          k.const("ident", H)[:, 0:H])
                mm.then_inc(cols_turned, 1)
                for n in range(2 * NT):
                    g, j = n // NT, n % NT
                    if n >= 2:
                        pe.wait_ge(cb_used, 4 * (n - 1))
                    pe.matmul(bank(k.ps, 1 + n % 2), act_x[:, NX + g, j * P:(j + 1) * P], act_x[:, NX + 2 + g, :],
                              start=True, stop=True).then_inc(cb_done, 1)
                for n in range(2 * NT):
                    j, half = n // 2, n % 2
                    if n >= 2:
                        pe.wait_ge(x_used, 2 * (n - 1))
                    for q in range(NT):
                        mm = pe.transpose(k.ps[:, 3 + n % 2, q * P:(q + 1) * P],
                                          act_x[:, NT * half + q, j * P:(j + 1) * P], k.const("ident"))
                    mm.then_inc(x_turned, 1)

            @block.scalar
            def _(act):
                act.wait_ge(cols_turned, 1)
                act.activation(coldt[:, :, :, :], small[:, :, 2:4, :], ACT.Copy).then_inc(dt_cols_ready, 1)
                act.activation(colneg[:, :, :, :], small[:, :, 0:2, :], ACT.Copy, scale=-1.0).then_inc(cols_ready, 1)

            @block.vector
            def _(dve):
                for n in range(2 * NT):
                    g, j = n // NT, n % NT
                    dve.wait_ge(cb_done, n + 1)
                    src, o, fw = bank(k.ps, 1 + n % 2), cbm[:, g, j, :], T - j * P
                    dve.tensor_tensor(o[:, 0:P], src[:, j * P:(j + 1) * P], k.const("le"), ALU.mult)\
                        .then_inc(cb_used, 1)
                    if fw > P:
                        dve.tensor_copy(o[:, P:fw], src[:, (j + 1) * P:T]).then_inc(cb_used, 1)
                    if j:
                        dve.tensor_copy(o[:, fw:fw + j * P], src[:, 0:j * P]).then_inc(cb_used, 1)
                    ins = dve.tensor_tensor(o[:, fw + j * P:fw + (j + 1) * P], src[:, j * P:(j + 1) * P],
                                            k.const("ge"), ALU.mult)
                    ins.then_inc(cb_used, 2 if j in (0, NT - 1) else 1)
                dve.wait_ge(dt_cols_ready, 1)
                for n in range(2 * NT):
                    j, half = n // 2, n % 2
                    dve.wait_ge(x_turned, n + 1)
                    for r in range(2):
                        o = xdt[r][:, j, half * T:(half + 1) * T].rearrange("p (h d) -> p h d", d=SSM_P)
                        dve.tensor_tensor(o, bank(k.ps, 3 + n % 2).rearrange("p (h d) -> p h d", d=SSM_P),
                                          coldt[:, j, r, 8 * half:8 * half + 8, None].broadcast_to([P, 8, SSM_P]),
                                          ALU.mult).then_inc(x_used, 1)

        with ExitStack() as inner:
            spread, bounded, decayed, prob_ready, tile_used, y_ready = semaphores(
                k, inner, "spread bounded decayed prob_ready tile_used y_ready")
            block = inner.enter_context(nc.Block())

            @block.tensor
            def _(pe):
                def spread_head(h):
                    if h >= 2:
                        pe.wait_ge(bounded, 2 * NT * (h - 1))
                    for r in range(2):
                        mm = pe.matmul(bank(k.ps, 2 * (h % 2) + r), k.const("ident", H)[:, h:h + 1].broadcast_to([H, P]),
                                       acum[:, r, :], start=True, stop=True)
                    mm.then_inc(spread, 1)

                spread_head(0)
                for h in range(H):
                    if h + 1 < H:
                        spread_head(h + 1)
                    bk, half = 4 + (h // 2) % 2, h % 2
                    if h % 2 == 0 and h >= 4:
                        pe.wait_ge(y_ready, h // 2 - 1)
                    for j in range(NT):
                        n = NT * h + j
                        pe.wait_ge(prob_ready, n + 1)
                        o = k.ps[64 * half:64 * half + 64, bk, :]
                        pe.matmul(o[:, j * P:T], xdt[0][:, j, h * SSM_P:(h + 1) * SSM_P],
                                  prob[:, n % 2, 0:T - j * P], start=(j == 0), stop=False)
                        mm = pe.matmul(o[:, 0:(j + 1) * P], xdt[1][:, j, h * SSM_P:(h + 1) * SSM_P],
                                       prob[:, n % 2, T - j * P:T + P], start=False, stop=(j == NT - 1))
                        mm.then_inc(tile_used, 1)

            @block.scalar
            def _(act):
                for h in range(H):
                    for j in range(NT):
                        n = NT * h + j
                        act.wait_ge(bounded, 2 * n + 2)
                        act.activation(decay[:, n % 2, :], decay[:, n % 2, :], ACT.Exp).then_inc(decayed, 1)

            @block.vector
            def _(dve):
                for h in range(H):
                    dve.wait_ge(spread, h + 1)
                    for j in range(NT):
                        n = NT * h + j
                        if n >= 2:
                            dve.wait_ge(prob_ready, n - 1)
                        for r, (a, b, at) in enumerate(((0, T - j * P, j * P), (T - j * P, T + P, 0))):
                            dve.tensor_scalar(decay[:, n % 2, a:b], k.ps[:, 2 * (h % 2) + r, at:at + b - a],
                                              colneg[:, j, r, h:h + 1], 0.0, ALU.add, ALU.min).then_inc(bounded, 1)
                        if n >= 2:
                            dve.wait_ge(tile_used, n - 1)
                        dve.wait_ge(decayed, n + 1)
                        dve.tensor_tensor(prob[:, n % 2, :], decay[:, n % 2, :], cbm[:, h // 8, j, :],
                                          ALU.mult).then_inc(prob_ready, 1)
                    if h % 2:
                        m = h // 2
                        dve.wait_ge(tile_used, NT * (h + 1))
                        dve.scalar_tensor_tensor(out=y[:, m, :], in0=act_x[:, m, :], scalar=k.col("d_skip", m),
                                                 in1=bank(k.ps, 4 + m % 2), op0=ALU.mult, op1=ALU.add)\
                            .then_inc(y_ready, 1)

        z = raw[:, :, :].rearrange("p a b -> p (a b)")[:, 0:8 * T].rearrange("p (m t) -> p m t", m=8)
        project(k, [(k.dram["w_z"], k.xn, z, 1.0)])
        with ExitStack() as inner:
            gate_ready, gated = semaphores(k, inner, "gate_ready gated")
            block = inner.enter_context(nc.Block())

            @block.scalar
            def _(act):
                for m in range(8):
                    act.activation(z[:, m, :], z[:, m, :], ACT.Silu).then_inc(gate_ready, 1)

            @block.vector
            def _(dve):
                for m in range(8):
                    dve.wait_ge(gate_ready, m + 1)
                    dve.tensor_tensor(y[:, m, :], y[:, m, :], z[:, m, :], ALU.mult).then_inc(gated, 1)
    rms_norm(k, y[:, 0:8, :], y[:, 0:8, :], "ssm_norm")


def flat(ap):
    return ap.rearrange("p a b -> p (a b)")


def rwkv_branch(k, y):
    nc = k.nc
    NM = RWKV_COLS // P
    Q = RWKV_W // P
    with ExitStack() as ctx:
        sb = lambda name, shape: k.sbuf(ctx, name, shape)
        mix = sb("mixed", [P, NM, T])
        kk = sb("kk", [P, Q, T])
        ka = sb("kk_a", [P, Q, T])
        store = sb("transfer", [P, 8192 + 2048])
        fm = sb("factors", [P, 9, T])
        raw = store[:, 0:NM * (T + 2)].rearrange("p (m t) -> p m t", m=NM)
        lora = sb("lora", [P, 2 * RWKV_W])
        g_up = k.wbuf[:, 0, 0:RWKV_W]
        r_, k_, v_ = mix[:, 0:Q, :], mix[:, Q:2 * Q, :], mix[:, 2 * Q:3 * Q, :]

        project(k, [(k.dram["w_rwkv"], k.xn, raw[:, :, 1:T + 1], 1.0)])

        with ExitStack() as inner:
            diff = fm[:, 0:4, :]
            edges, diffed, shifted, lora_in = semaphores(k, inner, "edges diffed shifted lora_in")
            block = inner.enter_context(nc.Block())

            @block.sync
            def _(sp):
                sp.dma_start(lora[:, :], k.dram["w_lora"]).then_inc(lora_in, 16)
                sp.wait_ge(lora_in, 16)

            @block.gpsimd
            def _(pool):
                pool.memset(raw[:, :, 0:1], 0.0).then_inc(edges, 1)
                pool.memset(raw[:, :, T + 1:T + 2], 0.0).then_inc(edges, 1)
                pool.wait_ge(edges, 2)
                for m in range(NM):
                    if m >= 2:
                        pool.wait_ge(shifted, 2 * (m - 1))
                    for s in range(2):
                        pool.tensor_tensor(diff[:, 2 * (m % 2) + s, :], raw[:, m, 2 * s:2 * s + T],
                                           raw[:, m, 1:T + 1], ALU.subtract).then_inc(diffed, 1)

            @block.vector
            def _(dve):
                for m in range(NM):
                    for s in range(2):
                        dve.wait_ge(diffed, 2 * m + s + 1)
                        if s:
                            dve.wait_ge(shifted, 2 * m + 1)
                        dve.scalar_tensor_tensor(out=mix[:, m, :], in0=diff[:, 2 * (m % 2) + s, :],
                                                 scalar=k.col("mu", s * NM + m),
                                                 in1=mix[:, m, :] if s else raw[:, m, 1:T + 1],
                                                 op0=ALU.mult, op1=ALU.add).then_inc(shifted, 1)

        with ExitStack() as inner:
            low, a_done, a_ready, kx_ready, kx_squared, kx_summed, root, inverse, made = semaphores(
                k, inner, "low a_done a_ready kx_ready kx_squared kx_summed root inverse made")
            block = inner.enter_context(nc.Block())
            a_, sq, rt = fm[:, 0:2, :], fm[:, 2:4, :], fm[:, 4:6, :]

            @block.scalar
            def _(act):
                act.activation(mix[0:64, 12, :], mix[0:64, 12, :], ACT.Tanh).then_inc(low, 1)
                act.activation(mix[:, 13, :], mix[:, 13, :], ACT.Sigmoid).then_inc(low, 1)
                for q in range(Q):
                    act.wait_ge(a_done, q + 1)
                    if q >= 2:
                        act.wait_ge(made, 4 * (q - 1))
                    act.activation(a_[:, q % 2, :], bank(k.ps, q % 2), ACT.Sigmoid, bias=k.col("a0", q))\
                        .then_inc(a_ready, 1)
                    act.wait_ge(kx_ready, q + 1)
                    act.activation(sq[:, q % 2, :], kk[:, q, :], ACT.Square).then_inc(kx_squared, 1)
                    act.wait_ge(kx_summed, q + 1)
                    act.activation(rt[:, q % 2, :], bank(k.ps, 2 + q % 2), ACT.Sqrt, bias=k.const("eps")[:, 2:3])\
                        .then_inc(root, 1)

            @block.tensor
            def _(pe):
                for q in range(Q):
                    if q >= 2:
                        pe.wait_ge(a_ready, q - 1)
                    pe.matmul(bank(k.ps, q % 2), lora[64:128, q * P:(q + 1) * P], mix[64:128, 12, :],
                              start=True, stop=True).then_inc(a_done, 1)
                    pe.wait_ge(kx_squared, q + 1)
                    if q >= 2:
                        pe.wait_ge(root, q - 1)
                    pe.matmul(bank(k.ps, 2 + q % 2), k.const("pair"), sq[:, q % 2, :], start=True, stop=True)\
                        .then_inc(kx_summed, 1)

            @block.vector
            def _(dve):
                for q in range(Q):
                    dve.tensor_scalar(kk[:, q, :], k_[:, q, :], k.col("k_k", q), None, ALU.mult).then_inc(kx_ready, 1)
                for q in range(Q):
                    r = rt[:, q % 2, :]
                    dve.wait_ge(root, q + 1)
                    dve.reciprocal(r, r).then_inc(inverse, 1)
                    dve.wait_ge(inverse, q + 1)
                    dve.tensor_tensor(kk[:, q, :], kk[:, q, :], r, ALU.mult).then_inc(made, 1)
                    dve.wait_ge(made, 4 * q + 1)
                    dve.wait_ge(a_ready, q + 1)
                    dve.tensor_tensor(ka[:, q, :], kk[:, q, :], a_[:, q % 2, :], ALU.mult).then_inc(made, 1)
                    dve.tensor_scalar(a_[:, q % 2, :], a_[:, q % 2, :], -1.0, k.col("k_a", q), ALU.add, ALU.mult)\
                        .then_inc(made, 1)
                    dve.wait_ge(made, 4 * q + 3)
                    dve.scalar_tensor_tensor(out=k_[:, q, :], in0=a_[:, q % 2, :], scalar=1.0, in1=k_[:, q, :],
                                             op0=ALU.add, op1=ALU.mult).then_inc(made, 1)

        gh = store[:, 0:8192].rearrange("p (q c n) -> p q c n", q=Q, c=NC)
        q1 = store[:, 8192:].rearrange("p (q t) -> p q t", q=Q)
        for back in range(2):
            rwkv_transfer(k, back, mix, kk, ka, fm, lora, gh, q1, y)
            rwkv_chain(k, back, gh, q1, y)

        with ExitStack() as inner:
            (mean_done, centred, squared, var_done, root, inverse, scaled, normed, rk_ready, rk_scaled, rk_done,
             bonus_ready, summed, g_done, y_ready, g_up_in) = semaphores(
                k, inner, "mean_done centred squared var_done root inverse scaled normed rk_ready rk_scaled "
                "rk_done bonus_ready summed g_done y_ready g_up_in")
            block = inner.enter_context(nc.Block())
            sq, rt, rk = fm[:, 0:2, :], fm[:, 2:4, :], fm[:, 4:6, :]

            @block.sync
            def _(sp):
                sp.dma_start(g_up, k.dram["w_g_up"]).then_inc(g_up_in, 16)

            @block.tensor
            def _(pe):
                pe.wait_ge(g_up_in, 16)
                for q in range(Q):
                    b = 4 * (q % 2)
                    if q >= 2:
                        pe.wait_ge(y_ready, q - 1)
                    pe.matmul(bank(k.ps, b), k.const("pair"), y[:, q, :], start=True, stop=True).then_inc(mean_done, 1)
                    pe.wait_ge(rk_ready, q + 1)
                    pe.matmul(bank(k.ps, b + 2), k.const("pair"), rk[:, q % 2, :], start=True, stop=True)\
                        .then_inc(rk_done, 1)
                    pe.matmul(bank(k.ps, b + 3), g_up[:, q * P:(q + 1) * P], mix[:, 13, :], start=True, stop=True)\
                        .then_inc(g_done, 1)
                    pe.wait_ge(squared, q + 1)
                    pe.matmul(bank(k.ps, b + 1), k.const("pair"), sq[:, q % 2, :], start=True, stop=True)\
                        .then_inc(var_done, 1)

            @block.scalar
            def _(act):
                for q in range(Q):
                    act.wait_ge(centred, q + 1)
                    act.activation(sq[:, q % 2, :], y[:, q, :], ACT.Square).then_inc(squared, 1)
                    act.wait_ge(var_done, q + 1)
                    act.activation(rt[:, q % 2, :], bank(k.ps, 4 * (q % 2) + 1), ACT.Sqrt,
                                   bias=k.const("eps")[:, 1:2], scale=1.0 / 64).then_inc(root, 1)
                    act.wait_ge(scaled, q + 1)
                    act.activation(y[:, q, :], y[:, q, :], ACT.Identity, scale=k.col("ln_w", q),
                                   bias=k.col("ln_b", q)).then_inc(normed, 1)

            @block.vector
            def _(dve):
                for q in range(Q):
                    b = 4 * (q % 2)
                    dve.wait_ge(mean_done, q + 1)
                    dve.scalar_tensor_tensor(out=y[:, q, :], in0=bank(k.ps, b), scalar=-1.0 / 64, in1=y[:, q, :],
                                             op0=ALU.mult, op1=ALU.add).then_inc(centred, 1)
                    dve.tensor_tensor(rk[:, q % 2, :], r_[:, q, :], k_[:, q, :], ALU.mult).then_inc(rk_scaled, 1)
                    dve.wait_ge(rk_scaled, q + 1)
                    dve.tensor_scalar(rk[:, q % 2, :], rk[:, q % 2, :], k.col("r_k", q), None, ALU.mult)\
                        .then_inc(rk_ready, 1)
                    dve.wait_ge(rk_done, q + 1)
                    dve.tensor_tensor(rk[:, q % 2, :], bank(k.ps, b + 2), v_[:, q, :], ALU.mult)\
                        .then_inc(bonus_ready, 1)
                    dve.wait_ge(root, q + 1)
                    dve.reciprocal(rt[:, q % 2, :], rt[:, q % 2, :]).then_inc(inverse, 1)
                    dve.wait_ge(inverse, q + 1)
                    dve.wait_ge(centred, q + 1)
                    dve.tensor_tensor(y[:, q, :], y[:, q, :], rt[:, q % 2, :], ALU.mult).then_inc(scaled, 1)
                    dve.wait_ge(normed, q + 1)
                    dve.wait_ge(bonus_ready, q + 1)
                    dve.tensor_tensor(y[:, q, :], y[:, q, :], rk[:, q % 2, :], ALU.add).then_inc(summed, 1)
                    dve.wait_ge(summed, q + 1)
                    dve.wait_ge(g_done, q + 1)
                    dve.tensor_tensor(y[:, q, :], y[:, q, :], bank(k.ps, b + 3), ALU.mult).then_inc(y_ready, 1)


def rwkv_transfer(k, back, mix, kk, ka, fm, lora, gh, q1, y):
    nc = k.nc
    Q = RWKV_W // P
    step = -1 if back else 1
    end = 0 if back else CH - 1
    strict, strict_t, incl = ("c_gt", "c_lt", "c_ge") if back else ("c_lt", "c_gt", "c_le")
    r_, k_, v_ = mix[:, 0:Q, :], mix[:, Q:2 * Q, :], mix[:, 2 * Q:3 * Q, :]
    logw, L, e_l, at, rt, bt, kt, bh, kh = [fm[:, n, :] for n in range(9)]
    wb = flat(k.wbuf[:, :, :]).rearrange("p (n t) -> p n t", t=T)
    tile4 = lambda n: wb[:, n, :].rearrange("p (j t) -> p j t", j=NT)
    N_, NT_, AK, ARB, ARK, Z = [[tile4(2 * n + h) for h in range(2)] for n in range(6)]
    bh_tok, kh_tok, v_tok = [tile4(12 + n) for n in range(3)]
    diag = wb[:, 15, :]
    ident = k.const("ident")
    with ExitStack() as inner:
        (w_done, sg_ready, logw_ready, L_ready, e_ready, factor_ready, turned, turned_used, gram_done, gram_used,
         av_done, av_used, z_done, n_done, z_used, n_used, q_done, q_used, gh_done, gh_used, diag_ready,
         diag_added) = semaphores(
            k, inner, "w_done sg_ready logw_ready L_ready e_ready factor_ready turned turned_used gram_done "
            "gram_used av_done av_used z_done n_done z_used n_used q_done q_used gh_done gh_used diag_ready "
            "diag_added")
        block = inner.enter_context(nc.Block())
        ROUNDS = 5
        NSQ = 2 * (ROUNDS - 1) - 1

        @block.tensor
        def _(pe):
            for u in range(Q):
                if u:
                    pe.wait_ge(q_used, 2 * u)
                pe.matmul(bank(k.ps, 7), lora[0:64, back * RWKV_W + u * P:back * RWKV_W + (u + 1) * P],
                          mix[0:64, 12, :],
                          start=True, stop=True).then_inc(w_done, 1)
                for n, src in enumerate((at, bh, kh, v_[:, u, :])):
                    if n == 0:
                        pe.wait_ge(factor_ready, 6 * u + 6)
                        pe.wait_ge(gh_used, 4 * u) if u else None
                    for j in range(NT):
                        mm = pe.transpose(k.ps[:, 4 + n, j * P:(j + 1) * P], src[:, j * P:(j + 1) * P], ident)
                    mm.then_inc(turned, 1)
                n = 0
                for lhs, rhs in ((bt, at), (at, bt), (kt, at), (bt, rt), (kt, rt)):
                    for h in range(2):
                        if n >= 4:
                            pe.wait_ge(gram_used, 10 * u + n - 3)
                        rows = slice(64 * h, 64 * h + 64)
                        for j in range(NT):
                            c = slice(j * P, (j + 1) * P)
                            mm = pe.matmul(k.ps[:, n % 4, c], lhs[rows, c], rhs[rows, c], start=True, stop=True)
                        mm.then_inc(gram_done, 1)
                        n += 1
                pe.wait_ge(turned_used, 5 * u + 5)
                for h in range(2):
                    pe.wait_ge(gram_used, 10 * u + 5 + h)
                    for j in range(NT):
                        mm = pe.matmul(k.ps[:, 4 + h, j * P:j * P + 64], AK[h][:, j, :],
                                       v_tok[:, j, 64 * h:64 * h + 64], start=True, stop=True)
                    mm.then_inc(av_done, 1)
                pe.wait_ge(gram_used, 10 * u + 10)
                for i in range(ROUNDS):
                    for h in range(2):
                        if i == 0:
                            pe.wait_ge(av_used, 2 * u + 2)
                        else:
                            pe.wait_ge(z_used, 2 * ROUNDS * u + 2 * (i - 1) + h + 1)
                            pe.wait_ge(n_used, 2 * NSQ * u + (4 * (i - 1) + 2 * h + 2 if i < ROUNDS - 1
                                                              else 4 * (i - 1) + h + 1))
                        for j in range(NT):
                            mm = pe.matmul(k.ps[:, 3 * h, j * P:(j + 1) * P], N_[h][:, j, :], Z[h][:, j, :],
                                           start=True, stop=True)
                        mm.then_inc(z_done, 1)
                        for s in range(2 if i < ROUNDS - 2 else 1 if i < ROUNDS - 1 else 0):
                            a, b = (N_[h], NT_[h]) if s else (NT_[h], N_[h])
                            for j in range(NT):
                                mm = pe.matmul(k.ps[:, 3 * h + 1 + s, j * P:(j + 1) * P], a[:, j, :], b[:, j, :],
                                               start=True, stop=True)
                            mm.then_inc(n_done, 1)
                pe.wait_ge(z_used, 2 * ROUNDS * (u + 1))
                for h in range(2):
                    rows = slice(64 * h, 64 * h + 64)
                    for j in range(NT):
                        c = slice(j * P, (j + 1) * P)
                        mm = pe.matmul(k.ps[rows, 6, c], Z[h][:, j, 0:64], ARB[h][:, j, :], start=True, stop=True)
                mm.then_inc(q_done, 1)
                for h in range(2):
                    rows = slice(64 * h, 64 * h + 64)
                    for j in range(NT):
                        c = slice(j * P, (j + 1) * P)
                        pe.matmul(k.ps[rows, 7, c], Z[h][:, j, 64:128], ARB[h][:, j, :], start=True, stop=False)
                        mm = pe.matmul(k.ps[rows, 7, c], v_tok[:, j, 64 * h:64 * h + 64], ARK[h][:, j, :],
                                       start=False, stop=True)
                mm.then_inc(q_done, 1)
                for c in range(NT):
                    tok = slice(CH * c, CH * c + CH)
                    for h in range(2):
                        rows, ch = slice(64 * h, 64 * h + 64), slice(64 * h, 64 * h + 64)
                        for j in range(NT):
                            o = k.ps[rows, c, j * P:(j + 1) * P]
                            pe.matmul(o[:, 0:64], Z[h][tok, j, 0:64], bh_tok[tok, j, ch], start=True, stop=True,
                                      tile_position=(CH * c, 64 * h))
                            pe.matmul(o[:, 64:128], bh_tok[tok, j, ch], Z[h][tok, j, 64:128], start=True, stop=False,
                                      tile_position=(CH * c, 64 * h))
                            mm = pe.matmul(o[:, 64:128], kh_tok[tok, j, ch], v_tok[tok, j, ch], start=False,
                                           stop=True, tile_position=(CH * c, 64 * h))
                    mm.then_inc(gh_done, 1)

        @block.scalar
        def _(act):
            for u in range(Q):
                if u:
                    act.wait_ge(diag_added, 2 * u)
                act.wait_ge(w_done, u + 1)
                act.activation(e_l, bank(k.ps, 7), ACT.Sigmoid, bias=k.col("w0", back * Q + u)).then_inc(sg_ready, 1)
                act.wait_ge(L_ready, 2 * u + 2)
                act.activation(e_l, L, ACT.Exp).then_inc(e_ready, 1)
                act.activation(at, logw, ACT.Exp).then_inc(e_ready, 1)
                act.activation(bt, L, ACT.Exp, scale=-1.0).then_inc(e_ready, 1)
                act.wait_ge(turned, 4 * u + 1)
                for h in range(2):
                    act.activation(Z[h][:, :, 0:64], bank(k.ps, 4).rearrange("p (j c) -> p j c", j=NT)[:, :, 64 * h:64 * h + 64],
                                   ACT.Copy).then_inc(turned_used, 1)
                for n, o in enumerate((bh_tok, kh_tok, v_tok)):
                    act.wait_ge(turned, 4 * u + n + 2)
                    act.activation(o, bank(k.ps, 5 + n).rearrange("p (j c) -> p j c", j=NT), ACT.Copy)\
                        .then_inc(turned_used, 1)
                for h in range(2):
                    act.wait_ge(av_done, 2 * u + h + 1)
                    act.activation(Z[h][:, :, 64:128], bank(k.ps, 4 + h).rearrange("p (j c) -> p j c", j=NT)[:, :, 0:64],
                                   ACT.Copy).then_inc(av_used, 1)
                n = 2 * NSQ * u
                for i in range(ROUNDS - 1):
                    for h in range(2):
                        squarings = 2 if i < ROUNDS - 2 else 1
                        act.wait_ge(n_done, n + squarings)
                        n += squarings
                        for s in range(squarings):
                            act.activation((NT_ if s else N_)[h],
                                           bank(k.ps, 3 * h + 1 + s).rearrange("p (j c) -> p j c", j=NT), ACT.Copy)\
                                .then_inc(n_used, 1)
                for c in range(NT):
                    act.wait_ge(gh_done, 4 * u + c + 1)
                    act.activation(gh[:, u, c::NT, :], bank(k.ps, c).rearrange("p (j n) -> p j n", j=NT), ACT.Copy)\
                        .then_inc(gh_used, 1)

        @block.vector
        def _(dve):
            for u in range(Q):
                dve.wait_ge(sg_ready, u + 1)
                dve.tensor_scalar(logw, e_l, -RWKV_DECAY, None, ALU.mult).then_inc(logw_ready, 1)
                dve.wait_ge(logw_ready, u + 1)
                reset = k.const("reset")[:, back * T:(back + 1) * T]
                dve.tensor_tensor_scan(L[:, ::step], reset[:, ::step], logw[:, ::step], 0.0, ALU.mult, ALU.add)\
                    .then_inc(L_ready, 1)
                dve.wait_ge(L_ready, 2 * u + 1)
                dve.tensor_tensor(logw, L, logw, ALU.subtract).then_inc(L_ready, 1)
                dve.wait_ge(e_ready, 3 * u + 1)
                dve.tensor_tensor(rt, r_[:, u, :], e_l, ALU.mult).then_inc(factor_ready, 1)
                dve.wait_ge(e_ready, 3 * u + 2)
                dve.scalar_tensor_tensor(out=at, in0=kk[:, u, :], scalar=-1.0, in1=at, op0=ALU.mult, op1=ALU.mult)\
                    .then_inc(factor_ready, 1)
                dve.wait_ge(e_ready, 3 * u + 3)
                dve.tensor_tensor(kt, k_[:, u, :], bt, ALU.mult).then_inc(factor_ready, 1)
                dve.tensor_tensor(bt, ka[:, u, :], bt, ALU.mult).then_inc(factor_ready, 1)
                dve.wait_ge(factor_ready, 6 * u + 4)
                chunks = lambda ap: ap.rearrange("p (c t) -> p c t", t=CH)
                e_end = chunks(e_l)[:, :, end:end + 1]
                for o, src in ((kh, kt), (bh, bt)):
                    dve.tensor_tensor(chunks(o), chunks(src), e_end.broadcast_to([P, NC, CH]), ALU.mult)\
                        .then_inc(factor_ready, 1)
                n = 0
                for dst, mask in ((N_, strict), (NT_, strict_t), (AK, strict), (ARB, incl), (ARK, incl)):
                    for h in range(2):
                        dve.wait_ge(gram_done, 10 * u + n + 1)
                        dve.tensor_tensor(dst[h], bank(k.ps, n % 4).rearrange("p (j c) -> p j c", j=NT),
                                          wide(k.const(mask), NT), ALU.mult).then_inc(gram_used, 1)
                        n += 1
                for i in range(ROUNDS):
                    for h in range(2):
                        dve.wait_ge(z_done, 2 * ROUNDS * u + 2 * i + h + 1)
                        if i:
                            dve.wait_ge(z_used, 2 * ROUNDS * u + 2 * (i - 1) + h + 1)
                        dve.tensor_tensor(Z[h], Z[h], bank(k.ps, 3 * h).rearrange("p (j c) -> p j c", j=NT), ALU.add)\
                            .then_inc(z_used, 1)
                dve.wait_ge(q_done, 2 * u + 1)
                dve.tensor_tensor(q1[:, u, :], bank(k.ps, 6), rt, ALU.add).then_inc(q_used, 1)
                dve.wait_ge(q_done, 2 * u + 2)
                if back:
                    dve.tensor_tensor(y[:, u, :], y[:, u, :], bank(k.ps, 7), ALU.add).then_inc(q_used, 1)
                else:
                    dve.tensor_copy(y[:, u, :], bank(k.ps, 7)).then_inc(q_used, 1)
                dve.wait_ge(gh_used, 4 * u + 4)
                for half in range(2):
                    cs = slice(8 * half, 8 * half + 8)
                    d3 = diag.rearrange("p (c n) -> p c n", n=64)
                    if 2 * u + half:
                        dve.wait_ge(diag_added, 2 * u + half)
                    dve.tensor_tensor(d3, wide(k.const("eye64"), 8), e_end[:, cs, :].broadcast_to([P, 8, 64]),
                                      ALU.mult).then_inc(diag_ready, 1)
                    dve.wait_ge(diag_ready, 2 * u + half + 1)
                    dve.tensor_tensor(gh[:, u, cs, 0:64], gh[:, u, cs, 0:64], d3, ALU.add).then_inc(diag_added, 1)


def rwkv_chain(k, back, gh, q1, y):
    nc = k.nc
    Q = RWKV_W // P
    order = list(range(NC))[::-1] if back else list(range(NC))
    with ExitStack() as inner:
        state_done, state_ready, out_done, out_used = semaphores(
            k, inner, "state_done state_ready out_done out_used")
        block = inner.enter_context(nc.Block())

        @block.tensor
        def _(pe):
            for i in range(1, NC):
                c, before = order[i], order[i - 1]
                if i > 1:
                    pe.wait_ge(state_ready, i - 1)
                if i < NC - 1:
                    for q in range(Q):
                        for h in range(2):
                            rows = slice(64 * h, 64 * h + 64)
                            mm = pe.matmul(k.ps[rows, 2 * (i % 2) + h, q * 64:(q + 1) * 64], gh[rows, q, c, 0:64],
                                           gh[rows, q, before, 64:128], start=True, stop=True)
                    mm.then_inc(state_done, 1)
                for q in range(Q):
                    for h in range(2):
                        rows = slice(64 * h, 64 * h + 64)
                        mm = pe.matmul(k.ps[rows, 4 + q, CH * c:CH * c + CH], gh[rows, q, before, 64:128],
                                       q1[rows, q, CH * c:CH * c + CH], start=True, stop=True)
            mm.then_inc(out_done, 1)

        @block.vector
        def _(dve):
            for i in range(1, NC - 1):
                c = order[i]
                dve.wait_ge(state_done, i)
                for h in range(2):
                    rows = slice(64 * h, 64 * h + 64)
                    ins = dve.tensor_tensor(gh[rows, :, c, 64:128], gh[rows, :, c, 64:128],
                                            k.ps[rows, 2 * (i % 2) + h, 0:Q * 64].rearrange("p (q n) -> p q n", q=Q),
                                            ALU.add)
                ins.then_inc(state_ready, 1)
            dve.wait_ge(out_done, 1)
            part = slice(0, T - CH) if back else slice(CH, T)
            for q in range(Q):
                dve.tensor_tensor(y[:, q, part], y[:, q, part], k.ps[:, 4 + q, part], ALU.add).then_inc(out_used, 1)


def hgrn_branch(k, y):
    nc = k.nc
    HH = HGRN_W // P
    with ExitStack() as ctx:
        sb = lambda name, shape: k.sbuf(ctx, name, shape)
        p = sb("hgrn_in", [P, 5 * HH, T])
        buf = sb("hgrn_buffers", [P, 2, 12, T])
        lbs = sb("lower_bound", [P, 5, HH])
        dec = sb("chunk_decay", [P, 2, NC])
        project(k, [(k.dram["w_hgrn"], k.xn, p[:, :, :], 1.0)])
        q_, f_, i_, g_ = p[:, 0:HH, :], p[:, HH:3 * HH, :], p[:, 3 * HH:4 * HH, :], p[:, 4 * HH:5 * HH, :]

        with ExitStack() as inner:
            bound, exped, sig_ready, f_ready, g_ready = semaphores(k, inner, "bound exped sig_ready f_ready g_ready")
            block = inner.enter_context(nc.Block())
            a, b = k.col_at["lb"]
            logits = k.cols[:, a:b]

            @block.vector
            def _(dve):
                dve.tensor_tensor(lbs[:, 0, :], logits, logits, ALU.subtract).then_inc(bound, 1)
                dve.wait_ge(exped, 1)
                dve.reciprocal(lbs[:, 2, :], lbs[:, 1, :]).then_inc(bound, 1)
                dve.wait_ge(bound, 2)
                dve.tensor_tensor(lbs[:, 2, :], lbs[:, 2, :], lbs[:, 1, :], ALU.mult).then_inc(bound, 1)
                dve.wait_ge(bound, 3)
                dve.tensor_tensor(lbs[:, 3, :], lbs[:, 2, :], lbs[:, 2, :], ALU.subtract).then_inc(bound, 1)
                dve.wait_ge(bound, 4)
                dve.tensor_scalar(lbs[:, 4, :], lbs[:, 3, :], -1.0, 1.0, ALU.mult, ALU.add).then_inc(bound, 1)
                dve.wait_ge(bound, 5)
                for n in range(2 * HH):
                    dve.wait_ge(sig_ready, n + 1)
                    dve.tensor_scalar(f_[:, n, :], f_[:, n, :], lbs[:, 4, n % HH:n % HH + 1],
                                      lbs[:, 3, n % HH:n % HH + 1], ALU.mult, ALU.add).then_inc(f_ready, 1)

            @block.scalar
            def _(act):
                act.wait_ge(bound, 1)
                act.activation(lbs[:, 1, :], lbs[:, 0, :], ACT.Exp).then_inc(exped, 1)
                for n in range(2 * HH):
                    act.activation(f_[:, n, :], f_[:, n, :], ACT.Sigmoid).then_inc(sig_ready, 1)
                for n in range(HH):
                    act.activation(g_[:, n, :], g_[:, n, :], ACT.Silu).then_inc(g_ready, 1)

        with ExitStack() as inner:
            (log_ready, prep, exps, turned, turned_used, scored, masked, inputs_done, state_ready, out_done,
             y_used) = semaphores(k, inner, "log_ready prep exps turned turned_used scored masked inputs_done "
                                  "state_ready out_done y_used")
            block = inner.enter_context(nc.Block())
            UNITS = 2 * HH
            PREP = 10
            chunks = lambda ap: ap.rearrange("p (c t) -> p c t", t=CH)
            tiles = lambda ap: ap.rearrange("p (j t) -> p j t", j=NT)

            def parts(u):
                b = buf[:, u % 2, :, :]
                return [b[:, n, :] for n in range(8)] + [b[:, 8:12, :].rearrange("p a t -> p (a t)")
                                                         .rearrange("p (c v) -> p c v", c=NC)]

            def order(u):
                return list(range(NC))[::-1] if u >= HH else list(range(NC))

            @block.scalar
            def _(act):
                for u in range(UNITS + 1):
                    if u < UNITS:
                        L, qs, ks, qb, kh, sc, kh_tok, v_tok, S = parts(u)
                        if u >= 2:
                            act.wait_ge(y_used, u - 1)
                        act.activation(qs, f_[:, u, :], ACT.Ln).then_inc(log_ready, 1)
                        act.wait_ge(prep, PREP * u + 4)
                        act.activation(ks, qs, ACT.Exp, scale=-1.0).then_inc(exps, 1)
                        act.activation(qb, L, ACT.Exp).then_inc(exps, 1)
                        act.activation(kh, kh, ACT.Exp).then_inc(exps, 1)
                        act.wait_ge(exps, 4 * u + 1)
                        act.activation(qs, qs, ACT.Exp).then_inc(exps, 1)
                    if u:
                        _, _, _, _, _, _, kh_tok, v_tok, _ = parts(u - 1)
                        for n, o in enumerate((kh_tok, v_tok)):
                            act.wait_ge(turned, 2 * (u - 1) + n + 1)
                            act.activation(o, bank(k.ps, 1 + n), ACT.Copy).then_inc(turned_used, 1)

            @block.vector
            def _(dve):
                for u in range(UNITS + 1):
                    if u < UNITS:
                        L, qs, ks, qb, kh, sc, kh_tok, v_tok, S = parts(u)
                        back, h = u // HH, u % HH
                        step, end, mid = (-1, 0, CH // 2) if back else (1, CH - 1, CH // 2 - 1)
                        reset = k.const("reset")[:, back * T:(back + 1) * T]
                        n0 = PREP * u
                        dve.wait_ge(log_ready, u + 1)
                        dve.tensor_tensor_scan(L[:, ::step], reset[:, ::step], qs[:, ::step], 0.0, ALU.mult, ALU.add)\
                            .then_inc(prep, 1)
                        dve.wait_ge(prep, n0 + 1)
                        dve.tensor_tensor(chunks(qs), chunks(L), chunks(L)[:, :, mid:mid + 1].broadcast_to([P, NC, CH]),
                                          ALU.subtract).then_inc(prep, 1)
                        dve.tensor_tensor(chunks(kh), chunks(L)[:, :, end:end + 1].broadcast_to([P, NC, CH]),
                                          chunks(L), ALU.subtract).then_inc(prep, 1)
                        dve.wait_ge(prep, n0 + 2)
                        dve.tensor_scalar(qs, qs, -43.0, 43.0, ALU.max, ALU.min).then_inc(prep, 1)
                        dve.tensor_scalar(f_[:, u, :], f_[:, u, :], -1.0, 1.0, ALU.mult, ALU.add).then_inc(prep, 1)
                        dve.wait_ge(exps, 4 * u + 4)
                        dve.wait_ge(prep, n0 + 5)
                        dve.tensor_copy(dec[:, u % 2, :], chunks(qb)[:, :, end]).then_inc(prep, 1)
                        dve.tensor_tensor(qs, qs, q_[:, h, :], ALU.mult).then_inc(prep, 1)
                        dve.tensor_tensor(ks, ks, f_[:, u, :], ALU.mult).then_inc(prep, 1)
                        dve.tensor_tensor(kh, kh, f_[:, u, :], ALU.mult).then_inc(prep, 1)
                        dve.wait_ge(prep, n0 + 6)
                        dve.tensor_tensor(qb, qb, q_[:, h, :], ALU.mult).then_inc(prep, 1)
                    if u:
                        w = u - 1
                        _, _, _, _, _, sc, _, _, S = parts(w)
                        back, h = w // HH, w % HH
                        dve.wait_ge(scored, w + 1)
                        dve.tensor_tensor(tiles(sc), tiles(bank(k.ps, 0)), wide(k.const("c_ge" if back else "c_le"), NT),
                                          ALU.mult).then_inc(masked, 1)
                        dve.wait_ge(inputs_done, w + 1)
                        for i, c in enumerate(order(w)[:-1]):
                            src = k.ps[:, 3 + c % NT, (c // NT) * P:(c // NT + 1) * P]
                            if i == 0:
                                dve.tensor_copy(S[:, c, :], src).then_inc(state_ready, 1)
                                continue
                            before = order(w)[i - 1]
                            dve.wait_ge(state_ready, (NC - 1) * w + i)
                            dve.scalar_tensor_tensor(out=S[:, c, :], in0=S[:, before, :],
                                                     scalar=dec[:, w % 2, c:c + 1], in1=src,
                                                     op0=ALU.mult, op1=ALU.add).then_inc(state_ready, 1)
                        dve.wait_ge(out_done, w + 1)
                        if back:
                            dve.tensor_tensor(y[:, h, :], y[:, h, :], bank(k.ps, 7), ALU.add).then_inc(y_used, 1)
                        else:
                            dve.tensor_copy(y[:, h, :], bank(k.ps, 7)).then_inc(y_used, 1)

            @block.tensor
            def _(pe):
                for u in range(UNITS):
                    L, qs, ks, qb, kh, sc, kh_tok, v_tok, S = parts(u)
                    pe.wait_ge(prep, PREP * (u + 1))
                    for n, src in enumerate((kh, i_[:, u % HH, :])):
                        if u:
                            pe.wait_ge(turned_used, 2 * u)
                        for j in range(NT):
                            mm = pe.transpose(k.ps[:, 1 + n, j * P:(j + 1) * P], src[:, j * P:(j + 1) * P],
                                              k.const("ident"))
                        mm.then_inc(turned, 1)
                    if u:
                        pe.wait_ge(masked, u)
                    for j in range(NT):
                        c = slice(j * P, (j + 1) * P)
                        mm = pe.matmul(k.ps[:, 0, c], ks[:, c], qs[:, c], start=True, stop=True)
                    mm.then_inc(scored, 1)
                    pe.wait_ge(turned_used, 2 * u + 2)
                    if u:
                        pe.wait_ge(state_ready, (NC - 1) * u)
                    for j in range(NT):
                        for c in range(NT):
                            rows = slice(CH * c, CH * c + CH)
                            mm = pe.matmul(k.ps[:, 3 + c, j * P:(j + 1) * P], kh_tok[rows, j * P:(j + 1) * P],
                                           v_tok[rows, j * P:(j + 1) * P], start=True, stop=True,
                                           tile_position=(CH * c, 0))
                    mm.then_inc(inputs_done, 1)
                    pe.wait_ge(masked, u + 1)
                    if u:
                        pe.wait_ge(y_used, u)
                    for j in range(NT):
                        c = slice(j * P, (j + 1) * P)
                        pe.matmul(k.ps[:, 7, c], v_tok[:, c], sc[:, c], start=(j == 0), stop=False,
                                  skip_group_check=True)
                    pe.wait_ge(state_ready, (NC - 1) * (u + 1))
                    for i, c in enumerate(order(u)[1:]):
                        ts = slice(CH * c, CH * c + CH)
                        mm = pe.matmul(k.ps[:, 7, ts], S[:, order(u)[i], :], qb[:, ts], start=False,
                                       stop=(i == NC - 2), skip_group_check=True)
                    mm.then_inc(out_done, 1)

        head_norm(k, y, HH, P, "hgrn_norm", k.const("eps")[:, 0:1], g_)


def head_norm(k, y, tiles, head, weight, eps, gate, factor=1.0):
    nc = k.nc
    over = k.const("ones") if head == P else k.const("pair")
    with ExitStack() as inner:
        sq = k.sbuf(inner, "squares", [P, 2, T])
        rt = k.sbuf(inner, "rstd", [P, 2, T])
        squared, summed, root, inverse, scaled, normed = semaphores(
            k, inner, "squared summed root inverse scaled normed")
        block = inner.enter_context(nc.Block())

        @block.scalar
        def _(act):
            for m in range(tiles):
                if m >= 2:
                    act.wait_ge(summed, m - 1)
                    act.wait_ge(scaled, m - 1)
                act.activation(sq[:, m % 2, :], y[:, m, :], ACT.Square).then_inc(squared, 1)
                act.wait_ge(summed, m + 1)
                act.activation(rt[:, m % 2, :], bank(k.ps, m % 2), ACT.Sqrt, bias=eps,
                               scale=1.0 / (head * factor * factor))\
                    .then_inc(root, 1)

        @block.tensor
        def _(pe):
            for m in range(tiles):
                pe.wait_ge(squared, m + 1)
                if m >= 2:
                    pe.wait_ge(root, m - 1)
                pe.matmul(bank(k.ps, m % 2), over, sq[:, m % 2, :], start=True, stop=True).then_inc(summed, 1)

        @block.vector
        def _(dve):
            for m in range(tiles):
                dve.wait_ge(root, m + 1)
                dve.reciprocal(rt[:, m % 2, :], rt[:, m % 2, :]).then_inc(inverse, 1)
                dve.wait_ge(inverse, m + 1)
                dve.scalar_tensor_tensor(out=y[:, m, :], in0=y[:, m, :], scalar=k.col(weight, m),
                                         in1=rt[:, m % 2, :], op0=ALU.mult, op1=ALU.mult).then_inc(scaled, 1)
                if gate is not None:
                    dve.wait_ge(scaled, m + 1)
                    dve.tensor_tensor(y[:, m, :], y[:, m, :], gate[:, m, :], ALU.mult).then_inc(normed, 1)


def project_tokens(k, jobs):
    nc = k.nc
    with ExitStack() as ctx:
        weights_in = semaphores(k, ctx, "weights_in_0 weights_in_1")
        done, taken = semaphores(k, ctx, "done taken")
        block = ctx.enter_context(nc.Block())

        @block.sync
        def _(sp):
            for n, (w, dst) in enumerate(jobs):
                if n >= 2:
                    sp.wait_ge(done, NT * (n - 1))
                sp.dma_start(k.wbuf[:, n % 2, 0:w.shape[1]], w).then_inc(weights_in[n % 2], 16)

        @block.tensor
        def _(pe):
            for n, (w, dst) in enumerate(jobs):
                width = w.shape[1] // KD
                pe.wait_ge(weights_in[n % 2], 16 * (n // 2 + 1))
                for j in range(NT):
                    if n:
                        pe.wait_ge(taken, NT * (n - 1) + j + 1)
                    for q in range(KD):
                        mm = pe.matmul(k.ps[:, j, 0:width], k.xn[:, q, j * P:(j + 1) * P],
                                       k.wbuf[:, n % 2, q * width:(q + 1) * width], start=(q == 0), stop=(q == KD - 1))
                    mm.then_inc(done, 1)

        @block.scalar
        def _(act):
            for n, (w, dst) in enumerate(jobs):
                for j in range(NT):
                    act.wait_ge(done, NT * n + j + 1)
                    act.activation(dst[:, j, :], k.ps[:, j, 0:w.shape[1] // KD], ACT.Copy).then_inc(taken, 1)


def mlstm_branch(k, n_layer, y):
    nc = k.nc
    H, N, PAD = A_HEADS, 2 * A_WIDTH // P, A_CONV // 2
    n = n_layer
    with ExitStack() as ctx:
        sb = lambda name, shape: k.sbuf(ctx, name, shape)
        raw = sb("qk_raw", [P, N, T + 2 * PAD])
        qk = sb("qk", [P, N, T])
        v_tok = sb("v_tok", [P, NT, A_WIDTH])
        o_gate = sb("o_gate", [P, H, T])
        rows = sb("gate_rows", [16, T])
        gates = sb("gate_kinds", [H, 4, T])
        work = sb("gate_work", [H, 2, T])
        b_, g_, M_, m_ = [sb(name, [H, 2, T]) for name in ("b_rows", "g_rows", "max_rows", "m_rows")]
        g_col = sb("g_cols", [P, NT, 2, H])
        project(k, [(k.dram[f"w_a_qk{n}"], k.xn, raw[:, :, PAD:PAD + T], 1.0),
                    (k.dram[f"w_a_o{n}"], k.xn, o_gate[:, :, :], 1.0)])
        project_tokens(k, [(k.dram[f"w_a_v{n}"][0, :, :], v_tok)])
        skinny(k, k.dram[f"w_a_gates{n}"][0, :, :], k.xn, [(0, 16, rows[:, :])], None)

        with ExitStack() as inner:
            tap = k.sbuf(inner, "tap", [P, 2, T])
            (edges, tapped, activated, biased, picked, steps, logs, rows_ready, m_ready, cols_turned,
             cols_ready, o_ready) = semaphores(
                k, inner, "edges tapped activated biased picked steps logs rows_ready m_ready cols_turned "
                "cols_ready o_ready")
            block = inner.enter_context(nc.Block())

            @block.gpsimd
            def _(pool):
                pool.memset(raw[:, :, 0:PAD], 0.0).then_inc(edges, 1)
                pool.memset(raw[:, :, PAD + T:], 0.0).then_inc(edges, 1)

            @block.tensor
            def _(pe):
                pe.wait_ge(biased, 1)
                for r in range(4):
                    mm = pe.matmul(k.ps[0:H, r, :], k.const("ident", 16)[:, H * r:H * r + H], rows[:, :],
                                   start=True, stop=True)
                mm.then_inc(picked, 1)
                cols = k.ps[:, 4, 0:NT * 2 * H].rearrange("p (j r h) -> p j r h", j=NT, r=2)
                pe.wait_ge(rows_ready, 10)
                for j in range(NT):
                    for r in range(2):
                        mm = pe.transpose(cols[:, j, r, :], g_[:, r, j * P:(j + 1) * P], k.const("ident", H)[:, 0:H])
                mm.then_inc(cols_turned, 1)

            @block.scalar
            def _(act):
                act.activation(rows[:, :], rows[:, :], ACT.Identity, bias=k.col(f"a_bias{n}", 0, 16)).then_inc(biased, 1)
                act.wait_ge(picked, 1)
                for r in range(4):
                    act.activation(gates[:, r, :], k.ps[0:H, r, :], ACT.Copy).then_inc(steps, 1)
                act.wait_ge(steps, 4)
                act.activation(work[:, :, :], gates[:, 1::2, :], ACT.Abs).then_inc(logs, 1)
                act.wait_ge(logs, 1)
                act.activation(work[:, :, :], work[:, :, :], ACT.Exp, scale=-1.0).then_inc(logs, 1)
                act.wait_ge(logs, 2)
                act.activation(work[:, :, :], work[:, :, :], ACT.Ln, bias=k.const("ones", H)[:, 0:1]).then_inc(logs, 1)
                act.wait_ge(rows_ready, 10)
                act.activation(m_[:, :, :], m_[:, :, :], ACT.Exp, scale=-1.0).then_inc(m_ready, 1)
                act.wait_ge(cols_turned, 1)
                cols = k.ps[:, 4, 0:NT * 2 * H].rearrange("p (j r h) -> p j r h", j=NT, r=2)
                act.activation(g_col[:, :, :, :], cols, ACT.Copy).then_inc(cols_ready, 1)
                for m in range(H):
                    act.activation(o_gate[:, m, :], o_gate[:, m, :], ACT.Sigmoid).then_inc(o_ready, 1)
                for m in range(N):
                    act.wait_ge(tapped, A_CONV * (m + 1))
                    act.activation(qk[:, m, :], tap[:, m % 2, :], ACT.Silu).then_inc(activated, 1)
                act.wait_ge(activated, N)
                act.activation(qk[:, H:N, :], qk[:, H:N, :], ACT.Copy, scale=float(P) ** -0.5).then_inc(activated, 1)

            @block.vector
            def _(dve):
                dve.wait_ge(logs, 3)
                for r in range(2):
                    step = -1 if r else 1
                    base = 5 * r
                    dve.scalar_tensor_tensor(out=work[:, r, :], in0=gates[:, 2 * r + 1, :], scalar=0.0,
                                             in1=work[:, r, :], op0=ALU.min, op1=ALU.subtract).then_inc(rows_ready, 1)
                    dve.wait_ge(rows_ready, base + 1)
                    dve.tensor_tensor_scan(b_[:, r, ::step], k.const("ones", H)[:, 0:1].broadcast_to([H, T]),
                                           work[:, r, ::step], 0.0, ALU.mult, ALU.add).then_inc(rows_ready, 1)
                    dve.wait_ge(rows_ready, base + 2)
                    dve.tensor_tensor(g_[:, r, :], gates[:, 2 * r, :], b_[:, r, :], ALU.subtract).then_inc(rows_ready, 1)
                    dve.wait_ge(rows_ready, base + 3)
                    dve.tensor_tensor_scan(M_[:, r, ::step], g_[:, r, ::step], g_[:, r, ::step], 0.0, ALU.max, ALU.max)\
                        .then_inc(rows_ready, 1)
                    dve.wait_ge(rows_ready, base + 4)
                    dve.tensor_tensor(m_[:, r, :], b_[:, r, :], M_[:, r, :], ALU.add).then_inc(rows_ready, 1)
                dve.wait_ge(edges, 2)
                for m in range(N):
                    o = tap[:, m % 2, :]
                    if m >= 2:
                        dve.wait_ge(activated, m - 1)
                    dve.tensor_scalar(o, raw[:, m, 0:T], k.col(f"a_conv{n}", m), None, ALU.mult).then_inc(tapped, 1)
                    for j in range(1, A_CONV):
                        dve.wait_ge(tapped, A_CONV * m + j)
                        dve.scalar_tensor_tensor(out=o, in0=raw[:, m, j:j + T], scalar=k.col(f"a_conv{n}", j * N + m),
                                                 in1=o, op0=ALU.mult, op1=ALU.add).then_inc(tapped, 1)

        with ExitStack() as inner:
            dist = k.sbuf(inner, "exponents", [P, 2, T])
            prob = k.sbuf(inner, "prob", [P, 2, T])
            den = k.sbuf(inner, "denominator", [P, 2, T])
            (spread, bounded, exped, masked, qk_done, prob_ready, pv_done, floor_spread, den_ready, den_step,
             h_ready) = semaphores(
                k, inner, "spread bounded exped masked qk_done prob_ready pv_done floor_spread den_ready "
                "den_step h_ready")
            block = inner.enter_context(nc.Block())
            UNITS = 2 * H
            STEPS = UNITS * NT

            def place(s):
                u = s // NT
                back, h = u % 2, u // 2
                j = NT - 1 - s % NT if back else s % NT
                return u, back, h, j, (slice(0, (j + 1) * P) if back else slice(j * P, T))

            @block.tensor
            def _(pe):
                def weigh(s):
                    u, back, h, j, ts = place(s)
                    pe.wait_ge(prob_ready, s + 1)
                    if s % NT == 0 and u >= 2:
                        pe.wait_ge(h_ready, u - 1)
                    pr = prob[:, s % 2, ts]
                    pe.matmul(k.ps[:, 4 + u % 2, ts], v_tok[:, j, h * P:(h + 1) * P], pr, start=(s % NT == 0),
                              stop=(s % NT == NT - 1))
                    pe.matmul(k.ps[:, 6 + u % 2, ts], k.const("ones"), pr, start=(s % NT == 0),
                              stop=(s % NT == NT - 1)).then_inc(pv_done, 1)
                    if s % NT == NT - 1:
                        pe.wait_ge(bounded, s + 1)
                        pe.matmul(bank(k.ps, u % 2), k.const("ident", H)[:, h:h + 1].broadcast_to([H, P]),
                                  m_[:, back, :], start=True, stop=True).then_inc(floor_spread, 1)

                for s in range(STEPS):
                    u, back, h, j, ts = place(s)
                    if s % NT == 0:
                        if u >= 2:
                            pe.wait_ge(h_ready, u - 1)
                        pe.matmul(bank(k.ps, u % 2), k.const("ident", H)[:, h:h + 1].broadcast_to([H, P]),
                                  M_[:, back, :], start=True, stop=True).then_inc(spread, 1)
                    if s >= 2:
                        pe.wait_ge(prob_ready, s - 1)
                    pe.matmul(k.ps[:, 2 + s % 2, ts], qk[:, H + h, j * P:(j + 1) * P], qk[:, h, ts],
                              start=True, stop=True).then_inc(qk_done, 1)
                    if s:
                        weigh(s - 1)
                weigh(STEPS - 1)

            @block.gpsimd
            def _(pool):
                for s in range(STEPS):
                    u, back, h, j, ts = place(s)
                    pool.wait_ge(exped, s + 1)
                    d = dist[:, s % 2, j * P:(j + 1) * P]
                    pool.tensor_tensor(d, d, k.const("ge" if back else "le"), ALU.mult).then_inc(masked, 1)

            @block.scalar
            def _(act):
                def absolute(u):
                    act.wait_ge(pv_done, NT * (u + 1))
                    act.activation(den[:, u % 2, :], bank(k.ps, 6 + u % 2), ACT.Abs).then_inc(den_ready, 1)
                for s in range(STEPS):
                    u, back, h, j, ts = place(s)
                    act.wait_ge(bounded, s + 1)
                    act.activation(dist[:, s % 2, ts], dist[:, s % 2, ts], ACT.Exp, scale=-1.0).then_inc(exped, 1)
                    if s % NT == 2 and u:
                        absolute(u - 1)
                absolute(UNITS - 1)

            @block.vector
            def _(dve):
                def weight(s):
                    u, back, h, j, ts = place(s)
                    dve.wait_ge(masked, s + 1)
                    dve.wait_ge(qk_done, s + 1)
                    if s >= 2:
                        dve.wait_ge(pv_done, s - 1)
                    dve.tensor_tensor(prob[:, s % 2, ts], dist[:, s % 2, ts], k.ps[:, 2 + s % 2, ts], ALU.mult)\
                        .then_inc(prob_ready, 1)

                def finish(u):
                    back, h, d = u % 2, u // 2, den[:, u % 2, :]
                    dve.wait_ge(den_ready, u + 1)
                    dve.wait_ge(floor_spread, u + 1)
                    dve.tensor_tensor(d, d, bank(k.ps, u % 2), ALU.max).then_inc(den_step, 1)
                    dve.wait_ge(den_step, 3 * u + 1)
                    dve.reciprocal(d, d).then_inc(den_step, 1)
                    dve.wait_ge(den_step, 3 * u + 2)
                    if back:
                        dve.tensor_tensor(d, d, bank(k.ps, 4 + u % 2), ALU.mult).then_inc(den_step, 1)
                        dve.wait_ge(den_step, 3 * u + 3)
                        dve.tensor_tensor(y[:, h, :], y[:, h, :], d, ALU.add).then_inc(h_ready, 1)
                    else:
                        dve.tensor_tensor(y[:, h, :], d, bank(k.ps, 4 + u % 2), ALU.mult).then_inc(h_ready, 1)
                        dve.wait_ge(h_ready, u + 1)
                        dve.tensor_copy(d[:, 0:1], y[:, h, 0:1]).then_inc(den_step, 1)

                for s in range(STEPS):
                    u, back, h, j, ts = place(s)
                    dve.wait_ge(spread, u + 1)
                    if s >= 2:
                        dve.wait_ge(prob_ready, s - 1)
                    dve.tensor_scalar(dist[:, s % 2, ts], k.ps[:, u % 2, ts], g_col[:, j, back, h:h + 1], 0.0,
                                      ALU.subtract, ALU.max).then_inc(bounded, 1)
                    if s:
                        weight(s - 1)
                    if s % NT == 2 and u:
                        finish(u - 1)
                weight(STEPS - 1)
                finish(UNITS - 1)

        with ExitStack() as inner:
            mean_done, centred = semaphores(k, inner, "mean_done centred")
            block = inner.enter_context(nc.Block())

            @block.tensor
            def _(pe):
                for m in range(H):
                    pe.matmul(bank(k.ps, m), k.const("ones"), y[:, m, :], start=True, stop=True).then_inc(mean_done, 1)

            @block.vector
            def _(dve):
                for m in range(H):
                    dve.wait_ge(mean_done, m + 1)
                    dve.scalar_tensor_tensor(out=y[:, m, :], in0=bank(k.ps, m), scalar=-1.0 / P, in1=y[:, m, :],
                                             op0=ALU.mult, op1=ALU.add).then_inc(centred, 1)
        head_norm(k, y, H, P, f"a_norm{n}", k.const("eps")[:, 0:1], o_gate[:, :, :])


def attention(k, y, heads, maps, q_of, k_of, v_of, width, bias_of=None, neg_lambda=None, prepare=None):
    nc = k.nc
    with ExitStack() as ctx:
        sb = lambda name, shape: k.sbuf(ctx, name, shape)
        RS, RE = 3, 4
        logits = sb("logits", [P, RS, T]) if bias_of else None
        expd = sb("exps", [P, RE, T])
        pt = sb("prob_t", [P, 2, NT, T])
        stat = sb("statistics", [P, 4, 8])
        (scores_done, fronts, exps, norms, turned, taken, pv_done, y_used, bias_ready) = semaphores(
            k, ctx, "scores_done fronts exps norms turned taken pv_done y_used bias_ready")
        block = ctx.enter_context(nc.Block())
        N = heads * NT * maps
        NPC = 2 if maps == 1 else 5

        def place(n):
            m = n // maps
            return m // NT, m % NT, n % maps

        @block.tensor
        def _(pe):
            def turn(m):
                pe.wait_ge(norms, NPC * (m + 1))
                if m >= 2:
                    pe.wait_ge(taken, m - 1)
                for j in range(NT):
                    mm = pe.transpose(k.ps[:, 3 + m % 2, j * P:(j + 1) * P],
                                      expd[:, (maps * m) % RE, j * P:(j + 1) * P], k.const("ident"))
                mm.then_inc(turned, 1)

            def weigh(h):
                pe.wait_ge(taken, NT * (h + 1))
                if h >= 2:
                    pe.wait_ge(y_used, h - 1)
                r0 = 0 if width == P else 64 * (h % 2)
                for j in range(NT):
                    mm = pe.matmul(k.ps[r0:r0 + width, 5 + h % 2, :], v_of(h, j), pt[:, h % 2, j, :],
                                   start=(j == 0), stop=(j == NT - 1))
                mm.then_inc(pv_done, 1)

            for n in range(N + 4):
                if n < N:
                    h, i, c = place(n)
                    if n >= RS:
                        pe.wait_ge(exps if bias_of is None else fronts,
                                   n - RS + 1 if bias_of is None else 2 * (n - RS) + 2)
                    pe.matmul(bank(k.ps, n % RS), q_of(h, c)[:, i * P:(i + 1) * P], k_of(h, c),
                              start=True, stop=True).then_inc(scores_done, 1)
                if 0 <= n - 2 < N and (n - 1) % maps == 0:
                    turn((n - 2) // maps)
                if 0 <= n - 3 < N and (n - 2) % (NT * maps) == 0:
                    weigh((n - 3) // (NT * maps))

        if prepare is not None:
            @block.gpsimd
            def _(pool):
                for h in range(heads):
                    if h >= 2:
                        pool.wait_ge(fronts, 2 * NT * maps * (h - 1))
                    prepare(pool, h).then_inc(bias_ready, 1)

        @block.scalar
        def _(act):
            def take(m):
                h, i = m // NT, m % NT
                act.wait_ge(turned, m + 1)
                if i == 0 and h >= 2:
                    act.wait_ge(pv_done, h - 1)
                act.activation(pt[:, h % 2, :, i * P:(i + 1) * P],
                               bank(k.ps, 3 + m % 2).rearrange("p (j t) -> p j t", j=NT), ACT.Copy).then_inc(taken, 1)

            for n in range(N + 2):
                if n < N:
                    act.wait_ge(fronts, 2 * n + 2)
                    if n >= RE:
                        act.wait_ge(turned, (n - RE) // maps + 1)
                    act.activation(expd[:, n % RE, :], bank(k.ps, n % RS) if bias_of is None else logits[:, n % RS, :],
                                   ACT.Exp, bias=stat[:, 1, n % 8:n % 8 + 1],
                                   accum_out=stat[:, 2, n % 8:n % 8 + 1]).then_inc(exps, 1)
                if 0 <= n - 2 < N and (n - 1) % maps == 0:
                    take((n - 2) // maps)

        @block.vector
        def _(dve):
            def normalise(n):
                h, i, c = place(n)
                m = n // maps
                s = slice(n % 8, n % 8 + 1)
                e = expd[:, n % RE, :]
                base = NPC * m + (2 if c else 0)
                dve.wait_ge(exps, n + 1)
                dve.reciprocal(stat[:, 3, s], stat[:, 2, s]).then_inc(norms, 1)
                dve.wait_ge(norms, base + 1)
                if c == 0:
                    dve.tensor_scalar(e, e, stat[:, 3, s], None, ALU.mult).then_inc(norms, 1)
                    return
                dve.tensor_scalar(stat[:, 3, s], stat[:, 3, s], neg_lambda, None, ALU.mult).then_inc(norms, 1)
                dve.wait_ge(norms, base + 2)
                first = expd[:, (n - 1) % RE, :]
                dve.scalar_tensor_tensor(out=first, in0=e, scalar=stat[:, 3, s], in1=first, op0=ALU.mult,
                                         op1=ALU.add).then_inc(norms, 1)

            def output(h):
                dve.wait_ge(pv_done, h + 1)
                if width == P:
                    dve.tensor_copy(y[:, h, :], bank(k.ps, 5 + h % 2)).then_inc(y_used, 1)
                else:
                    r = slice(64 * (h % 2), 64 * (h % 2) + 64)
                    dve.tensor_copy(y[r, h // 2, :], k.ps[r, 5 + h % 2, :]).then_inc(y_used, 1)

            for n in range(N + 5):
                if n < N:
                    h, i, c = place(n)
                    s = slice(n % 8, n % 8 + 1)
                    dve.wait_ge(scores_done, n + 1)
                    if bias_of is None:
                        dve.tensor_reduce(stat[:, 0, s], bank(k.ps, n % RS), AX.X, ALU.max).then_inc(fronts, 1)
                    else:
                        if prepare is not None:
                            dve.wait_ge(bias_ready, h + 1)
                        if n >= RS:
                            dve.wait_ge(exps, n - RS + 1)
                        dve.tensor_tensor_reduce(out=logits[:, n % RS, :], in0=bank(k.ps, n % RS), in1=bias_of(h, i),
                                                 scale=1.0, scalar=-3.0e38, op0=ALU.add, op1=ALU.max,
                                                 accum_out=stat[:, 0, s]).then_inc(fronts, 1)
                    dve.wait_ge(fronts, 2 * n + 1)
                    dve.tensor_scalar(stat[:, 1, s], stat[:, 0, s], -1.0, None, ALU.mult).then_inc(fronts, 1)
                if 0 <= n - 1 < N:
                    normalise(n - 1)
                if 0 <= n - 4 < N and (n - 3) % (NT * maps) == 0:
                    output((n - 4) // (NT * maps))


def gqa_branch(k, n, y):
    nc = k.nc
    with ExitStack() as ctx:
        sb = lambda name, shape: k.sbuf(ctx, name, shape)
        qk = sb("qk", [P, 5, T])
        k2 = sb("keys_twice", [P, 2, T])
        v_tok = sb("v_tok", [P, NT, P])
        project(k, [(k.dram[f"w_b_q{n}"], k.xn, qk[:, 0:4, :], 1.0)])
        project(k, [(k.dram[f"w_b_k{n}"], k.xn, qk[:, 4:5, :], 1.0)])
        project_tokens(k, [(k.dram[f"w_b_v{n}"][0, :, :], v_tok)])
        with ExitStack() as inner:
            sq = k.sbuf(inner, "squares", [P, 2, T])
            rt = k.sbuf(inner, "rstd", [P, 2, T])
            squared, summed, root, inverse, normed, rotated, roped, doubled, keys_ready = semaphores(
                k, inner, "squared summed root inverse normed rotated roped doubled keys_ready")
            block = inner.enter_context(nc.Block())

            @block.scalar
            def _(act):
                for m in range(5):
                    if m >= 2:
                        act.wait_ge(roped, 3 * (m - 1))
                    act.activation(sq[:, m % 2, :], qk[:, m, :], ACT.Square).then_inc(squared, 1)
                    act.wait_ge(summed, m + 1)
                    key = m == 4
                    act.activation(rt[:, m % 2, :], bank(k.ps, m % 2), ACT.Sqrt,
                                   bias=k.const("eps")[:, 0:1] if key else k.const("eps")[:, 3:4],
                                   scale=1.0 / 64 if key else 1.0).then_inc(root, 1)
                for g in range(2):
                    act.wait_ge(doubled, g + 1)
                    act.activation(k2[:, g, :], bank(k.ps, 4 + g), ACT.Copy).then_inc(keys_ready, 1)

            @block.tensor
            def _(pe):
                for m in range(5):
                    pe.wait_ge(squared, m + 1)
                    pe.matmul(bank(k.ps, m % 2), k.const("pair"), sq[:, m % 2, :], start=True, stop=True)\
                        .then_inc(summed, 1)
                    pe.wait_ge(normed, m + 1)
                    pe.matmul(bank(k.ps, 2 + m % 2), k.const("turn"), qk[:, m, :], start=True, stop=True)\
                        .then_inc(rotated, 1)
                pe.wait_ge(roped, 15)
                for g in range(2):
                    pe.matmul(bank(k.ps, 4 + g), k.const("dup")[:, g * P:(g + 1) * P], qk[:, 4, :],
                              start=True, stop=True).then_inc(doubled, 1)

            @block.vector
            def _(dve):
                for m in range(5):
                    r, s = rt[:, m % 2, :], sq[:, m % 2, :]
                    dve.wait_ge(root, m + 1)
                    dve.reciprocal(r, r).then_inc(inverse, 1)
                    dve.wait_ge(inverse, m + 1)
                    dve.scalar_tensor_tensor(out=qk[:, m, :], in0=qk[:, m, :],
                                             scalar=k.col(f"b_knorm{n}" if m == 4 else f"b_qnorm{n}"),
                                             in1=r, op0=ALU.mult, op1=ALU.mult).then_inc(normed, 1)
                    dve.wait_ge(rotated, m + 1)
                    dve.tensor_tensor(s, bank(k.ps, 2 + m % 2), k.const("sin"), ALU.mult).then_inc(roped, 1)
                    dve.tensor_tensor(r, qk[:, m, :], k.const("cos"), ALU.mult).then_inc(roped, 1)
                    dve.wait_ge(roped, 3 * m + 2)
                    dve.tensor_tensor(qk[:, m, :], r, s, ALU.add).then_inc(roped, 1)

        half = lambda h: slice(64 * (h % 2), 64 * (h % 2) + 64)
        attention(k, y, B_HEADS, 1, lambda h, c: qk[half(h), h // 2, :],
                  lambda h, c: k2[half(h), h // 4, :], lambda h, j: v_tok[:, j, 64 * (h // 4):64 * (h // 4) + 64], 64)


def natten_branch(k, n, y):
    nc = k.nc
    with ExitStack() as ctx:
        sb = lambda name, shape: k.sbuf(ctx, name, shape)
        qk = sb("qk", [P, 8, T])
        v_tok = sb("v_tok", [P, NT, 512])
        table = sb("bias_table", [P, C_HEADS, 16, GRID_W])
        project(k, [(k.dram[f"w_c_qk{n}"], k.xn, qk[:, :, :], 1.0)])
        project_tokens(k, [(k.dram[f"w_c_v{n}"][0, :, :], v_tok)])
        with ExitStack() as inner:
            rpb = k.sbuf(inner, "rpb", [P, P])
            rpb_in, shifted, table_ready, scaled = semaphores(k, inner, "rpb_in shifted table_ready scaled")
            block = inner.enter_context(nc.Block())
            band = k.const("band", 64)

            @block.sync
            def _(sp):
                sp.dma_start(rpb[:, :], k.dram[f"rpb{n}"]).then_inc(rpb_in, 16)

            @block.scalar
            def _(act):
                act.activation(qk[:, 0:4, :], qk[:, 0:4, :], ACT.Copy, scale=0.125).then_inc(scaled, 1)

            @block.tensor
            def _(pe):
                pe.wait_ge(rpb_in, 16)
                for kc in range(GRID_W):
                    g = kc // 4
                    if kc % 4 == 0 and g >= 2:
                        pe.wait_ge(table_ready, g - 1)
                    mm = pe.matmul(k.ps[:, g % 2, (kc % 4) * P:(kc % 4 + 1) * P], band[:, 63 - kc:191 - kc],
                                   rpb[0:64, :], start=True, stop=True)
                    if kc % 4 == 3:
                        mm.then_inc(shifted, 1)

            @block.vector
            def _(dve):
                flat_table = table[:, :, :, :].rearrange("p h j c -> p c (h j)")
                for g in range(GRID_W // 4):
                    dve.wait_ge(shifted, g + 1)
                    cs = slice(4 * g, 4 * g + 4)
                    dve.tensor_tensor(flat_table[:, cs, :], bank(k.ps, g % 2).rearrange("p (c m) -> p c m", c=4),
                                      k.const("window")[:, cs, None].broadcast_to([P, 4, P]), ALU.add)\
                        .then_inc(table_ready, 1)

        half = lambda h: slice(64 * (h % 2), 64 * (h % 2) + 64)
        attention(k, y, C_HEADS, 1, lambda h, c: qk[half(h), h // 2, :], lambda h, c: qk[half(h), 4 + h // 2, :],
                  lambda h, j: v_tok[:, j, 64 * h:64 * h + 64], 64,
                  bias_of=lambda h, i: table[:, h, 7 - 2 * i:15 - 2 * i, :].rearrange("p j c -> p (j c)"))


def diff_branch(k, n, y):
    nc = k.nc
    with ExitStack() as ctx:
        sb = lambda name, shape: k.sbuf(ctx, name, shape)
        qk = sb("qk", [P, 8, T])
        v_tok = sb("v_tok", [P, NT, 512])
        lam = sb("lambda", [P, 8])
        slope = sb("distance_bias", [P, 2, 896])
        project(k, [(k.dram[f"w_d_qk{n}"], k.xn, qk[:, :, :], 1.0)])
        project_tokens(k, [(k.dram[f"w_d_v{n}"][0, :, :], v_tok)])
        with ExitStack() as inner:
            scaled, products, dots, dots_exp, lam_ready = semaphores(
                k, inner, "scaled products dots dots_exp lam_ready")
            block = inner.enter_context(nc.Block())
            a, _ = k.col_at[f"lambda{n}"]

            @block.scalar
            def _(act):
                act.activation(qk[:, 0:4, :], qk[:, 0:4, :], ACT.Copy, scale=0.125).then_inc(scaled, 1)
                act.wait_ge(dots, 1)
                act.activation(lam[:, 2:4], k.ps[:, 0, 0:2], ACT.Exp).then_inc(dots_exp, 1)

            @block.tensor
            def _(pe):
                pe.wait_ge(products, 1)
                pe.matmul(k.ps[:, 0, 0:2], k.const("ones"), lam[:, 0:2], start=True, stop=True).then_inc(dots, 1)

            @block.vector
            def _(dve):
                dve.tensor_tensor(lam[:, 0:2], k.cols[:, a:a + 2], k.cols[:, a + 2:a + 4], ALU.mult)\
                    .then_inc(products, 1)
                dve.wait_ge(dots_exp, 1)
                dve.tensor_tensor(lam[:, 4:5], lam[:, 3:4], lam[:, 2:3], ALU.subtract).then_inc(lam_ready, 1)
                dve.wait_ge(lam_ready, 1)
                dve.tensor_scalar(lam[:, 5:6], lam[:, 4:5], -LAMBDA_INIT[n], None, ALU.add).then_inc(lam_ready, 1)

        def prepare(pool, h):
            return pool.tensor_scalar(slope[:, h % 2, :], k.const("distance"), -(2.0 ** (-8.0 * (h + 1) / D_HEADS)),
                                      None, ALU.mult)

        half = lambda h: slice(64 * (h % 2), 64 * (h % 2) + 64)
        attention(k, y, D_HEADS, 2, lambda h, c: qk[half(h), 2 * c + h // 2, :],
                  lambda h, c: qk[half(h), 4 + 2 * c + h // 2, :], lambda h, j: v_tok[:, j, P * h:P * h + P], P,
                  bias_of=lambda h, i: slope[:, h % 2, 384 - P * i:896 - P * i],
                  neg_lambda=lam[:, 5:6], prepare=prepare)
        head_norm(k, y, D_HEADS, P, f"d_subln{n}", k.const("eps")[:, 4 + n:5 + n], None,
                  1.0 - LAMBDA_INIT[n])


def merge_and_feed(k, branches, w_out, norm, w_ffn, w_down):
    with ExitStack() as ctx:
        mixed = k.sbuf(ctx, "mixed", [P, KD, T])
        for b, (w, src) in enumerate(branches):
            gated_product(k, k.dram[w], k.xn, src, ACT.Sigmoid, mixed, b > 0)
        project(k, [(k.dram[w_out], mixed, k.x, "add")])
    rms_norm(k, k.x, k.xn, norm)
    with ExitStack() as ctx:
        hidden = k.sbuf(ctx, "hidden", [P, KF, T])
        gated_product(k, k.dram[w_ffn], k.xn, k.xn, ACT.Silu, hidden, False)
        project(k, [(k.dram[w_down], hidden, k.x, "add")])


def hybrid_program(nc, dram, const_at, n_const, col_at, n_col):
    k = Kernel(nc, dram, const_at, col_at)
    with ExitStack() as ctx:
        sb = lambda name, shape: ctx.enter_context(nc.sbuf_tensor(name, shape, F32))
        k.x = sb("x", [P, KD, T])
        k.xn = sb("xn", [P, KD, T])
        k.wbuf = sb("weights", [P, 2, 4096])
        k.consts = sb("consts", [P, n_const])
        k.cols = sb("cols", [P, n_col])
        y = sb("y", [P, 16, T])
        k.ps = ctx.enter_context(nc.psum_tensor("ps", [P, 8, T], F32))
        load_constants(k, dram["cols"])
        load_x(k)
        rms_norm(k, k.x, k.xn, "norm1")
        ssm_branch(k, y)
        rwkv_branch(k, y[:, 8:12, :])
        hgrn_branch(k, y[:, 12:16, :])
        merge_and_feed(k, [("w_mix_ssm", y[:, 0:8, :]), ("w_mix_rwkv", y[:, 8:12, :]), ("w_mix_hgrn", y[:, 12:16, :])],
                       "w_out", "norm2", "w_ffn", "w_down")
        rms_norm(k, k.x, k.x, "norm3")
        for n in range(LAYERS):
            rms_norm(k, k.x, k.xn, f"norm1_{n}")
            mlstm_branch(k, n, y[:, 0:4, :])
            gqa_branch(k, n, y[:, 4:8, :])
            natten_branch(k, n, y[:, 8:12, :])
            diff_branch(k, n, y[:, 12:16, :])
            merge_and_feed(k, [(f"w_mix_{name}{n}", y[:, 4 * b:4 * b + 4, :]) for b, name in enumerate("abcd")],
                           f"w_out{n}", f"norm2_{n}", f"w_ffn{n}", f"w_down{n}")
        rms_norm(k, k.x, k.xn, "final")
        store_x(k, k.xn)


def kernel(**inputs):
    import concourse.bacc as bacc
    from concourse.bass_utils import run_bass_kernel_spmd

    x = {name: np.asarray(a) for name, a in inputs.items()}
    weights, cols = first_layout(x)
    more_weights, more_cols = second_layout(x)
    weights, cols, consts = weights | more_weights, cols | more_cols, constants()
    const_at, n_const = places({n: v.shape[1] for n, v in consts.items()})
    col_at, n_col = places({n: v.shape[1] for n, v in cols.items()})
    given = weights | {
        "x": x["x"].reshape(T, D),
        "consts": np.concatenate(list(consts.values()), 1),
        "cols": np.concatenate(list(cols.values()), 1),
    }
    nc = bacc.Bacc("TRN2", target_bir_lowering=False, num_devices=1, dynamic_dma_scratch_size=1024)
    arrays, dram = {}, {}
    for name, a in given.items():
        a = np.ascontiguousarray(a)
        arrays[f"in_{name}_dram"] = a
        dram[name] = nc.dram_tensor(f"in_{name}_dram", a.shape, mybir.dt.from_np(a.dtype), kind="ExternalInput").ap()
    dram["out"] = nc.dram_tensor("out_0_dram", (T, D), F32, kind="ExternalOutput").ap()
    hybrid_program(nc, dram, const_at, n_const, col_at, n_col)
    r = run_bass_kernel_spmd(nc, [arrays], core_ids=[0])
    return r.results[0]["out_0_dram"].reshape(1, T, D)
```

```python
from contextlib import ExitStack

import concourse.bass as bass
import numpy as np
from concourse import mybir

F32 = mybir.dt.float32
F32R = mybir.dt.float32r
ALU = mybir.AluOpType
ACT = mybir.ActivationFunctionType
AX = mybir.AxisListType

P = 128
T = 512
NT = T // P
D = 1024
KD = D // P

SSM_HEADS, SSM_P, SSM_CONV = 16, 64, 5
SSM_INNER, SSM_XBC = 1024, 1536
RWKV_W = 512
RWKV_COLS = 3 * RWKV_W + 256
RWKV_DECAY = 0.6065306597
HGRN_W = 512
D_FF = 2816
KF = D_FF // P
NORM_EPS = 1e-6
RWKV_LN_EPS = 64e-5
CH = 32
NC = T // CH
LAYERS = 2
GRID_W, WIN_R, WIN_C = 64, 8, 16
A_HEADS, A_CONV, A_WIDTH = 4, 3, 512
B_HEADS, C_HEADS, D_HEADS = 8, 8, 4
LAMBDA_INIT = [0.8 - 0.6 * float(np.exp(-0.3 * n)) for n in range(LAYERS)]


def constants():
    p = np.arange(P)
    s, t = p[:, None], p[None, :]
    block = (s // CH) == (t // CH)
    tok = np.arange(T)
    both = {
        "ident": np.eye(P),
        "ones": np.ones((P, P)),
        "pair": (s // 64) == (t // 64),
        "le": s <= t,
        "ge": s >= t,
        "eps": np.broadcast_to(np.array([[NORM_EPS, RWKV_LN_EPS, 1e-12, 64 * NORM_EPS]
                                        + [NORM_EPS / (1 - LAMBDA_INIT[n]) ** 2 for n in range(LAYERS)]]),
                               (P, 4 + LAYERS)),
    }
    first = {
        "eye64": s % 64 == t[:, :64],
        "c_le": block & (s <= t),
        "c_lt": block & (s < t),
        "c_ge": block & (s >= t),
        "c_gt": block & (s > t),
        "reset": np.broadcast_to(np.stack([tok % CH != 0, tok % CH != CH - 1]).reshape(1, -1), (P, 2 * T)),
    }
    c = {}
    d = p % 64
    inv = (10000.0 ** (-np.arange(16, dtype=np.float32) / 16)).astype(np.float32)
    pos = np.where((d < 32)[:, None], tok[None] // GRID_W, tok[None] % GRID_W).astype(np.float32)
    ang = (pos * inv[d % 16][:, None]).astype(np.float32)
    c["cos"], c["sin"] = np.cos(ang), np.sin(ang)
    turn = np.zeros((P, P))
    low = (p % 32) < 16
    turn[(p + 16)[low], p[low]] = -1.0
    turn[(p - 16)[~low], p[~low]] = 1.0
    c["turn"] = turn
    c["dup"] = np.concatenate([(s == t % 64), (s == 64 + t % 64)], 1)
    c["distance"] = np.abs(s - (np.arange(896)[None] - 384))
    band = np.zeros((P, 191))
    for a in range(2):
        for o in range(31):
            band[32 * a + o, 64 * a + 78 - o] = 1.0
    c["band"] = band
    col = p % 64
    start = np.clip(col - WIN_C // 2, 0, GRID_W - WIN_C)
    kc = np.arange(64)[None]
    c["window"] = np.where((kc >= start[:, None]) & (kc < start[:, None] + WIN_C), 0.0, -1e30)
    return [{n: np.ascontiguousarray(np.broadcast_to(v, (P, v.shape[1])), dtype=np.float32)
             for n, v in kind.items()} for kind in (both, first, c)]


def places(widths, at=0):
    out = {}
    for name, w in widths.items():
        out[name] = (at, at + w)
        at += w
    return out, at


def grouped(w, width=P):
    k, n = w.shape
    return np.ascontiguousarray(
        w.reshape(k // P, P, n // width, width).transpose(2, 1, 0, 3)).reshape(n // width, P, -1)


def side_by_side(a, b):
    return np.concatenate([grouped(a), grouped(b)], axis=2)


def padded(w):
    return grouped(np.concatenate([w, np.zeros((w.shape[0], P - w.shape[1]), w.dtype)], 1))


def columns(v):
    v = np.asarray(v).reshape(-1, P)
    return v.T


def short(v):
    v = np.asarray(v).reshape(-1)
    out = np.zeros((P, 1), v.dtype)
    out[: len(v), 0] = v
    return out


def first_layout(x):
    w = x["w_in"][0]
    o_xbc = SSM_INNER
    o_dt = o_xbc + SSM_XBC
    o_rwkv = o_dt + 2 * SSM_HEADS
    o_hgrn = o_rwkv + RWKV_COLS
    o_gate = o_hgrn + 5 * HGRN_W
    gate = w[:, o_gate:]
    weights = {
        "w_z": grouped(w[:, :o_xbc]),
        "w_xbc": grouped(w[:, o_xbc:o_dt]),
        "w_dt": np.concatenate([padded(w[:, o_dt + r * SSM_HEADS:o_dt + (r + 1) * SSM_HEADS]) for r in range(2)], 0),
        "w_rwkv": grouped(w[:, o_rwkv:o_hgrn]),
        "w_hgrn": grouped(w[:, o_hgrn:o_gate]),
        "w_mix_ssm": side_by_side(gate[:, :D], x["w_branch_ssm"][0]),
        "w_mix_rwkv": side_by_side(gate[:, D:2 * D], x["w_branch_rwkv"][0]),
        "w_mix_hgrn": side_by_side(gate[:, 2 * D:], x["w_branch_hgrn"][0]),
        "w_out": grouped(x["w_out"][0]),
        "w_ffn": side_by_side(x["ffn_w_in"][0][:, :D_FF], x["ffn_w_in"][0][:, D_FF:]),
        "w_down": grouped(x["ffn_w_down"][0]),
        "w_lora": np.concatenate([
            np.concatenate([x["rwkv_w_up"][0, 0], x["rwkv_w_up"][0, 1]], 1),
            np.concatenate([x["rwkv_a_up"][0], np.zeros_like(x["rwkv_a_up"][0])], 1)], 0),
        "w_g_up": x["rwkv_g_up"][0],
    }
    heads = lambda v: np.repeat(np.asarray(v).reshape(-1), 64)
    cols = {
        "norm1": columns(x["norm1_w"][0]),
        "conv_w": np.concatenate([columns(x["ssm_conv_w"][0, j, 0]) for j in range(SSM_CONV)], 1),
        "conv_b": columns(x["ssm_conv_b"][0]),
        "dt_bias": np.concatenate([short(x["ssm_dt_bias"][0, r]) for r in range(2)], 1),
        "a_log": np.concatenate([short(x["ssm_a_log"][0, r]) for r in range(2)], 1),
        "d_skip": columns(heads(x["ssm_d"][0])),
        "ssm_norm": columns(x["ssm_norm_w"][0]),
        "mu": np.concatenate([columns(x["rwkv_mu"][0, r]) for r in range(2)], 1),
        "w0": np.concatenate([columns(x["rwkv_w0"][0, r]) for r in range(2)], 1),
        "a0": columns(x["rwkv_a0"][0]),
        "k_k": columns(x["rwkv_k_k"][0]),
        "k_a": columns(x["rwkv_k_a"][0]),
        "r_k": columns(x["rwkv_r_k"][0]),
        "ln_w": columns(x["rwkv_ln_w"][0]),
        "ln_b": columns(x["rwkv_ln_b"][0]),
        "lb": columns(x["hgrn_lb_logits"][0]),
        "hgrn_norm": columns(x["hgrn_norm_w"][0]),
        "norm2": columns(x["norm2_w"][0]),
        "norm3": columns(x["final_norm_w"]),
    }
    return weights, cols


def second_layout(x):
    weights, cols = {}, {}
    widths = {"aq": 512, "ak": 512, "av": 512, "ao": 512, "ag": 16, "bq": 512, "bk": 128, "bv": 128,
              "cq": 512, "ck": 512, "cv": 512, "dq": 512, "dk": 512, "dv": 512, "gate": 4 * D}
    at, _ = places(widths)
    for n in range(LAYERS):
        w = x["w_in_2"][n]
        part = lambda *names: np.concatenate([w[:, at[m][0]:at[m][1]] for m in names], 1)
        weights |= {
            f"w_a_qk{n}": grouped(part("aq", "ak")),
            f"w_a_o{n}": grouped(part("ao")),
            f"w_a_gates{n}": padded(part("ag")),
            f"w_a_v{n}": grouped(part("av"), 512),
            f"w_b_q{n}": grouped(part("bq")),
            f"w_b_k{n}": grouped(part("bk")),
            f"w_b_v{n}": grouped(part("bv"), P),
            f"w_c_qk{n}": grouped(part("cq", "ck")),
            f"w_c_v{n}": grouped(part("cv"), 512),
            f"w_d_qk{n}": grouped(part("dq", "dk")),
            f"w_d_v{n}": grouped(part("dv"), 512),
            f"w_out{n}": grouped(x["w_out_2"][n]),
            f"w_ffn{n}": side_by_side(x["w_ffn_gate_2"][n], x["w_ffn_up_2"][n]),
            f"w_down{n}": grouped(x["w_ffn_down_2"][n]),
        }
        for b, name in enumerate("abcd"):
            g = part("gate")[:, b * D:(b + 1) * D]
            weights[f"w_mix_{name}{n}"] = side_by_side(g, x[f"w_up_{name}_2"][n])
        rpb = np.zeros((P, C_HEADS, 16), np.float32)
        for a in range(2):
            rpb[32 * a:32 * a + 31, :, a:a + 15] = np.asarray(x["c_rpb_2"][n]).transpose(2, 0, 1)
        weights[f"rpb{n}"] = rpb.reshape(P, -1)
        twice = lambda v: np.concatenate([short(v)[:64], short(v)[:64]], 0)
        cols |= {
            f"norm1_{n}": columns(x["norm1_g_2"][n]),
            f"a_conv{n}": np.concatenate([columns(x["a_conv_w_2"][n, j]) for j in range(A_CONV)], 1),
            f"a_bias{n}": short(x["a_gate_bias_2"][n]),
            f"a_norm{n}": columns(x["a_norm_g_2"][n]),
            f"b_qnorm{n}": twice(x["b_qnorm_g_2"][n]),
            f"b_knorm{n}": twice(x["b_knorm_g_2"][n]),
            f"lambda{n}": np.concatenate([short(x[f"d_lambda_{m}_2"][n]) for m in ("q1", "q2", "k1", "k2")], 1),
            f"d_subln{n}": np.repeat(columns(x["d_subln_g_2"][n]), D_HEADS, 1),
            f"norm2_{n}": columns(x["norm2_g_2"][n]),
        }
    cols["final"] = columns(x["final_g_2"])
    return weights, cols


class Kernel:

    def __init__(self, nc, dram, const_at, col_at):
        self.nc, self.dram, self.const_at, self.col_at = nc, dram, const_at, col_at
        self.made = 0
        self.free = sorted(nc.free_semaphores)

    def sbuf(self, ctx, name, shape):
        self.made += 1
        return ctx.enter_context(self.nc.sbuf_tensor(f"{name}_{self.made}", shape, F32))

    def both_kinds(self, ctx, name, shape):
        at = (self.nc.sbuf_base + 31) // 32 * 32
        whole = self.sbuf(ctx, name, shape)
        rounded = self.nc.alloc_sbuf_tensor_at(f"{name}_r_{self.made}", shape, F32R, offset=at)
        return whole, rounded

    def const(self, name, rows=P):
        a, b = self.const_at[name]
        return self.consts[0:rows, a:b]

    def col(self, name, j=0, rows=P):
        a, _ = self.col_at[name]
        return self.cols[0:rows, a + j:a + j + 1]


def semaphores(k, ctx, names):
    sems = [k.nc.alloc_semaphore(f"{n}_{k.nc.next_id()}", num=k.free.pop(0)) for n in names.split()]

    def give_back():
        for s in sems:
            k.nc.gpsimd.sem_clear(s)
            k.nc.release_semaphore(s)
            k.free.append(s.num)

    ctx.callback(give_back)
    return sems


def bank(ps, b):
    return ps[:, b, :]


def wide(ap, n):
    rows, m = ap.shape
    return ap[:, None, :].broadcast_to([rows, n, m])


def load_constants(k, col_array):
    nc = k.nc
    with ExitStack() as ctx:
        consts_in, cols_in = semaphores(k, ctx, "consts_in cols_in")
        block = ctx.enter_context(nc.Block())

        @block.sync
        def _(sp):
            sp.dma_start(k.consts[:, 0:k.dram["consts"].shape[1]], k.dram["consts"]).then_inc(consts_in, 16)
            sp.wait_ge(consts_in, 16)

        @block.scalar
        def _(act):
            act.dma_start(k.cols[:, 0:col_array.shape[1]], col_array).then_inc(cols_in, 16)
            act.wait_ge(cols_in, 16)


def load_x(k, more_consts=None):
    nc = k.nc
    with ExitStack() as ctx:
        rows = k.sbuf(ctx, "x_rows", [P, NT, D])
        x_in, turned, x_ready, more_in = semaphores(k, ctx, "x_in turned x_ready more_in")
        block = ctx.enter_context(nc.Block())

        @block.sync
        def _(sp):
            sp.dma_start(rows[:, :, :], k.dram["x"].rearrange("(j p) d -> p j d", p=P)).then_inc(x_in, 16)
            if more_consts:
                array, at = more_consts
                sp.dma_start(k.consts[:, at:at + array.shape[1]], array).then_inc(more_in, 16)
                sp.wait_ge(more_in, 16)

        @block.tensor
        def _(pe):
            pe.wait_ge(x_in, 16)
            for m in range(KD):
                if m >= 2:
                    pe.wait_ge(x_ready, m - 1)
                for j in range(NT):
                    mm = pe.transpose(k.ps[:, m % 2, j * P:(j + 1) * P], rows[:, j, m * P:(m + 1) * P],
                                      k.const("ident"))
                mm.then_inc(turned, 1)

        @block.scalar
        def _(act):
            for m in range(KD):
                act.wait_ge(turned, m + 1)
                act.activation(k.x[:, m, :], bank(k.ps, m % 2), ACT.Copy).then_inc(x_ready, 1)


def store_x(k, src):
    nc = k.nc
    with ExitStack() as ctx:
        rows = k.sbuf(ctx, "out_rows", [P, NT, D])
        turned, row_ready, stored = semaphores(k, ctx, "turned row_ready stored")
        block = ctx.enter_context(nc.Block())

        @block.tensor
        def _(pe):
            for n in range(2 * NT):
                j, half = n // 2, n % 2
                if n >= 2:
                    pe.wait_ge(row_ready, n - 1)
                for q in range(NT):
                    mm = pe.transpose(k.ps[:, n % 2, q * P:(q + 1) * P],
                                      src[:, NT * half + q, j * P:(j + 1) * P], k.const("ident"))
                mm.then_inc(turned, 1)

        @block.scalar
        def _(act):
            for n in range(2 * NT):
                act.wait_ge(turned, n + 1)
                act.activation(rows[:, n // 2, (n % 2) * T:(n % 2 + 1) * T], bank(k.ps, n % 2),
                               ACT.Copy).then_inc(row_ready, 1)

        @block.sync
        def _(sp):
            for j in range(NT):
                sp.wait_ge(row_ready, 2 * j + 2)
                sp.dma_start(k.dram["out"][j * P:(j + 1) * P, :], rows[:, j, :]).then_inc(stored, 16)
            sp.wait_ge(stored, 16 * NT)


def rms_norm(k, src, dst, weight, tiles=KD, name="n"):
    nc = k.nc
    with ExitStack() as ctx:
        sq = k.sbuf(ctx, "squares", [P, 3, T])
        rstd = k.sbuf(ctx, "rstd", [P, T])
        squared, summed, root, inverse, normed = semaphores(k, ctx, "squared summed root inverse normed")
        block = ctx.enter_context(nc.Block())

        @block.scalar
        def _(act):
            for m in range(tiles):
                if m >= 3:
                    act.wait_ge(summed, m - 2)
                act.activation(sq[:, m % 3, :], src[:, m, :], ACT.Square).then_inc(squared, 1)
            act.wait_ge(summed, tiles)
            act.activation(rstd[:, :], bank(k.ps, 0), ACT.Sqrt, bias=k.const("eps")[:, 0:1],
                           scale=1.0 / (tiles * P)).then_inc(root, 1)

        @block.tensor
        def _(pe):
            for m in range(tiles):
                pe.wait_ge(squared, m + 1)
                pe.matmul(bank(k.ps, 0), k.const("ones"), sq[:, m % 3, :], start=(m == 0),
                          stop=(m == tiles - 1)).then_inc(summed, 1)

        @block.vector
        def _(dve):
            dve.wait_ge(root, 1)
            dve.reciprocal(rstd[:, :], rstd[:, :]).then_inc(inverse, 1)
            dve.wait_ge(inverse, 1)
            for m in range(tiles):
                dve.scalar_tensor_tensor(out=dst[:, m, :], in0=src[:, m, :], scalar=k.col(weight, m),
                                         in1=rstd[:, :], op0=ALU.mult, op1=ALU.mult).then_inc(normed, 1)


AHEAD_RAW, AHEAD_PARTS = 4, 2


class Chunk:

    def __init__(self, name, row, at, width):
        self.name, self.row, self.at, self.width = name, row, at, width

    def key(self):
        return self.name, self.row, self.at, self.width


def step_chunks(name, row, runs):
    out, at = [], 0
    for run in runs:
        while run:
            n = min(run, KD)
            out.append(Chunk(name, row, at * P, n * P))
            at, run = at + n, run - n
    return out


def planned(name, rows, *runs, first=0):
    return [c for r in range(first, first + rows) for c in step_chunks(name, r, runs)]


class Stream:

    def __init__(self, k, plan):
        self.k, self.plan, self.stops = k, [], []
        for item in plan:
            if item is None:
                self.stops.append(len(self.plan))
            else:
                self.plan += item
        self.stops.append(len(self.plan))
        one = lambda name: k.nc.alloc_semaphore(name, num=k.free.pop(0))
        self.weights_in = [one(f"weights_in_{n}") for n in range(AHEAD_RAW)]
        self.hi_made, self.parts_ready, self.chunk_used = one("hi_made"), one("parts_ready"), one("chunk_used")
        self.at = self.loaded = self.split = 0

    def stop(self):
        return min(s for s in self.stops if s > self.at)

    def enter(self, jobs):
        at = self.at
        for job in jobs:
            job.g0 = at
            for p in range(job.per * job.bodies):
                assert self.plan[at].key() == job.chunk(p).key(), (self.plan[at].key(), job.chunk(p).key())
                at += 1
        return at

    def leave(self, end):
        stop = self.stop()
        self.at = end
        self.loaded = max(self.loaded, min(end + AHEAD_RAW, stop))
        self.split = max(self.split, min(end + AHEAD_PARTS, stop))

    def load(self, sp, g, chunk, i=0, job=None):
        w, per = self.k.dram[chunk.name], job.per if job else 0
        if job:
            row = sp.snap(i * job.body + chunk.row)
            w = w[bass.ds(row, 1), :, :].rearrange("a p n -> (a p) n")
        else:
            w = w[chunk.row, :, :]
        if job or g >= AHEAD_RAW:
            sp.wait_ge(self.parts_ready, i * per + (g - AHEAD_RAW + 1))
        slot = g % AHEAD_RAW
        sp.dma_start(self.k.raw[:, slot, 0:chunk.width], w[:, chunk.at:chunk.at + chunk.width])\
            .then_inc(self.weights_in[slot], 16)

    def make_hi(self, act, g, chunk, i=0, job=None):
        per, slot = job.per if job else 0, g % AHEAD_RAW
        act.wait_ge(self.weights_in[slot], i * (per // AHEAD_RAW * 16) + 16 * (g // AHEAD_RAW + 1))
        if job or g >= AHEAD_PARTS:
            act.wait_ge(self.chunk_used, i * per + (g - AHEAD_PARTS + 1))
        act.activation(self.k.w_hi[:, g % 2, 0:chunk.width], self.k.raw[:, slot, 0:chunk.width], ACT.Copy)\
            .then_inc(self.hi_made, 1)

    def make_lo(self, dve, g, chunk, i=0, job=None):
        per, slot = job.per if job else 0, g % AHEAD_RAW
        dve.wait_ge(self.hi_made, i * per + (g + 1))
        dve.tensor_tensor(self.k.w_lo[:, g % 2, 0:chunk.width], self.k.raw[:, slot, 0:chunk.width],
                          self.k.w_hi[:, g % 2, 0:chunk.width].bitcast(F32), ALU.subtract)\
            .then_inc(self.parts_ready, 1)

    def catch_up(self, do, eng, done, by):
        for g in range(done, min(self.at + by, self.stop())):
            do(eng, g, self.plan[g])

    def run_ahead(self, do, eng, job, i, last, p, by):
        if last or isinstance(i, int):
            g = job.g0 + job.per * (job.bodies - 1 if last else i) + p + by
            if g < self.stop():
                do(eng, g, self.plan[g])
        else:
            do(eng, job.g0 + p + by, job.chunk(p + by), i, job)


class Job:

    def __init__(self, name, steps, body, runs, t0=0, first=0):
        self.name, self.body, self.runs, self.t0, self.first = name, body, runs, t0, first
        self.bodies = steps // body
        self.per_step = len(step_chunks(name, 0, runs))
        self.per = body * self.per_step
        assert steps % body == 0 and (self.bodies < 4 or self.per % AHEAD_RAW == 0)

    def chunk(self, p):
        step, c = divmod(p, self.per_step)
        return step_chunks(self.name, self.first + step, self.runs)[c]


def walk(eng, job, body):
    n = job.bodies
    if n < 4:
        for i in range(n):
            body(i, i == n - 1)
        return
    body(0, False)
    with eng.Fori(1, n - 1) as i:
        body(i, False)
    body(n - 1, True)


class Parts:

    def __init__(self, full, lo, hi):
        self.full, self.lo, self.hi, self.shape = full, lo, hi, full.shape

    def make_hi(self, act, q):
        return act.activation(self.hi[:, q, :], self.full[:, q, :], ACT.Copy)

    def make_lo(self, dve, q):
        return dve.tensor_tensor(self.lo[:, q, :], self.full[:, q, :], self.hi[:, q, :].bitcast(F32), ALU.subtract)


def three_passes(pe, out, w_hi, w_lo, x_hi, x_lo, start, stop):
    pe.matmul(out, w_hi, x_hi, start=start, stop=False)
    pe.matmul(out, w_hi, x_lo, start=False, stop=False)
    return pe.matmul(out, w_lo, x_hi, start=False, stop=stop)


class Ready:
    tiles = 0

    def open(self, k, ctx):
        pass

    def scalar(self, act, upto):
        pass

    vector = tensor = scalar


class Split:

    def __init__(self, src):
        self.src, self.tiles = src, src.shape[1]

    def open(self, k, ctx):
        self.source_hi, self.source_ready = semaphores(k, ctx, "source_hi source_ready")
        self.done = {}

    def todo(self, engine, upto):
        a, b = self.done.get(engine, 0), min(upto, self.tiles)
        self.done[engine] = max(a, b)
        return range(a, b)

    def scalar(self, act, upto):
        for q in self.todo("scalar", upto):
            self.src.make_hi(act, q).then_inc(self.source_hi, 1)

    def vector(self, dve, upto):
        for q in self.todo("vector", upto):
            dve.wait_ge(self.source_hi, q + 1)
            self.src.make_lo(dve, q).then_inc(self.source_ready, 1)

    def tensor(self, pe, upto):
        for q in self.todo("tensor", upto):
            pe.wait_ge(self.source_ready, q + 1)


class Norm(Split):

    def __init__(self, x, src, weight, spare=None):
        Split.__init__(self, src)
        self.x, self.weight, self.spare = x, weight, spare

    def open(self, k, ctx):
        Split.open(self, k, ctx)
        self.k = k
        work = self.spare if self.spare is not None else k.sbuf(ctx, "norm_work", [P, 3, T])
        self.sq, self.rstd = work[:, 0:2, :], work[:, 2, :]
        self.squared, self.summed, self.root, self.inverse, self.normed = semaphores(
            k, ctx, "squared summed root inverse normed")

    def scalar(self, act, upto):
        k, tiles = self.k, self.todo("scalar", self.tiles)
        for m in tiles:
            if m >= 2:
                act.wait_ge(self.summed, m - 1)
            act.activation(self.sq[:, m % 2, :], self.x[:, m, :], ACT.Square).then_inc(self.squared, 1)
        if tiles:
            act.wait_ge(self.summed, self.tiles)
            act.activation(self.rstd, bank(k.ps, 7), ACT.Sqrt, bias=k.const("eps")[:, 0:1],
                           scale=1.0 / (self.tiles * P)).then_inc(self.root, 1)
        for q in tiles:
            act.wait_ge(self.normed, q + 1)
            self.src.make_hi(act, q).then_inc(self.source_hi, 1)

    def tensor(self, pe, upto):
        k = self.k
        if not self.done.get("sums"):
            self.done["sums"] = 1
            for m in range(self.tiles):
                pe.wait_ge(self.squared, m + 1)
                pe.matmul(bank(k.ps, 7), k.const("ones"), self.sq[:, m % 2, :], start=(m == 0),
                          stop=(m == self.tiles - 1)).then_inc(self.summed, 1)
        Split.tensor(self, pe, upto)

    def vector(self, dve, upto):
        k, tiles = self.k, self.todo("vector", self.tiles)
        if tiles:
            dve.wait_ge(self.root, 1)
            dve.reciprocal(self.rstd, self.rstd).then_inc(self.inverse, 1)
            dve.wait_ge(self.inverse, 1)
            for m in range(self.tiles + 1):
                if m < self.tiles:
                    dve.scalar_tensor_tensor(out=self.src.full[:, m, :], in0=self.x[:, m, :],
                                             scalar=k.col(self.weight, m), in1=self.rstd, op0=ALU.mult,
                                             op1=ALU.mult).then_inc(self.normed, 1)
                if m:
                    dve.wait_ge(self.source_hi, m)
                    self.src.make_lo(dve, m - 1).then_inc(self.source_ready, 1)


def project(k, outputs, src, source=Ready(), tokens=None):
    nc, stream, kt = k.nc, k.stream, src.shape[1]
    with ExitStack() as ctx:
        jobs, t0 = [], 0
        for name, dst, scale in outputs:
            tiles = dst.shape[1]
            whole = tiles // 4 * 4
            for first, steps, body in ((0, whole, 4), (whole, tiles - whole, tiles - whole)):
                if steps:
                    job = Job(name, steps, body, (kt,), t0, first)
                    job.dst, job.scale = dst[:, first:first + steps, :], scale
                    jobs.append(job)
                    t0 += steps
        tok = None
        if tokens:
            width = tokens[1].shape[2]
            tok = Job(tokens[0], 1, 1, (KD * width // P,), t0)
        end = stream.enter(jobs + ([tok] if tok else []))
        every = jobs + ([tok] if tok else [])
        adding = jobs[0].scale == "add"
        source.open(k, ctx)
        tile_used, tokens_used = semaphores(k, ctx, "tile_used tokens_used")
        block = ctx.enter_context(nc.Block())

        @block.sync
        def _(sp):
            stream.catch_up(stream.load, sp, stream.loaded, AHEAD_RAW)
            for job in every:
                def load(i, last):
                    for p in range(job.per):
                        stream.run_ahead(stream.load, sp, job, i, last, p, AHEAD_RAW)
                walk(sp, job, load)

        @block.tensor
        def _(pe):
            for job in jobs:
                def multiply(i, last):
                    for s in range(job.body):
                        t = job.t0 + s
                        out, q = bank(k.ps, t % 4), 0
                        if not isinstance(i, int) or t + i * job.body >= 4:
                            pe.wait_ge(tile_used, i * job.body + (t - 3))
                        for c in range(job.per_step):
                            p = s * job.per_step + c
                            g = job.g0 + p
                            pe.wait_ge(stream.parts_ready, i * job.per + (g + 1))
                            for n in range(job.chunk(p).width // P):
                                if isinstance(i, int):
                                    source.tensor(pe, q + 1)
                                at = slice(n * P, n * P + P)
                                mm = three_passes(pe, out, k.w_hi[:, g % 2, at], k.w_lo[:, g % 2, at],
                                                  src.hi[:, q, :], src.lo[:, q, :], q == 0, q == kt - 1)
                                q += 1
                            mm.then_inc(stream.chunk_used, 1)
                walk(pe, job, multiply)
            if tok:
                per = KD // tok.per
                for c in range(tok.per):
                    g = tok.g0 + c
                    pe.wait_ge(stream.parts_ready, g + 1)
                    for j in range(NT):
                        for q in range(c * per, c * per + per):
                            at = slice((q - c * per) * width, (q - c * per + 1) * width)
                            mm = three_passes(pe, k.ps[:, 4 + j, 0:width],
                                              src.hi[:, q, j * P:(j + 1) * P], src.lo[:, q, j * P:(j + 1) * P],
                                              k.w_hi[:, g % 2, at], k.w_lo[:, g % 2, at], q == 0, q == KD - 1)
                    mm.then_inc(stream.chunk_used, 1)

        @block.scalar
        def _(act):
            stream.catch_up(stream.make_hi, act, stream.split, AHEAD_PARTS)
            for job in every:
                def take(i, last):
                    for p in range(job.per):
                        if isinstance(i, int):
                            source.scalar(act, KD * (p + 1))
                        stream.run_ahead(stream.make_hi, act, job, i, last, p, AHEAD_PARTS)
                        if job is tok or adding or p % job.per_step < job.per_step - 1:
                            continue
                        s = p // job.per_step
                        rows = job.dst.shape[0]
                        act.wait_ge(stream.chunk_used, i * job.per + (job.g0 + p + 1))
                        o = job.dst[:, bass.ds(i * job.body + s, 1), :].rearrange("p a t -> p (a t)")
                        act.activation(o, k.ps[0:rows, (job.t0 + s) % 4, :], ACT.Copy, scale=job.scale)\
                            .then_inc(tile_used, 1)
                walk(act, job, take)
            if tok:
                act.wait_ge(stream.chunk_used, tok.g0 + tok.per)
                for j in range(NT):
                    act.activation(tokens[1][:, j, :], k.ps[:, 4 + j, 0:width], ACT.Copy).then_inc(tokens_used, 1)

        @block.vector
        def _(dve):
            stream.catch_up(stream.make_lo, dve, stream.split, AHEAD_PARTS)
            for job in every:
                def take(i, last):
                    for p in range(job.per):
                        if isinstance(i, int):
                            source.vector(dve, KD * (p + 1))
                        stream.run_ahead(stream.make_lo, dve, job, i, last, p, AHEAD_PARTS)
                        if not adding or p % job.per_step < job.per_step - 1:
                            continue
                        s = p // job.per_step
                        dve.wait_ge(stream.chunk_used, i * job.per + (job.g0 + p + 1))
                        o = job.dst[:, bass.ds(i * job.body + s, 1), :].rearrange("p a t -> p (a t)")
                        dve.tensor_tensor(o, o, bank(k.ps, (job.t0 + s) % 4), ALU.add).then_inc(tile_used, 1)
                walk(dve, job, take)
        stream.leave(end)


def gated_product(k, name, src_a, src_b, func, dst, accumulate, source, source_is_b, gate):
    nc, stream = k.nc, k.stream
    ka, kb = src_a.shape[1], src_b.shape[1]
    with ExitStack() as ctx:
        job = Job(name, dst.shape[1], 2, (ka, kb))
        end = stream.enter([job])
        source.open(k, ctx)
        gate_ready, tile_used, product_ready = semaphores(k, ctx, "gate_ready tile_used product_ready")
        block = ctx.enter_context(nc.Block())

        @block.sync
        def _(sp):
            stream.catch_up(stream.load, sp, stream.loaded, AHEAD_RAW)

            def load(i, last):
                for p in range(job.per):
                    stream.run_ahead(stream.load, sp, job, i, last, p, AHEAD_RAW)
            walk(sp, job, load)

        @block.tensor
        def _(pe):
            def multiply(i, last):
                for s in range(2):
                    if not isinstance(i, int) or i > 0:
                        pe.wait_ge(tile_used, i * 2 + (s - 1))
                    for c, (src, kt) in enumerate(((src_a, ka), (src_b, kb))):
                        g = job.g0 + 2 * s + c
                        pe.wait_ge(stream.parts_ready, i * 4 + (g + 1))
                        for q in range(kt):
                            if isinstance(i, int) and c == source_is_b:
                                source.tensor(pe, q + 1)
                            at = slice(q * P, q * P + P)
                            mm = three_passes(pe, bank(k.ps, 2 * s + c), k.w_hi[:, g % 2, at], k.w_lo[:, g % 2, at],
                                              src.hi[:, q, :], src.lo[:, q, :], q == 0, q == kt - 1)
                        mm.then_inc(stream.chunk_used, 1)
            walk(pe, job, multiply)

        @block.scalar
        def _(act):
            stream.catch_up(stream.make_hi, act, stream.split, AHEAD_PARTS)

            def gates(i, last):
                for s in range(2):
                    for c in range(2):
                        if isinstance(i, int):
                            source.scalar(act, KD)
                        stream.run_ahead(stream.make_hi, act, job, i, last, 2 * s + c, AHEAD_PARTS)
                        if c == 0:
                            act.wait_ge(stream.chunk_used, i * 4 + (job.g0 + 2 * s + 1))
                            if not isinstance(i, int) or i > 0:
                                act.wait_ge(tile_used, i * 2 + (s - 1))
                            act.activation(gate[:, s, :], bank(k.ps, 2 * s), func).then_inc(gate_ready, 1)
            walk(act, job, gates)

        @block.vector
        def _(dve):
            stream.catch_up(stream.make_lo, dve, stream.split, AHEAD_PARTS)

            def products(i, last):
                for s in range(2):
                    for c in range(2):
                        if isinstance(i, int):
                            source.vector(dve, KD)
                        stream.run_ahead(stream.make_lo, dve, job, i, last, 2 * s + c, AHEAD_PARTS)
                    dve.wait_ge(gate_ready, i * 2 + (s + 1))
                    dve.wait_ge(stream.chunk_used, i * 4 + (job.g0 + 2 * s + 2))
                    o = dst[:, bass.ds(i * 2 + s, 1), :].rearrange("p a t -> p (a t)")
                    g = gate[:, s, :]
                    if not accumulate:
                        dve.tensor_tensor(o, g, bank(k.ps, 2 * s + 1), ALU.mult).then_inc(tile_used, 1)
                        continue
                    dve.tensor_tensor(g, g, bank(k.ps, 2 * s + 1), ALU.mult).then_inc(product_ready, 1)
                    dve.wait_ge(product_ready, i * 2 + (s + 1))
                    dve.tensor_tensor(o, o, g, ALU.add).then_inc(tile_used, 1)
            walk(dve, job, products)
        stream.leave(end)


def ssm_branch(k, y, norm):
    nc = k.nc
    H, N, PAD = SSM_HEADS, SSM_XBC // P, SSM_CONV // 2
    W2 = T + 2 * PAD
    NX = SSM_INNER // P
    with ExitStack() as ctx:
        sb = lambda name, shape: k.sbuf(ctx, name, shape)
        raw = sb("xbc_raw", [P, N, W2])
        act_x = sb("xbc", [P, N, T])
        cbm = sb("cb_masked", [P, 2, NT, T + P])
        decay = sb("decay", [P, 2, T + P])
        prob = sb("prob", [P, 2, T + P])
        dt_raw = decay[0:H, :, 0:T]
        dt = sb("dt", [H, 2, T])
        acum = sb("acum", [H, 2, T])
        colneg = sb("acum_cols", [P, NT, 2, H])
        coldt = sb("dt_cols", [P, NT, 2, H])
        a_exp = sb("a_exp", [H, 2])
        xdt = [raw[:, :, :].rearrange("p a b -> p (a b)")[:, 0:NT * D].rearrange("p (j d) -> p j d", j=NT),
               y[:, 8:16, :].rearrange("p a t -> p (a t)").rearrange("p (j d) -> p j d", j=NT)]

        project(k, [("w_xbc", raw[:, :, PAD:PAD + T], 1.0), ("w_dt", dt_raw, 1.0)], k.xn, norm)

        with ExitStack() as inner:
            tap = prob[:, :, 0:T]
            edges, tapped, activated, dt_steps, dt_ready, scanned = semaphores(
                k, inner, "edges tapped activated dt_steps dt_ready scanned")
            block = inner.enter_context(nc.Block())

            @block.gpsimd
            def _(pool):
                pool.memset(raw[:, :, 0:PAD], 0.0).then_inc(edges, 1)
                pool.memset(raw[:, :, PAD + T:W2], 0.0).then_inc(edges, 1)

            @block.vector
            def _(dve):
                dve.wait_ge(edges, 2)
                for m in range(N):
                    o = tap[:, m % 2, :]
                    if m >= 2:
                        dve.wait_ge(activated, m - 1)
                    dve.tensor_scalar(o, raw[:, m, 0:T], k.col("conv_w", m), k.col("conv_b", m),
                                      ALU.mult, ALU.add).then_inc(tapped, 1)
                    for j in range(1, SSM_CONV):
                        dve.wait_ge(tapped, SSM_CONV * m + j)
                        dve.scalar_tensor_tensor(out=o, in0=raw[:, m, j:j + T], scalar=k.col("conv_w", j * N + m),
                                                 in1=o, op0=ALU.mult, op1=ALU.add).then_inc(tapped, 1)
                for r in range(2):
                    dve.wait_ge(dt_ready, r + 1)
                    dve.scalar_tensor_tensor(out=dt[:, r, :], in0=dt_raw[:, r, :], scalar=0.0, in1=dt[:, r, :],
                                             op0=ALU.max, op1=ALU.add).then_inc(scanned, 1)
                    dve.wait_ge(scanned, 3 * r + 1)
                    dve.tensor_scalar(dt_raw[:, r, :], dt[:, r, :], a_exp[:, r:r + 1], -1.0, ALU.mult,
                                      ALU.mult).then_inc(scanned, 1)
                    dve.wait_ge(scanned, 3 * r + 2)
                    step = -1 if r else 1
                    dve.tensor_tensor_scan(acum[:, r, ::step], k.const("ones", H)[:, 0:1].broadcast_to([H, T]),
                                           dt_raw[:, r, ::step], 0.0, ALU.mult, ALU.add).then_inc(scanned, 1)

            @block.scalar
            def _(act):
                for r in range(2):
                    act.activation(dt_raw[:, r, :], dt_raw[:, r, :], ACT.Identity,
                                   bias=k.col("dt_bias", r, H)).then_inc(dt_steps, 1)
                    act.wait_ge(dt_steps, 4 * r + 1)
                    act.activation(dt[:, r, :], dt_raw[:, r, :], ACT.Abs).then_inc(dt_steps, 1)
                    act.wait_ge(dt_steps, 4 * r + 2)
                    act.activation(dt[:, r, :], dt[:, r, :], ACT.Exp, scale=-1.0).then_inc(dt_steps, 1)
                    act.activation(a_exp[:, r:r + 1], k.col("a_log", r, H), ACT.Exp).then_inc(dt_steps, 1)
                    act.wait_ge(dt_steps, 4 * r + 4)
                    act.activation(dt[:, r, :], dt[:, r, :], ACT.Ln, bias=k.const("ones", H)[:, 0:1])\
                        .then_inc(dt_ready, 1)
                for m in range(N):
                    act.wait_ge(tapped, SSM_CONV * (m + 1))
                    act.activation(act_x[:, m, :], tap[:, m % 2, :], ACT.Silu).then_inc(activated, 1)

        with ExitStack() as inner:
            cols_turned, cols_ready, dt_cols_ready, x_turned, x_used, cb_done, cb_used = semaphores(
                k, inner, "cols_turned cols_ready dt_cols_ready x_turned x_used cb_done cb_used")
            block = inner.enter_context(nc.Block())
            small = k.ps[:, 0, 0:NT * 4 * H].rearrange("p (j r h) -> p j r h", j=NT, r=4)

            @block.tensor
            def _(pe):
                for j in range(NT):
                    for r in range(2):
                        pe.transpose(small[:, j, r, :], acum[:, r, j * P:(j + 1) * P], k.const("ident", H)[:, 0:H])
                        mm = pe.transpose(small[:, j, 2 + r, :], dt[:, r, j * P:(j + 1) * P],
                                          k.const("ident", H)[:, 0:H])
                mm.then_inc(cols_turned, 1)
                for n in range(2 * NT):
                    g, j = n // NT, n % NT
                    if n >= 2:
                        pe.wait_ge(cb_used, 4 * (n - 1))
                    pe.matmul(bank(k.ps, 1 + n % 2), act_x[:, NX + g, j * P:(j + 1) * P], act_x[:, NX + 2 + g, :],
                              start=True, stop=True).then_inc(cb_done, 1)
                for n in range(2 * NT):
                    j, half = n // 2, n % 2
                    if n >= 2:
                        pe.wait_ge(x_used, 2 * (n - 1))
                    for q in range(NT):
                        mm = pe.transpose(k.ps[:, 3 + n % 2, q * P:(q + 1) * P],
                                          act_x[:, NT * half + q, j * P:(j + 1) * P], k.const("ident"))
                    mm.then_inc(x_turned, 1)

            @block.scalar
            def _(act):
                act.wait_ge(cols_turned, 1)
                act.activation(coldt[:, :, :, :], small[:, :, 2:4, :], ACT.Copy).then_inc(dt_cols_ready, 1)
                act.activation(colneg[:, :, :, :], small[:, :, 0:2, :], ACT.Copy, scale=-1.0).then_inc(cols_ready, 1)

            @block.vector
            def _(dve):
                for n in range(2 * NT):
                    g, j = n // NT, n % NT
                    dve.wait_ge(cb_done, n + 1)
                    src, o, fw = bank(k.ps, 1 + n % 2), cbm[:, g, j, :], T - j * P
                    dve.tensor_tensor(o[:, 0:P], src[:, j * P:(j + 1) * P], k.const("le"), ALU.mult)\
                        .then_inc(cb_used, 1)
                    if fw > P:
                        dve.tensor_copy(o[:, P:fw], src[:, (j + 1) * P:T]).then_inc(cb_used, 1)
                    if j:
                        dve.tensor_copy(o[:, fw:fw + j * P], src[:, 0:j * P]).then_inc(cb_used, 1)
                    ins = dve.tensor_tensor(o[:, fw + j * P:fw + (j + 1) * P], src[:, j * P:(j + 1) * P],
                                            k.const("ge"), ALU.mult)
                    ins.then_inc(cb_used, 2 if j in (0, NT - 1) else 1)
                dve.wait_ge(dt_cols_ready, 1)
                for n in range(2 * NT):
                    j, half = n // 2, n % 2
                    dve.wait_ge(x_turned, n + 1)
                    for r in range(2):
                        o = xdt[r][:, j, half * T:(half + 1) * T].rearrange("p (h d) -> p h d", d=SSM_P)
                        dve.tensor_tensor(o, bank(k.ps, 3 + n % 2).rearrange("p (h d) -> p h d", d=SSM_P),
                                          coldt[:, j, r, 8 * half:8 * half + 8, None].broadcast_to([P, 8, SSM_P]),
                                          ALU.mult).then_inc(x_used, 1)

        with ExitStack() as inner:
            spread, bounded, decayed, prob_ready, tile_used, y_ready = semaphores(
                k, inner, "spread bounded decayed prob_ready tile_used y_ready")
            block = inner.enter_context(nc.Block())

            @block.tensor
            def _(pe):
                def spread_head(h):
                    if h >= 2:
                        pe.wait_ge(bounded, 2 * NT * (h - 1))
                    for r in range(2):
                        mm = pe.matmul(bank(k.ps, 2 * (h % 2) + r), k.const("ident", H)[:, h:h + 1].broadcast_to([H, P]),
                                       acum[:, r, :], start=True, stop=True)
                    mm.then_inc(spread, 1)

                spread_head(0)
                for h in range(H):
                    if h + 1 < H:
                        spread_head(h + 1)
                    bk, half = 4 + (h // 2) % 2, h % 2
                    if h % 2 == 0 and h >= 4:
                        pe.wait_ge(y_ready, h // 2 - 1)
                    for j in range(NT):
                        n = NT * h + j
                        pe.wait_ge(prob_ready, n + 1)
                        o = k.ps[64 * half:64 * half + 64, bk, :]
                        pe.matmul(o[:, j * P:T], xdt[0][:, j, h * SSM_P:(h + 1) * SSM_P],
                                  prob[:, n % 2, 0:T - j * P], start=(j == 0), stop=False)
                        mm = pe.matmul(o[:, 0:(j + 1) * P], xdt[1][:, j, h * SSM_P:(h + 1) * SSM_P],
                                       prob[:, n % 2, T - j * P:T + P], start=False, stop=(j == NT - 1))
                        mm.then_inc(tile_used, 1)

            @block.scalar
            def _(act):
                for h in range(H):
                    for j in range(NT):
                        n = NT * h + j
                        act.wait_ge(bounded, 2 * n + 2)
                        act.activation(decay[:, n % 2, :], decay[:, n % 2, :], ACT.Exp).then_inc(decayed, 1)

            @block.vector
            def _(dve):
                for h in range(H):
                    dve.wait_ge(spread, h + 1)
                    for j in range(NT):
                        n = NT * h + j
                        if n >= 2:
                            dve.wait_ge(prob_ready, n - 1)
                        for r, (a, b, at) in enumerate(((0, T - j * P, j * P), (T - j * P, T + P, 0))):
                            dve.tensor_scalar(decay[:, n % 2, a:b], k.ps[:, 2 * (h % 2) + r, at:at + b - a],
                                              colneg[:, j, r, h:h + 1], 0.0, ALU.add, ALU.min).then_inc(bounded, 1)
                        if n >= 2:
                            dve.wait_ge(tile_used, n - 1)
                        dve.wait_ge(decayed, n + 1)
                        dve.tensor_tensor(prob[:, n % 2, :], decay[:, n % 2, :], cbm[:, h // 8, j, :],
                                          ALU.mult).then_inc(prob_ready, 1)
                    if h % 2:
                        m = h // 2
                        dve.wait_ge(tile_used, NT * (h + 1))
                        dve.scalar_tensor_tensor(out=y[:, m, :], in0=act_x[:, m, :], scalar=k.col("d_skip", m),
                                                 in1=bank(k.ps, 4 + m % 2), op0=ALU.mult, op1=ALU.add)\
                            .then_inc(y_ready, 1)

        z = raw[:, :, :].rearrange("p a b -> p (a b)")[:, 0:8 * T].rearrange("p (m t) -> p m t", m=8)
        project(k, [("w_z", z, 1.0)], k.xn)
        with ExitStack() as inner:
            gate_ready, gated = semaphores(k, inner, "gate_ready gated")
            block = inner.enter_context(nc.Block())

            @block.scalar
            def _(act):
                for m in range(8):
                    act.activation(z[:, m, :], z[:, m, :], ACT.Silu).then_inc(gate_ready, 1)

            @block.vector
            def _(dve):
                for m in range(8):
                    dve.wait_ge(gate_ready, m + 1)
                    dve.tensor_tensor(y[:, m, :], y[:, m, :], z[:, m, :], ALU.mult).then_inc(gated, 1)
    rms_norm(k, y[:, 0:8, :], y[:, 0:8, :], "ssm_norm")


def flat(ap):
    return ap.rearrange("p a b -> p (a b)")


def rwkv_branch(k, y):
    nc = k.nc
    NM = RWKV_COLS // P
    Q = RWKV_W // P
    with ExitStack() as ctx:
        sb = lambda name, shape: k.sbuf(ctx, name, shape)
        mix = sb("mixed", [P, NM, T])
        kk = sb("kk", [P, Q, T])
        ka = sb("kk_a", [P, Q, T])
        store = sb("transfer", [P, 8192 + 2048])
        fm = sb("factors", [P, 9, T])
        raw = store[:, 0:NM * (T + 2)].rearrange("p (m t) -> p m t", m=NM)
        lora = sb("lora", [P, 2 * RWKV_W])
        g_up = k.raw[:, 0, 0:RWKV_W]
        r_, k_, v_ = mix[:, 0:Q, :], mix[:, Q:2 * Q, :], mix[:, 2 * Q:3 * Q, :]

        project(k, [("w_rwkv", raw[:, :, 1:T + 1], 1.0)], k.xn)

        with ExitStack() as inner:
            diff = fm[:, 0:4, :]
            edges, diffed, shifted, lora_in = semaphores(k, inner, "edges diffed shifted lora_in")
            block = inner.enter_context(nc.Block())

            @block.sync
            def _(sp):
                sp.dma_start(lora[:, :], k.dram["w_lora"]).then_inc(lora_in, 16)
                sp.wait_ge(lora_in, 16)

            @block.gpsimd
            def _(pool):
                pool.memset(raw[:, :, 0:1], 0.0).then_inc(edges, 1)
                pool.memset(raw[:, :, T + 1:T + 2], 0.0).then_inc(edges, 1)
                pool.wait_ge(edges, 2)
                for m in range(NM):
                    if m >= 2:
                        pool.wait_ge(shifted, 2 * (m - 1))
                    for s in range(2):
                        pool.tensor_tensor(diff[:, 2 * (m % 2) + s, :], raw[:, m, 2 * s:2 * s + T],
                                           raw[:, m, 1:T + 1], ALU.subtract).then_inc(diffed, 1)

            @block.vector
            def _(dve):
                for m in range(NM):
                    for s in range(2):
                        dve.wait_ge(diffed, 2 * m + s + 1)
                        if s:
                            dve.wait_ge(shifted, 2 * m + 1)
                        dve.scalar_tensor_tensor(out=mix[:, m, :], in0=diff[:, 2 * (m % 2) + s, :],
                                                 scalar=k.col("mu", s * NM + m),
                                                 in1=mix[:, m, :] if s else raw[:, m, 1:T + 1],
                                                 op0=ALU.mult, op1=ALU.add).then_inc(shifted, 1)

        with ExitStack() as inner:
            low, a_done, a_ready, kx_ready, kx_squared, kx_summed, root, inverse, made = semaphores(
                k, inner, "low a_done a_ready kx_ready kx_squared kx_summed root inverse made")
            block = inner.enter_context(nc.Block())
            a_, sq, rt = fm[:, 0:2, :], fm[:, 2:4, :], fm[:, 4:6, :]

            @block.scalar
            def _(act):
                act.activation(mix[0:64, 12, :], mix[0:64, 12, :], ACT.Tanh).then_inc(low, 1)
                act.activation(mix[:, 13, :], mix[:, 13, :], ACT.Sigmoid).then_inc(low, 1)
                for q in range(Q):
                    act.wait_ge(a_done, q + 1)
                    if q >= 2:
                        act.wait_ge(made, 4 * (q - 1))
                    act.activation(a_[:, q % 2, :], bank(k.ps, q % 2), ACT.Sigmoid, bias=k.col("a0", q))\
                        .then_inc(a_ready, 1)
                    act.wait_ge(kx_ready, q + 1)
                    act.activation(sq[:, q % 2, :], kk[:, q, :], ACT.Square).then_inc(kx_squared, 1)
                    act.wait_ge(kx_summed, q + 1)
                    act.activation(rt[:, q % 2, :], bank(k.ps, 2 + q % 2), ACT.Sqrt, bias=k.const("eps")[:, 2:3])\
                        .then_inc(root, 1)

            @block.tensor
            def _(pe):
                for q in range(Q):
                    if q >= 2:
                        pe.wait_ge(a_ready, q - 1)
                    pe.matmul(bank(k.ps, q % 2), lora[64:128, q * P:(q + 1) * P], mix[64:128, 12, :],
                              start=True, stop=True).then_inc(a_done, 1)
                    pe.wait_ge(kx_squared, q + 1)
                    if q >= 2:
                        pe.wait_ge(root, q - 1)
                    pe.matmul(bank(k.ps, 2 + q % 2), k.const("pair"), sq[:, q % 2, :], start=True, stop=True)\
                        .then_inc(kx_summed, 1)

            @block.vector
            def _(dve):
                for q in range(Q):
                    dve.tensor_scalar(kk[:, q, :], k_[:, q, :], k.col("k_k", q), None, ALU.mult).then_inc(kx_ready, 1)
                for q in range(Q):
                    r = rt[:, q % 2, :]
                    dve.wait_ge(root, q + 1)
                    dve.reciprocal(r, r).then_inc(inverse, 1)
                    dve.wait_ge(inverse, q + 1)
                    dve.tensor_tensor(kk[:, q, :], kk[:, q, :], r, ALU.mult).then_inc(made, 1)
                    dve.wait_ge(made, 4 * q + 1)
                    dve.wait_ge(a_ready, q + 1)
                    dve.tensor_tensor(ka[:, q, :], kk[:, q, :], a_[:, q % 2, :], ALU.mult).then_inc(made, 1)
                    dve.tensor_scalar(a_[:, q % 2, :], a_[:, q % 2, :], -1.0, k.col("k_a", q), ALU.add, ALU.mult)\
                        .then_inc(made, 1)
                    dve.wait_ge(made, 4 * q + 3)
                    dve.scalar_tensor_tensor(out=k_[:, q, :], in0=a_[:, q % 2, :], scalar=1.0, in1=k_[:, q, :],
                                             op0=ALU.add, op1=ALU.mult).then_inc(made, 1)

        gh = store[:, 0:8192].rearrange("p (q c n) -> p q c n", q=Q, c=NC)
        q1 = store[:, 8192:].rearrange("p (q t) -> p q t", q=Q)
        for back in range(2):
            rwkv_transfer(k, back, mix, kk, ka, fm, lora, gh, q1, y)
            rwkv_chain(k, back, gh, q1, y)

        with ExitStack() as inner:
            (mean_done, centred, squared, var_done, root, inverse, scaled, normed, rk_ready, rk_scaled, rk_done,
             bonus_ready, summed, g_done, y_ready, g_up_in) = semaphores(
                k, inner, "mean_done centred squared var_done root inverse scaled normed rk_ready rk_scaled "
                "rk_done bonus_ready summed g_done y_ready g_up_in")
            block = inner.enter_context(nc.Block())
            sq, rt, rk = fm[:, 0:2, :], fm[:, 2:4, :], fm[:, 4:6, :]

            @block.sync
            def _(sp):
                sp.dma_start(g_up, k.dram["w_g_up"]).then_inc(g_up_in, 16)

            @block.tensor
            def _(pe):
                pe.wait_ge(g_up_in, 16)
                for q in range(Q):
                    b = 4 * (q % 2)
                    if q >= 2:
                        pe.wait_ge(y_ready, q - 1)
                    pe.matmul(bank(k.ps, b), k.const("pair"), y[:, q, :], start=True, stop=True).then_inc(mean_done, 1)
                    pe.wait_ge(rk_ready, q + 1)
                    pe.matmul(bank(k.ps, b + 2), k.const("pair"), rk[:, q % 2, :], start=True, stop=True)\
                        .then_inc(rk_done, 1)
                    pe.matmul(bank(k.ps, b + 3), g_up[:, q * P:(q + 1) * P], mix[:, 13, :], start=True, stop=True)\
                        .then_inc(g_done, 1)
                    pe.wait_ge(squared, q + 1)
                    pe.matmul(bank(k.ps, b + 1), k.const("pair"), sq[:, q % 2, :], start=True, stop=True)\
                        .then_inc(var_done, 1)

            @block.scalar
            def _(act):
                for q in range(Q):
                    act.wait_ge(centred, q + 1)
                    act.activation(sq[:, q % 2, :], y[:, q, :], ACT.Square).then_inc(squared, 1)
                    act.wait_ge(var_done, q + 1)
                    act.activation(rt[:, q % 2, :], bank(k.ps, 4 * (q % 2) + 1), ACT.Sqrt,
                                   bias=k.const("eps")[:, 1:2], scale=1.0 / 64).then_inc(root, 1)
                    act.wait_ge(scaled, q + 1)
                    act.activation(y[:, q, :], y[:, q, :], ACT.Identity, scale=k.col("ln_w", q),
                                   bias=k.col("ln_b", q)).then_inc(normed, 1)

            @block.vector
            def _(dve):
                for q in range(Q):
                    b = 4 * (q % 2)
                    dve.wait_ge(mean_done, q + 1)
                    dve.scalar_tensor_tensor(out=y[:, q, :], in0=bank(k.ps, b), scalar=-1.0 / 64, in1=y[:, q, :],
                                             op0=ALU.mult, op1=ALU.add).then_inc(centred, 1)
                    dve.tensor_tensor(rk[:, q % 2, :], r_[:, q, :], k_[:, q, :], ALU.mult).then_inc(rk_scaled, 1)
                    dve.wait_ge(rk_scaled, q + 1)
                    dve.tensor_scalar(rk[:, q % 2, :], rk[:, q % 2, :], k.col("r_k", q), None, ALU.mult)\
                        .then_inc(rk_ready, 1)
                    dve.wait_ge(rk_done, q + 1)
                    dve.tensor_tensor(rk[:, q % 2, :], bank(k.ps, b + 2), v_[:, q, :], ALU.mult)\
                        .then_inc(bonus_ready, 1)
                    dve.wait_ge(root, q + 1)
                    dve.reciprocal(rt[:, q % 2, :], rt[:, q % 2, :]).then_inc(inverse, 1)
                    dve.wait_ge(inverse, q + 1)
                    dve.wait_ge(centred, q + 1)
                    dve.tensor_tensor(y[:, q, :], y[:, q, :], rt[:, q % 2, :], ALU.mult).then_inc(scaled, 1)
                    dve.wait_ge(normed, q + 1)
                    dve.wait_ge(bonus_ready, q + 1)
                    dve.tensor_tensor(y[:, q, :], y[:, q, :], rk[:, q % 2, :], ALU.add).then_inc(summed, 1)
                    dve.wait_ge(summed, q + 1)
                    dve.wait_ge(g_done, q + 1)
                    dve.tensor_tensor(y[:, q, :], y[:, q, :], bank(k.ps, b + 3), ALU.mult).then_inc(y_ready, 1)


def rwkv_transfer(k, back, mix, kk, ka, fm, lora, gh, q1, y):
    nc = k.nc
    Q = RWKV_W // P
    step = -1 if back else 1
    end = 0 if back else CH - 1
    strict, strict_t, incl = ("c_gt", "c_lt", "c_ge") if back else ("c_lt", "c_gt", "c_le")
    r_, k_, v_ = mix[:, 0:Q, :], mix[:, Q:2 * Q, :], mix[:, 2 * Q:3 * Q, :]
    logw, L, e_l, at, rt, bt, kt, bh, kh = [fm[:, n, :] for n in range(9)]
    rings = [flat(k.raw[:, 0:2, :]), flat(k.raw[:, 2:4, :]), flat(k.idle_hi[:, :, :]), flat(k.idle_lo[:, :, :])]
    scratch = lambda n: rings[n // 4][:, n % 4 * T:(n % 4 + 1) * T]
    tile4 = lambda n: scratch(n).rearrange("p (j t) -> p j t", j=NT)
    N_, NT_, AK, ARB, ARK, Z = [[tile4(2 * n + h) for h in range(2)] for n in range(6)]
    bh_tok, kh_tok, v_tok = [tile4(12 + n) for n in range(3)]
    diag = scratch(15)
    ident = k.const("ident")
    with ExitStack() as inner:
        (w_done, sg_ready, logw_ready, L_ready, e_ready, factor_ready, turned, turned_used, gram_done, gram_used,
         av_done, av_used, z_done, n_done, z_used, n_used, q_done, q_used, gh_done, gh_used, diag_ready,
         diag_added) = semaphores(
            k, inner, "w_done sg_ready logw_ready L_ready e_ready factor_ready turned turned_used gram_done "
            "gram_used av_done av_used z_done n_done z_used n_used q_done q_used gh_done gh_used diag_ready "
            "diag_added")
        block = inner.enter_context(nc.Block())
        ROUNDS = 5
        NSQ = 2 * (ROUNDS - 1) - 1

        @block.tensor
        def _(pe):
            for u in range(Q):
                if u:
                    pe.wait_ge(q_used, 2 * u)
                pe.matmul(bank(k.ps, 7), lora[0:64, back * RWKV_W + u * P:back * RWKV_W + (u + 1) * P],
                          mix[0:64, 12, :],
                          start=True, stop=True).then_inc(w_done, 1)
                for n, src in enumerate((at, bh, kh, v_[:, u, :])):
                    if n == 0:
                        pe.wait_ge(factor_ready, 6 * u + 6)
                        pe.wait_ge(gh_used, 4 * u) if u else None
                    for j in range(NT):
                        mm = pe.transpose(k.ps[:, 4 + n, j * P:(j + 1) * P], src[:, j * P:(j + 1) * P], ident)
                    mm.then_inc(turned, 1)
                n = 0
                for lhs, rhs in ((bt, at), (at, bt), (kt, at), (bt, rt), (kt, rt)):
                    for h in range(2):
                        if n >= 4:
                            pe.wait_ge(gram_used, 10 * u + n - 3)
                        rows = slice(64 * h, 64 * h + 64)
                        for j in range(NT):
                            c = slice(j * P, (j + 1) * P)
                            mm = pe.matmul(k.ps[:, n % 4, c], lhs[rows, c], rhs[rows, c], start=True, stop=True)
                        mm.then_inc(gram_done, 1)
                        n += 1
                pe.wait_ge(turned_used, 5 * u + 5)
                for h in range(2):
                    pe.wait_ge(gram_used, 10 * u + 5 + h)
                    for j in range(NT):
                        mm = pe.matmul(k.ps[:, 4 + h, j * P:j * P + 64], AK[h][:, j, :],
                                       v_tok[:, j, 64 * h:64 * h + 64], start=True, stop=True)
                    mm.then_inc(av_done, 1)
                pe.wait_ge(gram_used, 10 * u + 10)
                for i in range(ROUNDS):
                    for h in range(2):
                        if i == 0:
                            pe.wait_ge(av_used, 2 * u + 2)
                        else:
                            pe.wait_ge(z_used, 2 * ROUNDS * u + 2 * (i - 1) + h + 1)
                            pe.wait_ge(n_used, 2 * NSQ * u + (4 * (i - 1) + 2 * h + 2 if i < ROUNDS - 1
                                                              else 4 * (i - 1) + h + 1))
                        for j in range(NT):
                            mm = pe.matmul(k.ps[:, 3 * h, j * P:(j + 1) * P], N_[h][:, j, :], Z[h][:, j, :],
                                           start=True, stop=True)
                        mm.then_inc(z_done, 1)
                        for s in range(2 if i < ROUNDS - 2 else 1 if i < ROUNDS - 1 else 0):
                            a, b = (N_[h], NT_[h]) if s else (NT_[h], N_[h])
                            for j in range(NT):
                                mm = pe.matmul(k.ps[:, 3 * h + 1 + s, j * P:(j + 1) * P], a[:, j, :], b[:, j, :],
                                               start=True, stop=True)
                            mm.then_inc(n_done, 1)
                pe.wait_ge(z_used, 2 * ROUNDS * (u + 1))
                for h in range(2):
                    rows = slice(64 * h, 64 * h + 64)
                    for j in range(NT):
                        c = slice(j * P, (j + 1) * P)
                        mm = pe.matmul(k.ps[rows, 6, c], Z[h][:, j, 0:64], ARB[h][:, j, :], start=True, stop=True)
                mm.then_inc(q_done, 1)
                for h in range(2):
                    rows = slice(64 * h, 64 * h + 64)
                    for j in range(NT):
                        c = slice(j * P, (j + 1) * P)
                        pe.matmul(k.ps[rows, 7, c], Z[h][:, j, 64:128], ARB[h][:, j, :], start=True, stop=False)
                        mm = pe.matmul(k.ps[rows, 7, c], v_tok[:, j, 64 * h:64 * h + 64], ARK[h][:, j, :],
                                       start=False, stop=True)
                mm.then_inc(q_done, 1)
                for c in range(NT):
                    tok = slice(CH * c, CH * c + CH)
                    for h in range(2):
                        rows, ch = slice(64 * h, 64 * h + 64), slice(64 * h, 64 * h + 64)
                        for j in range(NT):
                            o = k.ps[rows, c, j * P:(j + 1) * P]
                            pe.matmul(o[:, 0:64], Z[h][tok, j, 0:64], bh_tok[tok, j, ch], start=True, stop=True,
                                      tile_position=(CH * c, 64 * h))
                            pe.matmul(o[:, 64:128], bh_tok[tok, j, ch], Z[h][tok, j, 64:128], start=True, stop=False,
                                      tile_position=(CH * c, 64 * h))
                            mm = pe.matmul(o[:, 64:128], kh_tok[tok, j, ch], v_tok[tok, j, ch], start=False,
                                           stop=True, tile_position=(CH * c, 64 * h))
                    mm.then_inc(gh_done, 1)

        @block.scalar
        def _(act):
            for u in range(Q):
                if u:
                    act.wait_ge(diag_added, 2 * u)
                act.wait_ge(w_done, u + 1)
                act.activation(e_l, bank(k.ps, 7), ACT.Sigmoid, bias=k.col("w0", back * Q + u)).then_inc(sg_ready, 1)
                act.wait_ge(L_ready, 2 * u + 2)
                act.activation(e_l, L, ACT.Exp).then_inc(e_ready, 1)
                act.activation(at, logw, ACT.Exp).then_inc(e_ready, 1)
                act.activation(bt, L, ACT.Exp, scale=-1.0).then_inc(e_ready, 1)
                act.wait_ge(turned, 4 * u + 1)
                for h in range(2):
                    act.activation(Z[h][:, :, 0:64], bank(k.ps, 4).rearrange("p (j c) -> p j c", j=NT)[:, :, 64 * h:64 * h + 64],
                                   ACT.Copy).then_inc(turned_used, 1)
                for n, o in enumerate((bh_tok, kh_tok, v_tok)):
                    act.wait_ge(turned, 4 * u + n + 2)
                    act.activation(o, bank(k.ps, 5 + n).rearrange("p (j c) -> p j c", j=NT), ACT.Copy)\
                        .then_inc(turned_used, 1)
                for h in range(2):
                    act.wait_ge(av_done, 2 * u + h + 1)
                    act.activation(Z[h][:, :, 64:128], bank(k.ps, 4 + h).rearrange("p (j c) -> p j c", j=NT)[:, :, 0:64],
                                   ACT.Copy).then_inc(av_used, 1)
                n = 2 * NSQ * u
                for i in range(ROUNDS - 1):
                    for h in range(2):
                        squarings = 2 if i < ROUNDS - 2 else 1
                        act.wait_ge(n_done, n + squarings)
                        n += squarings
                        for s in range(squarings):
                            act.activation((NT_ if s else N_)[h],
                                           bank(k.ps, 3 * h + 1 + s).rearrange("p (j c) -> p j c", j=NT), ACT.Copy)\
                                .then_inc(n_used, 1)
                for c in range(NT):
                    act.wait_ge(gh_done, 4 * u + c + 1)
                    act.activation(gh[:, u, c::NT, :], bank(k.ps, c).rearrange("p (j n) -> p j n", j=NT), ACT.Copy)\
                        .then_inc(gh_used, 1)

        @block.vector
        def _(dve):
            for u in range(Q):
                dve.wait_ge(sg_ready, u + 1)
                dve.tensor_scalar(logw, e_l, -RWKV_DECAY, None, ALU.mult).then_inc(logw_ready, 1)
                dve.wait_ge(logw_ready, u + 1)
                reset = k.const("reset")[:, back * T:(back + 1) * T]
                dve.tensor_tensor_scan(L[:, ::step], reset[:, ::step], logw[:, ::step], 0.0, ALU.mult, ALU.add)\
                    .then_inc(L_ready, 1)
                dve.wait_ge(L_ready, 2 * u + 1)
                dve.tensor_tensor(logw, L, logw, ALU.subtract).then_inc(L_ready, 1)
                dve.wait_ge(e_ready, 3 * u + 1)
                dve.tensor_tensor(rt, r_[:, u, :], e_l, ALU.mult).then_inc(factor_ready, 1)
                dve.wait_ge(e_ready, 3 * u + 2)
                dve.scalar_tensor_tensor(out=at, in0=kk[:, u, :], scalar=-1.0, in1=at, op0=ALU.mult, op1=ALU.mult)\
                    .then_inc(factor_ready, 1)
                dve.wait_ge(e_ready, 3 * u + 3)
                dve.tensor_tensor(kt, k_[:, u, :], bt, ALU.mult).then_inc(factor_ready, 1)
                dve.tensor_tensor(bt, ka[:, u, :], bt, ALU.mult).then_inc(factor_ready, 1)
                dve.wait_ge(factor_ready, 6 * u + 4)
                chunks = lambda ap: ap.rearrange("p (c t) -> p c t", t=CH)
                e_end = chunks(e_l)[:, :, end:end + 1]
                for o, src in ((kh, kt), (bh, bt)):
                    dve.tensor_tensor(chunks(o), chunks(src), e_end.broadcast_to([P, NC, CH]), ALU.mult)\
                        .then_inc(factor_ready, 1)
                n = 0
                for dst, mask in ((N_, strict), (NT_, strict_t), (AK, strict), (ARB, incl), (ARK, incl)):
                    for h in range(2):
                        dve.wait_ge(gram_done, 10 * u + n + 1)
                        dve.tensor_tensor(dst[h], bank(k.ps, n % 4).rearrange("p (j c) -> p j c", j=NT),
                                          wide(k.const(mask), NT), ALU.mult).then_inc(gram_used, 1)
                        n += 1
                for i in range(ROUNDS):
                    for h in range(2):
                        dve.wait_ge(z_done, 2 * ROUNDS * u + 2 * i + h + 1)
                        if i:
                            dve.wait_ge(z_used, 2 * ROUNDS * u + 2 * (i - 1) + h + 1)
                        dve.tensor_tensor(Z[h], Z[h], bank(k.ps, 3 * h).rearrange("p (j c) -> p j c", j=NT), ALU.add)\
                            .then_inc(z_used, 1)
                dve.wait_ge(q_done, 2 * u + 1)
                dve.tensor_tensor(q1[:, u, :], bank(k.ps, 6), rt, ALU.add).then_inc(q_used, 1)
                dve.wait_ge(q_done, 2 * u + 2)
                if back:
                    dve.tensor_tensor(y[:, u, :], y[:, u, :], bank(k.ps, 7), ALU.add).then_inc(q_used, 1)
                else:
                    dve.tensor_copy(y[:, u, :], bank(k.ps, 7)).then_inc(q_used, 1)
                dve.wait_ge(gh_used, 4 * u + 4)
                for half in range(2):
                    cs = slice(8 * half, 8 * half + 8)
                    d3 = diag.rearrange("p (c n) -> p c n", n=64)
                    if 2 * u + half:
                        dve.wait_ge(diag_added, 2 * u + half)
                    dve.tensor_tensor(d3, wide(k.const("eye64"), 8), e_end[:, cs, :].broadcast_to([P, 8, 64]),
                                      ALU.mult).then_inc(diag_ready, 1)
                    dve.wait_ge(diag_ready, 2 * u + half + 1)
                    dve.tensor_tensor(gh[:, u, cs, 0:64], gh[:, u, cs, 0:64], d3, ALU.add).then_inc(diag_added, 1)


def rwkv_chain(k, back, gh, q1, y):
    nc = k.nc
    Q = RWKV_W // P
    order = list(range(NC))[::-1] if back else list(range(NC))
    with ExitStack() as inner:
        state_done, state_ready, out_done, out_used = semaphores(
            k, inner, "state_done state_ready out_done out_used")
        block = inner.enter_context(nc.Block())

        @block.tensor
        def _(pe):
            for i in range(1, NC):
                c, before = order[i], order[i - 1]
                if i > 1:
                    pe.wait_ge(state_ready, i - 1)
                if i < NC - 1:
                    for q in range(Q):
                        for h in range(2):
                            rows = slice(64 * h, 64 * h + 64)
                            mm = pe.matmul(k.ps[rows, 2 * (i % 2) + h, q * 64:(q + 1) * 64], gh[rows, q, c, 0:64],
                                           gh[rows, q, before, 64:128], start=True, stop=True)
                    mm.then_inc(state_done, 1)
                for q in range(Q):
                    for h in range(2):
                        rows = slice(64 * h, 64 * h + 64)
                        mm = pe.matmul(k.ps[rows, 4 + q, CH * c:CH * c + CH], gh[rows, q, before, 64:128],
                                       q1[rows, q, CH * c:CH * c + CH], start=True, stop=True)
            mm.then_inc(out_done, 1)

        @block.vector
        def _(dve):
            for i in range(1, NC - 1):
                c = order[i]
                dve.wait_ge(state_done, i)
                for h in range(2):
                    rows = slice(64 * h, 64 * h + 64)
                    ins = dve.tensor_tensor(gh[rows, :, c, 64:128], gh[rows, :, c, 64:128],
                                            k.ps[rows, 2 * (i % 2) + h, 0:Q * 64].rearrange("p (q n) -> p q n", q=Q),
                                            ALU.add)
                ins.then_inc(state_ready, 1)
            dve.wait_ge(out_done, 1)
            part = slice(0, T - CH) if back else slice(CH, T)
            for q in range(Q):
                dve.tensor_tensor(y[:, q, part], y[:, q, part], k.ps[:, 4 + q, part], ALU.add).then_inc(out_used, 1)


def hgrn_branch(k, y):
    nc = k.nc
    HH = HGRN_W // P
    with ExitStack() as ctx:
        sb = lambda name, shape: k.sbuf(ctx, name, shape)
        p = sb("hgrn_in", [P, 5 * HH, T])
        buf = sb("hgrn_buffers", [P, 2, 12, T])
        lbs = sb("lower_bound", [P, 5, HH])
        dec = sb("chunk_decay", [P, 2, NC])
        project(k, [("w_hgrn", p[:, :, :], 1.0)], k.xn)
        q_, f_, i_, g_ = p[:, 0:HH, :], p[:, HH:3 * HH, :], p[:, 3 * HH:4 * HH, :], p[:, 4 * HH:5 * HH, :]

        with ExitStack() as inner:
            bound, exped, sig_ready, f_ready, g_ready = semaphores(k, inner, "bound exped sig_ready f_ready g_ready")
            block = inner.enter_context(nc.Block())
            a, b = k.col_at["lb"]
            logits = k.cols[:, a:b]

            @block.vector
            def _(dve):
                dve.tensor_tensor(lbs[:, 0, :], logits, logits, ALU.subtract).then_inc(bound, 1)
                dve.wait_ge(exped, 1)
                dve.reciprocal(lbs[:, 2, :], lbs[:, 1, :]).then_inc(bound, 1)
                dve.wait_ge(bound, 2)
                dve.tensor_tensor(lbs[:, 2, :], lbs[:, 2, :], lbs[:, 1, :], ALU.mult).then_inc(bound, 1)
                dve.wait_ge(bound, 3)
                dve.tensor_tensor(lbs[:, 3, :], lbs[:, 2, :], lbs[:, 2, :], ALU.subtract).then_inc(bound, 1)
                dve.wait_ge(bound, 4)
                dve.tensor_scalar(lbs[:, 4, :], lbs[:, 3, :], -1.0, 1.0, ALU.mult, ALU.add).then_inc(bound, 1)
                dve.wait_ge(bound, 5)
                for n in range(2 * HH):
                    dve.wait_ge(sig_ready, n + 1)
                    dve.tensor_scalar(f_[:, n, :], f_[:, n, :], lbs[:, 4, n % HH:n % HH + 1],
                                      lbs[:, 3, n % HH:n % HH + 1], ALU.mult, ALU.add).then_inc(f_ready, 1)

            @block.scalar
            def _(act):
                act.wait_ge(bound, 1)
                act.activation(lbs[:, 1, :], lbs[:, 0, :], ACT.Exp).then_inc(exped, 1)
                for n in range(2 * HH):
                    act.activation(f_[:, n, :], f_[:, n, :], ACT.Sigmoid).then_inc(sig_ready, 1)
                for n in range(HH):
                    act.activation(g_[:, n, :], g_[:, n, :], ACT.Silu).then_inc(g_ready, 1)

        with ExitStack() as inner:
            (log_ready, prep, exps, turned, turned_used, scored, masked, inputs_done, state_ready, out_done,
             y_used) = semaphores(k, inner, "log_ready prep exps turned turned_used scored masked inputs_done "
                                  "state_ready out_done y_used")
            block = inner.enter_context(nc.Block())
            UNITS = 2 * HH
            PREP = 10
            chunks = lambda ap: ap.rearrange("p (c t) -> p c t", t=CH)
            tiles = lambda ap: ap.rearrange("p (j t) -> p j t", j=NT)

            def parts(u):
                b = buf[:, u % 2, :, :]
                return [b[:, n, :] for n in range(8)] + [b[:, 8:12, :].rearrange("p a t -> p (a t)")
                                                         .rearrange("p (c v) -> p c v", c=NC)]

            def order(u):
                return list(range(NC))[::-1] if u >= HH else list(range(NC))

            @block.scalar
            def _(act):
                for u in range(UNITS + 1):
                    if u < UNITS:
                        L, qs, ks, qb, kh, sc, kh_tok, v_tok, S = parts(u)
                        if u >= 2:
                            act.wait_ge(y_used, u - 1)
                        act.activation(qs, f_[:, u, :], ACT.Ln).then_inc(log_ready, 1)
                        act.wait_ge(prep, PREP * u + 4)
                        act.activation(ks, qs, ACT.Exp, scale=-1.0).then_inc(exps, 1)
                        act.activation(qb, L, ACT.Exp).then_inc(exps, 1)
                        act.activation(kh, kh, ACT.Exp).then_inc(exps, 1)
                        act.wait_ge(exps, 4 * u + 1)
                        act.activation(qs, qs, ACT.Exp).then_inc(exps, 1)
                    if u:
                        _, _, _, _, _, _, kh_tok, v_tok, _ = parts(u - 1)
                        for n, o in enumerate((kh_tok, v_tok)):
                            act.wait_ge(turned, 2 * (u - 1) + n + 1)
                            act.activation(o, bank(k.ps, 1 + n), ACT.Copy).then_inc(turned_used, 1)

            @block.vector
            def _(dve):
                for u in range(UNITS + 1):
                    if u < UNITS:
                        L, qs, ks, qb, kh, sc, kh_tok, v_tok, S = parts(u)
                        back, h = u // HH, u % HH
                        step, end, mid = (-1, 0, CH // 2) if back else (1, CH - 1, CH // 2 - 1)
                        reset = k.const("reset")[:, back * T:(back + 1) * T]
                        n0 = PREP * u
                        dve.wait_ge(log_ready, u + 1)
                        dve.tensor_tensor_scan(L[:, ::step], reset[:, ::step], qs[:, ::step], 0.0, ALU.mult, ALU.add)\
                            .then_inc(prep, 1)
                        dve.wait_ge(prep, n0 + 1)
                        dve.tensor_tensor(chunks(qs), chunks(L), chunks(L)[:, :, mid:mid + 1].broadcast_to([P, NC, CH]),
                                          ALU.subtract).then_inc(prep, 1)
                        dve.tensor_tensor(chunks(kh), chunks(L)[:, :, end:end + 1].broadcast_to([P, NC, CH]),
                                          chunks(L), ALU.subtract).then_inc(prep, 1)
                        dve.wait_ge(prep, n0 + 2)
                        dve.tensor_scalar(qs, qs, -43.0, 43.0, ALU.max, ALU.min).then_inc(prep, 1)
                        dve.tensor_scalar(f_[:, u, :], f_[:, u, :], -1.0, 1.0, ALU.mult, ALU.add).then_inc(prep, 1)
                        dve.wait_ge(exps, 4 * u + 4)
                        dve.wait_ge(prep, n0 + 5)
                        dve.tensor_copy(dec[:, u % 2, :], chunks(qb)[:, :, end]).then_inc(prep, 1)
                        dve.tensor_tensor(qs, qs, q_[:, h, :], ALU.mult).then_inc(prep, 1)
                        dve.tensor_tensor(ks, ks, f_[:, u, :], ALU.mult).then_inc(prep, 1)
                        dve.tensor_tensor(kh, kh, f_[:, u, :], ALU.mult).then_inc(prep, 1)
                        dve.wait_ge(prep, n0 + 6)
                        dve.tensor_tensor(qb, qb, q_[:, h, :], ALU.mult).then_inc(prep, 1)
                    if u:
                        w = u - 1
                        _, _, _, _, _, sc, _, _, S = parts(w)
                        back, h = w // HH, w % HH
                        dve.wait_ge(scored, w + 1)
                        dve.tensor_tensor(tiles(sc), tiles(bank(k.ps, 0)), wide(k.const("c_ge" if back else "c_le"), NT),
                                          ALU.mult).then_inc(masked, 1)
                        dve.wait_ge(inputs_done, w + 1)
                        for i, c in enumerate(order(w)[:-1]):
                            src = k.ps[:, 3 + c % NT, (c // NT) * P:(c // NT + 1) * P]
                            if i == 0:
                                dve.tensor_copy(S[:, c, :], src).then_inc(state_ready, 1)
                                continue
                            before = order(w)[i - 1]
                            dve.wait_ge(state_ready, (NC - 1) * w + i)
                            dve.scalar_tensor_tensor(out=S[:, c, :], in0=S[:, before, :],
                                                     scalar=dec[:, w % 2, c:c + 1], in1=src,
                                                     op0=ALU.mult, op1=ALU.add).then_inc(state_ready, 1)
                        dve.wait_ge(out_done, w + 1)
                        if back:
                            dve.tensor_tensor(y[:, h, :], y[:, h, :], bank(k.ps, 7), ALU.add).then_inc(y_used, 1)
                        else:
                            dve.tensor_copy(y[:, h, :], bank(k.ps, 7)).then_inc(y_used, 1)

            @block.tensor
            def _(pe):
                for u in range(UNITS):
                    L, qs, ks, qb, kh, sc, kh_tok, v_tok, S = parts(u)
                    pe.wait_ge(prep, PREP * (u + 1))
                    for n, src in enumerate((kh, i_[:, u % HH, :])):
                        if u:
                            pe.wait_ge(turned_used, 2 * u)
                        for j in range(NT):
                            mm = pe.transpose(k.ps[:, 1 + n, j * P:(j + 1) * P], src[:, j * P:(j + 1) * P],
                                              k.const("ident"))
                        mm.then_inc(turned, 1)
                    if u:
                        pe.wait_ge(masked, u)
                    for j in range(NT):
                        c = slice(j * P, (j + 1) * P)
                        mm = pe.matmul(k.ps[:, 0, c], ks[:, c], qs[:, c], start=True, stop=True)
                    mm.then_inc(scored, 1)
                    pe.wait_ge(turned_used, 2 * u + 2)
                    if u:
                        pe.wait_ge(state_ready, (NC - 1) * u)
                    for j in range(NT):
                        for c in range(NT):
                            rows = slice(CH * c, CH * c + CH)
                            mm = pe.matmul(k.ps[:, 3 + c, j * P:(j + 1) * P], kh_tok[rows, j * P:(j + 1) * P],
                                           v_tok[rows, j * P:(j + 1) * P], start=True, stop=True,
                                           tile_position=(CH * c, 0))
                    mm.then_inc(inputs_done, 1)
                    pe.wait_ge(masked, u + 1)
                    if u:
                        pe.wait_ge(y_used, u)
                    for j in range(NT):
                        c = slice(j * P, (j + 1) * P)
                        pe.matmul(k.ps[:, 7, c], v_tok[:, c], sc[:, c], start=(j == 0), stop=False,
                                  skip_group_check=True)
                    pe.wait_ge(state_ready, (NC - 1) * (u + 1))
                    for i, c in enumerate(order(u)[1:]):
                        ts = slice(CH * c, CH * c + CH)
                        mm = pe.matmul(k.ps[:, 7, ts], S[:, order(u)[i], :], qb[:, ts], start=False,
                                       stop=(i == NC - 2), skip_group_check=True)
                    mm.then_inc(out_done, 1)

        head_norm(k, y, HH, P, "hgrn_norm", k.const("eps")[:, 0:1], g_)


def head_norm(k, y, tiles, head, weight, eps, gate, factor=1.0):
    nc = k.nc
    over = k.const("ones") if head == P else k.const("pair")
    with ExitStack() as inner:
        sq = k.sbuf(inner, "squares", [P, 2, T])
        rt = k.sbuf(inner, "rstd", [P, 2, T])
        squared, summed, root, inverse, scaled, normed = semaphores(
            k, inner, "squared summed root inverse scaled normed")
        block = inner.enter_context(nc.Block())

        @block.scalar
        def _(act):
            for m in range(tiles):
                if m >= 2:
                    act.wait_ge(summed, m - 1)
                    act.wait_ge(scaled, m - 1)
                act.activation(sq[:, m % 2, :], y[:, m, :], ACT.Square).then_inc(squared, 1)
                act.wait_ge(summed, m + 1)
                act.activation(rt[:, m % 2, :], bank(k.ps, m % 2), ACT.Sqrt, bias=eps,
                               scale=1.0 / (head * factor * factor))\
                    .then_inc(root, 1)

        @block.tensor
        def _(pe):
            for m in range(tiles):
                pe.wait_ge(squared, m + 1)
                if m >= 2:
                    pe.wait_ge(root, m - 1)
                pe.matmul(bank(k.ps, m % 2), over, sq[:, m % 2, :], start=True, stop=True).then_inc(summed, 1)

        @block.vector
        def _(dve):
            for m in range(tiles):
                dve.wait_ge(root, m + 1)
                dve.reciprocal(rt[:, m % 2, :], rt[:, m % 2, :]).then_inc(inverse, 1)
                dve.wait_ge(inverse, m + 1)
                dve.scalar_tensor_tensor(out=y[:, m, :], in0=y[:, m, :], scalar=k.col(weight, m),
                                         in1=rt[:, m % 2, :], op0=ALU.mult, op1=ALU.mult).then_inc(scaled, 1)
                if gate is not None:
                    dve.wait_ge(scaled, m + 1)
                    dve.tensor_tensor(y[:, m, :], y[:, m, :], gate[:, m, :], ALU.mult).then_inc(normed, 1)


def mlstm_branch(k, n_layer, y, norm):
    nc = k.nc
    H, N, PAD = A_HEADS, 2 * A_WIDTH // P, A_CONV // 2
    n = n_layer
    with ExitStack() as ctx:
        sb = lambda name, shape: k.sbuf(ctx, name, shape)
        raw = sb("qk_raw", [P, N, T + 2 * PAD])
        qk = sb("qk", [P, N, T])
        v_tok = sb("v_tok", [P, NT, A_WIDTH])
        o_gate = sb("o_gate", [P, H, T])
        rows = sb("gate_rows", [16, 1, T])
        gates = sb("gate_kinds", [H, 4, T])
        work = sb("gate_work", [H, 2, T])
        b_, g_, M_, m_ = [sb(name, [H, 2, T]) for name in ("b_rows", "g_rows", "max_rows", "m_rows")]
        g_col = sb("g_cols", [P, NT, 2, H])
        project(k, [(f"w_a_qk{n}", raw[:, :, PAD:PAD + T], 1.0), (f"w_a_o{n}", o_gate[:, :, :], 1.0),
                    (f"w_a_gates{n}", rows, 1.0)], k.xn, norm, tokens=(f"w_a_v{n}", v_tok))
        rows = rows[:, 0, :]

        with ExitStack() as inner:
            tap = k.sbuf(inner, "tap", [P, 2, T])
            (edges, tapped, activated, biased, picked, steps, logs, rows_ready, m_ready, cols_turned,
             cols_ready, o_ready) = semaphores(
                k, inner, "edges tapped activated biased picked steps logs rows_ready m_ready cols_turned "
                "cols_ready o_ready")
            block = inner.enter_context(nc.Block())

            @block.gpsimd
            def _(pool):
                pool.memset(raw[:, :, 0:PAD], 0.0).then_inc(edges, 1)
                pool.memset(raw[:, :, PAD + T:], 0.0).then_inc(edges, 1)

            @block.tensor
            def _(pe):
                pe.wait_ge(biased, 1)
                for r in range(4):
                    mm = pe.matmul(k.ps[0:H, r, :], k.const("ident", 16)[:, H * r:H * r + H], rows[:, :],
                                   start=True, stop=True)
                mm.then_inc(picked, 1)
                cols = k.ps[:, 4, 0:NT * 2 * H].rearrange("p (j r h) -> p j r h", j=NT, r=2)
                pe.wait_ge(rows_ready, 10)
                for j in range(NT):
                    for r in range(2):
                        mm = pe.transpose(cols[:, j, r, :], g_[:, r, j * P:(j + 1) * P], k.const("ident", H)[:, 0:H])
                mm.then_inc(cols_turned, 1)

            @block.scalar
            def _(act):
                act.activation(rows[:, :], rows[:, :], ACT.Identity, bias=k.col(f"a_bias{n}", 0, 16)).then_inc(biased, 1)
                act.wait_ge(picked, 1)
                for r in range(4):
                    act.activation(gates[:, r, :], k.ps[0:H, r, :], ACT.Copy).then_inc(steps, 1)
                act.wait_ge(steps, 4)
                act.activation(work[:, :, :], gates[:, 1::2, :], ACT.Abs).then_inc(logs, 1)
                act.wait_ge(logs, 1)
                act.activation(work[:, :, :], work[:, :, :], ACT.Exp, scale=-1.0).then_inc(logs, 1)
                act.wait_ge(logs, 2)
                act.activation(work[:, :, :], work[:, :, :], ACT.Ln, bias=k.const("ones", H)[:, 0:1]).then_inc(logs, 1)
                act.wait_ge(rows_ready, 10)
                act.activation(m_[:, :, :], m_[:, :, :], ACT.Exp, scale=-1.0).then_inc(m_ready, 1)
                act.wait_ge(cols_turned, 1)
                cols = k.ps[:, 4, 0:NT * 2 * H].rearrange("p (j r h) -> p j r h", j=NT, r=2)
                act.activation(g_col[:, :, :, :], cols, ACT.Copy).then_inc(cols_ready, 1)
                for m in range(H):
                    act.activation(o_gate[:, m, :], o_gate[:, m, :], ACT.Sigmoid).then_inc(o_ready, 1)
                for m in range(N):
                    act.wait_ge(tapped, A_CONV * (m + 1))
                    act.activation(qk[:, m, :], tap[:, m % 2, :], ACT.Silu).then_inc(activated, 1)
                act.wait_ge(activated, N)
                act.activation(qk[:, H:N, :], qk[:, H:N, :], ACT.Copy, scale=float(P) ** -0.5).then_inc(activated, 1)

            @block.vector
            def _(dve):
                dve.wait_ge(logs, 3)
                for r in range(2):
                    step = -1 if r else 1
                    base = 5 * r
                    dve.scalar_tensor_tensor(out=work[:, r, :], in0=gates[:, 2 * r + 1, :], scalar=0.0,
                                             in1=work[:, r, :], op0=ALU.min, op1=ALU.subtract).then_inc(rows_ready, 1)
                    dve.wait_ge(rows_ready, base + 1)
                    dve.tensor_tensor_scan(b_[:, r, ::step], k.const("ones", H)[:, 0:1].broadcast_to([H, T]),
                                           work[:, r, ::step], 0.0, ALU.mult, ALU.add).then_inc(rows_ready, 1)
                    dve.wait_ge(rows_ready, base + 2)
                    dve.tensor_tensor(g_[:, r, :], gates[:, 2 * r, :], b_[:, r, :], ALU.subtract).then_inc(rows_ready, 1)
                    dve.wait_ge(rows_ready, base + 3)
                    dve.tensor_tensor_scan(M_[:, r, ::step], g_[:, r, ::step], g_[:, r, ::step], 0.0, ALU.max, ALU.max)\
                        .then_inc(rows_ready, 1)
                    dve.wait_ge(rows_ready, base + 4)
                    dve.tensor_tensor(m_[:, r, :], b_[:, r, :], M_[:, r, :], ALU.add).then_inc(rows_ready, 1)
                dve.wait_ge(edges, 2)
                for m in range(N):
                    o = tap[:, m % 2, :]
                    if m >= 2:
                        dve.wait_ge(activated, m - 1)
                    dve.tensor_scalar(o, raw[:, m, 0:T], k.col(f"a_conv{n}", m), None, ALU.mult).then_inc(tapped, 1)
                    for j in range(1, A_CONV):
                        dve.wait_ge(tapped, A_CONV * m + j)
                        dve.scalar_tensor_tensor(out=o, in0=raw[:, m, j:j + T], scalar=k.col(f"a_conv{n}", j * N + m),
                                                 in1=o, op0=ALU.mult, op1=ALU.add).then_inc(tapped, 1)

        with ExitStack() as inner:
            dist, prob, den = [raw[:, :, :].rearrange("p a b -> p (a b)")[:, 2 * n * T:2 * (n + 1) * T].rearrange(
                "p (a t) -> p a t", a=2) for n in range(3)]
            (spread, bounded, exped, masked, qk_done, prob_ready, pv_done, floor_spread, den_ready, den_step,
             h_ready) = semaphores(
                k, inner, "spread bounded exped masked qk_done prob_ready pv_done floor_spread den_ready "
                "den_step h_ready")
            block = inner.enter_context(nc.Block())
            UNITS = 2 * H
            STEPS = UNITS * NT

            def place(s):
                u = s // NT
                back, h = u % 2, u // 2
                j = NT - 1 - s % NT if back else s % NT
                return u, back, h, j, (slice(0, (j + 1) * P) if back else slice(j * P, T))

            @block.tensor
            def _(pe):
                def weigh(s):
                    u, back, h, j, ts = place(s)
                    pe.wait_ge(prob_ready, s + 1)
                    if s % NT == 0 and u >= 2:
                        pe.wait_ge(h_ready, u - 1)
                    pr = prob[:, s % 2, ts]
                    pe.matmul(k.ps[:, 4 + u % 2, ts], v_tok[:, j, h * P:(h + 1) * P], pr, start=(s % NT == 0),
                              stop=(s % NT == NT - 1))
                    pe.matmul(k.ps[:, 6 + u % 2, ts], k.const("ones"), pr, start=(s % NT == 0),
                              stop=(s % NT == NT - 1)).then_inc(pv_done, 1)
                    if s % NT == NT - 1:
                        pe.wait_ge(bounded, s + 1)
                        pe.matmul(bank(k.ps, u % 2), k.const("ident", H)[:, h:h + 1].broadcast_to([H, P]),
                                  m_[:, back, :], start=True, stop=True).then_inc(floor_spread, 1)

                for s in range(STEPS):
                    u, back, h, j, ts = place(s)
                    if s % NT == 0:
                        if u >= 2:
                            pe.wait_ge(h_ready, u - 1)
                        pe.matmul(bank(k.ps, u % 2), k.const("ident", H)[:, h:h + 1].broadcast_to([H, P]),
                                  M_[:, back, :], start=True, stop=True).then_inc(spread, 1)
                    if s >= 2:
                        pe.wait_ge(prob_ready, s - 1)
                    pe.matmul(k.ps[:, 2 + s % 2, ts], qk[:, H + h, j * P:(j + 1) * P], qk[:, h, ts],
                              start=True, stop=True).then_inc(qk_done, 1)
                    if s:
                        weigh(s - 1)
                weigh(STEPS - 1)

            @block.gpsimd
            def _(pool):
                for s in range(STEPS):
                    u, back, h, j, ts = place(s)
                    pool.wait_ge(exped, s + 1)
                    d = dist[:, s % 2, j * P:(j + 1) * P]
                    pool.tensor_tensor(d, d, k.const("ge" if back else "le"), ALU.mult).then_inc(masked, 1)

            @block.scalar
            def _(act):
                def absolute(u):
                    act.wait_ge(pv_done, NT * (u + 1))
                    act.activation(den[:, u % 2, :], bank(k.ps, 6 + u % 2), ACT.Abs).then_inc(den_ready, 1)
                for s in range(STEPS):
                    u, back, h, j, ts = place(s)
                    act.wait_ge(bounded, s + 1)
                    act.activation(dist[:, s % 2, ts], dist[:, s % 2, ts], ACT.Exp, scale=-1.0).then_inc(exped, 1)
                    if s % NT == 2 and u:
                        absolute(u - 1)
                absolute(UNITS - 1)

            @block.vector
            def _(dve):
                def weight(s):
                    u, back, h, j, ts = place(s)
                    dve.wait_ge(masked, s + 1)
                    dve.wait_ge(qk_done, s + 1)
                    if s >= 2:
                        dve.wait_ge(pv_done, s - 1)
                    dve.tensor_tensor(prob[:, s % 2, ts], dist[:, s % 2, ts], k.ps[:, 2 + s % 2, ts], ALU.mult)\
                        .then_inc(prob_ready, 1)

                def finish(u):
                    back, h, d = u % 2, u // 2, den[:, u % 2, :]
                    dve.wait_ge(den_ready, u + 1)
                    dve.wait_ge(floor_spread, u + 1)
                    dve.tensor_tensor(d, d, bank(k.ps, u % 2), ALU.max).then_inc(den_step, 1)
                    dve.wait_ge(den_step, 3 * u + 1)
                    dve.reciprocal(d, d).then_inc(den_step, 1)
                    dve.wait_ge(den_step, 3 * u + 2)
                    if back:
                        dve.tensor_tensor(d, d, bank(k.ps, 4 + u % 2), ALU.mult).then_inc(den_step, 1)
                        dve.wait_ge(den_step, 3 * u + 3)
                        dve.tensor_tensor(y[:, h, :], y[:, h, :], d, ALU.add).then_inc(h_ready, 1)
                    else:
                        dve.tensor_tensor(y[:, h, :], d, bank(k.ps, 4 + u % 2), ALU.mult).then_inc(h_ready, 1)
                        dve.wait_ge(h_ready, u + 1)
                        dve.tensor_copy(d[:, 0:1], y[:, h, 0:1]).then_inc(den_step, 1)

                for s in range(STEPS):
                    u, back, h, j, ts = place(s)
                    dve.wait_ge(spread, u + 1)
                    if s >= 2:
                        dve.wait_ge(prob_ready, s - 1)
                    dve.tensor_scalar(dist[:, s % 2, ts], k.ps[:, u % 2, ts], g_col[:, j, back, h:h + 1], 0.0,
                                      ALU.subtract, ALU.max).then_inc(bounded, 1)
                    if s:
                        weight(s - 1)
                    if s % NT == 2 and u:
                        finish(u - 1)
                weight(STEPS - 1)
                finish(UNITS - 1)

        with ExitStack() as inner:
            mean_done, centred = semaphores(k, inner, "mean_done centred")
            block = inner.enter_context(nc.Block())

            @block.tensor
            def _(pe):
                for m in range(H):
                    pe.matmul(bank(k.ps, m), k.const("ones"), y[:, m, :], start=True, stop=True).then_inc(mean_done, 1)

            @block.vector
            def _(dve):
                for m in range(H):
                    dve.wait_ge(mean_done, m + 1)
                    dve.scalar_tensor_tensor(out=y[:, m, :], in0=bank(k.ps, m), scalar=-1.0 / P, in1=y[:, m, :],
                                             op0=ALU.mult, op1=ALU.add).then_inc(centred, 1)
        head_norm(k, y, H, P, f"a_norm{n}", k.const("eps")[:, 0:1], o_gate[:, :, :])


def attention(k, y, heads, maps, q_of, k_of, v_of, width, bias_of=None, neg_lambda=None, prepare=None):
    nc = k.nc
    with ExitStack() as ctx:
        sb = lambda name, shape: k.sbuf(ctx, name, shape)
        RS, RE = 3, 4
        logits = sb("logits", [P, RS, T]) if bias_of else None
        expd = sb("exps", [P, RE, T])
        pt = sb("prob_t", [P, 2, NT, T])
        stat = sb("statistics", [P, 4, 8])
        (scores_done, fronts, exps, norms, turned, taken, pv_done, y_used, bias_ready) = semaphores(
            k, ctx, "scores_done fronts exps norms turned taken pv_done y_used bias_ready")
        block = ctx.enter_context(nc.Block())
        N = heads * NT * maps
        NPC = 2 if maps == 1 else 5

        def place(n):
            m = n // maps
            return m // NT, m % NT, n % maps

        @block.tensor
        def _(pe):
            def turn(m):
                pe.wait_ge(norms, NPC * (m + 1))
                if m >= 2:
                    pe.wait_ge(taken, m - 1)
                for j in range(NT):
                    mm = pe.transpose(k.ps[:, 3 + m % 2, j * P:(j + 1) * P],
                                      expd[:, (maps * m) % RE, j * P:(j + 1) * P], k.const("ident"))
                mm.then_inc(turned, 1)

            def weigh(h):
                pe.wait_ge(taken, NT * (h + 1))
                if h >= 2:
                    pe.wait_ge(y_used, h - 1)
                r0 = 0 if width == P else 64 * (h % 2)
                for j in range(NT):
                    mm = pe.matmul(k.ps[r0:r0 + width, 5 + h % 2, :], v_of(h, j), pt[:, h % 2, j, :],
                                   start=(j == 0), stop=(j == NT - 1))
                mm.then_inc(pv_done, 1)

            for n in range(N + 4):
                if n < N:
                    h, i, c = place(n)
                    if n >= RS:
                        pe.wait_ge(exps if bias_of is None else fronts,
                                   n - RS + 1 if bias_of is None else 2 * (n - RS) + 2)
                    pe.matmul(bank(k.ps, n % RS), q_of(h, c)[:, i * P:(i + 1) * P], k_of(h, c),
                              start=True, stop=True).then_inc(scores_done, 1)
                if 0 <= n - 2 < N and (n - 1) % maps == 0:
                    turn((n - 2) // maps)
                if 0 <= n - 3 < N and (n - 2) % (NT * maps) == 0:
                    weigh((n - 3) // (NT * maps))

        if prepare is not None:
            @block.gpsimd
            def _(pool):
                for h in range(heads):
                    if h >= 2:
                        pool.wait_ge(fronts, 2 * NT * maps * (h - 1))
                    prepare(pool, h).then_inc(bias_ready, 1)

        @block.scalar
        def _(act):
            def take(m):
                h, i = m // NT, m % NT
                act.wait_ge(turned, m + 1)
                if i == 0 and h >= 2:
                    act.wait_ge(pv_done, h - 1)
                act.activation(pt[:, h % 2, :, i * P:(i + 1) * P],
                               bank(k.ps, 3 + m % 2).rearrange("p (j t) -> p j t", j=NT), ACT.Copy).then_inc(taken, 1)

            for n in range(N + 2):
                if n < N:
                    act.wait_ge(fronts, 2 * n + 2)
                    if n >= RE:
                        act.wait_ge(turned, (n - RE) // maps + 1)
                    act.activation(expd[:, n % RE, :], bank(k.ps, n % RS) if bias_of is None else logits[:, n % RS, :],
                                   ACT.Exp, bias=stat[:, 1, n % 8:n % 8 + 1],
                                   accum_out=stat[:, 2, n % 8:n % 8 + 1]).then_inc(exps, 1)
                if 0 <= n - 2 < N and (n - 1) % maps == 0:
                    take((n - 2) // maps)

        @block.vector
        def _(dve):
            def normalise(n):
                h, i, c = place(n)
                m = n // maps
                s = slice(n % 8, n % 8 + 1)
                e = expd[:, n % RE, :]
                base = NPC * m + (2 if c else 0)
                dve.wait_ge(exps, n + 1)
                dve.reciprocal(stat[:, 3, s], stat[:, 2, s]).then_inc(norms, 1)
                dve.wait_ge(norms, base + 1)
                if c == 0:
                    dve.tensor_scalar(e, e, stat[:, 3, s], None, ALU.mult).then_inc(norms, 1)
                    return
                dve.tensor_scalar(stat[:, 3, s], stat[:, 3, s], neg_lambda, None, ALU.mult).then_inc(norms, 1)
                dve.wait_ge(norms, base + 2)
                first = expd[:, (n - 1) % RE, :]
                dve.scalar_tensor_tensor(out=first, in0=e, scalar=stat[:, 3, s], in1=first, op0=ALU.mult,
                                         op1=ALU.add).then_inc(norms, 1)

            def output(h):
                dve.wait_ge(pv_done, h + 1)
                if width == P:
                    dve.tensor_copy(y[:, h, :], bank(k.ps, 5 + h % 2)).then_inc(y_used, 1)
                else:
                    r = slice(64 * (h % 2), 64 * (h % 2) + 64)
                    dve.tensor_copy(y[r, h // 2, :], k.ps[r, 5 + h % 2, :]).then_inc(y_used, 1)

            for n in range(N + 5):
                if n < N:
                    h, i, c = place(n)
                    s = slice(n % 8, n % 8 + 1)
                    dve.wait_ge(scores_done, n + 1)
                    if bias_of is None:
                        dve.tensor_reduce(stat[:, 0, s], bank(k.ps, n % RS), AX.X, ALU.max).then_inc(fronts, 1)
                    else:
                        if prepare is not None:
                            dve.wait_ge(bias_ready, h + 1)
                        if n >= RS:
                            dve.wait_ge(exps, n - RS + 1)
                        dve.tensor_tensor_reduce(out=logits[:, n % RS, :], in0=bank(k.ps, n % RS), in1=bias_of(h, i),
                                                 scale=1.0, scalar=-3.0e38, op0=ALU.add, op1=ALU.max,
                                                 accum_out=stat[:, 0, s]).then_inc(fronts, 1)
                    dve.wait_ge(fronts, 2 * n + 1)
                    dve.tensor_scalar(stat[:, 1, s], stat[:, 0, s], -1.0, None, ALU.mult).then_inc(fronts, 1)
                if 0 <= n - 1 < N:
                    normalise(n - 1)
                if 0 <= n - 4 < N and (n - 3) % (NT * maps) == 0:
                    output((n - 4) // (NT * maps))


def gqa_branch(k, n, y):
    nc = k.nc
    with ExitStack() as ctx:
        sb = lambda name, shape: k.sbuf(ctx, name, shape)
        qk = sb("qk", [P, 5, T])
        k2 = sb("keys_twice", [P, 2, T])
        v_tok = sb("v_tok", [P, NT, P])
        project(k, [(f"w_b_q{n}", qk[:, 0:4, :], 1.0), (f"w_b_k{n}", qk[:, 4:5, :], 1.0)], k.xn,
                tokens=(f"w_b_v{n}", v_tok))
        with ExitStack() as inner:
            sq = k.sbuf(inner, "squares", [P, 2, T])
            rt = k.sbuf(inner, "rstd", [P, 2, T])
            squared, summed, root, inverse, normed, rotated, roped, doubled, keys_ready = semaphores(
                k, inner, "squared summed root inverse normed rotated roped doubled keys_ready")
            block = inner.enter_context(nc.Block())

            @block.scalar
            def _(act):
                for m in range(5):
                    if m >= 2:
                        act.wait_ge(roped, 3 * (m - 1))
                    act.activation(sq[:, m % 2, :], qk[:, m, :], ACT.Square).then_inc(squared, 1)
                    act.wait_ge(summed, m + 1)
                    key = m == 4
                    act.activation(rt[:, m % 2, :], bank(k.ps, m % 2), ACT.Sqrt,
                                   bias=k.const("eps")[:, 0:1] if key else k.const("eps")[:, 3:4],
                                   scale=1.0 / 64 if key else 1.0).then_inc(root, 1)
                for g in range(2):
                    act.wait_ge(doubled, g + 1)
                    act.activation(k2[:, g, :], bank(k.ps, 4 + g), ACT.Copy).then_inc(keys_ready, 1)

            @block.tensor
            def _(pe):
                for m in range(5):
                    pe.wait_ge(squared, m + 1)
                    pe.matmul(bank(k.ps, m % 2), k.const("pair"), sq[:, m % 2, :], start=True, stop=True)\
                        .then_inc(summed, 1)
                    pe.wait_ge(normed, m + 1)
                    pe.matmul(bank(k.ps, 2 + m % 2), k.const("turn"), qk[:, m, :], start=True, stop=True)\
                        .then_inc(rotated, 1)
                pe.wait_ge(roped, 15)
                for g in range(2):
                    pe.matmul(bank(k.ps, 4 + g), k.const("dup")[:, g * P:(g + 1) * P], qk[:, 4, :],
                              start=True, stop=True).then_inc(doubled, 1)

            @block.vector
            def _(dve):
                for m in range(5):
                    r, s = rt[:, m % 2, :], sq[:, m % 2, :]
                    dve.wait_ge(root, m + 1)
                    dve.reciprocal(r, r).then_inc(inverse, 1)
                    dve.wait_ge(inverse, m + 1)
                    dve.scalar_tensor_tensor(out=qk[:, m, :], in0=qk[:, m, :],
                                             scalar=k.col(f"b_knorm{n}" if m == 4 else f"b_qnorm{n}"),
                                             in1=r, op0=ALU.mult, op1=ALU.mult).then_inc(normed, 1)
                    dve.wait_ge(rotated, m + 1)
                    dve.tensor_tensor(s, bank(k.ps, 2 + m % 2), k.const("sin"), ALU.mult).then_inc(roped, 1)
                    dve.tensor_tensor(r, qk[:, m, :], k.const("cos"), ALU.mult).then_inc(roped, 1)
                    dve.wait_ge(roped, 3 * m + 2)
                    dve.tensor_tensor(qk[:, m, :], r, s, ALU.add).then_inc(roped, 1)

        half = lambda h: slice(64 * (h % 2), 64 * (h % 2) + 64)
        attention(k, y, B_HEADS, 1, lambda h, c: qk[half(h), h // 2, :],
                  lambda h, c: k2[half(h), h // 4, :], lambda h, j: v_tok[:, j, 64 * (h // 4):64 * (h // 4) + 64], 64)


def natten_branch(k, n, y):
    nc = k.nc
    with ExitStack() as ctx:
        sb = lambda name, shape: k.sbuf(ctx, name, shape)
        qk = sb("qk", [P, 8, T])
        v_tok = sb("v_tok", [P, NT, 512])
        table = sb("bias_table", [P, C_HEADS, 16, GRID_W])
        project(k, [(f"w_c_qk{n}", qk[:, :, :], 1.0)], k.xn, tokens=(f"w_c_v{n}", v_tok))
        with ExitStack() as inner:
            rpb = k.sbuf(inner, "rpb", [P, P])
            rpb_in, shifted, table_ready, scaled = semaphores(k, inner, "rpb_in shifted table_ready scaled")
            block = inner.enter_context(nc.Block())
            band = k.const("band", 64)

            @block.sync
            def _(sp):
                sp.dma_start(rpb[:, :], k.dram[f"rpb{n}"]).then_inc(rpb_in, 16)

            @block.scalar
            def _(act):
                act.activation(qk[:, 0:4, :], qk[:, 0:4, :], ACT.Copy, scale=0.125).then_inc(scaled, 1)

            @block.tensor
            def _(pe):
                pe.wait_ge(rpb_in, 16)
                for kc in range(GRID_W):
                    g = kc // 4
                    if kc % 4 == 0 and g >= 2:
                        pe.wait_ge(table_ready, g - 1)
                    mm = pe.matmul(k.ps[:, g % 2, (kc % 4) * P:(kc % 4 + 1) * P], band[:, 63 - kc:191 - kc],
                                   rpb[0:64, :], start=True, stop=True)
                    if kc % 4 == 3:
                        mm.then_inc(shifted, 1)

            @block.vector
            def _(dve):
                flat_table = table[:, :, :, :].rearrange("p h j c -> p c (h j)")
                for g in range(GRID_W // 4):
                    dve.wait_ge(shifted, g + 1)
                    cs = slice(4 * g, 4 * g + 4)
                    dve.tensor_tensor(flat_table[:, cs, :], bank(k.ps, g % 2).rearrange("p (c m) -> p c m", c=4),
                                      k.const("window")[:, cs, None].broadcast_to([P, 4, P]), ALU.add)\
                        .then_inc(table_ready, 1)

        half = lambda h: slice(64 * (h % 2), 64 * (h % 2) + 64)
        attention(k, y, C_HEADS, 1, lambda h, c: qk[half(h), h // 2, :], lambda h, c: qk[half(h), 4 + h // 2, :],
                  lambda h, j: v_tok[:, j, 64 * h:64 * h + 64], 64,
                  bias_of=lambda h, i: table[:, h, 7 - 2 * i:15 - 2 * i, :].rearrange("p j c -> p (j c)"))


def diff_branch(k, n, y):
    nc = k.nc
    with ExitStack() as ctx:
        sb = lambda name, shape: k.sbuf(ctx, name, shape)
        qk = sb("qk", [P, 8, T])
        v_tok = sb("v_tok", [P, NT, 512])
        lam = sb("lambda", [P, 8])
        slope = sb("distance_bias", [P, 2, 896])
        project(k, [(f"w_d_qk{n}", qk[:, :, :], 1.0)], k.xn, tokens=(f"w_d_v{n}", v_tok))
        with ExitStack() as inner:
            scaled, products, dots, dots_exp, lam_ready = semaphores(
                k, inner, "scaled products dots dots_exp lam_ready")
            block = inner.enter_context(nc.Block())
            a, _ = k.col_at[f"lambda{n}"]

            @block.scalar
            def _(act):
                act.activation(qk[:, 0:4, :], qk[:, 0:4, :], ACT.Copy, scale=0.125).then_inc(scaled, 1)
                act.wait_ge(dots, 1)
                act.activation(lam[:, 2:4], k.ps[:, 0, 0:2], ACT.Exp).then_inc(dots_exp, 1)

            @block.tensor
            def _(pe):
                pe.wait_ge(products, 1)
                pe.matmul(k.ps[:, 0, 0:2], k.const("ones"), lam[:, 0:2], start=True, stop=True).then_inc(dots, 1)

            @block.vector
            def _(dve):
                dve.tensor_tensor(lam[:, 0:2], k.cols[:, a:a + 2], k.cols[:, a + 2:a + 4], ALU.mult)\
                    .then_inc(products, 1)
                dve.wait_ge(dots_exp, 1)
                dve.tensor_tensor(lam[:, 4:5], lam[:, 3:4], lam[:, 2:3], ALU.subtract).then_inc(lam_ready, 1)
                dve.wait_ge(lam_ready, 1)
                dve.tensor_scalar(lam[:, 5:6], lam[:, 4:5], -LAMBDA_INIT[n], None, ALU.add).then_inc(lam_ready, 1)

        def prepare(pool, h):
            return pool.tensor_scalar(slope[:, h % 2, :], k.const("distance"), -(2.0 ** (-8.0 * (h + 1) / D_HEADS)),
                                      None, ALU.mult)

        half = lambda h: slice(64 * (h % 2), 64 * (h % 2) + 64)
        attention(k, y, D_HEADS, 2, lambda h, c: qk[half(h), 2 * c + h // 2, :],
                  lambda h, c: qk[half(h), 4 + 2 * c + h // 2, :], lambda h, j: v_tok[:, j, P * h:P * h + P], P,
                  bias_of=lambda h, i: slope[:, h % 2, 384 - P * i:896 - P * i],
                  neg_lambda=lam[:, 5:6], prepare=prepare)
        head_norm(k, y, D_HEADS, P, f"d_subln{n}", k.const("eps")[:, 4 + n:5 + n], None,
                  1.0 - LAMBDA_INIT[n])


def merge_and_feed(k, branches, spare, w_out, norm, w_ffn, w_down):
    with ExitStack() as ctx:
        mixed, mixed_lo = k.both_kinds(ctx, "mixed", [P, KD, T])
        y_hi = ctx.enter_context(k.nc.sbuf_tensor(f"y_hi_{k.nc.next_id()}", [P, KD, T], F32R))
        gate = k.sbuf(ctx, "gate", [P, 2, T])
        for b, (w, src, lo) in enumerate(branches):
            parts = Parts(src, lo, y_hi[:, 0:src.shape[1], :])
            gated_product(k, w, k.xn, parts, ACT.Sigmoid, mixed, b > 0, Split(parts), 1, gate)
        parts = Parts(mixed[:, :, :], mixed_lo[:, :, :], k.xn.hi)
        project(k, [(w_out, k.x, "add")], parts, Split(parts))
    with ExitStack() as ctx:
        hidden, hidden_lo = k.both_kinds(ctx, "hidden", [P, KF, T])
        hidden_hi = ctx.enter_context(k.nc.sbuf_tensor(f"hidden_hi_{k.nc.next_id()}", [P, KF, T], F32R))
        gated_product(k, w_ffn, k.xn, k.xn, ACT.Silu, hidden, False, Norm(k.x, k.xn, norm, spare[:, 0:3, :]), 0,
                      spare[:, 3:5, :])
        parts = Parts(hidden[:, :, :], hidden_lo[:, :, :], hidden_hi[:, :, :])
        project(k, [(w_down, k.x, "add")], parts, Split(parts))


def stream_plan():
    ffn = lambda n: [planned(f"w_out{n}", KD, KD), planned(f"w_ffn{n}", KF, KD, KD), planned(f"w_down{n}", KD, KF)]
    plan = [planned("w_xbc", SSM_XBC // P, KD), planned("w_dt", 2, KD), planned("w_z", KD, KD),
            planned("w_rwkv", RWKV_COLS // P, KD), None,
            planned("w_hgrn", 5 * HGRN_W // P, KD),
            planned("w_mix_ssm", KD, KD, KD), planned("w_mix_rwkv", KD, KD, 4), planned("w_mix_hgrn", KD, KD, 4)]
    plan += ffn("")
    for n in range(LAYERS):
        plan += [planned(f"w_a_qk{n}", 8, KD), planned(f"w_a_o{n}", 4, KD), planned(f"w_a_gates{n}", 1, KD),
                 planned(f"w_a_v{n}", 1, 32),
                 planned(f"w_b_q{n}", 4, KD), planned(f"w_b_k{n}", 1, KD), planned(f"w_b_v{n}", 1, KD),
                 planned(f"w_c_qk{n}", 8, KD), planned(f"w_c_v{n}", 1, 32),
                 planned(f"w_d_qk{n}", 8, KD), planned(f"w_d_v{n}", 1, 32)]
        plan += [planned(f"w_mix_{name}{n}", KD, KD, 4) for name in "abcd"] + ffn(n)
    return plan


def hybrid_program(nc, dram, const_at, n_const, col_at, n_col):
    k = Kernel(nc, dram, const_at, col_at)
    k.stream = Stream(k, stream_plan())
    with ExitStack() as ctx:
        sb = lambda name, shape, dtype=F32: ctx.enter_context(nc.sbuf_tensor(name, shape, dtype))
        (xn, xn_lo), xn_hi = k.both_kinds(ctx, "xn", [P, KD, T]), sb("xn_hi", [P, KD, T], F32R)
        k.xn = Parts(xn[:, :, :], xn_lo[:, :, :], xn_hi[:, :, :])
        k.raw = sb("raw_weights", [P, AHEAD_RAW, KD * P])
        (k.idle_hi, k.w_hi), (k.idle_lo, k.w_lo) = [
            k.both_kinds(ctx, name, [P, AHEAD_PARTS, KD * P]) for name in ("weights_hi", "weights_lo")]
        k.consts = sb("consts", [P, n_const])
        k.cols = sb("cols", [P, n_col])
        y, y_lo = k.both_kinds(ctx, "y", [P, 16, T])
        k.ps = ctx.enter_context(nc.psum_tensor("ps", [P, 8, T], F32))
        load_constants(k, dram["cols"])
        with ExitStack() as inner:
            k.x = k.sbuf(inner, "x", [P, KD, T])
            load_x(k)
            ssm_branch(k, y, Norm(k.x, k.xn, "norm1"))
        rwkv_branch(k, y[:, 8:12, :])
        hgrn_branch(k, y[:, 12:16, :])
        k.x = sb("x_again", [P, KD, T])
        load_x(k, (dram["consts_2"], const_at["cos"][0]))
        merge_and_feed(k, [(f"w_mix_{name}", y[:, a:b, :], y_lo[:, a:b, :])
                           for name, a, b in (("ssm", 0, 8), ("rwkv", 8, 12), ("hgrn", 12, 16))],
                       y, "w_out", "norm2", "w_ffn", "w_down")
        rms_norm(k, k.x, k.x, "norm3")
        for n in range(LAYERS):
            mlstm_branch(k, n, y[:, 0:4, :], Norm(k.x, k.xn, f"norm1_{n}"))
            gqa_branch(k, n, y[:, 4:8, :])
            natten_branch(k, n, y[:, 8:12, :])
            diff_branch(k, n, y[:, 12:16, :])
            merge_and_feed(k, [(f"w_mix_{name}{n}", y[:, 4 * b:4 * b + 4, :], y_lo[:, 4 * b:4 * b + 4, :])
                               for b, name in enumerate("abcd")],
                           y, f"w_out{n}", f"norm2_{n}", f"w_ffn{n}", f"w_down{n}")
        rms_norm(k, k.x, xn, "final")
        store_x(k, xn)


def kernel(**inputs):
    import concourse.bacc as bacc
    from concourse.bass_utils import run_bass_kernel_spmd

    x = {name: np.asarray(a) for name, a in inputs.items()}
    weights, cols = first_layout(x)
    more_weights, more_cols = second_layout(x)
    weights, cols, consts = weights | more_weights, cols | more_cols, constants()
    both, first, second = consts
    widths = lambda arrays: {n: v.shape[1] for n, v in arrays.items()}
    const_at, at = places(widths(both))
    first_at, first_end = places(widths(first), at)
    second_at, second_end = places(widths(second), at)
    const_at, n_const = const_at | first_at | second_at, max(first_end, second_end)
    col_at, n_col = places(widths(cols))
    given = weights | {
        "x": x["x"].reshape(T, D),
        "consts": np.concatenate(list(both.values()) + list(first.values()), 1),
        "consts_2": np.concatenate(list(second.values()), 1),
        "cols": np.concatenate(list(cols.values()), 1),
    }
    nc = bacc.Bacc("TRN2", target_bir_lowering=False, num_devices=1, dynamic_dma_scratch_size=1024)
    arrays, dram = {}, {}
    for name, a in given.items():
        a = np.ascontiguousarray(a)
        arrays[f"in_{name}_dram"] = a
        dram[name] = nc.dram_tensor(f"in_{name}_dram", a.shape, mybir.dt.from_np(a.dtype), kind="ExternalInput").ap()
    dram["out"] = nc.dram_tensor("out_0_dram", (T, D), F32, kind="ExternalOutput").ap()
    hybrid_program(nc, dram, const_at, n_const, col_at, n_col)
    r = run_bass_kernel_spmd(nc, [arrays], core_ids=[0])
    return r.results[0]["out_0_dram"].reshape(1, T, D)
```

```python
from contextlib import ExitStack

import concourse.bass as bass
import numpy as np
from concourse import mybir

F32 = mybir.dt.float32
F32R = mybir.dt.float32r
ALU = mybir.AluOpType
ACT = mybir.ActivationFunctionType
AX = mybir.AxisListType

P = 128
T = 512
NT = T // P
D = 1024
KD = D // P

SSM_HEADS, SSM_P, SSM_CONV = 16, 64, 5
SSM_INNER, SSM_XBC = 1024, 1536
RWKV_W = 512
RWKV_COLS = 3 * RWKV_W + 256
RWKV_DECAY = 0.6065306597
HGRN_W = 512
D_FF = 2816
KF = D_FF // P
NORM_EPS = 1e-6
RWKV_LN_EPS = 64e-5
CH = 32
NC = T // CH
LAYERS = 2
GRID_W, WIN_R, WIN_C = 64, 8, 16
A_HEADS, A_CONV, A_WIDTH = 4, 3, 512
B_HEADS, C_HEADS, D_HEADS = 8, 8, 4
LAMBDA_INIT = [0.8 - 0.6 * float(np.exp(-0.3 * n)) for n in range(LAYERS)]


def constants():
    p = np.arange(P)
    s, t = p[:, None], p[None, :]
    block = (s // CH) == (t // CH)
    tok = np.arange(T)
    both = {
        "ident": np.eye(P),
        "ones": np.ones((P, P)),
        "pair": (s // 64) == (t // 64),
        "le": s <= t,
        "ge": s >= t,
        "eps": np.broadcast_to(np.array([[NORM_EPS, RWKV_LN_EPS, 1e-12, 64 * NORM_EPS]
                                        + [NORM_EPS / (1 - LAMBDA_INIT[n]) ** 2 for n in range(LAYERS)]]),
                               (P, 4 + LAYERS)),
    }
    first = {
        "eye64": s % 64 == t[:, :64],
        "c_le": block & (s <= t),
        "c_lt": block & (s < t),
        "c_ge": block & (s >= t),
        "c_gt": block & (s > t),
        "reset": np.broadcast_to(np.stack([tok % CH != 0, tok % CH != CH - 1]).reshape(1, -1), (P, 2 * T)),
    }
    c = {}
    d = p % 64
    inv = (10000.0 ** (-np.arange(16, dtype=np.float32) / 16)).astype(np.float32)
    pos = np.where((d < 32)[:, None], tok[None] // GRID_W, tok[None] % GRID_W).astype(np.float32)
    ang = (pos * inv[d % 16][:, None]).astype(np.float32)
    c["cos"], c["sin"] = np.cos(ang), np.sin(ang)
    turn = np.zeros((P, P))
    low = (p % 32) < 16
    turn[(p + 16)[low], p[low]] = -1.0
    turn[(p - 16)[~low], p[~low]] = 1.0
    c["turn"] = turn
    c["dup"] = np.concatenate([(s == t % 64), (s == 64 + t % 64)], 1)
    c["distance"] = np.abs(s - (np.arange(896)[None] - 384))
    band = np.zeros((P, 191))
    for a in range(2):
        for o in range(31):
            band[32 * a + o, 64 * a + 78 - o] = 1.0
    c["band"] = band
    col = p % 64
    start = np.clip(col - WIN_C // 2, 0, GRID_W - WIN_C)
    kc = np.arange(64)[None]
    c["window"] = np.where((kc >= start[:, None]) & (kc < start[:, None] + WIN_C), 0.0, -1e30)
    return [{n: np.ascontiguousarray(np.broadcast_to(v, (P, v.shape[1])), dtype=np.float32)
             for n, v in kind.items()} for kind in (both, first, c)]


def places(widths, at=0):
    out = {}
    for name, w in widths.items():
        out[name] = (at, at + w)
        at += w
    return out, at


def grouped(w, width=P):
    k, n = w.shape
    return np.ascontiguousarray(
        w.reshape(k // P, P, n // width, width).transpose(2, 1, 0, 3)).reshape(n // width, P, -1)


def side_by_side(a, b):
    return np.concatenate([grouped(a), grouped(b)], axis=2)


def padded(w):
    return grouped(np.concatenate([w, np.zeros((w.shape[0], P - w.shape[1]), w.dtype)], 1))


def columns(v):
    v = np.asarray(v).reshape(-1, P)
    return v.T


def short(v):
    v = np.asarray(v).reshape(-1)
    out = np.zeros((P, 1), v.dtype)
    out[: len(v), 0] = v
    return out


def first_layout(x):
    w = x["w_in"][0]
    o_xbc = SSM_INNER
    o_dt = o_xbc + SSM_XBC
    o_rwkv = o_dt + 2 * SSM_HEADS
    o_hgrn = o_rwkv + RWKV_COLS
    o_gate = o_hgrn + 5 * HGRN_W
    gate = w[:, o_gate:]
    weights = {
        "w_z": grouped(w[:, :o_xbc]),
        "w_xbc": grouped(w[:, o_xbc:o_dt]),
        "w_dt": np.concatenate([padded(w[:, o_dt + r * SSM_HEADS:o_dt + (r + 1) * SSM_HEADS]) for r in range(2)], 0),
        "w_rwkv": grouped(w[:, o_rwkv:o_hgrn]),
        "w_hgrn": grouped(w[:, o_hgrn:o_gate - HGRN_W]),
        "w_hgrn_gate": grouped(w[:, o_gate - HGRN_W:o_gate]),
        "w_mix_ssm": side_by_side(gate[:, :D], x["w_branch_ssm"][0]),
        "w_mix_rwkv": side_by_side(gate[:, D:2 * D], x["w_branch_rwkv"][0]),
        "w_mix_hgrn": side_by_side(gate[:, 2 * D:], x["w_branch_hgrn"][0]),
        "w_out": grouped(x["w_out"][0]),
        "w_ffn": side_by_side(x["ffn_w_in"][0][:, :D_FF], x["ffn_w_in"][0][:, D_FF:]),
        "w_down": grouped(x["ffn_w_down"][0]),
        "w_lora": np.concatenate([
            np.concatenate([x["rwkv_w_up"][0, 0], x["rwkv_w_up"][0, 1]], 1),
            np.concatenate([x["rwkv_a_up"][0], np.zeros_like(x["rwkv_a_up"][0])], 1)], 0),
        "w_g_up": x["rwkv_g_up"][0],
    }
    heads = lambda v: np.repeat(np.asarray(v).reshape(-1), 64)
    cols = {
        "norm1": columns(x["norm1_w"][0]),
        "conv_w": np.concatenate([columns(x["ssm_conv_w"][0, j, 0]) for j in range(SSM_CONV)], 1),
        "conv_b": columns(x["ssm_conv_b"][0]),
        "dt_bias": np.concatenate([short(x["ssm_dt_bias"][0, r]) for r in range(2)], 1),
        "a_log": np.concatenate([short(x["ssm_a_log"][0, r]) for r in range(2)], 1),
        "d_skip": columns(heads(x["ssm_d"][0])),
        "ssm_norm": columns(x["ssm_norm_w"][0]),
        "mu": np.concatenate([columns(x["rwkv_mu"][0, r]) for r in range(2)], 1),
        "w0": np.concatenate([columns(x["rwkv_w0"][0, r]) for r in range(2)], 1),
        "a0": columns(x["rwkv_a0"][0]),
        "k_k": columns(x["rwkv_k_k"][0]),
        "k_a": columns(x["rwkv_k_a"][0]),
        "r_k": columns(x["rwkv_r_k"][0]),
        "ln_w": columns(x["rwkv_ln_w"][0]),
        "ln_b": columns(x["rwkv_ln_b"][0]),
        "lb": columns(x["hgrn_lb_logits"][0]),
        "hgrn_norm": columns(x["hgrn_norm_w"][0]),
        "norm2": columns(x["norm2_w"][0]),
        "norm3": columns(x["final_norm_w"]),
    }
    return weights, cols


def second_layout(x):
    weights, cols = {}, {}
    widths = {"aq": 512, "ak": 512, "av": 512, "ao": 512, "ag": 16, "bq": 512, "bk": 128, "bv": 128,
              "cq": 512, "ck": 512, "cv": 512, "dq": 512, "dk": 512, "dv": 512, "gate": 4 * D}
    at, _ = places(widths)
    for n in range(LAYERS):
        w = x["w_in_2"][n]
        part = lambda *names: np.concatenate([w[:, at[m][0]:at[m][1]] for m in names], 1)
        weights |= {
            f"w_a_qk{n}": grouped(part("aq", "ak")),
            f"w_a_o{n}": grouped(part("ao")),
            f"w_a_gates{n}": padded(part("ag")),
            f"w_a_v{n}": grouped(part("av"), 512),
            f"w_b_q{n}": grouped(part("bq")),
            f"w_b_k{n}": grouped(part("bk")),
            f"w_b_v{n}": grouped(part("bv"), P),
            f"w_c_qk{n}": grouped(part("cq", "ck")),
            f"w_c_v{n}": grouped(part("cv"), 512),
            f"w_d_qk{n}": grouped(part("dq", "dk")),
            f"w_d_v{n}": grouped(part("dv"), 512),
            f"w_out{n}": grouped(x["w_out_2"][n]),
            f"w_ffn{n}": side_by_side(x["w_ffn_gate_2"][n], x["w_ffn_up_2"][n]),
            f"w_down{n}": grouped(x["w_ffn_down_2"][n]),
        }
        for b, name in enumerate("abcd"):
            g = part("gate")[:, b * D:(b + 1) * D]
            weights[f"w_mix_{name}{n}"] = side_by_side(g, x[f"w_up_{name}_2"][n])
        rpb = np.zeros((P, C_HEADS, 16), np.float32)
        for a in range(2):
            rpb[32 * a:32 * a + 31, :, a:a + 15] = np.asarray(x["c_rpb_2"][n]).transpose(2, 0, 1)
        weights[f"rpb{n}"] = rpb.reshape(P, -1)
        twice = lambda v: np.concatenate([short(v)[:64], short(v)[:64]], 0)
        cols |= {
            f"norm1_{n}": columns(x["norm1_g_2"][n]),
            f"a_conv{n}": np.concatenate([columns(x["a_conv_w_2"][n, j]) for j in range(A_CONV)], 1),
            f"a_bias{n}": short(x["a_gate_bias_2"][n]),
            f"a_norm{n}": columns(x["a_norm_g_2"][n]),
            f"b_qnorm{n}": twice(x["b_qnorm_g_2"][n]),
            f"b_knorm{n}": twice(x["b_knorm_g_2"][n]),
            f"lambda{n}": np.concatenate([short(x[f"d_lambda_{m}_2"][n]) for m in ("q1", "q2", "k1", "k2")], 1),
            f"d_subln{n}": np.repeat(columns(x["d_subln_g_2"][n]), D_HEADS, 1),
            f"norm2_{n}": columns(x["norm2_g_2"][n]),
        }
    cols["final"] = columns(x["final_g_2"])
    return weights, cols


class Kernel:

    def __init__(self, nc, dram, const_at, col_at):
        self.nc, self.dram, self.const_at, self.col_at = nc, dram, const_at, col_at
        self.made = 0
        self.free = sorted(nc.free_semaphores)

    def sbuf(self, ctx, name, shape, side="left"):
        self.made += 1
        return ctx.enter_context(self.nc.sbuf_tensor(f"{name}_{self.made}", shape, F32, side=side))

    def both_kinds(self, ctx, name, shape):
        at = (self.nc.sbuf_base + 31) // 32 * 32
        whole = self.sbuf(ctx, name, shape)
        rounded = self.nc.alloc_sbuf_tensor_at(f"{name}_r_{self.made}", shape, F32R, offset=at)
        return whole, rounded

    def const(self, name, rows=P):
        a, b = self.const_at[name]
        return self.consts[0:rows, a:b]

    def col(self, name, j=0, rows=P):
        a, _ = self.col_at[name]
        return self.cols[0:rows, a + j:a + j + 1]


def semaphores(k, ctx, names):
    sems = [k.nc.alloc_semaphore(f"{n}_{k.nc.next_id()}", num=k.free.pop(0)) for n in names.split()]

    def give_back():
        for s in sems:
            k.nc.gpsimd.sem_clear(s)
            k.nc.release_semaphore(s)
            k.free.append(s.num)

    ctx.callback(give_back)
    return sems


def bank(ps, b):
    return ps[:, b, :]


def wide(ap, n):
    rows, m = ap.shape
    return ap[:, None, :].broadcast_to([rows, n, m])


def load_constants(k, col_array):
    nc = k.nc
    with ExitStack() as ctx:
        consts_in, cols_in = semaphores(k, ctx, "consts_in cols_in")
        block = ctx.enter_context(nc.Block())

        @block.sync
        def _(sp):
            sp.dma_start(k.consts[:, 0:k.dram["consts"].shape[1]], k.dram["consts"]).then_inc(consts_in, 16)
            sp.wait_ge(consts_in, 16)

        @block.scalar
        def _(act):
            act.dma_start(k.cols[:, 0:col_array.shape[1]], col_array).then_inc(cols_in, 16)
            act.wait_ge(cols_in, 16)


def load_x(k):
    nc = k.nc
    with ExitStack() as ctx:
        rows = k.sbuf(ctx, "x_rows", [P, NT, D])
        x_in, turned, x_ready = semaphores(k, ctx, "x_in turned x_ready")
        block = ctx.enter_context(nc.Block())

        @block.sync
        def _(sp):
            sp.dma_start(rows[:, :, :], k.dram["x"].rearrange("(j p) d -> p j d", p=P)).then_inc(x_in, 16)

        @block.tensor
        def _(pe):
            pe.wait_ge(x_in, 16)
            for m in range(KD):
                if m >= 2:
                    pe.wait_ge(x_ready, m - 1)
                for j in range(NT):
                    mm = pe.transpose(k.ps[:, m % 2, j * P:(j + 1) * P], rows[:, j, m * P:(m + 1) * P],
                                      k.const("ident"))
                mm.then_inc(turned, 1)

        @block.scalar
        def _(act):
            for m in range(KD):
                act.wait_ge(turned, m + 1)
                act.activation(k.x[:, m, :], bank(k.ps, m % 2), ACT.Copy).then_inc(x_ready, 1)


def store_x(k, src):
    nc = k.nc
    with ExitStack() as ctx:
        rows = k.sbuf(ctx, "out_rows", [P, NT, D])
        turned, row_ready, stored = semaphores(k, ctx, "turned row_ready stored")
        block = ctx.enter_context(nc.Block())

        @block.tensor
        def _(pe):
            for n in range(2 * NT):
                j, half = n // 2, n % 2
                if n >= 2:
                    pe.wait_ge(row_ready, n - 1)
                for q in range(NT):
                    mm = pe.transpose(k.ps[:, n % 2, q * P:(q + 1) * P],
                                      src[:, NT * half + q, j * P:(j + 1) * P], k.const("ident"))
                mm.then_inc(turned, 1)

        @block.scalar
        def _(act):
            for n in range(2 * NT):
                act.wait_ge(turned, n + 1)
                act.activation(rows[:, n // 2, (n % 2) * T:(n % 2 + 1) * T], bank(k.ps, n % 2),
                               ACT.Copy).then_inc(row_ready, 1)

        @block.sync
        def _(sp):
            for j in range(NT):
                sp.wait_ge(row_ready, 2 * j + 2)
                sp.dma_start(k.dram["out"][j * P:(j + 1) * P, :], rows[:, j, :]).then_inc(stored, 16)
            sp.wait_ge(stored, 16 * NT)


def rms_norm(k, src, dst, weight, tiles=KD, sum_there=False):
    nc = k.nc
    with ExitStack() as ctx:
        sq = k.sbuf(ctx, "squares", [P, 3, T])
        rstd = k.sbuf(ctx, "rstd", [P, T])
        squared, summed, root, inverse, normed = semaphores(k, ctx, "squared summed root inverse normed")
        block = ctx.enter_context(nc.Block())

        @block.scalar
        def _(act):
            if not sum_there:
                for m in range(tiles):
                    if m >= 3:
                        act.wait_ge(summed, m - 2)
                    act.activation(sq[:, m % 3, :], src[:, m, :], ACT.Square).then_inc(squared, 1)
                act.wait_ge(summed, tiles)
            act.activation(rstd[:, :], bank(k.ps, 7), ACT.Sqrt, bias=k.const("eps")[:, 0:1],
                           scale=1.0 / (tiles * P)).then_inc(root, 1)

        @block.tensor
        def _(pe):
            if not sum_there:
                for m in range(tiles):
                    pe.wait_ge(squared, m + 1)
                    pe.matmul(bank(k.ps, 7), k.const("ones"), sq[:, m % 3, :], start=(m == 0),
                              stop=(m == tiles - 1)).then_inc(summed, 1)

        @block.vector
        def _(dve):
            dve.wait_ge(root, 1)
            dve.reciprocal(rstd[:, :], rstd[:, :]).then_inc(inverse, 1)
            dve.wait_ge(inverse, 1)
            for m in range(tiles):
                dve.scalar_tensor_tensor(out=dst[:, m, :], in0=src[:, m, :], scalar=k.col(weight, m),
                                         in1=rstd[:, :], op0=ALU.mult, op1=ALU.mult).then_inc(normed, 1)


AHEAD_RAW, AHEAD_PARTS = 4, 2


class Chunk:

    def __init__(self, name, row, at, width):
        self.name, self.row, self.at, self.width = name, row, at, width

    def key(self):
        return self.name, self.row, self.at, self.width


def step_chunks(name, row, runs):
    out, at = [], 0
    for run in runs:
        while run:
            n = min(run, KD)
            out.append(Chunk(name, row, at * P, n * P))
            at, run = at + n, run - n
    return out


def planned(name, rows, *runs, first=0):
    return [c for r in range(first, first + rows) for c in step_chunks(name, r, runs)]


class Stream:

    def __init__(self, k, plan):
        self.k, self.plan, self.stops = k, [], []
        for item in plan:
            if item is None:
                self.stops.append(len(self.plan))
            else:
                self.plan += item
        self.stops.append(len(self.plan))
        one = lambda name: k.nc.alloc_semaphore(name, num=k.free.pop(0))
        self.weights_in = [one(f"weights_in_{n}") for n in range(AHEAD_RAW)]
        self.hi_made, self.parts_ready, self.chunk_used = one("hi_made"), one("parts_ready"), one("chunk_used")
        self.at = self.loaded = self.split = 0

    def stop(self):
        return min(s for s in self.stops if s > self.at)

    def enter(self, jobs):
        at = self.at
        for job in jobs:
            job.g0 = at
            for p in range(job.per * job.bodies):
                assert self.plan[at].key() == job.chunk(p).key(), (self.plan[at].key(), job.chunk(p).key())
                at += 1
        return at

    def leave(self, end):
        stop = self.stop()
        self.at = end
        self.loaded = max(self.loaded, min(end + AHEAD_RAW, stop))
        self.split = max(self.split, min(end + AHEAD_PARTS, stop))

    def load(self, sp, g, chunk, i=0, job=None):
        w, per = self.k.dram[chunk.name], job.per if job else 0
        if job:
            row = sp.snap(i * job.body + chunk.row)
            w = w[bass.ds(row, 1), :, :].rearrange("a p n -> (a p) n")
        else:
            w = w[chunk.row, :, :]
        if job or g >= AHEAD_RAW:
            sp.wait_ge(self.parts_ready, i * per + (g - AHEAD_RAW + 1))
        slot = g % AHEAD_RAW
        sp.dma_start(self.k.raw[:, slot, 0:chunk.width], w[:, chunk.at:chunk.at + chunk.width])\
            .then_inc(self.weights_in[slot], 16)

    def make_hi(self, act, g, chunk, i=0, job=None):
        per, slot = job.per if job else 0, g % AHEAD_RAW
        act.wait_ge(self.weights_in[slot], i * (per // AHEAD_RAW * 16) + 16 * (g // AHEAD_RAW + 1))
        if job or g >= AHEAD_PARTS:
            act.wait_ge(self.chunk_used, i * per + (g - AHEAD_PARTS + 1))
        act.activation(self.k.w_hi[:, g % 2, 0:chunk.width], self.k.raw[:, slot, 0:chunk.width], ACT.Copy)\
            .then_inc(self.hi_made, 1)

    def make_lo(self, dve, g, chunk, i=0, job=None):
        per, slot = job.per if job else 0, g % AHEAD_RAW
        dve.wait_ge(self.hi_made, i * per + (g + 1))
        dve.tensor_tensor(self.k.w_lo[:, g % 2, 0:chunk.width], self.k.raw[:, slot, 0:chunk.width],
                          self.k.w_hi[:, g % 2, 0:chunk.width].bitcast(F32), ALU.subtract)\
            .then_inc(self.parts_ready, 1)

    def catch_up(self, do, eng, done, by):
        for g in range(done, min(self.at + by, self.stop())):
            do(eng, g, self.plan[g])

    def run_ahead(self, do, eng, job, i, last, p, by):
        if last or isinstance(i, int):
            g = job.g0 + job.per * (job.bodies - 1 if last else i) + p + by
            if g < self.stop():
                do(eng, g, self.plan[g])
        else:
            do(eng, job.g0 + p + by, job.chunk(p + by), i, job)


class Job:

    def __init__(self, name, steps, body, runs, t0=0, first=0):
        self.name, self.body, self.runs, self.t0, self.first = name, body, runs, t0, first
        self.bodies = steps // body
        self.per_step = len(step_chunks(name, 0, runs))
        self.per = body * self.per_step
        assert steps % body == 0 and (self.bodies < 4 or self.per % AHEAD_RAW == 0)

    def chunk(self, p):
        step, c = divmod(p, self.per_step)
        return step_chunks(self.name, self.first + step, self.runs)[c]


def walk(eng, job, body, unrolled=False):
    n = job.bodies
    if n < 4 or unrolled:
        for i in range(n):
            body(i, i == n - 1)
        return
    body(0, False)
    with eng.Fori(1, n - 1) as i:
        body(i, False)
    body(n - 1, True)


class Parts:

    def __init__(self, full, lo, hi):
        self.full, self.lo, self.hi, self.shape = full, lo, hi, full.shape

    def make_hi(self, act, q):
        return act.activation(self.hi[:, q, :], self.full[:, q, :], ACT.Copy)

    def make_lo(self, dve, q):
        return dve.tensor_tensor(self.lo[:, q, :], self.full[:, q, :], self.hi[:, q, :].bitcast(F32), ALU.subtract)


def three_passes(pe, out, w_hi, w_lo, x_hi, x_lo, start, stop):
    pe.matmul(out, w_hi, x_hi, start=start, stop=False)
    pe.matmul(out, w_hi, x_lo, start=False, stop=False)
    return pe.matmul(out, w_lo, x_hi, start=False, stop=stop)


class Nothing:

    def open(self, k, ctx):
        pass

    def tensor(self, pe):
        yield

    def scalar(self, act):
        yield

    def vector(self, dve):
        yield

    def gpsimd(self, pool):
        yield

    def sync(self, sp):
        pass

    def given(self, tile_used):
        self.tile_used = tile_used


class Together:

    def __init__(self, first, second):
        self.sides = (first, second)

    def open(self, k, ctx):
        for side in self.sides:
            side.open(k, ctx)

    def given(self, tile_used):
        for side in self.sides:
            side.given(tile_used)

    def sync(self, sp):
        for side in self.sides:
            side.sync(sp)

    def both(self, one, other):
        left = [one, other]
        while left:
            left = [g for g in left if next(g, "end") != "end"]
            yield

    def tensor(self, pe):
        return self.both(*[s.tensor(pe) for s in self.sides])

    def scalar(self, act):
        return self.both(*[s.scalar(act) for s in self.sides])

    def vector(self, dve):
        return self.both(*[s.vector(dve) for s in self.sides])

    def gpsimd(self, pool):
        return self.both(*[s.gpsimd(pool) for s in self.sides])


class Ready:
    tiles = 0

    def open(self, k, ctx):
        pass

    def scalar(self, act, upto):
        pass

    vector = tensor = scalar


class Split:

    def __init__(self, src):
        self.src, self.tiles = src, src.shape[1]

    def open(self, k, ctx):
        self.source_hi, self.source_ready = semaphores(k, ctx, "source_hi source_ready")
        self.done = {}

    def todo(self, engine, upto):
        a, b = self.done.get(engine, 0), min(upto, self.tiles)
        self.done[engine] = max(a, b)
        return range(a, b)

    def scalar(self, act, upto):
        for q in self.todo("scalar", upto):
            self.src.make_hi(act, q).then_inc(self.source_hi, 1)

    def vector(self, dve, upto):
        for q in self.todo("vector", upto):
            dve.wait_ge(self.source_hi, q + 1)
            self.src.make_lo(dve, q).then_inc(self.source_ready, 1)

    def tensor(self, pe, upto):
        for q in self.todo("tensor", upto):
            pe.wait_ge(self.source_ready, q + 1)


class Norm(Split):

    def __init__(self, x, src, weight, spare=None, sum_there=False):
        Split.__init__(self, src)
        self.x, self.weight, self.spare, self.sum_there = x, weight, spare, sum_there

    def open(self, k, ctx):
        Split.open(self, k, ctx)
        self.k = k
        work = self.spare if self.spare is not None else k.sbuf(ctx, "norm_work", [P, 3, T])
        self.sq, self.rstd = work[:, 0:2, :], work[:, 2, :]
        self.squared, self.summed, self.root, self.inverse, self.normed = semaphores(
            k, ctx, "squared summed root inverse normed")

    def scalar(self, act, upto):
        k, tiles = self.k, self.todo("scalar", self.tiles)
        for m in tiles if not self.sum_there else ():
            if m >= 2:
                act.wait_ge(self.summed, m - 1)
            act.activation(self.sq[:, m % 2, :], self.x[:, m, :], ACT.Square).then_inc(self.squared, 1)
        if tiles:
            if not self.sum_there:
                act.wait_ge(self.summed, self.tiles)
            act.activation(self.rstd, bank(k.ps, 7), ACT.Sqrt, bias=k.const("eps")[:, 0:1],
                           scale=1.0 / (self.tiles * P)).then_inc(self.root, 1)
        for q in tiles:
            act.wait_ge(self.normed, q + 1)
            self.src.make_hi(act, q).then_inc(self.source_hi, 1)

    def tensor(self, pe, upto):
        k = self.k
        if not self.done.get("sums") and not self.sum_there:
            self.done["sums"] = 1
            for m in range(self.tiles):
                pe.wait_ge(self.squared, m + 1)
                pe.matmul(bank(k.ps, 7), k.const("ones"), self.sq[:, m % 2, :], start=(m == 0),
                          stop=(m == self.tiles - 1)).then_inc(self.summed, 1)
        Split.tensor(self, pe, upto)

    def vector(self, dve, upto):
        k, tiles = self.k, self.todo("vector", self.tiles)
        if tiles:
            dve.wait_ge(self.root, 1)
            dve.reciprocal(self.rstd, self.rstd).then_inc(self.inverse, 1)
            dve.wait_ge(self.inverse, 1)
            for m in range(self.tiles + 1):
                if m < self.tiles:
                    dve.scalar_tensor_tensor(out=self.src.full[:, m, :], in0=self.x[:, m, :],
                                             scalar=k.col(self.weight, m), in1=self.rstd, op0=ALU.mult,
                                             op1=ALU.mult).then_inc(self.normed, 1)
                if m:
                    dve.wait_ge(self.source_hi, m)
                    self.src.make_lo(dve, m - 1).then_inc(self.source_ready, 1)


def project(k, outputs, src, source=Ready(), tokens=None, beside=None):
    nc, stream, kt = k.nc, k.stream, src.shape[1]
    with ExitStack() as ctx:
        jobs, t0 = [], 0
        for name, dst, scale in outputs:
            tiles = dst.shape[1]
            whole = tiles // 4 * 4
            for first, steps, body in ((0, whole, 4), (whole, tiles - whole, tiles - whole)):
                if steps:
                    job = Job(name, steps, body, (kt,), t0, first)
                    job.dst, job.scale = dst[:, first:first + steps, :], scale
                    jobs.append(job)
                    t0 += steps
        tok = None
        if tokens:
            width = tokens[1].shape[2]
            tok = Job(tokens[0], 1, 1, (KD * width // P,), t0)
        end = stream.enter(jobs + ([tok] if tok else []))
        every = jobs + ([tok] if tok else [])
        adding = jobs[0].scale == "add"
        source.open(k, ctx)
        side = beside or Nothing()
        side.open(k, ctx)
        unrolled = beside is not None
        tile_used, tokens_used = semaphores(k, ctx, "tile_used tokens_used")
        side.given(tile_used)
        block = ctx.enter_context(nc.Block())

        @block.sync
        def _(sp):
            stream.catch_up(stream.load, sp, stream.loaded, AHEAD_RAW)
            side.sync(sp)
            for job in every:
                def load(i, last):
                    for p in range(job.per):
                        stream.run_ahead(stream.load, sp, job, i, last, p, AHEAD_RAW)
                walk(sp, job, load)

        @block.tensor
        def _(pe):
            side_pieces = side.tensor(pe)
            for job in jobs:
                def multiply(i, last):
                    for s in range(job.body):
                        t = job.t0 + s
                        out, q = bank(k.ps, t % 4), 0
                        if not isinstance(i, int) or t + i * job.body >= 4:
                            pe.wait_ge(tile_used, i * job.body + (t - 3))
                        for c in range(job.per_step):
                            p = s * job.per_step + c
                            g = job.g0 + p
                            pe.wait_ge(stream.parts_ready, i * job.per + (g + 1))
                            for n in range(job.chunk(p).width // P):
                                if isinstance(i, int):
                                    source.tensor(pe, q + 1)
                                at = slice(n * P, n * P + P)
                                mm = three_passes(pe, out, k.w_hi[:, g % 2, at], k.w_lo[:, g % 2, at],
                                                  src.hi[:, q, :], src.lo[:, q, :], q == 0, q == kt - 1)
                                q += 1
                            mm.then_inc(stream.chunk_used, 1)
                            if unrolled:
                                next(side_pieces, None)
                walk(pe, job, multiply, unrolled)
            if tok:
                per = KD // tok.per
                for c in range(tok.per):
                    g = tok.g0 + c
                    pe.wait_ge(stream.parts_ready, g + 1)
                    for j in range(NT):
                        if c == 0 and t0 + j >= 4:
                            pe.wait_ge(tile_used, t0 + j - 3)
                        for q in range(c * per, c * per + per):
                            at = slice((q - c * per) * width, (q - c * per + 1) * width)
                            mm = three_passes(pe, k.ps[:, (t0 + j) % 4, 0:width],
                                              src.hi[:, q, j * P:(j + 1) * P], src.lo[:, q, j * P:(j + 1) * P],
                                              k.w_hi[:, g % 2, at], k.w_lo[:, g % 2, at], q == 0, q == KD - 1)
                    mm.then_inc(stream.chunk_used, 1)
                    if unrolled:
                        next(side_pieces, None)
            list(side_pieces)

        @block.scalar
        def _(act):
            side_pieces = side.scalar(act)
            stream.catch_up(stream.make_hi, act, stream.split, AHEAD_PARTS)
            for job in every:
                def take(i, last):
                    for p in range(job.per):
                        if unrolled and (i or p or job is not every[0]):
                            next(side_pieces, None)
                        if isinstance(i, int):
                            source.scalar(act, KD * (p + 1))
                        stream.run_ahead(stream.make_hi, act, job, i, last, p, AHEAD_PARTS)
                        if job is tok or adding or p % job.per_step < job.per_step - 1:
                            continue
                        s = p // job.per_step
                        rows = job.dst.shape[0]
                        act.wait_ge(stream.chunk_used, i * job.per + (job.g0 + p + 1))
                        o = job.dst[:, bass.ds(i * job.body + s, 1), :].rearrange("p a t -> p (a t)")
                        act.activation(o, k.ps[0:rows, (job.t0 + s) % 4, :], ACT.Copy, scale=job.scale)\
                            .then_inc(tile_used, 1)
                walk(act, job, take, unrolled)
            if tok:
                act.wait_ge(stream.chunk_used, tok.g0 + tok.per)
                for j in range(NT):
                    act.activation(tokens[1][:, j, :], k.ps[:, (t0 + j) % 4, 0:width], ACT.Copy).then_inc(tokens_used, 1)
            list(side_pieces)

        @block.vector
        def _(dve):
            side_pieces = side.vector(dve)
            stream.catch_up(stream.make_lo, dve, stream.split, AHEAD_PARTS)
            for job in every:
                def take(i, last):
                    for p in range(job.per):
                        if unrolled and (i or p or job is not every[0]):
                            next(side_pieces, None)
                        if isinstance(i, int):
                            source.vector(dve, KD * (p + 1))
                        stream.run_ahead(stream.make_lo, dve, job, i, last, p, AHEAD_PARTS)
                        if not adding or p % job.per_step < job.per_step - 1:
                            continue
                        s = p // job.per_step
                        dve.wait_ge(stream.chunk_used, i * job.per + (job.g0 + p + 1))
                        o = job.dst[:, bass.ds(i * job.body + s, 1), :].rearrange("p a t -> p (a t)")
                        dve.tensor_tensor(o, o, bank(k.ps, (job.t0 + s) % 4), ALU.add).then_inc(tile_used, 1)
                walk(dve, job, take, unrolled)
            list(side_pieces)

        @block.gpsimd
        def _(pool):
            list(side.gpsimd(pool))
        stream.leave(end)


class Gated:

    def __init__(self, name, src_a, src_b, func, accumulate, source, source_is_b, beside=None):
        self.name, self.sources, self.func, self.accumulate = name, (src_a, src_b), func, accumulate
        self.source, self.source_is_b, self.beside = source, source_is_b, beside


def gated_products(k, parts, dst, gate):
    nc, stream = k.nc, k.stream
    with ExitStack() as ctx:
        jobs, summed = [], 0
        for n, part in enumerate(parts):
            job = Job(part.name, dst.shape[1], 2, [src.shape[1] for src in part.sources], n * dst.shape[1])
            job.part, job.summed = part, summed
            summed += dst.shape[1] if part.accumulate else 0
            job.unrolled = part.beside is not None
            job.side = part.beside or Nothing()
            part.source.open(k, ctx)
            job.side.open(k, ctx)
            jobs.append(job)
        end = stream.enter(jobs)
        gate_ready, tile_used, product_ready = semaphores(k, ctx, "gate_ready tile_used product_ready")
        block = ctx.enter_context(nc.Block())

        @block.sync
        def _(sp):
            stream.catch_up(stream.load, sp, stream.loaded, AHEAD_RAW)
            for job in jobs:
                job.side.sync(sp)

                def load(i, last):
                    for p in range(job.per):
                        stream.run_ahead(stream.load, sp, job, i, last, p, AHEAD_RAW)
                walk(sp, job, load)

        @block.tensor
        def _(pe):
            for job in jobs:
                side_pieces = job.side.tensor(pe)

                def multiply(i, last):
                    for s in range(2):
                        if not isinstance(i, int) or i > 0 or job.t0:
                            pe.wait_ge(tile_used, i * 2 + (job.t0 + s - 1))
                        for c, src in enumerate(job.part.sources):
                            kt = src.shape[1]
                            g = job.g0 + 2 * s + c
                            pe.wait_ge(stream.parts_ready, i * 4 + (g + 1))
                            for q in range(kt):
                                if isinstance(i, int) and c == job.part.source_is_b:
                                    job.part.source.tensor(pe, q + 1)
                                at = slice(q * P, q * P + P)
                                mm = three_passes(pe, bank(k.ps, 2 * s + c), k.w_hi[:, g % 2, at],
                                                  k.w_lo[:, g % 2, at], src.hi[:, q, :], src.lo[:, q, :],
                                                  q == 0, q == kt - 1)
                            mm.then_inc(stream.chunk_used, 1)
                            if job.unrolled:
                                next(side_pieces, None)
                walk(pe, job, multiply, job.unrolled)
                list(side_pieces)

        @block.scalar
        def _(act):
            stream.catch_up(stream.make_hi, act, stream.split, AHEAD_PARTS)
            for job in jobs:
                side_pieces = job.side.scalar(act)

                def gates(i, last):
                    for s in range(2):
                        for c in range(2):
                            if job.unrolled and (i or s or c):
                                next(side_pieces, None)
                            if isinstance(i, int):
                                job.part.source.scalar(act, KD)
                            stream.run_ahead(stream.make_hi, act, job, i, last, 2 * s + c, AHEAD_PARTS)
                            if c == 0:
                                act.wait_ge(stream.chunk_used, i * 4 + (job.g0 + 2 * s + 1))
                                if not isinstance(i, int) or i > 0 or job.t0:
                                    act.wait_ge(tile_used, i * 2 + (job.t0 + s - 1))
                                act.activation(gate[:, s, :], bank(k.ps, 2 * s), job.part.func).then_inc(gate_ready, 1)
                walk(act, job, gates, job.unrolled)
                list(side_pieces)

        @block.vector
        def _(dve):
            stream.catch_up(stream.make_lo, dve, stream.split, AHEAD_PARTS)
            for job in jobs:
                side_pieces = job.side.vector(dve)

                def products(i, last):
                    for s in range(2):
                        for c in range(2):
                            if job.unrolled and (i or s or c):
                                next(side_pieces, None)
                            if isinstance(i, int):
                                job.part.source.vector(dve, KD)
                            stream.run_ahead(stream.make_lo, dve, job, i, last, 2 * s + c, AHEAD_PARTS)
                        dve.wait_ge(gate_ready, i * 2 + (job.t0 + s + 1))
                        dve.wait_ge(stream.chunk_used, i * 4 + (job.g0 + 2 * s + 2))
                        o = dst[:, bass.ds(i * 2 + s, 1), :].rearrange("p a t -> p (a t)")
                        g = gate[:, s, :]
                        if not job.part.accumulate:
                            dve.tensor_tensor(o, g, bank(k.ps, 2 * s + 1), ALU.mult).then_inc(tile_used, 1)
                            continue
                        dve.tensor_tensor(g, g, bank(k.ps, 2 * s + 1), ALU.mult).then_inc(product_ready, 1)
                        dve.wait_ge(product_ready, i * 2 + (job.summed + s + 1))
                        if job.t0 > 0 and isinstance(i, int):
                            dve.wait_ge(tile_used, job.t0)
                        dve.tensor_tensor(o, o, g, ALU.add).then_inc(tile_used, 1)
                walk(dve, job, products, job.unrolled)
                list(side_pieces)

        @block.gpsimd
        def _(pool):
            for job in jobs:
                list(job.side.gpsimd(pool))
        stream.leave(end)


class SquareSum(Nothing):

    def __init__(self, x, every, work):
        self.x, self.every, self.sq = x, every, work

    def open(self, k, ctx):
        self.k = k
        self.squared, self.summed = semaphores(k, ctx, "squared summed")

    def scalar(self, act):
        for m in range(KD):
            for _ in range(self.every - 1):
                yield
            act.wait_ge(self.tile_used, m + 1)
            if m >= 2:
                act.wait_ge(self.summed, m - 1)
            act.activation(self.sq[:, m % 2, :], self.x[:, m, :], ACT.Square).then_inc(self.squared, 1)
            yield

    def tensor(self, pe):
        k = self.k
        yield
        for m in range(KD):
            for _ in range(self.every - 1):
                yield
            pe.wait_ge(self.squared, m + 1)
            pe.matmul(bank(k.ps, 7), k.const("ones"), self.sq[:, m % 2, :], start=(m == 0),
                      stop=(m == KD - 1)).then_inc(self.summed, 1)
            yield


class LoadX(Nothing):

    def __init__(self, rows, array, at):
        self.rows, self.array, self.at = rows, array, at

    def open(self, k, ctx):
        self.k = k
        self.x_in, self.turned, self.x_ready, self.more_in = semaphores(k, ctx, "x_in turned x_ready more_in")

    def sync(self, sp):
        k = self.k
        sp.dma_start(self.rows[:, :, :], k.dram["x"].rearrange("(j p) d -> p j d", p=P)).then_inc(self.x_in, 16)
        sp.dma_start(k.consts[:, self.at:self.at + self.array.shape[1]], self.array).then_inc(self.more_in, 16)

    def gpsimd(self, pool):
        pool.wait_ge(self.more_in, 16)
        yield

    def tensor(self, pe):
        k = self.k
        yield
        pe.wait_ge(self.x_in, 16)
        for m in range(KD):
            if m >= 2:
                pe.wait_ge(self.x_ready, m - 1)
            for j in range(NT):
                mm = pe.transpose(k.ps[:, 4 + m % 2, j * P:(j + 1) * P], self.rows[:, j, m * P:(m + 1) * P],
                                  k.const("ident"))
            mm.then_inc(self.turned, 1)
            yield

    def scalar(self, act):
        k = self.k
        yield
        for m in range(KD):
            act.wait_ge(self.turned, m + 1)
            act.activation(k.x[:, m, :], bank(k.ps, 4 + m % 2), ACT.Copy).then_inc(self.x_ready, 1)
            yield


class SsmConvolution(Nothing):

    def __init__(self, raw, act_x, tap, dt_raw, dt, acum, a_exp):
        self.raw, self.act_x, self.tap = raw, act_x, tap
        self.dt_raw, self.dt, self.acum, self.a_exp = dt_raw, dt, acum, a_exp
        self.tiles = raw.shape[1]

    def open(self, k, ctx):
        self.k = k
        self.edges, self.tapped, self.activated, self.dt_steps, self.dt_ready, self.scanned = semaphores(
            k, ctx, "edges tapped activated dt_steps dt_ready scanned")

    def gpsimd(self, pool):
        raw, pad = self.raw, SSM_CONV // 2
        pool.memset(raw[:, :, 0:pad], 0.0).then_inc(self.edges, 1)
        pool.memset(raw[:, :, pad + T:], 0.0).then_inc(self.edges, 1)
        yield

    def scalar(self, act):
        k, dt, dt_raw, H = self.k, self.dt, self.dt_raw, SSM_HEADS
        for r in range(2):
            yield
            act.wait_ge(self.tile_used, r + 1)
            act.activation(dt_raw[:, r, :], dt_raw[:, r, :], ACT.Identity, bias=k.col("dt_bias", r, H))\
                .then_inc(self.dt_steps, 1)
            act.wait_ge(self.dt_steps, 4 * r + 1)
            act.activation(dt[:, r, :], dt_raw[:, r, :], ACT.Abs).then_inc(self.dt_steps, 1)
            act.wait_ge(self.dt_steps, 4 * r + 2)
            act.activation(dt[:, r, :], dt[:, r, :], ACT.Exp, scale=-1.0).then_inc(self.dt_steps, 1)
            act.activation(self.a_exp[:, r:r + 1], k.col("a_log", r, H), ACT.Exp).then_inc(self.dt_steps, 1)
            act.wait_ge(self.dt_steps, 4 * r + 4)
            act.activation(dt[:, r, :], dt[:, r, :], ACT.Ln, bias=k.const("ones", H)[:, 0:1])\
                .then_inc(self.dt_ready, 1)
        yield
        for m in range(self.tiles):
            yield
            act.wait_ge(self.tapped, SSM_CONV * (m + 1))
            act.activation(self.act_x[:, m, :], self.tap[:, m % 2, :], ACT.Silu).then_inc(self.activated, 1)

    def vector(self, dve):
        k, raw, dt, dt_raw, H = self.k, self.raw, self.dt, self.dt_raw, SSM_HEADS
        for r in range(2):
            yield
            dve.wait_ge(self.dt_ready, r + 1)
            dve.scalar_tensor_tensor(out=dt[:, r, :], in0=dt_raw[:, r, :], scalar=0.0, in1=dt[:, r, :],
                                     op0=ALU.max, op1=ALU.add).then_inc(self.scanned, 1)
            dve.wait_ge(self.scanned, 3 * r + 1)
            dve.tensor_scalar(dt_raw[:, r, :], dt[:, r, :], self.a_exp[:, r:r + 1], -1.0, ALU.mult,
                              ALU.mult).then_inc(self.scanned, 1)
            dve.wait_ge(self.scanned, 3 * r + 2)
            step = -1 if r else 1
            dve.tensor_tensor_scan(self.acum[:, r, ::step], k.const("ones", H)[:, 0:1].broadcast_to([H, T]),
                                   dt_raw[:, r, ::step], 0.0, ALU.mult, ALU.add).then_inc(self.scanned, 1)
        dve.wait_ge(self.edges, 2)
        for m in range(self.tiles):
            yield
            o = self.tap[:, m % 2, :]
            if m >= 2:
                dve.wait_ge(self.activated, m - 1)
            dve.wait_ge(self.tile_used, m + 3)
            dve.tensor_scalar(o, raw[:, m, 0:T], k.col("conv_w", m), k.col("conv_b", m), ALU.mult, ALU.add)\
                .then_inc(self.tapped, 1)
            for j in range(1, SSM_CONV):
                dve.wait_ge(self.tapped, SSM_CONV * m + j)
                dve.scalar_tensor_tensor(out=o, in0=raw[:, m, j:j + T], scalar=k.col("conv_w", j * self.tiles + m),
                                         in1=o, op0=ALU.mult, op1=ALU.add).then_inc(self.tapped, 1)


class SsmGate(Nothing):

    def __init__(self, z, y, sq):
        self.z, self.y, self.sq, self.tiles = z, y, sq, z.shape[1]

    def open(self, k, ctx):
        self.k = k
        self.gate_ready, self.gated, self.squared, self.summed = semaphores(
            k, ctx, "gate_ready gated squared summed")

    def scalar(self, act):
        for p in range(self.tiles + 1):
            if p < self.tiles:
                act.wait_ge(self.tile_used, p + 1)
                act.activation(self.z[:, p, :], self.z[:, p, :], ACT.Silu).then_inc(self.gate_ready, 1)
            m = p - 1
            if m >= 0:
                act.wait_ge(self.gated, m + 1)
                if m >= 2:
                    act.wait_ge(self.summed, m - 1)
                act.activation(self.sq[:, m % 2, :], self.y[:, m, :], ACT.Square).then_inc(self.squared, 1)
            yield

    def vector(self, dve):
        for m in range(self.tiles):
            dve.wait_ge(self.gate_ready, m + 1)
            dve.tensor_tensor(self.y[:, m, :], self.y[:, m, :], self.z[:, m, :], ALU.mult).then_inc(self.gated, 1)
            yield

    def tensor(self, pe):
        k = self.k
        yield
        yield
        for m in range(self.tiles):
            pe.wait_ge(self.squared, m + 1)
            pe.matmul(bank(k.ps, 7), k.const("ones"), self.sq[:, m % 2, :], start=(m == 0),
                      stop=(m == self.tiles - 1)).then_inc(self.summed, 1)
            yield


def ssm_branch(k, y, norm, spare):
    nc = k.nc
    H, N, PAD = SSM_HEADS, SSM_XBC // P, SSM_CONV // 2
    W2 = T + 2 * PAD
    NX = SSM_INNER // P
    with ExitStack() as ctx:
        sb = lambda name, shape: k.sbuf(ctx, name, shape)
        raw = sb("xbc_raw", [P, N, W2])
        act_x = sb("xbc", [P, N, T])
        cbm = sb("cb_masked", [P, 2, NT, T + P])
        decay = sb("decay", [P, 3, T + P])
        prob = sb("prob", [P, 2, T + P])
        dt_raw = decay[0:H, 0:2, 0:T]
        dt = sb("dt", [H, 2, T])
        acum = sb("acum", [H, 2, T])
        colneg = sb("acum_cols", [P, NT, 2, H])
        colpos = sb("acum_cols_pos", [P, NT, 2, H])
        coldt = sb("dt_cols", [P, NT, 2, H])
        a_exp = sb("a_exp", [H, 2])
        acum_hi, acum_lo = spare[0:H, 0:2, :], spare[0:H, 2:4, :]
        ident_r = spare[0:H, 4, 0:H]
        xdt = [raw[:, :, :].rearrange("p a b -> p (a b)")[:, 0:NT * D].rearrange("p (j d) -> p j d", j=NT),
               y[:, 8:16, :].rearrange("p a t -> p (a t)").rearrange("p (j d) -> p j d", j=NT)]

        project(k, [("w_dt", dt_raw, 1.0), ("w_xbc", raw[:, :, PAD:PAD + T], 1.0)], k.xn, norm,
                beside=SsmConvolution(raw, act_x, prob[:, :, 0:T], dt_raw, dt, acum, a_exp))

        with ExitStack() as inner:
            (acum_split, ident_copied, cols_turned, cols_ready, dt_cols_ready, x_turned, x_used, cb_done,
             cb_used) = semaphores(k, inner, "acum_split ident_copied cols_turned cols_ready dt_cols_ready "
                                   "x_turned x_used cb_done cb_used")
            block = inner.enter_context(nc.Block())
            small = k.ps[:, 0, 0:NT * 4 * H].rearrange("p (j r h) -> p j r h", j=NT, r=4)

            @block.tensor
            def _(pe):
                for j in range(NT):
                    for r in range(2):
                        pe.transpose(small[:, j, r, :], acum[:, r, j * P:(j + 1) * P], k.const("ident", H)[:, 0:H])
                        mm = pe.transpose(small[:, j, 2 + r, :], dt[:, r, j * P:(j + 1) * P],
                                          k.const("ident", H)[:, 0:H])
                mm.then_inc(cols_turned, 1)
                for n in range(2 * NT):
                    g, j = n // NT, n % NT
                    if n >= 2:
                        pe.wait_ge(cb_used, 4 * (n - 1))
                    pe.matmul(bank(k.ps, 1 + n % 2), act_x[:, NX + g, j * P:(j + 1) * P], act_x[:, NX + 2 + g, :],
                              start=True, stop=True).then_inc(cb_done, 1)
                for n in range(2 * NT):
                    j, half = n // 2, n % 2
                    if n >= 2:
                        pe.wait_ge(x_used, 2 * (n - 1))
                    for q in range(NT):
                        mm = pe.transpose(k.ps[:, 3 + n % 2, q * P:(q + 1) * P],
                                          act_x[:, NT * half + q, j * P:(j + 1) * P], k.const("ident"))
                    mm.then_inc(x_turned, 1)

            @block.scalar
            def _(act):
                act.activation(acum_hi, acum[:, :, :], ACT.Copy).then_inc(acum_split, 1)
                act.activation(ident_r, k.const("ident", H)[:, 0:H], ACT.Copy).then_inc(ident_copied, 1)
                act.wait_ge(cols_turned, 1)
                act.activation(coldt[:, :, :, :], small[:, :, 2:4, :], ACT.Copy).then_inc(dt_cols_ready, 1)
                act.activation(colneg[:, :, :, :], small[:, :, 0:2, :], ACT.Copy, scale=-1.0).then_inc(cols_ready, 1)
                act.activation(colpos[:, :, :, :], small[:, :, 0:2, :], ACT.Copy).then_inc(cols_ready, 1)

            @block.vector
            def _(dve):
                dve.wait_ge(acum_split, 1)
                dve.tensor_tensor(acum_lo, acum[:, :, :], acum_hi.bitcast(F32), ALU.subtract).then_inc(acum_split, 1)
                for n in range(2 * NT):
                    g, j = n // NT, n % NT
                    dve.wait_ge(cb_done, n + 1)
                    src, o, fw = bank(k.ps, 1 + n % 2), cbm[:, g, j, :], T - j * P
                    dve.tensor_tensor(o[:, 0:P], src[:, j * P:(j + 1) * P], k.const("le"), ALU.mult)\
                        .then_inc(cb_used, 1)
                    if fw > P:
                        dve.tensor_copy(o[:, P:fw], src[:, (j + 1) * P:T]).then_inc(cb_used, 1)
                    if j:
                        dve.tensor_copy(o[:, fw:fw + j * P], src[:, 0:j * P]).then_inc(cb_used, 1)
                    ins = dve.tensor_tensor(o[:, fw + j * P:fw + (j + 1) * P], src[:, j * P:(j + 1) * P],
                                            k.const("ge"), ALU.mult)
                    ins.then_inc(cb_used, 2 if j in (0, NT - 1) else 1)
                dve.wait_ge(dt_cols_ready, 1)
                for n in range(2 * NT):
                    j, half = n // 2, n % 2
                    dve.wait_ge(x_turned, n + 1)
                    for r in range(2):
                        o = xdt[r][:, j, half * T:(half + 1) * T].rearrange("p (h d) -> p h d", d=SSM_P)
                        dve.tensor_tensor(o, bank(k.ps, 3 + n % 2).rearrange("p (h d) -> p h d", d=SSM_P),
                                          coldt[:, j, r, 8 * half:8 * half + 8, None].broadcast_to([P, 8, SSM_P]),
                                          ALU.mult).then_inc(x_used, 1)

        with ExitStack() as inner:
            spread, bounded, own_bounded, decayed, prob_ready, tile_used, y_ready = semaphores(
                k, inner, "spread bounded own_bounded decayed prob_ready tile_used y_ready")
            OWN = NT // 2
            block = inner.enter_context(nc.Block())

            @block.tensor
            def _(pe):
                def spread_head(h):
                    if h >= 2:
                        pe.wait_ge(bounded, 2 * (NT - OWN) * (h - 1))
                        pe.wait_ge(own_bounded, 2 * OWN * (h - 1))
                    for r in range(2):
                        out, row = bank(k.ps, 4 + 2 * (h % 2) + r), ident_r[:, h:h + 1].broadcast_to([H, P])
                        pe.matmul(out, row, acum_hi[:, r, :], start=True, stop=False)
                        mm = pe.matmul(out, row, acum_lo[:, r, :], start=False, stop=True)
                    mm.then_inc(spread, 1)

                spread_head(0)
                for h in range(H):
                    if h + 1 < H:
                        spread_head(h + 1)
                    bk, half = 2 * (h // 2 % 2), h % 2
                    if h % 2 == 0 and h >= 4:
                        pe.wait_ge(y_ready, h // 2 - 1)
                    for j in range(NT):
                        n = NT * h + j
                        pe.wait_ge(prob_ready, n + 1)
                        o = k.ps[64 * half:64 * half + 64, bk, :]
                        pe.matmul(o[:, j * P:T], xdt[0][:, j, h * SSM_P:(h + 1) * SSM_P],
                                  prob[:, n % 2, 0:T - j * P], start=(j == 0), stop=False)
                        mm = pe.matmul(o[:, 0:(j + 1) * P], xdt[1][:, j, h * SSM_P:(h + 1) * SSM_P],
                                       prob[:, n % 2, T - j * P:T + P], start=False, stop=(j == NT - 1))
                        mm.then_inc(tile_used, 1)

            def parts(j):
                return (0, 0, T - j * P, j * P), (1, T - j * P, T + P, 0)

            @block.scalar
            def _(act):
                for n in range(NT * H):
                    h, j = divmod(n, NT)
                    d = decay[:, n % 3, :]
                    if j >= NT - OWN:
                        act.wait_ge(spread, h + 1)
                        if n >= 3:
                            act.wait_ge(prob_ready, n - 2)
                        for r, a, b, at in parts(j):
                            act.activation(d[:, a:b], k.ps[:, 4 + 2 * (h % 2) + r, at:at + b - a], ACT.Relu,
                                           bias=colpos[:, j, r, h:h + 1], scale=-1.0).then_inc(own_bounded, 1)
                        act.wait_ge(own_bounded, 2 * (OWN * h + j - (NT - OWN)) + 2)
                        act.activation(d, d, ACT.Exp, scale=-1.0).then_inc(decayed, 1)
                    else:
                        act.wait_ge(bounded, 2 * ((NT - OWN) * h + j) + 2)
                        act.activation(d, d, ACT.Exp).then_inc(decayed, 1)

            @block.vector
            def _(dve):
                def weigh(n):
                    h, j = divmod(n, NT)
                    if n >= 2:
                        dve.wait_ge(tile_used, n - 1)
                    dve.wait_ge(decayed, n + 1)
                    dve.tensor_tensor(prob[:, n % 2, :], decay[:, n % 3, :], cbm[:, h // 8, j, :],
                                      ALU.mult).then_inc(prob_ready, 1)

                def output(m):
                    dve.wait_ge(tile_used, 2 * NT * (m + 1))
                    dve.scalar_tensor_tensor(out=y[:, m, :], in0=act_x[:, m, :], scalar=k.col("d_skip", m),
                                             in1=bank(k.ps, 2 * (m % 2)), op0=ALU.mult, op1=ALU.add)\
                        .then_inc(y_ready, 1)

                for n in range(NT * H):
                    h, j = divmod(n, NT)
                    if j < NT - OWN:
                        dve.wait_ge(spread, h + 1)
                        if n >= 3:
                            dve.wait_ge(prob_ready, n - 2)
                        for r, a, b, at in parts(j):
                            dve.tensor_scalar(decay[:, n % 3, a:b], k.ps[:, 4 + 2 * (h % 2) + r, at:at + b - a],
                                              colneg[:, j, r, h:h + 1], 0.0, ALU.add, ALU.min).then_inc(bounded, 1)
                    if n:
                        weigh(n - 1)
                    if n >= 2 * NT and n % (2 * NT) == 2:
                        output(n // (2 * NT) - 1)
                weigh(NT * H - 1)
                output(H // 2 - 1)

        z = raw[:, :, :].rearrange("p a b -> p (a b)")[:, 0:8 * T].rearrange("p (m t) -> p m t", m=8)
        project(k, [("w_z", z, 1.0)], k.xn, beside=SsmGate(z, y, prob[:, :, 0:T]))
    rms_norm(k, y[:, 0:8, :], y[:, 0:8, :], "ssm_norm", sum_there=True)


def flat(ap):
    return ap.rearrange("p a b -> p (a b)")


class TokenShift(Nothing):

    def __init__(self, raw, mix, fm, lora, g_up):
        self.raw, self.mix, self.diff, self.lora, self.g_up = raw, mix, fm[:, 0:4, :], lora, g_up
        self.tiles = raw.shape[1]

    def open(self, k, ctx):
        self.k = k
        self.edges, self.diffed, self.shifted, self.small_in = semaphores(k, ctx, "edges diffed shifted small_in")

    def sync(self, sp):
        sp.dma_start(self.lora[:, :], self.k.dram["w_lora"]).then_inc(self.small_in, 16)
        sp.dma_start(self.g_up[:, :], self.k.dram["w_g_up"]).then_inc(self.small_in, 16)

    def gpsimd(self, pool):
        raw = self.raw
        pool.memset(raw[:, :, 0:1], 0.0).then_inc(self.edges, 1)
        pool.memset(raw[:, :, T + 1:T + 2], 0.0).then_inc(self.edges, 1)
        pool.wait_ge(self.edges, 2)
        for m in range(self.tiles):
            pool.wait_ge(self.tile_used, m + 1)
            if m >= 2:
                pool.wait_ge(self.shifted, 2 * (m - 1))
            for s in range(2):
                pool.tensor_tensor(self.diff[:, 2 * (m % 2) + s, :], raw[:, m, 2 * s:2 * s + T], raw[:, m, 1:T + 1],
                                   ALU.subtract).then_inc(self.diffed, 1)
        pool.wait_ge(self.small_in, 32)
        yield

    def vector(self, dve):
        k = self.k
        yield
        for m in range(self.tiles):
            yield
            for s in range(2):
                dve.wait_ge(self.diffed, 2 * m + s + 1)
                if s:
                    dve.wait_ge(self.shifted, 2 * m + 1)
                dve.scalar_tensor_tensor(out=self.mix[:, m, :], in0=self.diff[:, 2 * (m % 2) + s, :],
                                         scalar=k.col("mu", s * self.tiles + m),
                                         in1=self.mix[:, m, :] if s else self.raw[:, m, 1:T + 1],
                                         op0=ALU.mult, op1=ALU.add).then_inc(self.shifted, 1)


class RwkvOutput(Nothing):

    def __init__(self, mix, fm, g_up, y):
        Q = RWKV_W // P
        self.mix, self.g_up, self.y, self.tiles = mix, g_up, y, Q
        self.r_, self.k_, self.v_ = mix[:, 0:Q, :], mix[:, Q:2 * Q, :], mix[:, 2 * Q:3 * Q, :]
        self.sq, self.rt, self.rk = fm[:, 0:2, :], fm[:, 2:4, :], fm[:, 4:6, :]

    def open(self, k, ctx):
        self.k = k
        (self.mean_done, self.centred, self.squared, self.var_done, self.root, self.inverse, self.scaled,
         self.normed, self.rk_ready, self.rk_scaled, self.rk_done, self.bonus_ready, self.summed, self.g_done,
         self.y_ready) = semaphores(
            k, ctx, "mean_done centred squared var_done root inverse scaled normed rk_ready rk_scaled rk_done "
            "bonus_ready summed g_done y_ready")

    def tensor(self, pe):
        k, y = self.k, self.y
        for q in range(self.tiles):
            if q:
                pe.wait_ge(self.y_ready, q)
            pe.matmul(bank(k.ps, 4), k.const("pair"), y[:, q, :], start=True, stop=True).then_inc(self.mean_done, 1)
            pe.matmul(bank(k.ps, 7), self.g_up[:, q * P:(q + 1) * P], self.mix[:, 13, :], start=True, stop=True)\
                .then_inc(self.g_done, 1)
            yield
            pe.wait_ge(self.rk_ready, q + 1)
            pe.matmul(bank(k.ps, 6), k.const("pair"), self.rk[:, q % 2, :], start=True, stop=True)\
                .then_inc(self.rk_done, 1)
            yield
            pe.wait_ge(self.squared, q + 1)
            pe.matmul(bank(k.ps, 5), k.const("pair"), self.sq[:, q % 2, :], start=True, stop=True)\
                .then_inc(self.var_done, 1)
            yield
            yield

    def scalar(self, act):
        k, y = self.k, self.y
        for q in range(self.tiles):
            yield
            act.wait_ge(self.centred, q + 1)
            act.activation(self.sq[:, q % 2, :], y[:, q, :], ACT.Square).then_inc(self.squared, 1)
            yield
            act.wait_ge(self.var_done, q + 1)
            act.activation(self.rt[:, q % 2, :], bank(k.ps, 5), ACT.Sqrt, bias=k.const("eps")[:, 1:2],
                           scale=1.0 / 64).then_inc(self.root, 1)
            yield
            act.wait_ge(self.scaled, q + 1)
            act.activation(y[:, q, :], y[:, q, :], ACT.Identity, scale=k.col("ln_w", q), bias=k.col("ln_b", q))\
                .then_inc(self.normed, 1)
            yield

    def vector(self, dve):
        k, y, rt, rk = self.k, self.y, self.rt, self.rk
        for q in range(self.tiles):
            dve.tensor_tensor(rk[:, q % 2, :], self.r_[:, q, :], self.k_[:, q, :], ALU.mult).then_inc(self.rk_scaled, 1)
            dve.wait_ge(self.rk_scaled, q + 1)
            dve.tensor_scalar(rk[:, q % 2, :], rk[:, q % 2, :], k.col("r_k", q), None, ALU.mult)\
                .then_inc(self.rk_ready, 1)
            dve.wait_ge(self.mean_done, q + 1)
            dve.scalar_tensor_tensor(out=y[:, q, :], in0=bank(k.ps, 4), scalar=-1.0 / 64, in1=y[:, q, :],
                                     op0=ALU.mult, op1=ALU.add).then_inc(self.centred, 1)
            yield
            dve.wait_ge(self.rk_done, q + 1)
            dve.tensor_tensor(rk[:, q % 2, :], bank(k.ps, 6), self.v_[:, q, :], ALU.mult).then_inc(self.bonus_ready, 1)
            yield
            dve.wait_ge(self.root, q + 1)
            dve.reciprocal(rt[:, q % 2, :], rt[:, q % 2, :]).then_inc(self.inverse, 1)
            dve.wait_ge(self.inverse, q + 1)
            dve.wait_ge(self.centred, q + 1)
            dve.tensor_tensor(y[:, q, :], y[:, q, :], rt[:, q % 2, :], ALU.mult).then_inc(self.scaled, 1)
            yield
            dve.wait_ge(self.normed, q + 1)
            dve.wait_ge(self.bonus_ready, q + 1)
            dve.tensor_tensor(y[:, q, :], y[:, q, :], rk[:, q % 2, :], ALU.add).then_inc(self.summed, 1)
            dve.wait_ge(self.summed, q + 1)
            dve.wait_ge(self.g_done, q + 1)
            dve.tensor_tensor(y[:, q, :], y[:, q, :], bank(k.ps, 7), ALU.mult).then_inc(self.y_ready, 1)
            yield


def rwkv_branch(k, y, hgrn):
    nc = k.nc
    NM = RWKV_COLS // P
    Q = RWKV_W // P
    with ExitStack() as ctx:
        sb = lambda name, shape: k.sbuf(ctx, name, shape)
        mix = sb("mixed", [P, NM, T])
        fm = sb("factors", [P, 11, T])
        g_up = sb("g_up", [P, RWKV_W])
        middle = ctx.enter_context(ExitStack())
        sb = lambda name, shape: k.sbuf(middle, name, shape)
        kk = sb("kk", [P, Q, T])
        ka = sb("kk_a", [P, Q, T])
        store = sb("transfer", [P, 8192 + 2048])
        raw = store[:, 0:NM * (T + 2)].rearrange("p (m t) -> p m t", m=NM)
        lora = sb("lora", [P, 2 * RWKV_W])
        r_, k_, v_ = mix[:, 0:Q, :], mix[:, Q:2 * Q, :], mix[:, 2 * Q:3 * Q, :]

        project(k, [("w_rwkv", raw[:, :, 1:T + 1], 1.0)], k.xn, beside=TokenShift(raw, mix, fm, lora, g_up))

        with ExitStack() as inner:
            low, a_done, a_ready, kx_ready, kx_squared, kx_summed, root, inverse, made = semaphores(
                k, inner, "low a_done a_ready kx_ready kx_squared kx_summed root inverse made")
            block = inner.enter_context(nc.Block())
            a_, sq, rt = fm[:, 0:2, :], fm[:, 2:4, :], fm[:, 4:6, :]

            @block.scalar
            def _(act):
                act.activation(mix[0:64, 12, :], mix[0:64, 12, :], ACT.Tanh).then_inc(low, 1)
                act.activation(mix[:, 13, :], mix[:, 13, :], ACT.Sigmoid).then_inc(low, 1)
                for q in range(Q):
                    act.wait_ge(a_done, q + 1)
                    if q >= 2:
                        act.wait_ge(made, 4 * (q - 1))
                    act.activation(a_[:, q % 2, :], bank(k.ps, q % 2), ACT.Sigmoid, bias=k.col("a0", q))\
                        .then_inc(a_ready, 1)
                    act.wait_ge(kx_ready, q + 1)
                    act.activation(sq[:, q % 2, :], kk[:, q, :], ACT.Square).then_inc(kx_squared, 1)
                    act.wait_ge(kx_summed, q + 1)
                    act.activation(rt[:, q % 2, :], bank(k.ps, 2 + q % 2), ACT.Sqrt, bias=k.const("eps")[:, 2:3])\
                        .then_inc(root, 1)

            @block.tensor
            def _(pe):
                for q in range(Q):
                    if q >= 2:
                        pe.wait_ge(a_ready, q - 1)
                    pe.matmul(bank(k.ps, q % 2), lora[64:128, q * P:(q + 1) * P], mix[64:128, 12, :],
                              start=True, stop=True).then_inc(a_done, 1)
                    pe.wait_ge(kx_squared, q + 1)
                    if q >= 2:
                        pe.wait_ge(root, q - 1)
                    pe.matmul(bank(k.ps, 2 + q % 2), k.const("pair"), sq[:, q % 2, :], start=True, stop=True)\
                        .then_inc(kx_summed, 1)

            @block.vector
            def _(dve):
                for q in range(Q):
                    dve.tensor_scalar(kk[:, q, :], k_[:, q, :], k.col("k_k", q), None, ALU.mult).then_inc(kx_ready, 1)
                for q in range(Q):
                    r = rt[:, q % 2, :]
                    dve.wait_ge(root, q + 1)
                    dve.reciprocal(r, r).then_inc(inverse, 1)
                    dve.wait_ge(inverse, q + 1)
                    dve.tensor_tensor(kk[:, q, :], kk[:, q, :], r, ALU.mult).then_inc(made, 1)
                    dve.wait_ge(made, 4 * q + 1)
                    dve.wait_ge(a_ready, q + 1)
                    dve.tensor_tensor(ka[:, q, :], kk[:, q, :], a_[:, q % 2, :], ALU.mult).then_inc(made, 1)
                    dve.tensor_scalar(a_[:, q % 2, :], a_[:, q % 2, :], -1.0, k.col("k_a", q), ALU.add, ALU.mult)\
                        .then_inc(made, 1)
                    dve.wait_ge(made, 4 * q + 3)
                    dve.scalar_tensor_tensor(out=k_[:, q, :], in0=a_[:, q % 2, :], scalar=1.0, in1=k_[:, q, :],
                                             op0=ALU.add, op1=ALU.mult).then_inc(made, 1)

        gh = store[:, 0:8192].rearrange("p (q c n) -> p q c n", q=Q, c=NC)
        q1 = store[:, 8192:].rearrange("p (q t) -> p q t", q=Q)
        for back in range(2):
            rwkv_transfer(k, back, mix, kk, ka, fm, lora, gh, q1, y)
            rwkv_chain(k, back, gh, q1, y)

        middle.close()
        hgrn(RwkvOutput(mix, fm, g_up, y))


def rwkv_transfer(k, back, mix, kk, ka, fm, lora, gh, q1, y):
    nc = k.nc
    Q = RWKV_W // P
    step = -1 if back else 1
    end = 0 if back else CH - 1
    strict, strict_t, incl = ("c_gt", "c_lt", "c_ge") if back else ("c_lt", "c_gt", "c_le")
    r_, k_, v_ = mix[:, 0:Q, :], mix[:, Q:2 * Q, :], mix[:, 2 * Q:3 * Q, :]
    logw, L, at, bt, kt, bh, kh = [fm[:, n, :] for n in range(7)]
    e_l_of, rt_of = (lambda u: fm[:, 7 + u % 2, :]), (lambda u: fm[:, 9 + u % 2, :])
    rings = [flat(k.raw[:, 0:2, :]), flat(k.raw[:, 2:4, :]), flat(k.idle_hi[:, :, :]), flat(k.idle_lo[:, :, :])]
    scratch = lambda n: rings[n // 4][:, n % 4 * T:(n % 4 + 1) * T]
    tile4 = lambda n: scratch(n).rearrange("p (j t) -> p j t", j=NT)
    N_, NT_, AK, ARB, ARK, Z = [[tile4(2 * n + h) for h in range(2)] for n in range(6)]
    bh_tok, kh_tok, v_tok = [tile4(12 + n) for n in range(3)]
    diag = scratch(15)
    ident = k.const("ident")
    with ExitStack() as inner:
        (w_done, sg_ready, logw_ready, L_ready, e_ready, factor_ready, turned, turned_used, gram_done, gram_used,
         av_done, av_used, z_done, n_done, z_used, n_used, q_done, q_used, gh_done, gh_used, diag_ready,
         diag_added) = semaphores(
            k, inner, "w_done sg_ready logw_ready L_ready e_ready factor_ready turned turned_used gram_done "
            "gram_used av_done av_used z_done n_done z_used n_used q_done q_used gh_done gh_used diag_ready "
            "diag_added")
        block = inner.enter_context(nc.Block())
        ROUNDS = 5
        NSQ = 2 * (ROUNDS - 1) - 1

        @block.tensor
        def _(pe):
            def decay_logits(u):
                pe.matmul(bank(k.ps, 7), lora[0:64, back * RWKV_W + u * P:back * RWKV_W + (u + 1) * P],
                          mix[0:64, 12, :], start=True, stop=True).then_inc(w_done, 1)

            decay_logits(0)
            for u in range(Q):
                rt = rt_of(u)
                for n, src in enumerate((at, bh, kh, v_[:, u, :])):
                    if n == 0:
                        pe.wait_ge(factor_ready, 6 * u + 6)
                        if u:
                            pe.wait_ge(q_used, 2 * u)
                            pe.wait_ge(gh_used, 4 * u)
                    for j in range(NT):
                        mm = pe.transpose(k.ps[:, 4 + n, j * P:(j + 1) * P], src[:, j * P:(j + 1) * P], ident)
                    mm.then_inc(turned, 1)
                n = 0
                for lhs, rhs in ((bt, at), (at, bt), (kt, at), (bt, rt), (kt, rt)):
                    for h in range(2):
                        if n >= 4:
                            pe.wait_ge(gram_used, 10 * u + n - 3)
                        rows = slice(64 * h, 64 * h + 64)
                        for j in range(NT):
                            c = slice(j * P, (j + 1) * P)
                            mm = pe.matmul(k.ps[:, n % 4, c], lhs[rows, c], rhs[rows, c], start=True, stop=True)
                        mm.then_inc(gram_done, 1)
                        n += 1
                pe.wait_ge(turned_used, 5 * u + 5)
                for h in range(2):
                    pe.wait_ge(gram_used, 10 * u + 5 + h)
                    for j in range(NT):
                        mm = pe.matmul(k.ps[:, 4 + h, j * P:j * P + 64], AK[h][:, j, :],
                                       v_tok[:, j, 64 * h:64 * h + 64], start=True, stop=True)
                    mm.then_inc(av_done, 1)
                pe.wait_ge(gram_used, 10 * u + 10)
                if u + 1 < Q:
                    decay_logits(u + 1)
                for i in range(ROUNDS):
                    for h in range(2):
                        if i == 0:
                            pe.wait_ge(av_used, 2 * u + 2)
                        else:
                            pe.wait_ge(z_used, 2 * ROUNDS * u + 2 * (i - 1) + h + 1)
                            pe.wait_ge(n_used, 2 * NSQ * u + (4 * (i - 1) + 2 * h + 2 if i < ROUNDS - 1
                                                              else 4 * (i - 1) + h + 1))
                        for j in range(NT):
                            mm = pe.matmul(k.ps[:, 3 * h, j * P:(j + 1) * P], N_[h][:, j, :], Z[h][:, j, :],
                                           start=True, stop=True)
                        mm.then_inc(z_done, 1)
                        for s in range(2 if i < ROUNDS - 2 else 1 if i < ROUNDS - 1 else 0):
                            a, b = (N_[h], NT_[h]) if s else (NT_[h], N_[h])
                            for j in range(NT):
                                mm = pe.matmul(k.ps[:, 3 * h + 1 + s, j * P:(j + 1) * P], a[:, j, :], b[:, j, :],
                                               start=True, stop=True)
                            mm.then_inc(n_done, 1)
                pe.wait_ge(z_used, 2 * ROUNDS * (u + 1))
                if u + 1 < Q:
                    pe.wait_ge(sg_ready, u + 2)
                for h in range(2):
                    rows = slice(64 * h, 64 * h + 64)
                    for j in range(NT):
                        c = slice(j * P, (j + 1) * P)
                        mm = pe.matmul(k.ps[rows, 6, c], Z[h][:, j, 0:64], ARB[h][:, j, :], start=True, stop=True)
                mm.then_inc(q_done, 1)
                for h in range(2):
                    rows = slice(64 * h, 64 * h + 64)
                    for j in range(NT):
                        c = slice(j * P, (j + 1) * P)
                        pe.matmul(k.ps[rows, 7, c], Z[h][:, j, 64:128], ARB[h][:, j, :], start=True, stop=False)
                        mm = pe.matmul(k.ps[rows, 7, c], v_tok[:, j, 64 * h:64 * h + 64], ARK[h][:, j, :],
                                       start=False, stop=True)
                mm.then_inc(q_done, 1)
                for c in range(NT):
                    tok = slice(CH * c, CH * c + CH)
                    for h in range(2):
                        rows, ch = slice(64 * h, 64 * h + 64), slice(64 * h, 64 * h + 64)
                        for j in range(NT):
                            o = k.ps[rows, c, j * P:(j + 1) * P]
                            pe.matmul(o[:, 0:64], Z[h][tok, j, 0:64], bh_tok[tok, j, ch], start=True, stop=True,
                                      tile_position=(CH * c, 64 * h))
                            pe.matmul(o[:, 64:128], bh_tok[tok, j, ch], Z[h][tok, j, 64:128], start=True, stop=False,
                                      tile_position=(CH * c, 64 * h))
                            mm = pe.matmul(o[:, 64:128], kh_tok[tok, j, ch], v_tok[tok, j, ch], start=False,
                                           stop=True, tile_position=(CH * c, 64 * h))
                    mm.then_inc(gh_done, 1)

        @block.scalar
        def _(act):
            def prepare(u):
                e_l = e_l_of(u)
                if u >= 2:
                    act.wait_ge(diag_added, 2 * (u - 1))
                act.wait_ge(w_done, u + 1)
                act.activation(e_l, bank(k.ps, 7), ACT.Sigmoid, bias=k.col("w0", back * Q + u)).then_inc(sg_ready, 1)
                yield
                yield
                yield
                act.wait_ge(L_ready, 2 * u + 2)
                act.activation(e_l, L, ACT.Exp).then_inc(e_ready, 1)
                yield
                act.activation(at, logw, ACT.Exp).then_inc(e_ready, 1)
                yield
                act.activation(bt, L, ACT.Exp, scale=-1.0).then_inc(e_ready, 1)
                yield

            list(prepare(0))
            for u in range(Q):
                ahead = prepare(u + 1) if u + 1 < Q else iter(())
                act.wait_ge(turned, 4 * u + 1)
                for h in range(2):
                    act.activation(Z[h][:, :, 0:64], bank(k.ps, 4).rearrange("p (j c) -> p j c", j=NT)[:, :, 64 * h:64 * h + 64],
                                   ACT.Copy).then_inc(turned_used, 1)
                for n, o in enumerate((bh_tok, kh_tok, v_tok)):
                    act.wait_ge(turned, 4 * u + n + 2)
                    act.activation(o, bank(k.ps, 5 + n).rearrange("p (j c) -> p j c", j=NT), ACT.Copy)\
                        .then_inc(turned_used, 1)
                for h in range(2):
                    act.wait_ge(av_done, 2 * u + h + 1)
                    act.activation(Z[h][:, :, 64:128], bank(k.ps, 4 + h).rearrange("p (j c) -> p j c", j=NT)[:, :, 0:64],
                                   ACT.Copy).then_inc(av_used, 1)
                n = 2 * NSQ * u
                for i in range(ROUNDS - 1):
                    for h in range(2):
                        next(ahead, None)
                        squarings = 2 if i < ROUNDS - 2 else 1
                        act.wait_ge(n_done, n + squarings)
                        n += squarings
                        for s in range(squarings):
                            act.activation((NT_ if s else N_)[h],
                                           bank(k.ps, 3 * h + 1 + s).rearrange("p (j c) -> p j c", j=NT), ACT.Copy)\
                                .then_inc(n_used, 1)
                list(ahead)
                for c in range(NT):
                    act.wait_ge(gh_done, 4 * u + c + 1)
                    act.activation(gh[:, u, c::NT, :], bank(k.ps, c).rearrange("p (j n) -> p j n", j=NT), ACT.Copy)\
                        .then_inc(gh_used, 1)

        @block.vector
        def _(dve):
            chunks = lambda ap: ap.rearrange("p (c t) -> p c t", t=CH)
            end_of = lambda u: chunks(e_l_of(u))[:, :, end:end + 1]

            def prepare(u):
                e_l, rt, e_end = e_l_of(u), rt_of(u), end_of(u)
                dve.wait_ge(sg_ready, u + 1)
                dve.tensor_scalar(logw, e_l, -RWKV_DECAY, None, ALU.mult).then_inc(logw_ready, 1)
                yield
                dve.wait_ge(logw_ready, u + 1)
                reset = k.const("reset")[:, back * T:(back + 1) * T]
                dve.tensor_tensor_scan(L[:, ::step], reset[:, ::step], logw[:, ::step], 0.0, ALU.mult, ALU.add)\
                    .then_inc(L_ready, 1)
                yield
                dve.wait_ge(L_ready, 2 * u + 1)
                dve.tensor_tensor(logw, L, logw, ALU.subtract).then_inc(L_ready, 1)
                yield
                yield
                dve.wait_ge(e_ready, 3 * u + 1)
                if u >= 2:
                    dve.wait_ge(q_used, 2 * (u - 1))
                dve.tensor_tensor(rt, r_[:, u, :], e_l, ALU.mult).then_inc(factor_ready, 1)
                yield
                dve.wait_ge(e_ready, 3 * u + 2)
                dve.scalar_tensor_tensor(out=at, in0=kk[:, u, :], scalar=-1.0, in1=at, op0=ALU.mult, op1=ALU.mult)\
                    .then_inc(factor_ready, 1)
                yield
                dve.wait_ge(e_ready, 3 * u + 3)
                dve.tensor_tensor(kt, k_[:, u, :], bt, ALU.mult).then_inc(factor_ready, 1)
                yield
                dve.tensor_tensor(bt, ka[:, u, :], bt, ALU.mult).then_inc(factor_ready, 1)
                yield
                dve.wait_ge(factor_ready, 6 * u + 4)
                for o, src in ((kh, kt), (bh, bt)):
                    dve.tensor_tensor(chunks(o), chunks(src), e_end.broadcast_to([P, NC, CH]), ALU.mult)\
                        .then_inc(factor_ready, 1)
                    yield

            list(prepare(0))
            for u in range(Q):
                rt, e_end = rt_of(u), end_of(u)
                ahead = prepare(u + 1) if u + 1 < Q else iter(())
                n = 0
                for dst, mask in ((N_, strict), (NT_, strict_t), (AK, strict), (ARB, incl), (ARK, incl)):
                    for h in range(2):
                        dve.wait_ge(gram_done, 10 * u + n + 1)
                        dve.tensor_tensor(dst[h], bank(k.ps, n % 4).rearrange("p (j c) -> p j c", j=NT),
                                          wide(k.const(mask), NT), ALU.mult).then_inc(gram_used, 1)
                        n += 1
                for i in range(ROUNDS):
                    for h in range(2):
                        dve.wait_ge(z_done, 2 * ROUNDS * u + 2 * i + h + 1)
                        if i:
                            dve.wait_ge(z_used, 2 * ROUNDS * u + 2 * (i - 1) + h + 1)
                        dve.tensor_tensor(Z[h], Z[h], bank(k.ps, 3 * h).rearrange("p (j c) -> p j c", j=NT), ALU.add)\
                            .then_inc(z_used, 1)
                        next(ahead, None)
                list(ahead)
                dve.wait_ge(q_done, 2 * u + 1)
                dve.tensor_tensor(q1[:, u, :], bank(k.ps, 6), rt, ALU.add).then_inc(q_used, 1)
                dve.wait_ge(q_done, 2 * u + 2)
                if back:
                    dve.tensor_tensor(y[:, u, :], y[:, u, :], bank(k.ps, 7), ALU.add).then_inc(q_used, 1)
                else:
                    dve.tensor_copy(y[:, u, :], bank(k.ps, 7)).then_inc(q_used, 1)
                dve.wait_ge(gh_used, 4 * u + 4)
                for half in range(2):
                    cs = slice(8 * half, 8 * half + 8)
                    d3 = diag.rearrange("p (c n) -> p c n", n=64)
                    if 2 * u + half:
                        dve.wait_ge(diag_added, 2 * u + half)
                    dve.tensor_tensor(d3, wide(k.const("eye64"), 8), e_end[:, cs, :].broadcast_to([P, 8, 64]),
                                      ALU.mult).then_inc(diag_ready, 1)
                    dve.wait_ge(diag_ready, 2 * u + half + 1)
                    dve.tensor_tensor(gh[:, u, cs, 0:64], gh[:, u, cs, 0:64], d3, ALU.add).then_inc(diag_added, 1)


def rwkv_chain(k, back, gh, q1, y):
    nc = k.nc
    Q = RWKV_W // P
    order = list(range(NC))[::-1] if back else list(range(NC))
    with ExitStack() as inner:
        state_done, state_ready, out_done, out_used = semaphores(
            k, inner, "state_done state_ready out_done out_used")
        block = inner.enter_context(nc.Block())

        groups = [range(0, Q // 2), range(Q // 2, Q)]

        @block.tensor
        def _(pe):
            for i in range(1, NC):
                c, before = order[i], order[i - 1]
                for g, pairs in enumerate(groups):
                    if i > 1:
                        pe.wait_ge(state_ready, 2 * (i - 2) + g + 1)
                    if i < NC - 1:
                        for q in pairs:
                            for h in range(2):
                                rows = slice(64 * h, 64 * h + 64)
                                mm = pe.matmul(k.ps[rows, 2 * g + h, q % 2 * 64:(q % 2 + 1) * 64],
                                               gh[rows, q, c, 0:64], gh[rows, q, before, 64:128], start=True, stop=True)
                        mm.then_inc(state_done, 1)
                for q in range(Q):
                    for h in range(2):
                        rows = slice(64 * h, 64 * h + 64)
                        mm = pe.matmul(k.ps[rows, 4 + q, CH * c:CH * c + CH], gh[rows, q, before, 64:128],
                                       q1[rows, q, CH * c:CH * c + CH], start=True, stop=True)
            mm.then_inc(out_done, 1)

        @block.vector
        def _(dve):
            for i in range(1, NC - 1):
                c = order[i]
                for g, pairs in enumerate(groups):
                    dve.wait_ge(state_done, 2 * (i - 1) + g + 1)
                    for h in range(2):
                        rows, qs = slice(64 * h, 64 * h + 64), slice(pairs[0], pairs[-1] + 1)
                        src = k.ps[rows, 2 * g + h, 0:len(pairs) * 64].rearrange("p (q n) -> p q n", n=64)
                        ins = dve.tensor_tensor(gh[rows, qs, c, 64:128], gh[rows, qs, c, 64:128], src, ALU.add)
                    ins.then_inc(state_ready, 1)
            dve.wait_ge(out_done, 1)
            part = slice(0, T - CH) if back else slice(CH, T)
            for q in range(Q):
                dve.tensor_tensor(y[:, q, part], y[:, q, part], k.ps[:, 4 + q, part], ALU.add).then_inc(out_used, 1)


class HgrnGates(Nothing):

    def __init__(self, p, gate, log_f, lbs):
        self.f_, self.gate, self.log_f, self.lbs = p[:, 4:12, :], gate, log_f, lbs

    def open(self, k, ctx):
        self.k = k
        self.bound, self.exped, self.sig_ready, self.f_ready, self.g_ready, self.log_ready = semaphores(
            k, ctx, "bound exped sig_ready f_ready g_ready log_ready")

    def vector(self, dve):
        a, b = self.k.col_at["lb"]
        logits, lbs, HH = self.k.cols[:, a:b], self.lbs, HGRN_W // P
        dve.tensor_tensor(lbs[:, 0, :], logits, logits, ALU.subtract).then_inc(self.bound, 1)
        yield
        dve.wait_ge(self.exped, 1)
        dve.reciprocal(lbs[:, 2, :], lbs[:, 1, :]).then_inc(self.bound, 1)
        dve.wait_ge(self.bound, 2)
        dve.tensor_tensor(lbs[:, 2, :], lbs[:, 2, :], lbs[:, 1, :], ALU.mult).then_inc(self.bound, 1)
        dve.wait_ge(self.bound, 3)
        dve.tensor_tensor(lbs[:, 3, :], lbs[:, 2, :], lbs[:, 2, :], ALU.subtract).then_inc(self.bound, 1)
        dve.wait_ge(self.bound, 4)
        dve.tensor_scalar(lbs[:, 4, :], lbs[:, 3, :], -1.0, 1.0, ALU.mult, ALU.add).then_inc(self.bound, 1)
        dve.wait_ge(self.bound, 5)
        for _ in range(7):
            yield
        for n in range(2 * HH):
            dve.wait_ge(self.sig_ready, n + 1)
            dve.tensor_scalar(self.f_[:, n, :], self.f_[:, n, :], lbs[:, 4, n % HH:n % HH + 1],
                              lbs[:, 3, n % HH:n % HH + 1], ALU.mult, ALU.add).then_inc(self.f_ready, 1)
            yield

    def scalar(self, act):
        HH = HGRN_W // P
        act.wait_ge(self.bound, 1)
        act.activation(self.lbs[:, 1, :], self.lbs[:, 0, :], ACT.Exp).then_inc(self.exped, 1)
        for _ in range(4):
            yield
        for n in range(HH):
            act.wait_ge(self.tile_used, n + 1)
            act.activation(self.gate[:, n, :], self.gate[:, n, :], ACT.Silu).then_inc(self.g_ready, 1)
            yield
        for n in range(2 * HH):
            act.wait_ge(self.tile_used, 2 * HH + n + 1)
            act.activation(self.f_[:, n, :], self.f_[:, n, :], ACT.Sigmoid).then_inc(self.sig_ready, 1)
            yield
        yield
        for n in range(2 * HH):
            act.wait_ge(self.f_ready, n + 1)
            act.activation(self.log_f[:, n, :], self.f_[:, n, :], ACT.Ln).then_inc(self.log_ready, 1)
            if n % 3 == 2:
                yield


def hgrn_branch(k, y, p, log_f):
    nc = k.nc
    HH = HGRN_W // P
    with ExitStack() as ctx:
        sb = lambda name, shape: k.sbuf(ctx, name, shape)
        buf = sb("hgrn_buffers", [P, 2, 12, T])
        dec = sb("chunk_decay", [P, 2, NC])
        qb_ring = sb("hgrn_q", [P, 3, T])
        q_, f_, i_ = p[:, 0:HH, :], p[:, HH:3 * HH, :], p[:, 3 * HH:4 * HH, :]

        with ExitStack() as inner:
            (prep, exps, turned, turned_used, scored, masked, inputs_done, inputs_taken, state_ready, out_done,
             y_used) = semaphores(k, inner, "prep exps turned turned_used scored masked inputs_done "
                                  "inputs_taken state_ready out_done y_used")
            block = inner.enter_context(nc.Block())
            UNITS = 2 * HH
            PREP = 10
            chunks = lambda ap: ap.rearrange("p (c t) -> p c t", t=CH)
            tiles = lambda ap: ap.rearrange("p (j t) -> p j t", j=NT)

            def parts(u):
                b = buf[:, u % 2, :, :]
                rows = [b[:, n, :] for n in range(8)]
                rows[3] = qb_ring[:, u % 3, :]
                return rows + [b[:, 8:12, :].rearrange("p a t -> p (a t)")
                                                         .rearrange("p (c v) -> p c v", c=NC)]

            def order(u):
                return list(range(NC))[::-1] if u >= HH else list(range(NC))

            @block.scalar
            def _(act):
                def take_inputs(u):
                    S = parts(u)[8]
                    act.wait_ge(inputs_done, u + 1)
                    if u >= 2:
                        act.wait_ge(out_done, u - 1)
                    for c in range(NT):
                        act.activation(S[:, c::NT, :], bank(k.ps, 3 + c).rearrange("p (j v) -> p j v", j=NT),
                                       ACT.Copy).then_inc(inputs_taken, 1)

                for u in range(UNITS):
                    L, qs, ks, qb, kh, sc, kh_tok, v_tok, S = parts(u)
                    act.wait_ge(prep, PREP * u + 4)
                    act.activation(ks, qs, ACT.Exp, scale=-1.0).then_inc(exps, 1)
                    act.activation(qb, L, ACT.Exp).then_inc(exps, 1)
                    act.activation(kh, kh, ACT.Exp).then_inc(exps, 1)
                    act.wait_ge(exps, 4 * u + 1)
                    act.activation(qs, qs, ACT.Exp).then_inc(exps, 1)
                    if u:
                        take_inputs(u - 1)
                    for n, o in enumerate((kh_tok, v_tok)):
                        act.wait_ge(turned, 2 * u + n + 1)
                        act.activation(o, bank(k.ps, 1 + n), ACT.Copy).then_inc(turned_used, 1)
                take_inputs(UNITS - 1)

            @block.vector
            def _(dve):
                def output(w):
                    dve.wait_ge(out_done, w + 1)
                    h = w % HH
                    if w >= HH:
                        dve.tensor_tensor(y[:, h, :], y[:, h, :], bank(k.ps, 7), ALU.add).then_inc(y_used, 1)
                    else:
                        dve.tensor_copy(y[:, h, :], bank(k.ps, 7)).then_inc(y_used, 1)

                for u in range(UNITS + 1):
                    if u < UNITS:
                        L, qs, ks, qb, kh, sc, kh_tok, v_tok, S = parts(u)
                        back, h = u // HH, u % HH
                        step, end, mid = (-1, 0, CH // 2) if back else (1, CH - 1, CH // 2 - 1)
                        reset = k.const("reset")[:, back * T:(back + 1) * T]
                        n0 = PREP * u
                        if u >= 2:
                            dve.wait_ge(scored, u - 1)
                        dve.tensor_tensor_scan(L[:, ::step], reset[:, ::step], log_f[:, u, ::step], 0.0, ALU.mult,
                                               ALU.add)\
                            .then_inc(prep, 1)
                        dve.wait_ge(prep, n0 + 1)
                        dve.tensor_tensor(chunks(qs), chunks(L), chunks(L)[:, :, mid:mid + 1].broadcast_to([P, NC, CH]),
                                          ALU.subtract).then_inc(prep, 1)
                        dve.tensor_tensor(chunks(kh), chunks(L)[:, :, end:end + 1].broadcast_to([P, NC, CH]),
                                          chunks(L), ALU.subtract).then_inc(prep, 1)
                        dve.wait_ge(prep, n0 + 2)
                        dve.tensor_scalar(qs, qs, -43.0, 43.0, ALU.max, ALU.min).then_inc(prep, 1)
                        dve.tensor_scalar(f_[:, u, :], f_[:, u, :], -1.0, 1.0, ALU.mult, ALU.add).then_inc(prep, 1)
                        dve.wait_ge(exps, 4 * u + 4)
                        dve.wait_ge(prep, n0 + 5)
                        if u >= 2:
                            dve.wait_ge(state_ready, (NC - 2) * (u - 1))
                        dve.tensor_copy(dec[:, u % 2, :], chunks(qb)[:, :, end]).then_inc(prep, 1)
                        dve.tensor_tensor(qs, qs, q_[:, h, :], ALU.mult).then_inc(prep, 1)
                        dve.tensor_tensor(ks, ks, f_[:, u, :], ALU.mult).then_inc(prep, 1)
                        dve.tensor_tensor(kh, kh, f_[:, u, :], ALU.mult).then_inc(prep, 1)
                        dve.wait_ge(prep, n0 + 6)
                        dve.tensor_tensor(qb, qb, q_[:, h, :], ALU.mult).then_inc(prep, 1)
                        if u >= 2:
                            output(u - 2)
                    if u:
                        w = u - 1
                        _, _, _, _, _, sc, _, _, S = parts(w)
                        back, h = w // HH, w % HH
                        dve.wait_ge(scored, w + 1)
                        dve.tensor_tensor(tiles(sc), tiles(bank(k.ps, 0)), wide(k.const("c_ge" if back else "c_le"), NT),
                                          ALU.mult).then_inc(masked, 1)
                        dve.wait_ge(inputs_taken, NT * (w + 1))
                        for i, c in enumerate(order(w)[:-1]):
                            if i == 0:
                                continue
                            before = order(w)[i - 1]
                            if i > 1:
                                dve.wait_ge(state_ready, (NC - 2) * w + i - 1)
                            dve.scalar_tensor_tensor(out=S[:, c, :], in0=S[:, before, :],
                                                     scalar=dec[:, w % 2, c:c + 1], in1=S[:, c, :],
                                                     op0=ALU.mult, op1=ALU.add).then_inc(state_ready, 1)
                output(UNITS - 2)
                output(UNITS - 1)

            @block.tensor
            def _(pe):
                def output(u):
                    L, qs, ks, qb, kh, sc, kh_tok, v_tok, S = parts(u)
                    pe.wait_ge(masked, u + 1)
                    if u:
                        pe.wait_ge(y_used, u)
                    for j in range(NT):
                        c = slice(j * P, (j + 1) * P)
                        pe.matmul(k.ps[:, 7, c], v_tok[:, c], sc[:, c], start=(j == 0), stop=False,
                                  skip_group_check=True)
                    pe.wait_ge(state_ready, (NC - 2) * (u + 1))
                    for i, c in enumerate(order(u)[1:]):
                        ts = slice(CH * c, CH * c + CH)
                        mm = pe.matmul(k.ps[:, 7, ts], S[:, order(u)[i], :], qb[:, ts], start=False,
                                       stop=(i == NC - 2), skip_group_check=True)
                    mm.then_inc(out_done, 1)

                for u in range(UNITS):
                    L, qs, ks, qb, kh, sc, kh_tok, v_tok, S = parts(u)
                    pe.wait_ge(prep, PREP * (u + 1))
                    for n, src in enumerate((kh, i_[:, u % HH, :])):
                        if u:
                            pe.wait_ge(turned_used, 2 * u)
                        for j in range(NT):
                            mm = pe.transpose(k.ps[:, 1 + n, j * P:(j + 1) * P], src[:, j * P:(j + 1) * P],
                                              k.const("ident"))
                        mm.then_inc(turned, 1)
                    if u:
                        pe.wait_ge(masked, u)
                    for j in range(NT):
                        c = slice(j * P, (j + 1) * P)
                        mm = pe.matmul(k.ps[:, 0, c], ks[:, c], qs[:, c], start=True, stop=True)
                    mm.then_inc(scored, 1)
                    pe.wait_ge(turned_used, 2 * u + 2)
                    if u:
                        pe.wait_ge(inputs_taken, NT * u)
                    for j in range(NT):
                        for c in range(NT):
                            rows = slice(CH * c, CH * c + CH)
                            mm = pe.matmul(k.ps[:, 3 + c, j * P:(j + 1) * P], kh_tok[rows, j * P:(j + 1) * P],
                                           v_tok[rows, j * P:(j + 1) * P], start=True, stop=True,
                                           tile_position=(CH * c, 0))
                    mm.then_inc(inputs_done, 1)
                    if u:
                        output(u - 1)
                output(UNITS - 1)



class HeadNorm(Nothing):

    def __init__(self, y, tiles, head, weight, eps, gate, factor=1.0, centre=False, work=None):
        self.y, self.tiles, self.head, self.weight, self.eps = y, tiles, head, weight, eps
        self.gate, self.factor, self.centre, self.work = gate, factor, centre, work

    def open(self, k, ctx):
        self.k = k
        work = self.work if self.work is not None else k.sbuf(ctx, "head_norm_work", [P, 4, T])
        self.sq, self.rt = work[:, 0:2, :], work[:, 2:4, :]
        self.over = k.const("ones") if self.head == P else k.const("pair")
        (self.mean_done, self.centred, self.squared, self.summed, self.root, self.inverse, self.scaled,
         self.normed) = semaphores(k, ctx, "mean_done centred squared summed root inverse scaled normed")

    def tensor(self, pe):
        k = self.k
        for p in range(self.tiles + 2):
            m = p
            if self.centre and m < self.tiles:
                if m >= 2:
                    pe.wait_ge(self.centred, m - 1)
                pe.matmul(bank(k.ps, 4 + m % 2), self.over, self.y[:, m, :], start=True, stop=True)\
                    .then_inc(self.mean_done, 1)
            m = p - 2
            if m >= 0:
                pe.wait_ge(self.squared, m + 1)
                if m >= 2:
                    pe.wait_ge(self.root, m - 1)
                pe.matmul(bank(k.ps, 6 + m % 2), self.over, self.sq[:, m % 2, :], start=True, stop=True)\
                    .then_inc(self.summed, 1)
            yield

    def scalar(self, act):
        k = self.k
        for p in range(self.tiles + 2):
            m = p - 1
            if 0 <= m < self.tiles:
                if self.centre:
                    act.wait_ge(self.centred, m + 1)
                if m >= 2:
                    act.wait_ge(self.summed, m - 1)
                act.activation(self.sq[:, m % 2, :], self.y[:, m, :], ACT.Square).then_inc(self.squared, 1)
            m = p - 2
            if m >= 0:
                act.wait_ge(self.summed, m + 1)
                if m >= 2:
                    act.wait_ge(self.scaled, m - 1)
                act.activation(self.rt[:, m % 2, :], bank(k.ps, 6 + m % 2), ACT.Sqrt, bias=self.eps,
                               scale=1.0 / (self.head * self.factor * self.factor)).then_inc(self.root, 1)
            yield

    def vector(self, dve):
        k = self.k
        for p in range(self.tiles + 3):
            m = p
            if self.centre and m < self.tiles:
                dve.wait_ge(self.mean_done, m + 1)
                dve.scalar_tensor_tensor(out=self.y[:, m, :], in0=bank(k.ps, 4 + m % 2), scalar=-1.0 / self.head,
                                         in1=self.y[:, m, :], op0=ALU.mult, op1=ALU.add).then_inc(self.centred, 1)
            m = p - 3
            if m >= 0:
                rt = self.rt[:, m % 2, :]
                dve.wait_ge(self.root, m + 1)
                dve.reciprocal(rt, rt).then_inc(self.inverse, 1)
                dve.wait_ge(self.inverse, m + 1)
                if self.centre:
                    dve.wait_ge(self.centred, m + 1)
                dve.scalar_tensor_tensor(out=self.y[:, m, :], in0=self.y[:, m, :], scalar=k.col(self.weight, m),
                                         in1=rt, op0=ALU.mult, op1=ALU.mult).then_inc(self.scaled, 1)
                if self.gate is not None:
                    dve.wait_ge(self.scaled, m + 1)
                    dve.tensor_tensor(self.y[:, m, :], self.y[:, m, :], self.gate[:, m, :], ALU.mult)\
                        .then_inc(self.normed, 1)
            yield


class MlstmPreparation(Nothing):

    def __init__(self, n, raw, qk, tap, o_gate, rows, gates, work, b_, g_, M_, m_, g_col):
        self.n, self.raw, self.qk, self.tap, self.o_gate, self.rows, self.gates = n, raw, qk, tap, o_gate, rows, gates
        self.work, self.b_, self.g_, self.M_, self.m_, self.g_col = work, b_, g_, M_, m_, g_col

    def open(self, k, ctx):
        self.k = k
        (self.edges, self.tapped, self.activated, self.biased, self.picked, self.steps, self.logs, self.rows_ready,
         self.m_ready, self.cols_turned, self.cols_ready, self.o_ready) = semaphores(
            k, ctx, "edges tapped activated biased picked steps logs rows_ready m_ready cols_turned cols_ready "
            "o_ready")
        self.cols = k.ps[:, 4, 0:NT * 2 * A_HEADS].rearrange("p (j r h) -> p j r h", j=NT, r=2)

    def gpsimd(self, pool):
        pad = A_CONV // 2
        pool.memset(self.raw[:, :, 0:pad], 0.0).then_inc(self.edges, 1)
        pool.memset(self.raw[:, :, pad + T:], 0.0).then_inc(self.edges, 1)
        yield

    def tensor(self, pe):
        k, H = self.k, A_HEADS
        for _ in range(2):
            yield
        pe.wait_ge(self.biased, 1)
        for r in range(4):
            mm = pe.matmul(k.ps[0:H, 4 + r, :], k.const("ident", 16)[:, H * r:H * r + H], self.rows, start=True,
                           stop=True)
        mm.then_inc(self.picked, 1)
        for _ in range(6):
            yield
        pe.wait_ge(self.rows_ready, 10)
        for j in range(NT):
            for r in range(2):
                mm = pe.transpose(self.cols[:, j, r, :], self.g_[:, r, j * P:(j + 1) * P],
                                  k.const("ident", H)[:, 0:H])
        mm.then_inc(self.cols_turned, 1)

    def scalar(self, act):
        k, H, N, work, m_ = self.k, A_HEADS, 2 * A_WIDTH // P, self.work, self.m_
        yield
        act.wait_ge(self.tile_used, 1)
        act.activation(self.rows, self.rows, ACT.Identity, bias=k.col(f"a_bias{self.n}", 0, 16))\
            .then_inc(self.biased, 1)
        yield
        yield
        act.wait_ge(self.picked, 1)
        for r in range(4):
            act.activation(self.gates[:, r, :], k.ps[0:H, 4 + r, :], ACT.Copy).then_inc(self.steps, 1)
        act.wait_ge(self.steps, 4)
        act.activation(work[:, :, :], self.gates[:, 1::2, :], ACT.Abs).then_inc(self.logs, 1)
        yield
        act.wait_ge(self.logs, 1)
        act.activation(work[:, :, :], work[:, :, :], ACT.Exp, scale=-1.0).then_inc(self.logs, 1)
        act.wait_ge(self.logs, 2)
        act.activation(work[:, :, :], work[:, :, :], ACT.Ln, bias=k.const("ones", H)[:, 0:1]).then_inc(self.logs, 1)
        for m in range(N):
            yield
            act.wait_ge(self.tapped, A_CONV * (m + 1))
            act.activation(self.qk[:, m, :], self.tap[:, m % 2, :], ACT.Silu).then_inc(self.activated, 1)
        yield
        act.wait_ge(self.rows_ready, 10)
        act.activation(m_[:, :, :], m_[:, :, :], ACT.Exp, scale=-1.0).then_inc(self.m_ready, 1)
        act.wait_ge(self.cols_turned, 1)
        act.activation(self.g_col[:, :, :, :], self.cols, ACT.Copy).then_inc(self.cols_ready, 1)
        act.wait_ge(self.activated, N)
        act.activation(self.qk[:, H:N, :], self.qk[:, H:N, :], ACT.Copy, scale=float(P) ** -0.5)\
            .then_inc(self.activated, 1)
        yield
        for m in range(H):
            act.wait_ge(self.tile_used, 1 + N + m + 1)
            act.activation(self.o_gate[:, m, :], self.o_gate[:, m, :], ACT.Sigmoid).then_inc(self.o_ready, 1)
            yield

    def running(self, dve, r):
        k, H, work, gates = self.k, A_HEADS, self.work, self.gates
        b_, g_, M_, m_ = self.b_, self.g_, self.M_, self.m_
        step, base = -1 if r else 1, 5 * r
        dve.scalar_tensor_tensor(out=work[:, r, :], in0=gates[:, 2 * r + 1, :], scalar=0.0, in1=work[:, r, :],
                                 op0=ALU.min, op1=ALU.subtract).then_inc(self.rows_ready, 1)
        dve.wait_ge(self.rows_ready, base + 1)
        dve.tensor_tensor_scan(b_[:, r, ::step], k.const("ones", H)[:, 0:1].broadcast_to([H, T]),
                               work[:, r, ::step], 0.0, ALU.mult, ALU.add).then_inc(self.rows_ready, 1)
        dve.wait_ge(self.rows_ready, base + 2)
        dve.tensor_tensor(g_[:, r, :], gates[:, 2 * r, :], b_[:, r, :], ALU.subtract).then_inc(self.rows_ready, 1)
        dve.wait_ge(self.rows_ready, base + 3)
        dve.tensor_tensor_scan(M_[:, r, ::step], g_[:, r, ::step], g_[:, r, ::step], 0.0, ALU.max, ALU.max)\
            .then_inc(self.rows_ready, 1)
        dve.wait_ge(self.rows_ready, base + 4)
        dve.tensor_tensor(m_[:, r, :], b_[:, r, :], M_[:, r, :], ALU.add).then_inc(self.rows_ready, 1)

    def vector(self, dve):
        k, n, N, raw = self.k, self.n, 2 * A_WIDTH // P, self.raw
        for _ in range(4):
            yield
        dve.wait_ge(self.edges, 2)
        for m in range(N):
            o = self.tap[:, m % 2, :]
            dve.wait_ge(self.tile_used, m + 2)
            if m >= 2:
                dve.wait_ge(self.activated, m - 1)
            dve.tensor_scalar(o, raw[:, m, 0:T], k.col(f"a_conv{n}", m), None, ALU.mult).then_inc(self.tapped, 1)
            for j in range(1, A_CONV):
                dve.wait_ge(self.tapped, A_CONV * m + j)
                dve.scalar_tensor_tensor(out=o, in0=raw[:, m, j:j + T], scalar=k.col(f"a_conv{n}", j * N + m),
                                         in1=o, op0=ALU.mult, op1=ALU.add).then_inc(self.tapped, 1)
            if m in (1, 2):
                dve.wait_ge(self.logs, 3)
                self.running(dve, m - 1)
            yield


def mlstm_branch(k, n_layer, y, o_gate, norm):
    nc = k.nc
    H, N, PAD = A_HEADS, 2 * A_WIDTH // P, A_CONV // 2
    n = n_layer
    with ExitStack() as ctx:
        sb = lambda name, shape: k.sbuf(ctx, name, shape)
        raw = sb("qk_raw", [P, N, T + 2 * PAD])
        qk = sb("qk", [P, N, T])
        v_tok = sb("v_tok", [P, NT, A_WIDTH])
        tap = sb("tap", [P, 2, T])
        rows = sb("gate_rows", [16, 1, T])
        gates = sb("gate_kinds", [H, 4, T])
        work = sb("gate_work", [H, 2, T])
        b_, g_, M_, m_ = [sb(name, [H, 2, T]) for name in ("b_rows", "g_rows", "max_rows", "m_rows")]
        g_col = sb("g_cols", [P, NT, 2, H])
        project(k, [(f"w_a_gates{n}", rows, 1.0), (f"w_a_qk{n}", raw[:, :, PAD:PAD + T], 1.0),
                    (f"w_a_o{n}", o_gate, 1.0)], k.xn, norm, tokens=(f"w_a_v{n}", v_tok),
                beside=MlstmPreparation(n, raw, qk, tap, o_gate, rows[:, 0, :], gates, work, b_, g_, M_, m_, g_col))

        with ExitStack() as inner:
            dist, prob, den = [raw[:, :, :].rearrange("p a b -> p (a b)")[:, 2 * n * T:2 * (n + 1) * T].rearrange(
                "p (a t) -> p a t", a=2) for n in range(3)]
            (spread, bounded, exped, masked, qk_done, prob_ready, pv_done, floor_spread, den_ready, den_step,
             h_ready) = semaphores(
                k, inner, "spread bounded exped masked qk_done prob_ready pv_done floor_spread den_ready "
                "den_step h_ready")
            block = inner.enter_context(nc.Block())
            UNITS = 2 * H
            STEPS = UNITS * NT

            def place(s):
                u = s // NT
                back, h = u % 2, u // 2
                j = NT - 1 - s % NT if back else s % NT
                return u, back, h, j, (slice(0, (j + 1) * P) if back else slice(j * P, T))

            @block.tensor
            def _(pe):
                def weigh(s):
                    u, back, h, j, ts = place(s)
                    pe.wait_ge(prob_ready, s + 1)
                    if s % NT == 0 and u >= 2:
                        pe.wait_ge(h_ready, u - 1)
                    pr = prob[:, s % 2, ts]
                    pe.matmul(k.ps[:, 4 + u % 2, ts], v_tok[:, j, h * P:(h + 1) * P], pr, start=(s % NT == 0),
                              stop=(s % NT == NT - 1))
                    pe.matmul(k.ps[:, 6 + u % 2, ts], k.const("ones"), pr, start=(s % NT == 0),
                              stop=(s % NT == NT - 1)).then_inc(pv_done, 1)
                    if s % NT == NT - 1:
                        pe.wait_ge(bounded, s + 1)
                        pe.matmul(bank(k.ps, u % 2), k.const("ident", H)[:, h:h + 1].broadcast_to([H, P]),
                                  m_[:, back, :], start=True, stop=True).then_inc(floor_spread, 1)

                for s in range(STEPS):
                    u, back, h, j, ts = place(s)
                    if s % NT == 0:
                        if u >= 2:
                            pe.wait_ge(h_ready, u - 1)
                        pe.matmul(bank(k.ps, u % 2), k.const("ident", H)[:, h:h + 1].broadcast_to([H, P]),
                                  M_[:, back, :], start=True, stop=True).then_inc(spread, 1)
                    if s >= 2:
                        pe.wait_ge(prob_ready, s - 1)
                    pe.matmul(k.ps[:, 2 + s % 2, ts], qk[:, H + h, j * P:(j + 1) * P], qk[:, h, ts],
                              start=True, stop=True).then_inc(qk_done, 1)
                    if s:
                        weigh(s - 1)
                weigh(STEPS - 1)

            @block.gpsimd
            def _(pool):
                for s in range(STEPS):
                    u, back, h, j, ts = place(s)
                    pool.wait_ge(exped, s + 1)
                    d = dist[:, s % 2, j * P:(j + 1) * P]
                    pool.tensor_tensor(d, d, k.const("ge" if back else "le"), ALU.mult).then_inc(masked, 1)

            @block.scalar
            def _(act):
                def absolute(u):
                    act.wait_ge(pv_done, NT * (u + 1))
                    act.activation(den[:, u % 2, :], bank(k.ps, 6 + u % 2), ACT.Abs).then_inc(den_ready, 1)
                for s in range(STEPS):
                    u, back, h, j, ts = place(s)
                    act.wait_ge(bounded, s + 1)
                    act.activation(dist[:, s % 2, ts], dist[:, s % 2, ts], ACT.Exp, scale=-1.0).then_inc(exped, 1)
                    if s % NT == 2 and u:
                        absolute(u - 1)
                absolute(UNITS - 1)

            @block.vector
            def _(dve):
                def weight(s):
                    u, back, h, j, ts = place(s)
                    dve.wait_ge(masked, s + 1)
                    dve.wait_ge(qk_done, s + 1)
                    if s >= 2:
                        dve.wait_ge(pv_done, s - 1)
                    dve.tensor_tensor(prob[:, s % 2, ts], dist[:, s % 2, ts], k.ps[:, 2 + s % 2, ts], ALU.mult)\
                        .then_inc(prob_ready, 1)

                def finish(u):
                    back, h, d = u % 2, u // 2, den[:, u % 2, :]
                    dve.wait_ge(den_ready, u + 1)
                    dve.wait_ge(floor_spread, u + 1)
                    dve.tensor_tensor(d, d, bank(k.ps, u % 2), ALU.max).then_inc(den_step, 1)
                    dve.wait_ge(den_step, 3 * u + 1)
                    dve.reciprocal(d, d).then_inc(den_step, 1)
                    dve.wait_ge(den_step, 3 * u + 2)
                    if back:
                        dve.tensor_tensor(d, d, bank(k.ps, 4 + u % 2), ALU.mult).then_inc(den_step, 1)
                        dve.wait_ge(den_step, 3 * u + 3)
                        dve.tensor_tensor(y[:, h, :], y[:, h, :], d, ALU.add).then_inc(h_ready, 1)
                    else:
                        dve.tensor_tensor(y[:, h, :], d, bank(k.ps, 4 + u % 2), ALU.mult).then_inc(h_ready, 1)
                        dve.wait_ge(h_ready, u + 1)
                        dve.tensor_copy(d[:, 0:1], y[:, h, 0:1]).then_inc(den_step, 1)

                for s in range(STEPS):
                    u, back, h, j, ts = place(s)
                    dve.wait_ge(spread, u + 1)
                    if s >= 2:
                        dve.wait_ge(prob_ready, s - 1)
                    dve.tensor_scalar(dist[:, s % 2, ts], k.ps[:, u % 2, ts], g_col[:, j, back, h:h + 1], 0.0,
                                      ALU.subtract, ALU.max).then_inc(bounded, 1)
                    if s:
                        weight(s - 1)
                    if s % NT == 2 and u:
                        finish(u - 1)
                weight(STEPS - 1)
                finish(UNITS - 1)


def attention(k, y, heads, maps, q_of, k_of, v_of, width, bias_of=None, neg_lambda=None, prepare=None):
    nc = k.nc
    with ExitStack() as ctx:
        sb = lambda name, shape: k.sbuf(ctx, name, shape)
        RS, RE = 3, 4
        logits = sb("logits", [P, RS, T]) if bias_of else None
        expd = sb("exps", [P, RE, T])
        pt = sb("prob_t", [P, 2, NT, T])
        stat = sb("statistics", [P, 4, 8])
        (scores_done, fronts, exps, norms, turned, taken, pv_done, y_used, bias_ready) = semaphores(
            k, ctx, "scores_done fronts exps norms turned taken pv_done y_used bias_ready")
        block = ctx.enter_context(nc.Block())
        N = heads * NT * maps
        NPC = 2 if maps == 1 else 5

        def place(n):
            m = n // maps
            return m // NT, m % NT, n % maps

        @block.tensor
        def _(pe):
            def turn(m):
                pe.wait_ge(norms, NPC * (m + 1))
                if m >= 2:
                    pe.wait_ge(taken, m - 1)
                for j in range(NT):
                    mm = pe.transpose(k.ps[:, 3 + m % 2, j * P:(j + 1) * P],
                                      expd[:, (maps * m) % RE, j * P:(j + 1) * P], k.const("ident"))
                mm.then_inc(turned, 1)

            def weigh(h):
                pe.wait_ge(taken, NT * (h + 1))
                if h >= 2:
                    pe.wait_ge(y_used, h - 1)
                r0 = 0 if width == P else 64 * (h % 2)
                for j in range(NT):
                    mm = pe.matmul(k.ps[r0:r0 + width, 5 + h % 2, :], v_of(h, j), pt[:, h % 2, j, :],
                                   start=(j == 0), stop=(j == NT - 1))
                mm.then_inc(pv_done, 1)

            for n in range(N + 4):
                if n < N:
                    h, i, c = place(n)
                    if n >= RS:
                        pe.wait_ge(exps if bias_of is None else fronts,
                                   n - RS + 1 if bias_of is None else 2 * (n - RS) + 2)
                    pe.matmul(bank(k.ps, n % RS), q_of(h, c)[:, i * P:(i + 1) * P], k_of(h, c),
                              start=True, stop=True).then_inc(scores_done, 1)
                if 0 <= n - 2 < N and (n - 1) % maps == 0:
                    turn((n - 2) // maps)
                if 0 <= n - 3 < N and (n - 2) % (NT * maps) == 0:
                    weigh((n - 3) // (NT * maps))

        if prepare is not None:
            @block.gpsimd
            def _(pool):
                for h in range(heads):
                    if h >= 2:
                        pool.wait_ge(fronts, 2 * NT * maps * (h - 1))
                    prepare(pool, h).then_inc(bias_ready, 1)

        @block.scalar
        def _(act):
            def take(m):
                h, i = m // NT, m % NT
                act.wait_ge(turned, m + 1)
                if i == 0 and h >= 2:
                    act.wait_ge(pv_done, h - 1)
                act.activation(pt[:, h % 2, :, i * P:(i + 1) * P],
                               bank(k.ps, 3 + m % 2).rearrange("p (j t) -> p j t", j=NT), ACT.Copy).then_inc(taken, 1)

            for n in range(N + 2):
                if n < N:
                    act.wait_ge(fronts, 2 * n + 2)
                    if n >= RE:
                        act.wait_ge(turned, (n - RE) // maps + 1)
                    act.activation(expd[:, n % RE, :], bank(k.ps, n % RS) if bias_of is None else logits[:, n % RS, :],
                                   ACT.Exp, bias=stat[:, 1, n % 8:n % 8 + 1],
                                   accum_out=stat[:, 2, n % 8:n % 8 + 1]).then_inc(exps, 1)
                if 0 <= n - 2 < N and (n - 1) % maps == 0:
                    take((n - 2) // maps)

        @block.vector
        def _(dve):
            def normalise(n):
                h, i, c = place(n)
                m = n // maps
                s = slice(n % 8, n % 8 + 1)
                e = expd[:, n % RE, :]
                base = NPC * m + (2 if c else 0)
                dve.wait_ge(exps, n + 1)
                dve.reciprocal(stat[:, 3, s], stat[:, 2, s]).then_inc(norms, 1)
                dve.wait_ge(norms, base + 1)
                if c == 0:
                    dve.tensor_scalar(e, e, stat[:, 3, s], None, ALU.mult).then_inc(norms, 1)
                    return
                dve.tensor_scalar(stat[:, 3, s], stat[:, 3, s], neg_lambda, None, ALU.mult).then_inc(norms, 1)
                dve.wait_ge(norms, base + 2)
                first = expd[:, (n - 1) % RE, :]
                dve.scalar_tensor_tensor(out=first, in0=e, scalar=stat[:, 3, s], in1=first, op0=ALU.mult,
                                         op1=ALU.add).then_inc(norms, 1)

            def output(h):
                dve.wait_ge(pv_done, h + 1)
                if width == P:
                    dve.tensor_copy(y[:, h, :], bank(k.ps, 5 + h % 2)).then_inc(y_used, 1)
                else:
                    r = slice(64 * (h % 2), 64 * (h % 2) + 64)
                    dve.tensor_copy(y[r, h // 2, :], k.ps[r, 5 + h % 2, :]).then_inc(y_used, 1)

            for n in range(N + 5):
                if n < N:
                    h, i, c = place(n)
                    s = slice(n % 8, n % 8 + 1)
                    dve.wait_ge(scores_done, n + 1)
                    if bias_of is None:
                        dve.tensor_reduce(stat[:, 0, s], bank(k.ps, n % RS), AX.X, ALU.max).then_inc(fronts, 1)
                    else:
                        if prepare is not None:
                            dve.wait_ge(bias_ready, h + 1)
                        if n >= RS:
                            dve.wait_ge(exps, n - RS + 1)
                        dve.tensor_tensor_reduce(out=logits[:, n % RS, :], in0=bank(k.ps, n % RS), in1=bias_of(h, i),
                                                 scale=1.0, scalar=-3.0e38, op0=ALU.add, op1=ALU.max,
                                                 accum_out=stat[:, 0, s]).then_inc(fronts, 1)
                    dve.wait_ge(fronts, 2 * n + 1)
                    dve.tensor_scalar(stat[:, 1, s], stat[:, 0, s], -1.0, None, ALU.mult).then_inc(fronts, 1)
                if 0 <= n - 1 < N:
                    normalise(n - 1)
                if 0 <= n - 4 < N and (n - 3) % (NT * maps) == 0:
                    output((n - 4) // (NT * maps))


class Rotary(Nothing):

    def __init__(self, n, qk, k2, work):
        self.n, self.qk, self.k2 = n, qk, k2
        self.sq, self.rt = work[:, 0:2, :], work[:, 2:4, :]

    def open(self, k, ctx):
        self.k = k
        (self.squared, self.summed, self.root, self.inverse, self.normed, self.rotated, self.roped, self.doubled,
         self.keys_ready) = semaphores(
            k, ctx, "squared summed root inverse normed rotated roped doubled keys_ready")

    def scalar(self, act):
        k = self.k
        for m in range(5):
            if m >= 2:
                act.wait_ge(self.roped, 3 * (m - 1))
            act.activation(self.sq[:, m % 2, :], self.qk[:, m, :], ACT.Square).then_inc(self.squared, 1)
            yield
            act.wait_ge(self.summed, m + 1)
            key = m == 4
            act.activation(self.rt[:, m % 2, :], bank(k.ps, 4 + m % 2), ACT.Sqrt,
                           bias=k.const("eps")[:, 0:1] if key else k.const("eps")[:, 3:4],
                           scale=1.0 / 64 if key else 1.0).then_inc(self.root, 1)
            yield
        yield
        for g in range(2):
            act.wait_ge(self.doubled, g + 1)
            act.activation(self.k2[:, g, :], bank(k.ps, 4 + g), ACT.Copy).then_inc(self.keys_ready, 1)

    def tensor(self, pe):
        k = self.k
        yield
        for m in range(5):
            pe.wait_ge(self.squared, m + 1)
            pe.matmul(bank(k.ps, 4 + m % 2), k.const("pair"), self.sq[:, m % 2, :], start=True, stop=True)\
                .then_inc(self.summed, 1)
            yield
            pe.wait_ge(self.normed, m + 1)
            pe.matmul(bank(k.ps, 6 + m % 2), k.const("turn"), self.qk[:, m, :], start=True, stop=True)\
                .then_inc(self.rotated, 1)
            yield
        pe.wait_ge(self.roped, 15)
        for g in range(2):
            pe.matmul(bank(k.ps, 4 + g), k.const("dup")[:, g * P:(g + 1) * P], self.qk[:, 4, :],
                      start=True, stop=True).then_inc(self.doubled, 1)

    def vector(self, dve):
        k, qk = self.k, self.qk
        yield
        for m in range(5):
            r, s = self.rt[:, m % 2, :], self.sq[:, m % 2, :]
            dve.wait_ge(self.root, m + 1)
            dve.reciprocal(r, r).then_inc(self.inverse, 1)
            dve.wait_ge(self.inverse, m + 1)
            dve.scalar_tensor_tensor(out=qk[:, m, :], in0=qk[:, m, :],
                                     scalar=k.col(f"b_knorm{self.n}" if m == 4 else f"b_qnorm{self.n}"),
                                     in1=r, op0=ALU.mult, op1=ALU.mult).then_inc(self.normed, 1)
            yield
            dve.wait_ge(self.rotated, m + 1)
            dve.tensor_tensor(s, bank(k.ps, 6 + m % 2), k.const("sin"), ALU.mult).then_inc(self.roped, 1)
            dve.tensor_tensor(r, qk[:, m, :], k.const("cos"), ALU.mult).then_inc(self.roped, 1)
            dve.wait_ge(self.roped, 3 * m + 2)
            dve.tensor_tensor(qk[:, m, :], r, s, ALU.add).then_inc(self.roped, 1)
            yield


def gqa_attention(k, y, qk, k2, v_tok):
    half = lambda h: slice(64 * (h % 2), 64 * (h % 2) + 64)
    attention(k, y, B_HEADS, 1, lambda h, c: qk[half(h), h // 2, :],
              lambda h, c: k2[half(h), h // 4, :], lambda h, j: v_tok[:, j, 64 * (h // 4):64 * (h // 4) + 64], 64)


class BiasTable(Nothing):

    def __init__(self, n, table, rpb, qk):
        self.n, self.table, self.rpb, self.qk = n, table, rpb, qk
        self.groups = GRID_W // 4

    def open(self, k, ctx):
        self.k = k
        self.rpb_in, self.shifted, self.table_ready, self.scaled = semaphores(
            k, ctx, "rpb_in shifted table_ready scaled")

    def sync(self, sp):
        sp.dma_start(self.rpb[:, :], self.k.dram[f"rpb{self.n}"]).then_inc(self.rpb_in, 16)

    def scalar(self, act):
        yield
        for m in range(4):
            act.wait_ge(self.tile_used, m + 1)
            act.activation(self.qk[:, m, :], self.qk[:, m, :], ACT.Copy, scale=0.125).then_inc(self.scaled, 1)
            yield

    def tensor(self, pe):
        k, band = self.k, self.k.const("band", 64)
        yield
        pe.wait_ge(self.rpb_in, 16)
        for g in range(self.groups):
            if g >= 4:
                pe.wait_ge(self.table_ready, g - 3)
            for c in range(4):
                kc = 4 * g + c
                mm = pe.matmul(k.ps[:, 4 + g % 4, c * P:(c + 1) * P], band[:, 63 - kc:191 - kc],
                               self.rpb[0:64, :], start=True, stop=True)
            mm.then_inc(self.shifted, 1)
            if g % 2:
                yield

    def vector(self, dve):
        k = self.k
        flat_table = self.table[:, :, :, :].rearrange("p h j c -> p c (h j)")
        yield
        for g in range(self.groups):
            dve.wait_ge(self.shifted, g + 1)
            cs = slice(4 * g, 4 * g + 4)
            dve.tensor_tensor(flat_table[:, cs, :], bank(k.ps, 4 + g % 4).rearrange("p (c m) -> p c m", c=4),
                              k.const("window")[:, cs, None].broadcast_to([P, 4, P]), ALU.add)\
                .then_inc(self.table_ready, 1)
            if g % 2:
                yield


def natten_branch(k, n, y):
    with ExitStack() as ctx:
        sb = lambda name, shape: k.sbuf(ctx, name, shape)
        qk = sb("c_qk", [P, 8, T])
        v_tok = sb("c_v", [P, NT, 512])
        table = sb("bias_table", [P, C_HEADS, 16, GRID_W])
        with ExitStack() as inner:
            rpb = k.sbuf(inner, "rpb", [P, P])
            project(k, [(f"w_c_qk{n}", qk, 1.0)], k.xn, tokens=(f"w_c_v{n}", v_tok),
                    beside=BiasTable(n, table, rpb, qk))
        half = lambda h: slice(64 * (h % 2), 64 * (h % 2) + 64)
        attention(k, y, C_HEADS, 1, lambda h, c: qk[half(h), h // 2, :], lambda h, c: qk[half(h), 4 + h // 2, :],
                  lambda h, j: v_tok[:, j, 64 * h:64 * h + 64], 64,
                  bias_of=lambda h, i: table[:, h, 7 - 2 * i:15 - 2 * i, :].rearrange("p j c -> p (j c)"))


def diff_branch(k, n, y, qk, v_tok):
    nc = k.nc
    with ExitStack() as ctx:
        sb = lambda name, shape: k.sbuf(ctx, name, shape)
        lam = sb("lambda", [P, 8])
        slope = sb("distance_bias", [P, 2, 896])
        with ExitStack() as inner:
            scaled, products, dots, dots_exp, lam_ready = semaphores(
                k, inner, "scaled products dots dots_exp lam_ready")
            block = inner.enter_context(nc.Block())
            a, _ = k.col_at[f"lambda{n}"]

            @block.scalar
            def _(act):
                act.activation(qk[:, 0:4, :], qk[:, 0:4, :], ACT.Copy, scale=0.125).then_inc(scaled, 1)
                act.wait_ge(dots, 1)
                act.activation(lam[:, 2:4], k.ps[:, 0, 0:2], ACT.Exp).then_inc(dots_exp, 1)

            @block.tensor
            def _(pe):
                pe.wait_ge(products, 1)
                pe.matmul(k.ps[:, 0, 0:2], k.const("ones"), lam[:, 0:2], start=True, stop=True).then_inc(dots, 1)

            @block.vector
            def _(dve):
                dve.tensor_tensor(lam[:, 0:2], k.cols[:, a:a + 2], k.cols[:, a + 2:a + 4], ALU.mult)\
                    .then_inc(products, 1)
                dve.wait_ge(dots_exp, 1)
                dve.tensor_tensor(lam[:, 4:5], lam[:, 3:4], lam[:, 2:3], ALU.subtract).then_inc(lam_ready, 1)
                dve.wait_ge(lam_ready, 1)
                dve.tensor_scalar(lam[:, 5:6], lam[:, 4:5], -LAMBDA_INIT[n], None, ALU.add).then_inc(lam_ready, 1)

        def prepare(pool, h):
            return pool.tensor_scalar(slope[:, h % 2, :], k.const("distance"), -(2.0 ** (-8.0 * (h + 1) / D_HEADS)),
                                      None, ALU.mult)

        half = lambda h: slice(64 * (h % 2), 64 * (h % 2) + 64)
        attention(k, y, D_HEADS, 2, lambda h, c: qk[half(h), 2 * c + h // 2, :],
                  lambda h, c: qk[half(h), 4 + 2 * c + h // 2, :], lambda h, j: v_tok[:, j, P * h:P * h + P], P,
                  bias_of=lambda h, i: slope[:, h % 2, 384 - P * i:896 - P * i],
                  neg_lambda=lam[:, 5:6], prepare=prepare)


def merge(k, branches, w_out):
    with ExitStack() as ctx:
        mixed, mixed_lo = k.both_kinds(ctx, "mixed", [P, KD, T])
        y_hi = ctx.enter_context(k.nc.sbuf_tensor(f"y_hi_{k.nc.next_id()}", [P, 16, T], F32R))
        gate = k.sbuf(ctx, "gate", [P, 2, T])
        gated, at = [], 0
        for w, src, lo, beside in branches:
            parts = Parts(src, lo, y_hi[:, at:at + src.shape[1], :])
            at += src.shape[1]
            gated.append(Gated(w, k.xn, parts, ACT.Sigmoid, bool(gated), Split(parts), 1, beside))
        gated_products(k, gated, mixed, gate)
        parts = Parts(mixed[:, :, :], mixed_lo[:, :, :], k.xn.hi)
        project(k, [(w_out, k.x, "add")], parts, Split(parts), beside=SquareSum(k.x, 1, gate))


def feed_forward(k, spare, norm, w_ffn, w_down):
    with ExitStack() as ctx:
        hidden, hidden_lo = k.both_kinds(ctx, "hidden", [P, KF, T])
        hidden_hi = ctx.enter_context(k.nc.sbuf_tensor(f"hidden_hi_{k.nc.next_id()}", [P, KF, T], F32R))
        source = Norm(k.x, k.xn, norm, spare[:, 0:3, :], sum_there=True)
        gated_products(k, [Gated(w_ffn, k.xn, k.xn, ACT.Silu, False, source, 0)], hidden, spare[:, 3:5, :])
        parts = Parts(hidden[:, :, :], hidden_lo[:, :, :], hidden_hi[:, :, :])
        project(k, [(w_down, k.x, "add")], parts, Split(parts), beside=SquareSum(k.x, 3, spare[:, 3:5, :]))


def stream_plan():
    ffn = lambda n: [planned(f"w_out{n}", KD, KD), planned(f"w_ffn{n}", KF, KD, KD), planned(f"w_down{n}", KD, KF)]
    plan = [planned("w_dt", 2, KD), planned("w_xbc", SSM_XBC // P, KD), planned("w_z", KD, KD),
            planned("w_rwkv", RWKV_COLS // P, KD), None,
            planned("w_hgrn_gate", HGRN_W // P, KD), planned("w_hgrn", 4 * HGRN_W // P, KD),
            planned("w_mix_ssm", KD, KD, KD), planned("w_mix_rwkv", KD, KD, 4), planned("w_mix_hgrn", KD, KD, 4)]
    plan += ffn("")
    for n in range(LAYERS):
        plan += [planned(f"w_a_gates{n}", 1, KD), planned(f"w_a_qk{n}", 8, KD), planned(f"w_a_o{n}", 4, KD),
                 planned(f"w_a_v{n}", 1, 32),
                 planned(f"w_b_q{n}", 4, KD), planned(f"w_b_k{n}", 1, KD), planned(f"w_b_v{n}", 1, KD),
                 planned(f"w_d_qk{n}", 8, KD), planned(f"w_d_v{n}", 1, 32),
                 planned(f"w_c_qk{n}", 8, KD), planned(f"w_c_v{n}", 1, 32)]
        plan += [planned(f"w_mix_{name}{n}", KD, KD, 4) for name in "cbda"] + ffn(n)
    return plan


def layer_branches(k, n, y, o_gate):
    mlstm_branch(k, n, y[:, 0:4, :], o_gate, Norm(k.x, k.xn, f"norm1_{n}", sum_there=n > 0))
    with ExitStack() as ctx:
        d_qk = k.sbuf(ctx, "d_qk", [P, 8, T])
        d_v = k.sbuf(ctx, "d_v", [P, NT, 512])
        with ExitStack() as inner:
            b_qk = k.sbuf(inner, "b_qk", [P, 5, T])
            b_k2 = k.sbuf(inner, "b_keys_twice", [P, 2, T])
            b_v = k.sbuf(inner, "b_v", [P, NT, P])
            project(k, [(f"w_b_q{n}", b_qk[:, 0:4, :], 1.0), (f"w_b_k{n}", b_qk[:, 4:5, :], 1.0)], k.xn,
                    tokens=(f"w_b_v{n}", b_v))
            with ExitStack() as work:
                project(k, [(f"w_d_qk{n}", d_qk, 1.0)], k.xn, tokens=(f"w_d_v{n}", d_v),
                        beside=Rotary(n, b_qk, b_k2, k.sbuf(work, "rotary_work", [P, 4, T])))
            gqa_attention(k, y[:, 4:8, :], b_qk, b_k2, b_v)
        diff_branch(k, n, y[:, 12:16, :], d_qk, d_v)
    natten_branch(k, n, y[:, 8:12, :])


def hybrid_program(nc, dram, const_at, n_const, col_at, n_col):
    k = Kernel(nc, dram, const_at, col_at)
    k.stream = Stream(k, stream_plan())
    with ExitStack() as ctx:
        sb = lambda name, shape, dtype=F32: ctx.enter_context(nc.sbuf_tensor(name, shape, dtype))
        (xn, xn_lo), xn_hi = k.both_kinds(ctx, "xn", [P, KD, T]), sb("xn_hi", [P, KD, T], F32R)
        k.xn = Parts(xn[:, :, :], xn_lo[:, :, :], xn_hi[:, :, :])
        k.raw = sb("raw_weights", [P, AHEAD_RAW, KD * P])
        (k.idle_hi, k.w_hi), (k.idle_lo, k.w_lo) = [
            k.both_kinds(ctx, name, [P, AHEAD_PARTS, KD * P]) for name in ("weights_hi", "weights_lo")]
        k.consts = sb("consts", [P, n_const])
        k.cols = sb("cols", [P, n_col])
        y, y_lo = k.both_kinds(ctx, "y", [P, 16, T])
        k.ps = ctx.enter_context(nc.psum_tensor("ps", [P, 8, T], F32))
        load_constants(k, dram["cols"])
        with ExitStack() as inner:
            k.x, spare = k.both_kinds(inner, "x", [P, KD, T])
            load_x(k)
            ssm_branch(k, y, Norm(k.x, k.xn, "norm1"), spare)
        merging = ctx.enter_context(ExitStack())
        with ExitStack() as inner:
            held = {}

            def hgrn_projection(beside):
                held["gate"] = k.sbuf(merging, "hgrn_gate", [P, 4, T], "right")
                held["in"] = k.sbuf(inner, "hgrn_in", [P, 16, T], "right")
                held["log_f"] = k.sbuf(inner, "log_f", [P, 8, T], "right")
                gates = HgrnGates(held["in"], held["gate"], held["log_f"],
                                  k.sbuf(inner, "lower_bound", [P, 5, 4], "right"))
                project(k, [("w_hgrn_gate", held["gate"], 1.0), ("w_hgrn", held["in"], 1.0)], k.xn,
                        beside=Together(beside, gates))

            rwkv_branch(k, y[:, 8:12, :], hgrn_projection)
            hgrn_branch(k, y[:, 12:16, :], held["in"], held["log_f"])
        k.x = sb("x_again", [P, KD, T])
        rows = k.sbuf(merging, "x_rows", [P, NT, D], "right")
        beside = (HeadNorm(y[:, 12:16, :], 4, P, "hgrn_norm", k.const("eps")[:, 0:1], held["gate"]),
                  LoadX(rows, dram["consts_2"], const_at["cos"][0]), None)
        merge(k, [(f"w_mix_{name}", y[:, a:b, :], y_lo[:, a:b, :], stage)
                  for (name, a, b), stage in zip((("ssm", 0, 8), ("rwkv", 8, 12), ("hgrn", 12, 16)), beside)], "w_out")
        merging.close()
        feed_forward(k, y, "norm2", "w_ffn", "w_down")
        rms_norm(k, k.x, k.x, "norm3", sum_there=True)
        for n in range(LAYERS):
            with ExitStack() as inner:
                o_gate = k.sbuf(inner, "o_gate", [P, A_HEADS, T])
                layer_branches(k, n, y, o_gate)
                norm_d = HeadNorm(y[:, 12:16, :], D_HEADS, P, f"d_subln{n}", k.const("eps")[:, 4 + n:5 + n], None,
                                  1.0 - LAMBDA_INIT[n])
                norm_a = HeadNorm(y[:, 0:4, :], A_HEADS, P, f"a_norm{n}", k.const("eps")[:, 0:1], o_gate, centre=True)
                merge(k, [(f"w_mix_{name}{n}", y[:, a:a + 4, :], y_lo[:, a:a + 4, :], stage)
                          for name, a, stage in (("c", 8, norm_d), ("b", 4, norm_a), ("d", 12, None), ("a", 0, None))],
                      f"w_out{n}")
            feed_forward(k, y, f"norm2_{n}", f"w_ffn{n}", f"w_down{n}")
        rms_norm(k, k.x, xn, "final", sum_there=True)
        store_x(k, xn)


def kernel(**inputs):
    import concourse.bacc as bacc
    from concourse.bass_utils import run_bass_kernel_spmd

    x = {name: np.asarray(a) for name, a in inputs.items()}
    weights, cols = first_layout(x)
    more_weights, more_cols = second_layout(x)
    weights, cols, consts = weights | more_weights, cols | more_cols, constants()
    both, first, second = consts
    widths = lambda arrays: {n: v.shape[1] for n, v in arrays.items()}
    const_at, at = places(widths(both))
    first_at, first_end = places(widths(first), at)
    second_at, second_end = places(widths(second), at)
    const_at, n_const = const_at | first_at | second_at, max(first_end, second_end)
    col_at, n_col = places(widths(cols))
    given = weights | {
        "x": x["x"].reshape(T, D),
        "consts": np.concatenate(list(both.values()) + list(first.values()), 1),
        "consts_2": np.concatenate(list(second.values()), 1),
        "cols": np.concatenate(list(cols.values()), 1),
    }
    nc = bacc.Bacc("TRN2", target_bir_lowering=False, num_devices=1, dynamic_dma_scratch_size=1024)
    arrays, dram = {}, {}
    for name, a in given.items():
        a = np.ascontiguousarray(a)
        arrays[f"in_{name}_dram"] = a
        dram[name] = nc.dram_tensor(f"in_{name}_dram", a.shape, mybir.dt.from_np(a.dtype), kind="ExternalInput").ap()
    dram["out"] = nc.dram_tensor("out_0_dram", (T, D), F32, kind="ExternalOutput").ap()
    hybrid_program(nc, dram, const_at, n_const, col_at, n_col)
    r = run_bass_kernel_spmd(nc, [arrays], core_ids=[0])
    return r.results[0]["out_0_dram"].reshape(1, T, D)
```
